# Optimizing a Trainium2 kernel written in Bass

```python
import jax, jax.numpy as jnp
from jax import lax
import numpy as np
import math

D_MODEL = 1024
BATCH = 1
SEQ = 256
DEPTH = 1

CHUNK = 64
MIX_WIDTH = D_MODEL
RET_WIDTH = MIX_WIDTH // 2
RWKV_WIDTH = MIX_WIDTH - RET_WIDTH
RET_HEADS = 4
RET_HEAD_DIM = RET_WIDTH // RET_HEADS
RWKV_HEAD_DIM = 64
RWKV_HEADS = RWKV_WIDTH // RWKV_HEAD_DIM
DECAY_LORA = 64
AAA_LORA = 64
GATE_LORA = 128
RWKV_COLS = 3 * RWKV_WIDTH + DECAY_LORA + AAA_LORA + GATE_LORA
IN_COLS = 4 * RET_WIDTH + RWKV_COLS
N_GROUPS = 4
EXPERTS_PER_GROUP = 8
N_EXPERTS = N_GROUPS * EXPERTS_PER_GROUP
TOP_K = 2
D_EXPERT = 512
MOE_BLOCK = 128
ROPE_BASE = 10000.0
NORM_EPS = 1e-6
RET_GN_EPS = 1e-5
RWKV_GN_EPS = 64e-5


def rms_norm(x, gain):
    xf = x.astype(jnp.float32)
    y = xf * lax.rsqrt(jnp.mean(xf * xf, axis=-1, keepdims=True) + NORM_EPS)
    return (y * gain.astype(jnp.float32)).astype(x.dtype)

def head_norm(y, gain, eps):
    mu = jnp.mean(y, axis=-1, keepdims=True)
    yc = y - mu
    var = jnp.mean(yc * yc, axis=-1, keepdims=True)
    return yc * lax.rsqrt(var + eps) * gain.astype(jnp.float32)

def rotary(x):
    S, d = x.shape[1], x.shape[-1]
    half = d // 2
    inv = ROPE_BASE ** (-jnp.arange(half, dtype=jnp.float32) / half)
    ang = jnp.arange(S, dtype=jnp.float32)[:, None] * inv[None, :]
    cos = jnp.cos(ang)[None, :, None, :]
    sin = jnp.sin(ang)[None, :, None, :]
    x1, x2 = x[..., :half], x[..., half:]
    return jnp.concatenate([x1 * cos - x2 * sin, x1 * sin + x2 * cos], axis=-1)

def retention(q, k, v):
    B, S, H, d = q.shape
    NC = S // CHUNK
    log_g = jnp.log(1.0 - jnp.exp2(-5.0 - jnp.arange(H, dtype=jnp.float32)))
    idx = jnp.arange(CHUNK, dtype=jnp.float32)
    intra_decay = jnp.exp(log_g[:, None, None] * jnp.abs(idx[:, None] - idx[None, :]))
    k_decay = jnp.exp(log_g[:, None] * (CHUNK - 1.0 - idx)[None, :])
    q_decay = jnp.exp(log_g[:, None] * (idx + 1.0)[None, :])
    chunk_decay = jnp.exp(log_g * CHUNK)
    qc = q.reshape(B, NC, CHUNK, H, d)
    kc = k.reshape(B, NC, CHUNK, H, d) * (d ** -0.5)
    vc = v.reshape(B, NC, CHUNK, H, d)
    scores = jnp.einsum('bnchd,bnmhd->bnhcm', qc, kc) * intra_decay[None, None]
    intra = jnp.einsum('bnhcm,bnmhe->bnche', scores, vc)
    kv = jnp.einsum('bnmhd,hm,bnmhe->bnhde', kc, k_decay, vc)

    def step(state, kv_n):
        return state * chunk_decay[None, :, None, None] + kv_n, state

    _, prev = lax.scan(step, jnp.zeros((B, H, d, d), jnp.float32), jnp.moveaxis(kv, 1, 0))
    prev = jnp.moveaxis(prev, 0, 1)
    cross = jnp.einsum('bnchd,hc,bnhde->bnche', qc, q_decay, prev)
    return (intra + cross).reshape(B, S, H, d)

def token_shift_lerp(feat, mu):
    prev = jnp.concatenate([jnp.zeros_like(feat[:, :1]), feat[:, :-1]], axis=1)
    return feat + (prev - feat) * mu

def rwkv7_time_mix(feats, mu, w0, w_up, a0, a_up, g_up, k_k, k_a, r_k, gn_gain):
    B, S, _ = feats.shape
    H, N, W = RWKV_HEADS, RWKV_HEAD_DIM, RWKV_WIDTH
    f = token_shift_lerp(feats.astype(jnp.float32), mu.astype(jnp.float32))
    r = f[..., 0:W]
    k = f[..., W:2 * W]
    v = f[..., 2 * W:3 * W]
    o = 3 * W
    w_lo = f[..., o:o + DECAY_LORA]
    a_lo = f[..., o + DECAY_LORA:o + DECAY_LORA + AAA_LORA]
    g_lo = f[..., o + DECAY_LORA + AAA_LORA:]
    w = -jax.nn.softplus(-(w0 + jnp.tanh(w_lo) @ w_up)) - 0.5
    decay = jnp.exp(-jnp.exp(w))
    a = jax.nn.sigmoid(a0 + a_lo @ a_up)
    g = jax.nn.sigmoid(g_lo) @ g_up
    kk = (k * k_k).reshape(B, S, H, N)
    kk = kk / jnp.maximum(jnp.sqrt(jnp.sum(kk * kk, axis=-1, keepdims=True)), 1e-12)
    k = k * (1.0 + (a - 1.0) * k_a)
    rh = r.reshape(B, S, H, N)
    kh = k.reshape(B, S, H, N)
    vh = v.reshape(B, S, H, N)
    ah = a.reshape(B, S, H, N)
    dh = decay.reshape(B, S, H, N)
    a_vec = -kk
    b_vec = kk * ah

    def step(state, inp):
        r_t, k_t, v_t, w_t, a_t, b_t = inp
        sa = jnp.einsum('bhvk,bhk->bhv', state, a_t)
        state = state * w_t[:, :, None, :] + sa[..., None] * b_t[:, :, None, :] + v_t[..., None] * k_t[:, :, None, :]
        return state, jnp.einsum('bhvk,bhk->bhv', state, r_t)

    xs = tuple(jnp.moveaxis(t, 1, 0) for t in (rh, kh, vh, dh, a_vec, b_vec))
    _, y = lax.scan(step, jnp.zeros((B, H, N, N), jnp.float32), xs)
    y = jnp.moveaxis(y, 0, 1)
    y = head_norm(y, gn_gain.reshape(H, N), RWKV_GN_EPS)
    bonus = jnp.sum(rh * kh * r_k[None, None].astype(jnp.float32), axis=-1, keepdims=True) * vh
    return (y + bonus).reshape(B, S, W) * g

def hier_moe(xn, w_route_group, b_route_group, w_route_expert, b_route_expert, w_gate, w_up, w_down):
    B, S, D = xn.shape
    T = B * S
    xt = xn.reshape(T, D)
    group_logits = (xt @ w_route_group).astype(jnp.float32) + b_route_group.astype(jnp.float32)
    group_prob = jax.nn.softmax(group_logits, axis=-1)
    g_idx = jnp.argmax(group_logits, axis=-1).astype(jnp.int32)
    g_p = jnp.take_along_axis(group_prob, g_idx[:, None], axis=1)
    exp_logits = ((xt @ w_route_expert).astype(jnp.float32) + b_route_expert.astype(jnp.float32)).reshape(T, N_GROUPS, EXPERTS_PER_GROUP)
    in_group = jnp.take_along_axis(exp_logits, g_idx[:, None, None], axis=1)[:, 0]
    top_v, top_i = lax.top_k(in_group, TOP_K)
    top_w = jax.nn.softmax(top_v, axis=-1) * g_p
    expert_id = (g_idx[:, None] * EXPERTS_PER_GROUP + top_i.astype(jnp.int32)).reshape(-1)
    token_id = jnp.repeat(jnp.arange(T, dtype=jnp.int32), TOP_K)
    weight = top_w.reshape(-1)
    A = T * TOP_K
    order = jnp.argsort(expert_id)
    se, st, sw = expert_id[order], token_id[order], weight[order]
    counts = jax.ops.segment_sum(jnp.ones((A,), jnp.int32), expert_id, num_segments=N_EXPERTS)
    starts = jnp.cumsum(counts) - counts
    padded = (counts + MOE_BLOCK - 1) // MOE_BLOCK * MOE_BLOCK
    pad_ends = jnp.cumsum(padded)
    pad_starts = pad_ends - padded
    dest = pad_starts[se] + jnp.arange(A, dtype=jnp.int32) - starts[se]
    P = ((A + MOE_BLOCK - 1) // MOE_BLOCK + N_EXPERTS) * MOE_BLOCK
    NB = P // MOE_BLOCK
    slot_tok = jnp.full((P,), T, jnp.int32).at[dest].set(st)
    slot_w = jnp.zeros((P,), jnp.float32).at[dest].set(sw)
    block_expert = jnp.clip(jnp.searchsorted(pad_ends, jnp.arange(NB, dtype=jnp.int32) * MOE_BLOCK, side='right'), 0, N_EXPERTS - 1)
    x_pad = jnp.concatenate([xt, jnp.zeros((1, D), xt.dtype)], axis=0)
    xb = x_pad[slot_tok].reshape(NB, MOE_BLOCK, D)

    def expert_block(args):
        xblk, e = args
        hdn = jax.nn.silu(xblk @ w_gate[e]) * (xblk @ w_up[e])
        return hdn @ w_down[e]

    yb = lax.map(expert_block, (xb, block_expert)).reshape(P, D)
    y = jax.ops.segment_sum(yb.astype(jnp.float32) * slot_w[:, None], slot_tok, num_segments=T + 1)[:T]
    return y.reshape(B, S, D).astype(xn.dtype)

def first_inputs(seed: int = 0) -> dict:
    key = jax.random.key(seed)
    ks = jax.random.split(key, 24)
    L, D = DEPTH, D_MODEL
    nrm = lambda k, shape, s: jax.random.normal(k, shape, jnp.float32) * s
    return {
        'x': nrm(ks[0], (BATCH, SEQ, D), 1.0),
        'norm1_gain': 1.0 + nrm(ks[1], (L, D), 0.02),
        'w_in': nrm(ks[2], (L, D, IN_COLS), D ** -0.5),
        'ret_gn_gain': 1.0 + nrm(ks[3], (L, RET_WIDTH), 0.02),
        'rwkv_mu': jax.random.uniform(ks[4], (L, RWKV_COLS), jnp.float32),
        'rwkv_w0': nrm(ks[5], (L, RWKV_WIDTH), 0.5) + 0.5,
        'rwkv_w_up': nrm(ks[6], (L, DECAY_LORA, RWKV_WIDTH), 0.5 * DECAY_LORA ** -0.5),
        'rwkv_a0': nrm(ks[7], (L, RWKV_WIDTH), 0.5),
        'rwkv_a_up': nrm(ks[8], (L, AAA_LORA, RWKV_WIDTH), 0.5 * AAA_LORA ** -0.5),
        'rwkv_g_up': nrm(ks[9], (L, GATE_LORA, RWKV_WIDTH), GATE_LORA ** -0.5),
        'rwkv_k_k': 0.85 + nrm(ks[10], (L, RWKV_WIDTH), 0.05),
        'rwkv_k_a': 1.0 + nrm(ks[11], (L, RWKV_WIDTH), 0.05),
        'rwkv_r_k': nrm(ks[12], (L, RWKV_HEADS, RWKV_HEAD_DIM), 0.1),
        'rwkv_gn_gain': 1.0 + nrm(ks[13], (L, RWKV_WIDTH), 0.02),
        'w_out': nrm(ks[14], (L, MIX_WIDTH, D), MIX_WIDTH ** -0.5),
        'norm2_gain': 1.0 + nrm(ks[15], (L, D), 0.02),
        'w_route_group': nrm(ks[16], (L, D, N_GROUPS), D ** -0.5),
        'b_route_group': nrm(ks[17], (L, N_GROUPS), 0.01),
        'w_route_expert': nrm(ks[18], (L, D, N_EXPERTS), D ** -0.5),
        'b_route_expert': nrm(ks[19], (L, N_EXPERTS), 0.01),
        'w_gate': nrm(ks[20], (L, N_EXPERTS, D, D_EXPERT), D ** -0.5),
        'w_up': nrm(ks[21], (L, N_EXPERTS, D, D_EXPERT), D ** -0.5),
        'w_down': nrm(ks[22], (L, N_EXPERTS, D_EXPERT, D), D_EXPERT ** -0.5),
        'final_norm_gain': 1.0 + nrm(ks[23], (D,), 0.02),
    }

def first_block(x, norm1_gain, w_in, ret_gn_gain, rwkv_mu, rwkv_w0, rwkv_w_up, rwkv_a0, rwkv_a_up, rwkv_g_up, rwkv_k_k, rwkv_k_a, rwkv_r_k, rwkv_gn_gain, w_out, norm2_gain, w_route_group, b_route_group, w_route_expert, b_route_expert, w_gate, w_up, w_down, final_norm_gain):
    B, S, _ = x.shape
    h = x
    for l in range(DEPTH):
        xn = rms_norm(h, norm1_gain[l])
        proj = xn @ w_in[l]
        rp = proj[..., :4 * RET_WIDTH].astype(jnp.float32)
        q = rotary(rp[..., 0:RET_WIDTH].reshape(B, S, RET_HEADS, RET_HEAD_DIM))
        k = rotary(rp[..., RET_WIDTH:2 * RET_WIDTH].reshape(B, S, RET_HEADS, RET_HEAD_DIM))
        v = rp[..., 2 * RET_WIDTH:3 * RET_WIDTH].reshape(B, S, RET_HEADS, RET_HEAD_DIM)
        ret = head_norm(retention(q, k, v), ret_gn_gain[l].reshape(RET_HEADS, RET_HEAD_DIM), RET_GN_EPS)
        ret = jax.nn.silu(rp[..., 3 * RET_WIDTH:]) * ret.reshape(B, S, RET_WIDTH)
        rw = rwkv7_time_mix(proj[..., 4 * RET_WIDTH:], rwkv_mu[l], rwkv_w0[l], rwkv_w_up[l], rwkv_a0[l], rwkv_a_up[l], rwkv_g_up[l], rwkv_k_k[l], rwkv_k_a[l], rwkv_r_k[l], rwkv_gn_gain[l])
        mixed = jnp.concatenate([ret, rw], axis=-1).astype(x.dtype)
        h = h + mixed @ w_out[l]
        h = h + hier_moe(rms_norm(h, norm2_gain[l]), w_route_group[l], b_route_group[l], w_route_expert[l], b_route_expert[l], w_gate[l], w_up[l], w_down[l])
    return rms_norm(h, final_norm_gain)


HEAD_DIM = 64
MOBA_HEADS = 8
MOBA_WIDTH = MOBA_HEADS * HEAD_DIM
MOBA_BLOCK = 256
MOBA_TOPK = 3
MOBA_Q_CHUNK = 16
DIFF_HEADS = 4
DIFF_QK_DIM = HEAD_DIM
DIFF_V_DIM = 2 * HEAD_DIM
DIFF_WIDTH = DIFF_HEADS * DIFF_V_DIM
MIX_WIDTH_2 = MOBA_WIDTH + DIFF_WIDTH
IN_SPLITS = (MOBA_WIDTH, MOBA_WIDTH, MOBA_WIDTH,
             DIFF_HEADS * 2 * DIFF_QK_DIM, DIFF_HEADS * 2 * DIFF_QK_DIM, DIFF_WIDTH)
IN_COLS_2 = sum(IN_SPLITS)
ATTN_Q_BLOCK = 128
ROPE_THETA = 10000.0
EPS = 1e-6
NEG_INF = -1e30
PEER_HEADS = 8
PEER_NKEYS = 128
PEER_EXPERTS = PEER_NKEYS * PEER_NKEYS
PEER_DK = 256
PEER_HALF = PEER_DK // 2
PEER_TOPK = 16
PEER_TOK_CHUNK = 128


def rms_norm_2(x, gain):
    xf = x.astype(jnp.float32)
    y = xf * lax.rsqrt(jnp.mean(xf * xf, axis=-1, keepdims=True) + EPS)
    return (y * gain.astype(jnp.float32)).astype(x.dtype)

def rope_tables(seq):
    pos = jnp.arange(seq, dtype=jnp.float32)
    inv = 1.0 / (ROPE_THETA ** (jnp.arange(0, HEAD_DIM, 2, dtype=jnp.float32) / HEAD_DIM))
    ang = pos[:, None] * inv[None, :]
    return jnp.cos(ang), jnp.sin(ang)

def apply_rope(x, cos, sin):
    x1, x2 = jnp.split(x, 2, axis=-1)
    c = cos.astype(x.dtype)
    s = sin.astype(x.dtype)
    return jnp.concatenate([x1 * c - x2 * s, x2 * c + x1 * s], axis=-1)

def moba_attention(q, k, v):
    B, H, S, Dh = q.shape
    nb = -(-S // MOBA_BLOCK)
    pad = nb * MOBA_BLOCK - S
    kp = jnp.pad(k, ((0, 0), (0, 0), (0, pad), (0, 0)))
    vp = jnp.pad(v, ((0, 0), (0, 0), (0, pad), (0, 0)))
    k_blocks = kp.reshape(B, H, nb, MOBA_BLOCK, Dh)
    v_blocks = vp.reshape(B, H, nb, MOBA_BLOCK, Dh)
    k_mean = jnp.mean(k_blocks.astype(jnp.float32), axis=3)
    gate = jnp.einsum('bhsd,bhnd->bhsn', q.astype(jnp.float32), k_mean)
    q_block = jnp.arange(S) // MOBA_BLOCK
    past = jnp.arange(nb)[None, :] < q_block[:, None]
    gate = jnp.where(past, gate, NEG_INF)
    k_eff = min(MOBA_TOPK, nb)
    _, sel = lax.top_k(gate, k_eff)
    valid = sel < q_block[:, None]

    n_chunks = S // MOBA_Q_CHUNK

    def to_chunks(t):
        t = t.reshape(B, H, n_chunks, MOBA_Q_CHUNK, *t.shape[3:])
        return jnp.moveaxis(t, 2, 0)

    b_idx = jnp.arange(B)[:, None, None, None]
    h_idx = jnp.arange(H)[None, :, None, None]
    scale = Dh ** -0.5
    key_off = jnp.arange(MOBA_BLOCK)

    def chunk_fn(args):
        c, qc, selc, validc = args
        q_pos = c * MOBA_Q_CHUNK + jnp.arange(MOBA_Q_CHUNK)
        blk = (c * MOBA_Q_CHUNK) // MOBA_BLOCK
        k_sel = k_blocks[b_idx, h_idx, selc]
        v_sel = v_blocks[b_idx, h_idx, selc]
        s_sel = jnp.einsum('bhcd,bhckld->bhckl', qc, k_sel).astype(jnp.float32) * scale
        s_sel = jnp.where(validc[..., None], s_sel, NEG_INF)
        k_own = lax.dynamic_slice_in_dim(kp, blk * MOBA_BLOCK, MOBA_BLOCK, axis=2)
        v_own = lax.dynamic_slice_in_dim(vp, blk * MOBA_BLOCK, MOBA_BLOCK, axis=2)
        s_own = jnp.einsum('bhcd,bhld->bhcl', qc, k_own).astype(jnp.float32) * scale
        own_pos = blk * MOBA_BLOCK + key_off
        s_own = jnp.where(own_pos[None, :] <= q_pos[:, None], s_own, NEG_INF)
        n_sel = k_eff * MOBA_BLOCK
        logits = jnp.concatenate([s_sel.reshape(B, H, MOBA_Q_CHUNK, n_sel), s_own], axis=-1)
        p = jax.nn.softmax(logits, axis=-1).astype(v.dtype)
        p_sel = p[..., :n_sel].reshape(B, H, MOBA_Q_CHUNK, k_eff, MOBA_BLOCK)
        p_own = p[..., n_sel:]
        return (jnp.einsum('bhckl,bhckld->bhcd', p_sel, v_sel)
                + jnp.einsum('bhcl,bhld->bhcd', p_own, v_own))

    outs = lax.map(chunk_fn, (jnp.arange(n_chunks), to_chunks(q), to_chunks(sel), to_chunks(valid)))
    return jnp.moveaxis(outs, 0, 2).reshape(B, H, S, Dh)

def diff_attention(q, k, v, lam):
    B, H, _, S, Dk = q.shape
    Dv = v.shape[-1]
    nqb = S // ATTN_Q_BLOCK
    scale = Dk ** -0.5
    key_pos = jnp.arange(S)
    qb = jnp.moveaxis(q.reshape(B, H, 2, nqb, ATTN_Q_BLOCK, Dk), 3, 0)

    def block_fn(args):
        i, qi = args
        q_pos = i * ATTN_Q_BLOCK + jnp.arange(ATTN_Q_BLOCK)
        s = jnp.einsum('bhmqd,bhmkd->bhmqk', qi, k).astype(jnp.float32) * scale
        s = jnp.where(key_pos[None, :] <= q_pos[:, None], s, NEG_INF)
        p = jax.nn.softmax(s, axis=-1)
        a = p[:, :, 0] - lam * p[:, :, 1]
        return jnp.einsum('bhqk,bhkd->bhqd', a.astype(v.dtype), v)

    outs = lax.map(block_fn, (jnp.arange(nqb), qb))
    return jnp.moveaxis(outs, 0, 2).reshape(B, H, S, Dv)

def peer_ffn(x, w_query, sub_keys, expert_down, expert_up):
    B, S, D = x.shape
    T = B * S
    n_chunks = T // PEER_TOK_CHUNK
    xt = x.reshape(n_chunks, PEER_TOK_CHUNK, D)

    def chunk_fn(xc):
        C = xc.shape[0]
        q = (xc @ w_query).reshape(C, PEER_HEADS, 2, PEER_HALF)
        sc = jnp.einsum('thpd,hpnd->thpn', q, sub_keys).astype(jnp.float32)
        top_s, top_i = lax.top_k(sc, PEER_TOPK)
        cand_s = (top_s[:, :, 0, :, None] + top_s[:, :, 1, None, :]).reshape(C, PEER_HEADS, PEER_TOPK * PEER_TOPK)
        cand_i = (top_i[:, :, 0, :, None] * PEER_NKEYS + top_i[:, :, 1, None, :]).reshape(C, PEER_HEADS, PEER_TOPK * PEER_TOPK)
        best_s, best_pos = lax.top_k(cand_s, PEER_TOPK)
        experts = jnp.take_along_axis(cand_i, best_pos, axis=-1)
        gates = jax.nn.softmax(best_s, axis=-1)
        u = expert_down[experts]
        vv = expert_up[experts]
        act = jax.nn.gelu(jnp.einsum('cd,chkd->chk', xc, u).astype(jnp.float32), approximate=False)
        w = (gates * act).astype(xc.dtype)
        return jnp.einsum('chk,chkd->cd', w, vv)

    out = lax.map(chunk_fn, xt)
    return out.reshape(B, S, D)

def second_inputs(seed: int = 0) -> dict:
    key = jax.random.key(seed)
    ks = jax.random.split(key, 20)
    f32 = jnp.float32

    def nrm(k, shape, scale):
        return jax.random.normal(k, shape, f32) * scale

    def gain(k, shape):
        return 1.0 + 0.01 * jax.random.normal(k, shape, f32)

    L = DEPTH
    return {
        "x": jax.random.normal(ks[0], (BATCH, SEQ, D_MODEL), f32),
        "attn_norm": gain(ks[1], (L, D_MODEL)),
        "w_in": nrm(ks[2], (L, D_MODEL, IN_COLS_2), D_MODEL ** -0.5),
        "q_norm_moba": gain(ks[3], (L, HEAD_DIM)),
        "k_norm_moba": gain(ks[4], (L, HEAD_DIM)),
        "q_norm_diff": gain(ks[5], (L, 2, DIFF_QK_DIM)),
        "k_norm_diff": gain(ks[6], (L, 2, DIFF_QK_DIM)),
        "lambda_q1": nrm(ks[7], (L, DIFF_QK_DIM), 0.1),
        "lambda_k1": nrm(ks[8], (L, DIFF_QK_DIM), 0.1),
        "lambda_q2": nrm(ks[9], (L, DIFF_QK_DIM), 0.1),
        "lambda_k2": nrm(ks[10], (L, DIFF_QK_DIM), 0.1),
        "moba_out_gain": gain(ks[11], (L, MOBA_HEADS, HEAD_DIM)),
        "diff_out_gain": gain(ks[12], (L, DIFF_HEADS, DIFF_V_DIM)),
        "w_out": nrm(ks[13], (L, MIX_WIDTH_2, D_MODEL), MIX_WIDTH_2 ** -0.5),
        "ffn_norm": gain(ks[14], (L, D_MODEL)),
        "peer_query": nrm(ks[15], (L, D_MODEL, PEER_HEADS * PEER_DK), D_MODEL ** -0.5),
        "peer_sub_keys": nrm(ks[16], (L, PEER_HEADS, 2, PEER_NKEYS, PEER_HALF), PEER_HALF ** -0.5),
        "peer_down": nrm(ks[17], (L, PEER_EXPERTS, D_MODEL), D_MODEL ** -0.5),
        "peer_up": nrm(ks[18], (L, PEER_EXPERTS, D_MODEL), (PEER_HEADS * PEER_TOPK) ** -0.5),
    }

def second_block(x, attn_norm, w_in, q_norm_moba, k_norm_moba, q_norm_diff, k_norm_diff,
              lambda_q1, lambda_k1, lambda_q2, lambda_k2, moba_out_gain, diff_out_gain,
              w_out, ffn_norm, peer_query, peer_sub_keys, peer_down, peer_up):
    B, S, D = x.shape
    cos, sin = rope_tables(S)
    split_pts = [int(p) for p in np.cumsum(IN_SPLITS)[:-1]]
    for i in range(DEPTH):
        h = rms_norm_2(x, attn_norm[i])
        proj = h @ w_in[i]
        mq, mk, mv, dq, dk, dv = jnp.split(proj, split_pts, axis=-1)
        mq = mq.reshape(B, S, MOBA_HEADS, HEAD_DIM).transpose(0, 2, 1, 3)
        mk = mk.reshape(B, S, MOBA_HEADS, HEAD_DIM).transpose(0, 2, 1, 3)
        mv = mv.reshape(B, S, MOBA_HEADS, HEAD_DIM).transpose(0, 2, 1, 3)
        mq = apply_rope(rms_norm_2(mq, q_norm_moba[i]), cos, sin)
        mk = apply_rope(rms_norm_2(mk, k_norm_moba[i]), cos, sin)
        a_out = moba_attention(mq, mk, mv)
        a_out = rms_norm_2(a_out.transpose(0, 2, 1, 3), moba_out_gain[i])
        dq = dq.reshape(B, S, DIFF_HEADS, 2, DIFF_QK_DIM).transpose(0, 2, 3, 1, 4)
        dk = dk.reshape(B, S, DIFF_HEADS, 2, DIFF_QK_DIM).transpose(0, 2, 3, 1, 4)
        dv = dv.reshape(B, S, DIFF_HEADS, DIFF_V_DIM).transpose(0, 2, 1, 3)
        dq = apply_rope(rms_norm_2(dq, q_norm_diff[i][:, None, :]), cos, sin)
        dk = apply_rope(rms_norm_2(dk, k_norm_diff[i][:, None, :]), cos, sin)
        lambda_init = 0.8 - 0.6 * math.exp(-0.3 * i)
        lam = (jnp.exp(jnp.sum(lambda_q1[i].astype(jnp.float32) * lambda_k1[i].astype(jnp.float32)))
               - jnp.exp(jnp.sum(lambda_q2[i].astype(jnp.float32) * lambda_k2[i].astype(jnp.float32)))
               + lambda_init)
        b_out = diff_attention(dq, dk, dv, lam)
        b_out = rms_norm_2(b_out.transpose(0, 2, 1, 3), diff_out_gain[i]) * (1.0 - lambda_init)
        mixed = jnp.concatenate([a_out.reshape(B, S, MOBA_WIDTH),
                                 b_out.reshape(B, S, DIFF_WIDTH).astype(a_out.dtype)], axis=-1)
        x = x + mixed @ w_out[i]
        x = x + peer_ffn(rms_norm_2(x, ffn_norm[i]), peer_query[i], peer_sub_keys[i], peer_down[i], peer_up[i])
    return x


def setup_inputs(seed=0):
    out = dict(first_inputs(seed))
    for name, value in second_inputs(seed + 1).items():
        if name != "x":
            out[name + "_2"] = value
    return out


def reference(
    x, norm1_gain, w_in, ret_gn_gain, rwkv_mu, rwkv_w0, rwkv_w_up, rwkv_a0, rwkv_a_up,
    rwkv_g_up, rwkv_k_k, rwkv_k_a, rwkv_r_k, rwkv_gn_gain, w_out, norm2_gain, w_route_group,
    b_route_group, w_route_expert, b_route_expert, w_gate, w_up, w_down, final_norm_gain,
    attn_norm_2, w_in_2, q_norm_moba_2, k_norm_moba_2, q_norm_diff_2, k_norm_diff_2,
    lambda_q1_2, lambda_k1_2, lambda_q2_2, lambda_k2_2, moba_out_gain_2, diff_out_gain_2,
    w_out_2, ffn_norm_2, peer_query_2, peer_sub_keys_2, peer_down_2, peer_up_2,
):
    x = first_block(
        x, norm1_gain, w_in, ret_gn_gain, rwkv_mu, rwkv_w0, rwkv_w_up, rwkv_a0, rwkv_a_up,
        rwkv_g_up, rwkv_k_k, rwkv_k_a, rwkv_r_k, rwkv_gn_gain, w_out, norm2_gain, w_route_group,
        b_route_group, w_route_expert, b_route_expert, w_gate, w_up, w_down, final_norm_gain,
    )
    return second_block(
        x, attn_norm_2, w_in_2, q_norm_moba_2, k_norm_moba_2, q_norm_diff_2, k_norm_diff_2,
        lambda_q1_2, lambda_k1_2, lambda_q2_2, lambda_k2_2, moba_out_gain_2, diff_out_gain_2,
        w_out_2, ffn_norm_2, peer_query_2, peer_sub_keys_2, peer_down_2, peer_up_2,
    )


_drawn_inputs = setup_inputs


def setup_inputs(seed=0):
    import zlib

    import numpy as np

    out = dict(_drawn_inputs(seed))
    spreads = {}
    factors = {'ret_gn_gain': 2.711,
     'rwkv_k_k': 4.481,
     'b_route_group': 3.996,
     'attn_norm_2': 4.662,
     'q_norm_moba_2': 8.0,
     'k_norm_moba_2': 8.0,
     'q_norm_diff_2': 8.0,
     'k_norm_diff_2': 8.0,
     'lambda_q1_2': 3.144,
     'lambda_k2_2': 8.0,
     'moba_out_gain_2': 181.793,
     'diff_out_gain_2': 200.0,
     'ffn_norm_2': 174.021}
    for name, (base, spread) in spreads.items():
        noise = np.random.default_rng([zlib.crc32(name.encode()), seed]).standard_normal(out[name].shape)
        drawn = base * np.exp(spread * noise) if base else spread * noise
        out[name] = __import__('jax').numpy.asarray(drawn.astype(out[name].dtype))
    for name, factor in factors.items():
        out[name] = (out[name] * factor).astype(out[name].dtype)
    return out
```

```python
from contextlib import ExitStack

import numpy as np

import concourse.bass as bass
from concourse import mybir

F32 = mybir.dt.float32
U32 = mybir.dt.uint32
ALU = mybir.AluOpType
ACT = mybir.ActivationFunctionType
AX = mybir.AxisListType

P = 128
T = 256
TT = T // P
D = 1024
K = D // P
EPS = 1e-6

RET_HEADS, RET_DIM = 4, 128
RW_HEADS, RW_DIM = 8, 64
CHUNK = 64
CHUNKS = T // CHUNK
RET_EPS, RW_EPS = 1e-5, 64e-5
FEATURE_BLOCKS = 14

GROUPS, PER_GROUP = 4, 8
EXPERTS = GROUPS * PER_GROUP
FF = 512
FT = FF // P
PAIRS = EXPERTS // 2
SLOTS_E = 64

M_HEADS, M_DIM = 8, 64
F_HEADS, F_DIM = 4, 128
LAMBDA_INIT = 0.2
NEG = -1e30

P_HEADS = 8
NKEYS = 128
TOPK = 16
SLOTS = P_HEADS * TOPK

COLS = {}
_at = 0
for _name, _n in (("norm1", K), ("norm2", K), ("attn", K), ("ffn", K), ("mu", FEATURE_BLOCKS), ("w0", 4), ("a0", 4),
                  ("k_k", 4), ("k_a", 4), ("r_k", 4)):
    COLS[_name] = (_at, _n)
    _at += _n
N_COLS = _at

ROWS1 = {"ret_gain": (0, 512), "rw_gain": (512, 512), "route_bias": (1024, 36)}
N_ROWS1 = 1060
ROWS2 = {"final": (0, D), "mq": (1024, 64), "mk": (1088, 64), "dq": (1152, 128), "dk": (1280, 128),
         "lambda": (1408, 256), "m_out": (1664, 512), "d_out": (2176, 512)}
N_ROWS2 = 2688

SLOT = 4096
RING = 0
RING_SLOTS = 3
SPARE = RING_SLOTS * SLOT
WORK = 4 * SLOT
MORE = WORK + 16384
KEPT = MORE + 12288
END = 53200


class Order:

    def __init__(self, sem):
        self.sem, self.n = sem, 0

    def step(self, ins):
        ins.then_inc(self.sem, 1)
        self.n += 1
        return ins

    def settle(self, eng):
        eng.wait_ge(self.sem, self.n)


class Banks:

    def __init__(self, kernel, name, banks):
        self.banks = [kernel.psum[b] for b in banks]
        self.filled = kernel.sem(name + "_filled")
        self.emptied = kernel.sem(name + "_emptied")

    def free(self, pe, job):
        if job >= len(self.banks):
            pe.wait_ge(self.emptied, job - len(self.banks) + 1)
        return self.banks[job % len(self.banks)]

    def ready(self, eng, job):
        eng.wait_ge(self.filled, job + 1)
        return self.banks[job % len(self.banks)]


class Kernel:
    def __init__(self, nc, ctx, ins, out):
        self.nc, self.ctx, self.ins, self.out = nc, ctx, ins, out
        self.mem = ctx.enter_context(nc.sbuf_tensor("mem", [P, END], F32))
        self.psum = [ctx.enter_context(nc.psum_tensor(f"bank{i}", [P, 512], F32)) for i in range(8)]
        self.part_sems = []
        self.vec = Order(self.lasting_sem("vector_order"))
        self.place_kept()
        self.landed = [self.lasting_sem(f"slot{i}_landed") for i in range(6)]
        self.x_landed, self.const_landed = self.lasting_sem("x_landed"), self.lasting_sem("const_landed")
        self.loads = [0] * 6
        self.used_by = {}
        self.issued = 0
        i = self.ins
        self.chunks = [(i["w_in"][c], 512) for c in range(4)] + [(i["w_in_lora"], 256)]
        self.chunks += [(i["w_in"][c], 512) for c in range(4, 7)]
        self.chunks += [(i["w_out"][c], 512) for c in range(2)]
        self.first_half = len(self.chunks)
        self.chunks += [(i["w_in_2"][c], 512) for c in range(6)] + [(i["w_out_2"][c], 512) for c in range(2)]
        self.chunks += [(i["peer_query"][c], 512) for c in range(4)]

    def sem(self, name):
        handle = self.nc.alloc_semaphore(name=name)
        self.part_sems.append(handle)
        return handle

    def lasting_sem(self, name):
        return self.ctx.enter_context(self.nc.semaphore(name))

    def end_part(self):
        self.nc.clear_and_free_semaphores(self.part_sems)
        self.nc.all_engine_barrier()
        self.part_sems = []

    def at(self, off, *shape):
        n = int(np.prod(shape))
        assert off + n <= END, (off, shape)
        ap = self.mem[:, off:off + n]
        if len(shape) == 1:
            return ap
        names = "abcd"[:len(shape)]
        return ap.rearrange(f"p ({' '.join(names)}) -> p {' '.join(names)}",
                            **{x: s for x, s in zip(names[1:], shape[1:])})

    def place_kept(self):
        self.cursor = KEPT

        def keep(*shape):
            ap = self.at(self.cursor, *shape)
            self.cursor += int(np.prod(shape))
            return ap

        self.h = keep(TT, D)
        self.xT = keep(K, T)
        self.ident = keep(P)
        self.iota_all = keep(2 * P + 1)
        self.iota = self.iota_all[:, 0:P]
        self.slot_number = self.iota_all[:, P:P + 1]
        self.up_to = self.iota_all[:, P + 1:]
        self.cols = keep(N_COLS)
        self.small = keep(64)
        self.slot_i = keep(T)
        self.slot_j = keep(T)
        self.slot_g = keep(T)
        self.lt = keep(4)

    def col(self, name):
        o, n = COLS[name]
        return self.cols[:, o:o + n]


    def slot_of(self, c):
        return c % RING_SLOTS

    def issue(self, sync, upto):
        while self.issued < min(upto, len(self.chunks)):
            c = self.issued
            if c >= RING_SLOTS and not self.first_half <= c < self.first_half + RING_SLOTS:
                sync.wait_ge(*self.used_by[c - RING_SLOTS])
            src, n = self.chunks[c]
            s = self.slot_of(c)
            sync.dma_start(self.at(RING + s * SLOT, K, n), src).then_inc(self.landed[s], 16)
            self.loads[s] += 1
            self.issued += 1

    def plan_chunk(self, c):
        s = self.slot_of(c)
        n = sum(1 for b in range(c + 1) if self.slot_of(b) == s)
        if c >= self.first_half:
            n += EXPERTS // 2
        return s, 16 * n

    def chunk(self, pe, c):
        s, value = self.plan_chunk(c)
        pe.wait_ge(self.landed[s], value)
        return self.at(RING + s * SLOT, K, self.chunks[c][1])


    def rms_to_features(self, name, gain, first=False, scaled_at=WORK):
        nc, h, xT, ident = self.nc, self.h, self.xT, self.ident
        scaled = self.at(scaled_at, TT, D)
        ss, ms, root, rstd = (self.small[:, i * 2:i * 2 + 2] for i in range(4))
        squares, mean_ready, root_ready, scaled_ready = (
            self.sem(f"{name}_{x}") for x in ("squares", "mean", "root", "scaled"))
        turned = Banks(self, name + "_turned", [0, 1, 2, 3])
        order = self.vec
        with nc.Block() as block:
            if first:
                @block.sync
                def _(sync):
                    self.load_first(sync)

            @block.scalar
            def _(act):
                if first:
                    act.wait_ge(self.x_landed, 16)
                for t in range(TT):
                    act.activation(scaled[:, t, :], h[:, t, :], ACT.Square, accum_out=ss[:, t:t + 1]).then_inc(squares, 1)
                act.wait_ge(mean_ready, 1)
                act.activation(root, ms, ACT.Sqrt).then_inc(root_ready, 1)

            @block.vector
            def _(vec):
                vec.wait_ge(squares, TT)
                vec.tensor_scalar(ms, ss, 1.0 / D, EPS, ALU.mult, ALU.add).then_inc(mean_ready, 1)
                vec.wait_ge(root_ready, 1)
                order.step(vec.reciprocal(rstd, root))
                order.settle(vec)
                for t in range(TT):
                    vec.tensor_scalar(scaled[:, t, :], h[:, t, :], rstd[:, t:t + 1], None, ALU.mult).then_inc(scaled_ready, 1)
                if first:
                    vec.wait_ge(self.const_landed, 16 * self.n_const)
                g = self.col(gain)
                for job in range(2 * TT):
                    t, half = divmod(job, 2)
                    bank = turned.ready(vec, job)
                    ks = slice(4 * half, 4 * half + 4)
                    vec.tensor_tensor(xT[:, ks, t * P:(t + 1) * P], bank[:, :].rearrange("p (k t) -> p k t", k=4),
                                      g[:, ks].unsqueeze(2).broadcast_to([P, 4, P]), ALU.mult).then_inc(turned.emptied, 1)

            @block.tensor
            def _(pe):
                if first:
                    pe.wait_ge(self.const_landed, 16 * self.n_const)
                for job in range(2 * TT):
                    t, half = divmod(job, 2)
                    pe.wait_ge(scaled_ready, t + 1)
                    bank = turned.free(pe, job)
                    for k in range(4):
                        last = pe.transpose(bank[:, k * P:(k + 1) * P],
                                            scaled[:, t, (4 * half + k) * P:(4 * half + k + 1) * P], ident)
                    last.then_inc(turned.filled, 1)

    def load_first(self, sync):
        i = self.ins
        sync.dma_start(self.h, i["x"].rearrange("(t p) d -> p t d", p=P)).then_inc(self.x_landed, 16)
        for dst, src in self.consts:
            sync.dma_start(dst, src).then_inc(self.const_landed, 16)
        self.issue(sync, RING_SLOTS)


    def place_first(self):
        i = self.ins
        at = self.at
        o = WORK
        self.qkvg = at(o, 4, TT, 512)
        self.qkT = at(o + 4096, 2, RET_HEADS, T)
        self.rotated = at(o + 6144, 2, TT, 512)
        self.ret_decay = at(o + 8192, RET_HEADS, 384)
        self.ret_p = at(o + 9728, 2, 384)
        self.tok_b = at(o, TT, RW_HEADS, RW_DIM)
        self.tok_k = at(o + 1024, TT, RW_HEADS, RW_DIM)
        self.tok_au = at(o + 2048, TT, RW_HEADS, P)
        self.wz = at(o + 4096, TT, RW_HEADS, P)
        self.phi = at(o + 6144, CHUNKS, 4, 2, RW_DIM)
        self.q_hat = at(o + 8192, 4, T)
        self.y_local = at(o + 9216, TT, RW_HEADS, RW_DIM)
        o = WORK + 10496
        self.mixed = at(o, TT, D)
        self.tok_v = at(o + 2048, TT, RW_HEADS, RW_DIM)
        self.gate = at(o + 3072, TT, 512)
        self.tmp = at(o + 4096, 4, T)
        assert o + 5120 <= MORE
        self.lora = at(SPARE, 2, T)
        self.carry = at(SPARE + 512, 4, T)
        self.raw = at(SPARE + 1536, 4, T + 1)
        self.rows1 = at(SPARE + 2564, N_ROWS1)
        f = [at(MORE + 1024 * n, 4, T) for n in range(12)]
        self.f_r, self.f_k, self.f_v, self.f_l, self.f_a, self.f_kk, self.f_k2 = f[:7]
        self.f_b, self.f_kt, self.f_x = f[7], f[8], f[11]
        self.f_ar = at(MORE + 1024 * 9, 4, TT, 2, P)
        self.up_wa = at(MORE + 1024 * 9, 512)
        self.up_g = at(MORE + 1024 * 9 + 512, 512)
        o = MORE
        self.u_k = at(o, 4, 256)
        self.u_b = at(o + 1024, 4, 256)
        self.u_n = at(o + 2048, 5, 4, P)
        self.u_a = at(o + 4608, 4, P)
        self.u_x = at(o + 5120, 4, P)
        self.u_xt = at(o + 5632, 4, P)
        self.u_p = at(o + 6144, 4, P)
        c = self.cursor
        self.mask_pair = at(c, 2, P)
        self.mask_a = at(c + 256, P)
        self.mask_level = at(c + 384, 5, P)
        self.mask_two = at(c + 1024, 2, P)
        self.ones_head = at(c + 1280, P)
        self.ident64 = at(c + 1408, RW_DIM)
        self.rope1 = at(c + 1472, 2, TT, RET_DIM // 2)
        self.pair_ones = at(c + 1728, 2)
        self.decay_end = at(c + 1730, 4, CHUNKS)
        self.state = at(c + 1746, 4, RW_DIM)
        self.bonus = at(c + 2002, TT, RW_HEADS)
        self.stat = at(c + 2018, 12, 16)
        assert c + 2210 <= END, c + 2210
        self.consts = [(self.cols, i["cols"]), (self.ident, i["ident"]), (self.iota_all, i["iota"]),
                       (at(c, 1730), i["const1"]), (self.carry, i["carry"]),
                       (self.ret_decay, i["ret_decay"]), (at(MORE + 1024 * 9, 1024), i["lora_up"]),
                       (self.rows1, i["rows1"].partition_broadcast(P))]
        self.n_const = len(self.consts)

    def project_first(self):
        nc, xT = self.nc, self.xT
        tokens = Banks(self, "project_tokens", [0, 1, 2, 3])
        features = Banks(self, "project_features", [4, 5, 6, 7])
        raw_used, pad_ready = self.sem("raw_used"), self.sem("raw_pad_ready")
        targets = [self.lora[:, 0, :], self.lora[:, 1, :]]
        targets += [f[:, b, :] for f in (self.f_r, self.f_k, self.f_v) for b in range(4)]
        mu_of = [12, 13] + list(range(12))
        order = self.vec
        diff = self.tmp[:, 0, :]
        for c in range(4):
            self.used_by[c] = (tokens.filled, TT * (c + 1))
        for c in range(4, 8):
            self.used_by[c] = (features.filled, 2 + 4 * (c - 4))
        with nc.Block() as block:
            @block.sync
            def _(sync):
                self.issue(sync, 8 + 2)

            @block.tensor
            def _(pe):
                for c in range(4):
                    w = self.chunk(pe, c)
                    for t in range(TT):
                        bank = tokens.free(pe, c * TT + t)
                        for k in range(K):
                            last = pe.matmul(bank[:, :], xT[:, k, t * P:(t + 1) * P], w[:, k, :],
                                             start=(k == 0), stop=(k == K - 1))
                        last.then_inc(tokens.filled, 1)
                job = 0
                for c in range(4, 8):
                    w = self.chunk(pe, c)
                    for b in range(2 if c == 4 else 4):
                        bank = features.free(pe, job)
                        for k in range(K):
                            last = pe.matmul(bank[:, 0:T], w[:, k, b * P:(b + 1) * P], xT[:, k, :],
                                             start=(k == 0), stop=(k == K - 1))
                        last.then_inc(features.filled, 1)
                        job += 1

            @block.scalar
            def _(act):
                for job in range(4 * TT):
                    bank = tokens.ready(act, job)
                    act.activation(self.qkvg[:, job // TT, job % TT, :], bank[:, :], ACT.Copy).then_inc(tokens.emptied, 1)
                act.wait_ge(pad_ready, 1)
                for job in range(FEATURE_BLOCKS):
                    bank = features.ready(act, job)
                    if job >= 4:
                        act.wait_ge(raw_used, job - 3)
                    act.activation(self.raw[:, job % 4, 1:T + 1], bank[:, 0:T], ACT.Copy).then_inc(features.emptied, 1)

            @block.vector
            def _(vec):
                vec.memset(self.raw[:, :, 0:1], 0.0).then_inc(pad_ready, 1)
                cos, sin = self.rope1[:, 0], self.rope1[:, 1]
                half = RET_DIM // 2
                a = self.tmp[:, 1, :].rearrange("p (h d) -> p h d", h=4)
                b = self.tmp[:, 2, :].rearrange("p (h d) -> p h d", h=4)
                for n in range(2 * TT):
                    which, t = divmod(n, TT)
                    vec.wait_ge(tokens.emptied, n + 1)
                    x = self.qkvg[:, which, t, :].rearrange("p (h d) -> p h d", h=4)
                    y = self.rotated[:, which, t, :].rearrange("p (h d) -> p h d", h=4)
                    c4 = cos[:, t, :].unsqueeze(1).broadcast_to([P, 4, half])
                    s4 = sin[:, t, :].unsqueeze(1).broadcast_to([P, 4, half])
                    x1, x2 = x[:, :, 0:half], x[:, :, half:]
                    for out, u, v, op in ((y[:, :, 0:half], c4, s4, ALU.subtract), (y[:, :, half:], s4, c4, ALU.add)):
                        order.step(vec.tensor_tensor(a, x1, u, ALU.mult))
                        order.step(vec.tensor_tensor(b, x2, v, ALU.mult))
                        order.settle(vec)
                        order.step(vec.tensor_tensor(out, a, b, op))
                        order.settle(vec)
                mu = self.col("mu")
                for job in range(FEATURE_BLOCKS):
                    vec.wait_ge(features.emptied, job + 1)
                    now, before = self.raw[:, job % 4, 1:T + 1], self.raw[:, job % 4, 0:T]
                    order.step(vec.tensor_tensor(diff, before, now, ALU.subtract))
                    order.settle(vec)
                    vec.scalar_tensor_tensor(out=targets[job], in0=diff, scalar=mu[:, mu_of[job]:mu_of[job] + 1],
                                             in1=now, op0=ALU.mult, op1=ALU.add).then_inc(raw_used, 1)
                    vec.wait_ge(raw_used, job + 1)

    def retention(self):
        nc, ident = self.nc, self.ident
        turned = Banks(self, "ret_turned", [0, 1])
        scores = Banks(self, "ret_scores", [2, 3])
        outs = [self.psum[4], self.psum[5]]
        p_ready, outs_ready, gate_ready = self.sem("ret_p_ready"), self.sem("ret_outs_ready"), self.sem("ret_gate_ready")
        var_ready, root_ready = self.sem("ret_var_ready"), self.sem("ret_root_ready")
        scores.emptied = p_ready
        v = self.qkvg[:, 2]
        order = self.vec
        with nc.Block() as block:
            @block.tensor
            def _(pe):
                for job in range(2 * TT):
                    which, t = divmod(job, TT)
                    bank = turned.free(pe, job)
                    for h in range(RET_HEADS):
                        last = pe.transpose(bank[:, h * P:(h + 1) * P], self.rotated[:, which, t, h * P:(h + 1) * P], ident)
                    last.then_inc(turned.filled, 1)
                pe.wait_ge(turned.emptied, 2 * TT)
                for h in range(RET_HEADS + 1):
                    if h < RET_HEADS:
                        bank = scores.free(pe, h)
                        pe.matmul(bank[:, 0:T], self.qkT[:, 1, h, 0:P], self.qkT[:, 0, h, :], start=True, stop=True)
                        pe.matmul(bank[:, T:T + P], self.qkT[:, 1, h, P:T], self.qkT[:, 0, h, P:T],
                                  start=True, stop=True).then_inc(scores.filled, 1)
                    if h > 0:
                        g = h - 1
                        pe.wait_ge(p_ready, g + 1)
                        p = self.ret_p[:, g % 2]
                        hs = slice(g * P, (g + 1) * P)
                        pe.matmul(outs[0][:, hs], p[:, 0:P], v[:, 0, hs], start=True, stop=True)
                        pe.matmul(outs[1][:, hs], p[:, P:T], v[:, 0, hs], start=True, stop=False)
                        pe.matmul(outs[1][:, hs], p[:, T:T + P], v[:, 1, hs], start=False, stop=True).then_inc(outs_ready, 1)

            @block.scalar
            def _(act):
                for job in range(2 * TT):
                    which, t = divmod(job, TT)
                    bank = turned.ready(act, job)
                    act.activation(self.qkT[:, which, :, t * P:(t + 1) * P],
                                   bank[:, :].rearrange("p (h t) -> p h t", h=4), ACT.Copy).then_inc(turned.emptied, 1)
                for t in range(TT):
                    act.activation(self.rotated[:, 0, t, :], self.qkvg[:, 3, t, :], ACT.Silu).then_inc(gate_ready, 1)
                act.wait_ge(var_ready, 1)
                act.activation(self.stat[:, 4, 0:8], self.stat[:, 3, 0:8], ACT.Sqrt).then_inc(root_ready, 1)

            @block.vector
            def _(vec):
                for h in range(RET_HEADS):
                    bank = scores.ready(vec, h)
                    if h >= 2:
                        vec.wait_ge(outs_ready, h - 1)
                    vec.tensor_tensor(self.ret_p[:, h % 2], bank[:, 0:384], self.ret_decay[:, h], ALU.mult).then_inc(p_ready, 1)
                vec.wait_ge(outs_ready, RET_HEADS)
                total, mean, square, var, root, rstd = (self.stat[:, n, 0:8].rearrange("p (t h) -> p t h", t=2) for n in
                                                        (0, 1, 2, 3, 4, 5))
                centred = self.rotated[:, 1]
                sq = self.mixed[:, :, 512:1024]
                heads = "p (h d) -> p h d"

                def over(x):
                    return x.unsqueeze(2).broadcast_to([P, RET_HEADS, RET_DIM])

                for t in range(TT):
                    order.step(vec.tensor_reduce(total[:, t], outs[t][:, :].rearrange(heads, h=4), AX.X, ALU.add))
                order.settle(vec)
                order.step(vec.tensor_scalar(mean, total, 1.0 / RET_DIM, None, ALU.mult))
                order.settle(vec)
                for t in range(TT):
                    order.step(vec.tensor_tensor(centred[:, t].rearrange(heads, h=4), outs[t][:, :].rearrange(heads, h=4),
                                                 over(mean[:, t]), ALU.subtract))
                order.settle(vec)
                for t in range(TT):
                    order.step(vec.tensor_tensor(sq[:, t], centred[:, t], centred[:, t], ALU.mult))
                order.settle(vec)
                for t in range(TT):
                    order.step(vec.tensor_reduce(square[:, t], sq[:, t].rearrange(heads, h=4), AX.X, ALU.add))
                order.settle(vec)
                vec.tensor_scalar(var, square, 1.0 / RET_DIM, RET_EPS, ALU.mult, ALU.add).then_inc(var_ready, 1)
                vec.wait_ge(root_ready, 1)
                order.step(vec.reciprocal(rstd, root))
                order.settle(vec)
                o, n = ROWS1["ret_gain"]
                gain = self.rows1[:, o:o + n]
                vec.wait_ge(gate_ready, TT)
                for t in range(TT):
                    order.step(vec.tensor_tensor(sq[:, t].rearrange(heads, h=4), centred[:, t].rearrange(heads, h=4),
                                                 over(rstd[:, t]), ALU.mult))
                    order.step(vec.tensor_tensor(self.rotated[:, 0, t], self.rotated[:, 0, t], gain, ALU.mult))
                order.settle(vec)
                for t in range(TT):
                    order.step(vec.tensor_tensor(self.mixed[:, t, 0:512], sq[:, t], self.rotated[:, 0, t], ALU.mult))

    def rwkv_features(self):
        nc = self.nc
        lora_w, lora_a = Banks(self, "lora_w", [0, 1]), Banks(self, "lora_a", [2, 3])
        lora_g = Banks(self, "lora_g", [4, 5])
        norms = Banks(self, "kk_norms", [6, 7])
        bonus = Banks(self, "bonus", [0])
        squares_ready, bonus_in = self.sem("kk_squares_ready"), self.sem("bonus_in_ready")
        bounded, roots = self.sem("kk_bounded"), self.sem("kk_roots")
        tanh_ready, sig_ready = self.sem("tanh_ready"), self.sem("gate_sigmoid_ready")
        sums, excl, expd = self.sem("decay_sums_ready"), self.sem("decay_before_ready"), self.sem("decay_exps")
        order = self.vec
        f_r, f_k, f_l, f_a, f_kk, f_k2, f_x, tmp = (self.f_r, self.f_k, self.f_l, self.f_a, self.f_kk, self.f_k2,
                                                    self.f_x, self.tmp)

        def wide(name):
            return self.col(name).unsqueeze(2).broadcast_to([P, 4, T])

        with nc.Block() as block:
            @block.tensor
            def _(pe):
                pe.wait_ge(tanh_ready, 1)
                for stage, rows in ((lora_w, slice(0, 64)), (lora_a, slice(64, 128))):
                    for pair in range(2):
                        bank = stage.free(pe, pair)
                        for n in range(2):
                            b = 2 * pair + n
                            last = pe.matmul(bank[:, n * T:(n + 1) * T], self.up_wa[rows, b * P:(b + 1) * P],
                                             self.lora[rows, 0, :], start=True, stop=True)
                        last.then_inc(stage.filled, 1)
                pe.wait_ge(sig_ready, 1)
                for t in range(TT):
                    bank = lora_g.free(pe, t)
                    pe.matmul(bank[:, :], self.lora[:, 1, t * P:(t + 1) * P], self.up_g, start=True,
                              stop=True).then_inc(lora_g.filled, 1)
                pe.wait_ge(squares_ready, 1)
                for pair in range(2):
                    bank = norms.free(pe, pair)
                    pe.matmul(bank[:, :], self.ones_head, f_x[:, 2 * pair:2 * pair + 2, :], start=True,
                              stop=True).then_inc(norms.filled, 1)
                pe.wait_ge(bonus_in, 1)
                pe.wait_ge(lora_w.emptied, 2)
                bank = bonus.free(pe, 0)
                for t in range(TT):
                    for b in range(4):
                        last = pe.matmul(bank[:, t * 8 + 2 * b:t * 8 + 2 * b + 2], f_k[:, b, t * P:(t + 1) * P],
                                         self.pair_ones, start=True, stop=True)
                last.then_inc(bonus.filled, 1)

            @block.scalar
            def _(act):
                act.activation(self.lora[0:64, 0, :], self.lora[0:64, 0, :], ACT.Tanh).then_inc(tanh_ready, 1)
                act.activation(self.lora[:, 1, :], self.lora[:, 1, :], ACT.Sigmoid).then_inc(sig_ready, 1)
                for stage, dst, bias in ((lora_w, f_l, "w0"), (lora_a, f_a, "a0")):
                    for pair in range(2):
                        bank = stage.ready(act, pair)
                        for n in range(2):
                            b = 2 * pair + n
                            last = act.activation(dst[:, b, :], bank[:, n * T:(n + 1) * T], ACT.Sigmoid,
                                                  bias=self.col(bias)[:, b:b + 1])
                        last.then_inc(stage.emptied, 1)
                for t in range(TT):
                    bank = lora_g.ready(act, t)
                    act.activation(self.gate[:, t, :], bank[:, :], ACT.Copy).then_inc(lora_g.emptied, 1)
                act.wait_ge(bounded, 2)
                act.activation(f_x, tmp, ACT.Sqrt).then_inc(roots, 1)
                act.wait_ge(sums, 1)
                act.wait_ge(excl, 1)
                act.activation(f_l, f_l, ACT.Exp).then_inc(expd, 1)
                act.activation(tmp, f_x, ACT.Exp, scale=-1.0).then_inc(expd, 1)
                act.wait_ge(expd, 2)
                act.activation(f_x, f_x, ACT.Exp).then_inc(expd, 1)

            @block.vector
            def _(vec):
                order.step(vec.tensor_tensor(f_kk, f_k, wide("k_k"), ALU.mult))
                order.settle(vec)
                vec.tensor_tensor(f_x, f_kk, f_kk, ALU.mult).then_inc(squares_ready, 1)
                for pair in range(2):
                    bank = norms.ready(vec, pair)
                    vec.tensor_scalar(tmp[:, 2 * pair:2 * pair + 2, :].rearrange("p b t -> p (b t)"), bank[:, :], 1e-24,
                                      None, ALU.max).then_inc(bounded, 1)
                vec.wait_ge(roots, 1)
                order.step(vec.reciprocal(tmp, f_x))
                order.settle(vec)
                order.step(vec.tensor_tensor(f_kk, f_kk, tmp, ALU.mult))
                vec.wait_ge(lora_a.emptied, 2)
                order.settle(vec)
                order.step(vec.scalar_tensor_tensor(out=tmp, in0=f_a, scalar=1.0, in1=wide("k_a"), op0=ALU.subtract,
                                                    op1=ALU.mult))
                order.settle(vec)
                order.step(vec.scalar_tensor_tensor(out=f_k2, in0=tmp, scalar=1.0, in1=f_k, op0=ALU.add, op1=ALU.mult))
                order.settle(vec)
                order.step(vec.tensor_tensor(f_k, f_r, f_k2, ALU.mult))
                order.step(vec.tensor_tensor(f_a, f_a, f_kk, ALU.mult))
                order.settle(vec)
                vec.tensor_tensor(f_k, f_k, wide("r_k"), ALU.mult).then_inc(bonus_in, 1)
                order.step(vec.tensor_scalar(f_l, f_l, -float(np.exp(-0.5)), None, ALU.mult))
                order.settle(vec)
                flat = "p b t -> p (b t)"
                vec.tensor_tensor_scan(f_x.rearrange(flat), self.carry.rearrange(flat), f_l.rearrange(flat), 0.0,
                                       ALU.mult, ALU.add).then_inc(sums, 1)
                vec.wait_ge(sums, 1)
                vec.tensor_tensor(f_l, f_x, f_l, ALU.subtract).then_inc(excl, 1)
                vec.wait_ge(expd, 1)
                vec.wait_ge(lora_g.emptied, TT)
                pairs = "p b t a x -> p (b t) a x"
                ar = self.f_ar.rearrange(pairs)

                def tiles(x):
                    return x.rearrange("p b (t x) -> p (b t) x", t=TT)

                order.step(vec.scalar_tensor_tensor(out=ar[:, :, 0, :], in0=tiles(f_kk), scalar=-1.0, in1=tiles(f_l),
                                                    op0=ALU.mult, op1=ALU.mult))
                vec.wait_ge(expd, 2)
                order.step(vec.tensor_tensor(self.f_b, f_a, tmp, ALU.mult))
                order.step(vec.tensor_tensor(self.f_kt, f_k2, tmp, ALU.mult))
                vec.wait_ge(expd, 3)
                order.step(vec.tensor_tensor(ar[:, :, 1, :], tiles(f_r), tiles(f_x), ALU.mult))
                order.step(vec.tensor_copy(self.decay_end, f_x[:, :, CHUNK - 1::CHUNK]))
                bank = bonus.ready(vec, 0)
                order.step(vec.tensor_copy(self.bonus, bank[:, 0:16].rearrange("p (t h) -> p t h", t=2)))

    def rwkv_turn(self):
        nc, ident = self.nc, self.ident
        turned = Banks(self, "rwkv_turned", [0, 1, 2, 3])
        with nc.Block() as block:
            sources = [lambda b, t: self.f_v[:, b, t * P:(t + 1) * P], lambda b, t: self.f_ar[:, b, t, 0, :],
                       lambda b, t: self.f_b[:, b, t * P:(t + 1) * P], lambda b, t: self.f_kt[:, b, t * P:(t + 1) * P]]
            targets = [self.tok_v, self.tok_au[:, :, :, 0:RW_DIM], self.tok_b, self.tok_k]

            @block.tensor
            def _(pe):
                for job in range(4 * TT):
                    which, t = divmod(job, TT)
                    bank = turned.free(pe, job)
                    for b in range(4):
                        last = pe.transpose(bank[:, b * P:(b + 1) * P], sources[which](b, t), ident)
                    last.then_inc(turned.filled, 1)

            @block.scalar
            def _(act):
                for job in range(4 * TT):
                    which, t = divmod(job, TT)
                    bank = turned.ready(act, job)
                    act.activation(targets[which][:, t], bank[:, :].rearrange("p (h d) -> p h d", h=8),
                                   ACT.Copy).then_inc(turned.emptied, 1)

    def rwkv_units(self):
        nc = self.nc
        scores = Banks(self, "unit_scores", [0, 1, 2, 3, 4, 5])
        level_p, level_xt, level_x = (Banks(self, "unit_" + n, [b]) for n, b in (("p", 6), ("xt", 7), ("x", 0)))
        u_in, wz_in = Banks(self, "unit_u", [1]), Banks(self, "unit_wz", [2])
        q_in, y_in = Banks(self, "unit_q", [3]), Banks(self, "unit_y", [4])
        phi_in = Banks(self, "unit_phi", [5, 6])
        masked, level_masks = self.sem("unit_masked"), self.sem("unit_level_masks")
        x_ready = self.sem("unit_x_first")
        scores.emptied = masked
        order = self.vec
        LEVELS = 5
        GROUPS_ = 2 * TT
        with nc.Block() as block:
            def heads(g):
                return g // 2, 4 * (g % 2)

            def rows(h):
                return slice(64 * (h % 2), 64 * (h % 2) + 64)

            @block.tensor
            def _(pe):
                for g in range(GROUPS_):
                    t, h0 = heads(g)
                    cols = slice(t * P, (t + 1) * P)
                    if g > 0:
                        pe.wait_ge(q_in.emptied, g)
                        pe.wait_ge(y_in.emptied, g)
                        pe.wait_ge(phi_in.emptied, 2 * g)
                    for part in range(6):
                        kind, parity = divmod(part, 2)
                        bank = scores.free(pe, 6 * g + part)
                        for n in range(2):
                            h = h0 + parity + 2 * n
                            b, r = h // 2, rows(h)
                            if kind < 2:
                                left = (self.f_kt, self.f_b)[kind]
                                last = pe.matmul(bank[:, n * T:(n + 1) * T], left[r, b, cols],
                                                 self.f_ar[r, b, t].rearrange("p a x -> p (a x)"), start=True, stop=True)
                            else:
                                last = pe.matmul(bank[:, n * P:(n + 1) * P], self.f_ar[r, b, t, 0, :],
                                                 self.f_b[r, b, cols], start=True, stop=True)
                        last.then_inc(scores.filled, 1)
                    pe.wait_ge(x_ready, 2 * (g + 1))
                    for level in range(LEVELS):
                        n_done = g * LEVELS + level
                        pe.wait_ge(level_masks, n_done + 1)
                        pe.wait_ge(level_xt.emptied, n_done)
                        pe.wait_ge(level_x.emptied, n_done - g)
                        bank = level_p.free(pe, n_done)
                        for n in range(4):
                            last = pe.matmul(bank[:, n * P:(n + 1) * P], self.u_n[:, level, n, :], self.u_x[:, n, :],
                                             start=True, stop=True)
                        last.then_inc(level_p.filled, 1)
                        pe.wait_ge(level_p.emptied, n_done + 1)
                        bank = level_xt.free(pe, n_done)
                        for n in range(4):
                            last = pe.matmul(bank[:, n * P:(n + 1) * P], self.u_p[:, n, :], self.u_xt[:, n, :],
                                             start=True, stop=True)
                        last.then_inc(level_xt.filled, 1)
                        if level < LEVELS - 1:
                            bank = level_x.free(pe, n_done - g)
                            for n in range(4):
                                last = pe.matmul(bank[:, n * P:(n + 1) * P], self.u_xt[:, n, :], self.u_p[:, n, :],
                                                 start=True, stop=True)
                            last.then_inc(level_x.filled, 1)
                    bank = u_in.free(pe, g)
                    for n in range(4):
                        last = pe.matmul(bank[:, n * 64:(n + 1) * 64], self.u_k[:, n, 0:P], self.tok_v[:, t, h0 + n, :],
                                         start=True, stop=True)
                    last.then_inc(u_in.filled, 1)
                    pe.wait_ge(level_xt.emptied, LEVELS * (g + 1))
                    pe.wait_ge(u_in.emptied, g + 1)
                    bank = wz_in.free(pe, g)
                    for n in range(4):
                        last = pe.matmul(bank[:, n * P:(n + 1) * P], self.u_xt[:, n, :], self.tok_au[:, t, h0 + n, :],
                                         start=True, stop=True)
                    last.then_inc(wz_in.filled, 1)
                    pe.wait_ge(wz_in.emptied, g + 1)
                    bank = q_in.free(pe, g)
                    for n in range(4):
                        h = h0 + n
                        last = pe.matmul(bank[rows(h), (n // 2) * P:(n // 2 + 1) * P], self.wz[:, t, h, 0:64],
                                         self.u_b[:, n, P:2 * P], start=True, stop=True)
                    last.then_inc(q_in.filled, 1)
                    bank = y_in.free(pe, g)
                    for n in range(4):
                        h = h0 + n
                        pe.matmul(bank[:, n * 64:(n + 1) * 64], self.u_k[:, n, P:2 * P], self.tok_v[:, t, h, :],
                                  start=True, stop=False)
                        last = pe.matmul(bank[:, n * 64:(n + 1) * 64], self.u_b[:, n, P:2 * P], self.wz[:, t, h, 64:P],
                                         start=False, stop=True)
                    last.then_inc(y_in.filled, 1)
                    for c in range(2):
                        bank = phi_in.free(pe, 2 * g + c)
                        r = slice(64 * c, 64 * c + 64)
                        for n in range(4):
                            h = h0 + n
                            out = bank[rows(h), (n // 2) * P:(n // 2 + 1) * P]
                            pe.matmul(out[:, 0:64], self.wz[r, t, h, 0:64], self.tok_b[r, t, h, :], start=True, stop=True)
                            pe.matmul(out[:, 64:P], self.tok_b[r, t, h, :], self.wz[r, t, h, 64:P], start=True, stop=False)
                            last = pe.matmul(out[:, 64:P], self.tok_k[r, t, h, :], self.tok_v[r, t, h, :],
                                             start=False, stop=True)
                        last.then_inc(phi_in.filled, 1)

            @block.scalar
            def _(act):
                for g in range(GROUPS_):
                    t, h0 = heads(g)
                    for level in range(LEVELS):
                        bank = level_p.ready(act, g * LEVELS + level)
                        act.activation(self.u_p, bank[:, :].rearrange("p (n s) -> p n s", n=4),
                                       ACT.Copy).then_inc(level_p.emptied, 1)
                    bank = u_in.ready(act, g)
                    act.activation(self.tok_au[:, t, h0:h0 + 4, 64:P], bank[:, 0:T].rearrange("p (n v) -> p n v", n=4),
                                   ACT.Copy).then_inc(u_in.emptied, 1)
                    bank = wz_in.ready(act, g)
                    act.activation(self.wz[:, t, h0:h0 + 4, :], bank[:, :].rearrange("p (n v) -> p n v", n=4),
                                   ACT.Copy).then_inc(wz_in.emptied, 1)
                    bank = y_in.ready(act, g)
                    act.activation(self.y_local[:, t, h0:h0 + 4, :], bank[:, 0:T].rearrange("p (n v) -> p n v", n=4),
                                   ACT.Copy).then_inc(y_in.emptied, 1)

            @block.gpsimd
            def _(pool):
                for g in range(GROUPS_):
                    pool.wait_ge(masked, 6 * (g + 1))
                    for level in range(LEVELS):
                        pool.tensor_tensor(self.u_n[:, level], self.u_b[:, :, 0:P],
                                           self.mask_level[:, level, :].unsqueeze(1).broadcast_to([P, 4, P]),
                                           ALU.mult).then_inc(level_masks, 1)

            @block.vector
            def _(vec):
                for g in range(GROUPS_):
                    t, h0 = heads(g)
                    b0 = h0 // 2
                    for part in range(6):
                        kind, parity = divmod(part, 2)
                        bank = scores.ready(vec, 6 * g + part)
                        if kind < 2:
                            dst = (self.u_k, self.u_b)[kind][:, parity::2, :]
                            mask = self.mask_pair.rearrange("p a x -> p (a x)").unsqueeze(1).broadcast_to([P, 2, T])
                            src = bank[:, :].rearrange("p (n s) -> p n s", n=2)
                        else:
                            dst = self.u_a[:, parity::2, :]
                            mask = self.mask_a.unsqueeze(1).broadcast_to([P, 2, P])
                            src = bank[:, 0:T].rearrange("p (n s) -> p n s", n=2)
                        vec.tensor_tensor(dst, src, mask, ALU.mult).then_inc(masked, 1)
                    vec.wait_ge(masked, 6 * (g + 1))
                    for n, (x, src) in enumerate(((self.u_x, self.u_a), (self.u_xt, self.u_b[:, :, 0:P]))):
                        order.step(vec.tensor_tensor(x, src, self.mask_two[:, n, :].unsqueeze(1).broadcast_to([P, 4, P]),
                                                     ALU.mult))
                    order.settle(vec)
                    for x in (self.u_x, self.u_xt):
                        vec.tensor_tensor(x, x, self.ident.unsqueeze(1).broadcast_to([P, 4, P]),
                                          ALU.add).then_inc(x_ready, 1)
                    vec.wait_ge(x_ready, 2 * (g + 1))
                    for level in range(LEVELS):
                        bank = level_xt.ready(vec, g * LEVELS + level)
                        if level < LEVELS - 1:
                            level_x.ready(vec, g * LEVELS + level - g)
                        vec.tensor_tensor(self.u_xt, self.u_xt, bank[:, :].rearrange("p (n s) -> p n s", n=4),
                                          ALU.add).then_inc(level_xt.emptied, 1)
                        if level < LEVELS - 1:
                            bank = level_x.ready(vec, g * LEVELS + level - g)
                            vec.tensor_tensor(self.u_x, self.u_x, bank[:, :].rearrange("p (n s) -> p n s", n=4),
                                              ALU.add).then_inc(level_x.emptied, 1)
                            vec.wait_ge(level_x.emptied, g * LEVELS + level - g + 1)
                    bank = q_in.ready(vec, g)
                    vec.tensor_tensor(self.q_hat[:, b0:b0 + 2, t * P:(t + 1) * P],
                                      bank[:, 0:T].rearrange("p (n s) -> p n s", n=2), self.f_ar[:, b0:b0 + 2, t, 1, :],
                                      ALU.add).then_inc(q_in.emptied, 1)
                    for c in range(2):
                        bank = phi_in.ready(vec, 2 * g + c)
                        src = bank[:, 0:T].rearrange("p (n a x) -> p n a x", n=2, a=2)
                        dst = self.phi[:, 2 * t + c, b0:b0 + 2]
                        order.step(vec.tensor_copy(dst[:, :, 1, :], src[:, :, 1, :]))
                        vec.tensor_tensor(dst[:, :, 0, :], src[:, :, 0, :],
                                          self.ident64.unsqueeze(1).broadcast_to([P, 2, 64]),
                                          ALU.add).then_inc(phi_in.emptied, 1)

    def rwkv_scan(self):
        nc = self.nc
        cross = [[self.psum[2 * t + half] for half in range(2)] for t in range(TT)]
        nexts = [self.psum[4], self.psum[5]]
        cross_ready, next_ready = self.sem("cross_ready"), self.sem("next_state_ready")
        state_ready, var_ready, root_ready = (self.sem(n) for n in ("state_ready", "rwkv_var_ready", "rwkv_root_ready"))
        order = self.vec
        state = self.state
        with nc.Block() as block:
            @block.tensor
            def _(pe):
                for c in range(CHUNKS):
                    t, half_t = divmod(c, 2)
                    pe.wait_ge(state_ready, 2 * c + 1)
                    for par in range(2):
                        r = slice(64 * par, 64 * par + 64)
                        for b in range(4):
                            last = pe.matmul(cross[t][par][64 * half_t:64 * half_t + 64, b * 64:(b + 1) * 64],
                                             self.q_hat[r, b, c * CHUNK:(c + 1) * CHUNK], state[r, b, :],
                                             start=True, stop=True)
                    last.then_inc(cross_ready, 1)
                    if c < CHUNKS - 1:
                        for par in range(2):
                            r = slice(64 * par, 64 * par + 64)
                            for b in range(4):
                                last = pe.matmul(nexts[par][r, b * 64:(b + 1) * 64], self.phi[r, c, b, 0, :],
                                                 state[r, b, :], start=True, stop=True)
                        last.then_inc(next_ready, 1)

            @block.scalar
            def _(act):
                act.wait_ge(var_ready, 1)
                act.activation(self.stat[:, 4, :], self.stat[:, 3, :], ACT.Sqrt).then_inc(root_ready, 1)

            @block.vector
            def _(vec):
                vec.memset(state, 0.0).then_inc(state_ready, 1)
                for c in range(CHUNKS - 1):
                    vec.wait_ge(next_ready, c + 1)
                    vec.wait_ge(cross_ready, c + 1)
                    for par in range(2):
                        r = slice(64 * par, 64 * par + 64)
                        order.step(vec.tensor_tensor(state[r], nexts[par][r, 0:T].rearrange("p (b x) -> p b x", b=4),
                                                     self.phi[r, c, :, 1, :], ALU.add))
                    order.settle(vec)
                    for par in range(2):
                        r = slice(64 * par, 64 * par + 64)
                        vec.tensor_tensor(state[r], state[r],
                                          self.decay_end[r, :, c:c + 1].broadcast_to([64, 4, RW_DIM]),
                                          ALU.mult).then_inc(state_ready, 1)
                total, mean, square, var, root, rstd = (self.stat[:, n, :].rearrange("p (t h) -> p t h", t=2)
                                                        for n in range(6))
                y, wide = self.y_local, self.tmp.rearrange("p (t n) s -> p t (n s)", t=2)
                heads = "p (h d) -> p h d"

                def over(x):
                    return x.unsqueeze(2).broadcast_to([P, RW_HEADS, RW_DIM])

                vec.wait_ge(cross_ready, CHUNKS)
                for t in range(TT):
                    for par in range(2):
                        order.step(vec.tensor_tensor(y[:, t, par::2, :], y[:, t, par::2, :],
                                                     cross[t][par][:, 0:T].rearrange(heads, h=4), ALU.add))
                order.settle(vec)
                for t in range(TT):
                    order.step(vec.tensor_reduce(total[:, t], y[:, t], AX.X, ALU.add))
                order.settle(vec)
                order.step(vec.tensor_scalar(mean, total, 1.0 / RW_DIM, None, ALU.mult))
                order.settle(vec)
                for t in range(TT):
                    order.step(vec.tensor_tensor(y[:, t], y[:, t], over(mean[:, t]), ALU.subtract))
                order.settle(vec)
                for t in range(TT):
                    order.step(vec.tensor_tensor(wide[:, t].rearrange(heads, h=8), y[:, t], y[:, t], ALU.mult))
                order.settle(vec)
                for t in range(TT):
                    order.step(vec.tensor_reduce(square[:, t], wide[:, t].rearrange(heads, h=8), AX.X, ALU.add))
                order.settle(vec)
                vec.tensor_scalar(var, square, 1.0 / RW_DIM, RW_EPS, ALU.mult, ALU.add).then_inc(var_ready, 1)
                for t in range(TT):
                    order.step(vec.tensor_tensor(wide[:, t].rearrange(heads, h=8), self.tok_v[:, t], over(self.bonus[:, t]),
                                                 ALU.mult))
                vec.wait_ge(root_ready, 1)
                order.step(vec.reciprocal(rstd, root))
                order.settle(vec)
                for t in range(TT):
                    order.step(vec.tensor_tensor(y[:, t], y[:, t], over(rstd[:, t]), ALU.mult))
                order.settle(vec)
                o, n = ROWS1["rw_gain"]
                for t in range(TT):
                    order.step(vec.tensor_tensor(y[:, t], y[:, t], self.rows1[:, o:o + n].rearrange(heads, h=8), ALU.mult))
                order.settle(vec)
                for t in range(TT):
                    order.step(vec.tensor_tensor(y[:, t], y[:, t], wide[:, t].rearrange(heads, h=8), ALU.add))
                order.settle(vec)
                for t in range(TT):
                    order.step(vec.tensor_tensor(self.mixed[:, t, 512:1024].rearrange(heads, h=8), y[:, t],
                                                 self.gate[:, t].rearrange(heads, h=8), ALU.mult))

    def project_out(self, name, first_chunk, upto):
        nc, h, xT, ident, mixed = self.nc, self.h, self.xT, self.ident, self.mixed
        turned = Banks(self, name + "_turned", [0, 1])
        sums = Banks(self, name + "_sums", [4, 5])
        for c in range(2):
            self.used_by[first_chunk + c] = (sums.filled, TT * (c + 1))
        with nc.Block() as block:
            @block.sync
            def _(sync):
                self.issue(sync, upto)

            @block.tensor
            def _(pe):
                for job in range(2 * TT):
                    t, half = divmod(job, 2)
                    bank = turned.free(pe, job)
                    for k in range(4):
                        last = pe.transpose(bank[:, k * P:(k + 1) * P], mixed[:, t, (4 * half + k) * P:(4 * half + k + 1) * P],
                                            ident)
                    last.then_inc(turned.filled, 1)
                pe.wait_ge(turned.emptied, 2 * TT)
                for c in range(2):
                    w = self.chunk(pe, first_chunk + c)
                    for t in range(TT):
                        bank = sums.free(pe, c * TT + t)
                        for k in range(K):
                            last = pe.matmul(bank[:, :], xT[:, k, t * P:(t + 1) * P], w[:, k, :],
                                             start=(k == 0), stop=(k == K - 1))
                        last.then_inc(sums.filled, 1)

            @block.scalar
            def _(act):
                for job in range(2 * TT):
                    t, half = divmod(job, 2)
                    bank = turned.ready(act, job)
                    act.activation(xT[:, 4 * half:4 * half + 4, t * P:(t + 1) * P],
                                   bank[:, :].rearrange("p (k t) -> p k t", k=4), ACT.Copy).then_inc(turned.emptied, 1)

            @block.vector
            def _(vec):
                for job in range(2 * TT):
                    c, t = divmod(job, TT)
                    bank = sums.ready(vec, job)
                    part = h[:, t, c * 512:(c + 1) * 512]
                    vec.tensor_tensor(part, part, bank[:, :], ALU.add).then_inc(sums.emptied, 1)


    def place_experts(self):
        at = self.at
        self.pick = at(WORK + 8192, TT, PAIRS, P)
        self.put = at(WORK + 12288, PAIRS, T)
        self.normed = at(MORE, TT, D)
        self.gathered = at(MORE + 2048, K, P)
        self.gate_up = at(MORE + 3072, 2, 512)
        self.hid = at(MORE + 4096, 2, FT, SLOTS_E)
        self.slot_out = at(MORE + 4608, D)
        self.silu_s = at(MORE + 5632, FT, SLOTS_E)
        self.sum_t = at(MORE + 2048, K, T)
        self.expert_w = at(WORK + 8192, EXPERTS, T)
        self.hidden = at(MORE, 2, FT, T)
        self.silu = at(MORE + 2048, 2, T)
        self.rows2 = at(MORE + 5900, N_ROWS2)
        self.const2 = at(MORE + 5900 + N_ROWS2, 256)
        o = MORE + 5900 + N_ROWS2 + 256
        self.route = at(o, K, 36)
        self.logits = at(o + 288, TT, 36)
        self.small_moe = at(o + 360, 29, 64)
        self.weights_t = at(o + 2216, 2, T)
        self.zeros = at(o + 2728, 320).bitcast(mybir.dt.bfloat16)
        self.ones = at(o + 3048, P)
        self.over_flag = at(o + 3176, 1)
        self.iota8 = self.iota[:, 0:8]
        self.weights_left = self.at(o + 3177, TT, EXPERTS)
        self.route_bias = self.at(o + 3241, GROUPS + EXPERTS)

    def route_tokens(self):
        nc = self.nc
        s = self.small_moe
        route_landed = self.sem("route_landed")
        logits_ready, exp_in, exp_out, pair_in, pair_out = (
            self.sem("route_" + n) for n in ("logits", "exp_in", "exp_out", "pair_in", "pair_out"))
        weights_ready, weights_t_ready = self.sem("route_weights"), self.sem("route_weights_t")
        zeros_ready = self.zeros_ready = self.sem("zeros_ready")
        turned_ready = self.sem("route_turned")
        spread_w, spread_n = Banks(self, "spread_weights", [4, 5]), Banks(self, "spread_slots", [6, 7])
        counts_ready, chosen_ready = self.sem("slot_counts"), self.sem("chosen_experts")
        order = self.vec
        logits = self.logits

        def tile_view(n, width):
            return s[:, n, 0:TT * width].rearrange("p (t x) -> p t x", t=TT)

        gmax, shifted, gexp, gsum, gprob = tile_view(0, 1), tile_view(1, 4), tile_view(2, 4), tile_view(3, 1), tile_view(4, 1)
        equal, count, chosen, ones = tile_view(5, 4), tile_view(6, 4), tile_view(7, 4), s[:, 8, 0:4]
        product, inside, best = tile_view(9, 32), tile_view(10, 8), tile_view(11, 8)
        index, index_f = tile_view(12, 8).bitcast(U32), tile_view(13, 8)
        diff, ratio, denom, w0, w1 = (tile_view(14 + n, 1) for n in range(5))
        pick0, pick1 = tile_view(19, 8), tile_view(20, 8)
        weights, weights_all = tile_view(21, 32), self.weights_left
        mask, running, slot, fits = (tile_view(22 + n, 32) for n in range(4))
        picked, biggest = tile_view(26, 8), s[:, 27, 0:1]
        with nc.Block() as block:
            @block.sync
            def _(sync):
                sync.dma_start(self.route, self.ins["route"]).then_inc(route_landed, 16)
                o, n = ROWS1["route_bias"]
                sync.dma_start(self.route_bias, self.ins["rows1"][o:o + n].partition_broadcast(P)).then_inc(route_landed, 16)
                for e in range(2):
                    for n in range(3):
                        self.load_weight(sync, 0, e, n)

            @block.tensor
            def _(pe):
                pe.wait_ge(route_landed, 32)
                for t in range(TT):
                    for k in range(K):
                        last = pe.matmul(self.psum[t][:, 0:36], self.xT[:, k, t * P:(t + 1) * P], self.route[:, k, :],
                                         start=(k == 0), stop=(k == K - 1))
                    last.then_inc(logits_ready, 1)
                pe.wait_ge(chosen_ready, TT)
                pe.matmul(self.psum[3][:, 0:32], self.up_to, mask[:, 0, :], start=True, stop=True)
                pe.matmul(self.psum[3][:, 32:64], self.up_to, mask[:, 1, :], start=True, stop=False)
                pe.matmul(self.psum[3][:, 32:64], self.ones, mask[:, 0, :], start=False, stop=True)
                pe.matmul(self.psum[3][:, 64:96], self.ones, mask[:, 0, :], start=True, stop=False)
                pe.matmul(self.psum[3][:, 64:96], self.ones, mask[:, 1, :], start=False,
                          stop=True).then_inc(counts_ready, 1)
                pe.wait_ge(weights_ready, TT)
                for which, src in enumerate((weights, slot)):
                    for t in range(TT):
                        last = pe.transpose(self.psum[2][0:EXPERTS, (which * TT + t) * P:(which * TT + t + 1) * P],
                                            src[:, t, :], self.ident)
                last.then_inc(turned_ready, 1)
                pe.wait_ge(weights_t_ready, 1)
                for job in range(PAIRS // 2):
                    for which, stage in enumerate((spread_w, spread_n)):
                        bank = stage.free(pe, job)
                        for n in range(2):
                            q = 2 * job + n
                            for parity in range(2):
                                e = 2 * q + parity
                                row = self.ident[0:EXPERTS, e:e + 1].broadcast_to([EXPERTS, 64])
                                last = pe.matmul(bank[64 * parity:64 * parity + 64, n * T:(n + 1) * T], row,
                                                 self.weights_t[0:EXPERTS, which, :], start=True, stop=True)
                        last.then_inc(stage.filled, 1)

            @block.scalar
            def _(act):
                act.wait_ge(exp_in, 1)
                act.activation(gexp, shifted, ACT.Exp).then_inc(exp_out, 1)
                act.wait_ge(pair_in, 1)
                act.activation(ratio, diff, ACT.Exp).then_inc(pair_out, 1)
                for job in range(PAIRS // 2):
                    bank = spread_w.ready(act, job)
                    act.activation(self.put[:, 2 * job:2 * job + 2, :], bank[:, :].rearrange("p (n t) -> p n t", n=2),
                                   ACT.Copy).then_inc(spread_w.emptied, 1)

            @block.vector
            def _(vec):
                vec.memset(self.zeros, 0.0).then_inc(zeros_ready, 1)
                order.step(vec.memset(ones, 1.0))
                order.step(vec.memset(self.ones, 1.0))
                for t in range(TT):
                    vec.wait_ge(logits_ready, t + 1)
                    order.step(vec.tensor_tensor(logits[:, t, :], self.psum[t][:, 0:36], self.route_bias, ALU.add))
                order.settle(vec)
                order.step(vec.tensor_reduce(gmax, logits[:, :, 0:GROUPS], AX.X, ALU.max))
                order.settle(vec)
                wide = gmax.broadcast_to([P, TT, GROUPS])
                order.step(vec.tensor_tensor(equal, logits[:, :, 0:GROUPS], wide, ALU.is_equal))
                vec.tensor_tensor(shifted, logits[:, :, 0:GROUPS], wide, ALU.subtract).then_inc(exp_in, 1)
                order.settle(vec)
                for t in range(TT):
                    order.step(vec.tensor_tensor_scan(count[:, t], ones, equal[:, t], 0.0, ALU.mult, ALU.add))
                order.settle(vec)
                order.step(vec.scalar_tensor_tensor(out=chosen, in0=count, scalar=1.0, in1=equal, op0=ALU.is_equal,
                                                    op1=ALU.mult))
                vec.wait_ge(exp_out, 1)
                order.step(vec.tensor_reduce(gsum, gexp, AX.X, ALU.add))
                order.settle(vec)
                order.step(vec.reciprocal(gprob, gsum))
                for t in range(TT):
                    order.step(vec.tensor_tensor(product[:, t].rearrange("p (g e) -> p g e", g=GROUPS),
                                                 logits[:, t, GROUPS:36].rearrange("p (g e) -> p g e", g=GROUPS),
                                                 chosen[:, t].unsqueeze(2).broadcast_to([P, GROUPS, PER_GROUP]), ALU.mult))
                order.settle(vec)
                for t in range(TT):
                    order.step(vec.tensor_reduce(inside[:, t], product[:, t].rearrange("p (g e) -> p e g", g=GROUPS),
                                                 AX.X, ALU.add))
                order.settle(vec)
                for t in range(TT):
                    order.step(vec.max(best[:, t], inside[:, t]))
                order.settle(vec)
                for t in range(TT):
                    order.step(vec.max_index(index[:, t], best[:, t], inside[:, t]))
                vec.tensor_tensor(diff, best[:, :, 1:2], best[:, :, 0:1], ALU.subtract).then_inc(pair_in, 1)
                order.settle(vec)
                order.step(vec.tensor_copy(index_f, index))
                order.settle(vec)
                for t in range(TT):
                    for n, pick in enumerate((pick0, picked)):
                        order.step(vec.tensor_scalar(pick[:, t], self.iota8, index_f[:, t, n:n + 1], None, ALU.is_equal))
                order.settle(vec)
                order.step(vec.tensor_tensor(picked, picked, pick0, ALU.add))
                order.settle(vec)
                for t in range(TT):
                    vec.tensor_tensor(mask[:, t].rearrange("p (g e) -> p g e", g=GROUPS),
                                      picked[:, t].unsqueeze(1).broadcast_to([P, GROUPS, PER_GROUP]),
                                      chosen[:, t].unsqueeze(2).broadcast_to([P, GROUPS, PER_GROUP]),
                                      ALU.mult).then_inc(chosen_ready, 1)
                vec.wait_ge(pair_out, 1)
                order.step(vec.tensor_scalar(denom, ratio, 1.0, None, ALU.add))
                order.settle(vec)
                order.step(vec.reciprocal(w0, denom))
                order.settle(vec)
                order.step(vec.tensor_tensor(w0, w0, gprob, ALU.mult))
                order.settle(vec)
                order.step(vec.tensor_tensor(w1, w0, ratio, ALU.mult))
                order.settle(vec)
                for t in range(TT):
                    for n, (pick, w) in enumerate(((pick0, w0), (pick1, w1))):
                        order.step(vec.tensor_scalar(pick[:, t], self.iota8, index_f[:, t, n:n + 1], w[:, t], ALU.is_equal,
                                                     ALU.mult))
                order.settle(vec)
                order.step(vec.tensor_tensor(pick0, pick0, pick1, ALU.add))
                order.settle(vec)
                for t in range(TT):
                    order.step(vec.tensor_tensor(weights_all[:, t].rearrange("p (g e) -> p g e", g=GROUPS),
                                                 pick0[:, t].unsqueeze(1).broadcast_to([P, GROUPS, PER_GROUP]),
                                                 chosen[:, t].unsqueeze(2).broadcast_to([P, GROUPS, PER_GROUP]), ALU.mult))
                vec.wait_ge(counts_ready, 1)
                running_in = self.psum[3][:, 0:64].rearrange("p (t e) -> p t e", t=TT)
                order.step(vec.tensor_tensor(running, running_in, mask, ALU.mult))
                order.step(vec.tensor_reduce(biggest, self.psum[3][:, 64:96], AX.X, ALU.max))
                order.settle(vec)
                order.step(vec.tensor_scalar(self.over_flag.bitcast(mybir.dt.int32), biggest, float(SLOTS_E), None, ALU.is_gt))
                order.step(vec.tensor_scalar(fits, running, float(SLOTS_E), None, ALU.is_le))
                order.step(vec.tensor_scalar(slot, running, -1.0, None, ALU.add))
                order.settle(vec)
                vec.tensor_tensor(weights, weights_all, fits, ALU.mult).then_inc(weights_ready, 1)
                vec.wait_ge(weights_ready, 1)
                vec.tensor_tensor(weights_all, weights_all, weights, ALU.subtract).then_inc(weights_ready, 1)
                for t in range(TT):
                    for q in range(PAIRS):
                        for n in range(2):
                            order.step(vec.tensor_scalar(self.pick[:, t, q, n * 64:(n + 1) * 64], self.iota[:, 0:64],
                                                         slot[:, t, 2 * q + n:2 * q + n + 1], None, ALU.is_equal))
                vec.wait_ge(turned_ready, 1)
                vec.tensor_copy(self.weights_t[0:EXPERTS].rearrange("p a t -> p (a t)"),
                                self.psum[2][0:EXPERTS, :]).then_inc(weights_t_ready, 1)
                for job in range(PAIRS // 2):
                    vec.wait_ge(spread_w.emptied, job + 1)
                    bank = spread_n.ready(vec, job)
                    put = self.put[:, 2 * job:2 * job + 2, :].rearrange("p n t -> p (n t)")
                    vec.scalar_tensor_tensor(out=put, in0=bank[:, :], scalar=self.slot_number, in1=put,
                                             op0=ALU.is_equal, op1=ALU.mult).then_inc(spread_n.emptied, 1)

    def load_weight(self, sync, q, parity, n):
        s = 3 * parity + n
        dst = self.at(RING + s * SLOT, FT, D) if n == 2 else self.at(RING + s * SLOT, K, FF)
        src = self.ins[("w_gate", "w_up", "w_down")[n]][q * 2 + parity]
        sync.dma_start(dst, src).then_inc(self.landed[s], 16)

    def experts(self):
        nc, ident = self.nc, self.ident
        acc = [self.psum[n] for n in range(4)]
        wide = [self.psum[4], self.psum[5]]
        gu_bank, turn_bank = self.psum[6], self.psum[7]
        base = [self.loads[s] for s in range(6)]
        for s in range(6):
            self.loads[s] += PAIRS
        (gather_ready, gather_used, gu_ready, gu_used, turn_ready, silu_ready, hid_ready, down_ready, down_used,
         scatter_done, all_done, sum_ready) = (self.sem("pair_" + n) for n in (
            "gathered", "gathered_used", "gate_up", "gate_up_used", "turned", "silu", "hidden", "down", "down_used",
            "scattered", "all", "sum_copied"))
        back = Banks(self, "sum_turned", [4, 5])
        rows_landed = self.rows2_landed = self.sem("rows2_landed")
        gain = self.col("norm2")
        order = self.vec

        def slot(s, *shape):
            return self.at(RING + s * SLOT, *shape)

        with nc.Block() as block:
            @block.sync
            def _(sync):
                sync.dma_start(self.rows2, self.ins["rows2"].partition_broadcast(P)).then_inc(rows_landed, 16)
                sync.dma_start(self.const2, self.ins["const2"]).then_inc(rows_landed, 16)
                with sync.Fori(1, PAIRS) as q:
                    sync.wait_ge(gu_ready, q * 2 - 1)
                    self.load_weight(sync, q, 0, 0)
                    self.load_weight(sync, q, 0, 1)
                    sync.wait_ge(gu_ready, q * 2)
                    self.load_weight(sync, q, 1, 0)
                    self.load_weight(sync, q, 1, 1)
                    sync.wait_ge(down_ready, q)
                    self.load_weight(sync, q, 0, 2)
                    self.load_weight(sync, q, 1, 2)

            @block.tensor
            def _(pe):
                pe.wait_ge(self.zeros_ready, 1)

                def touch(start):
                    for bank in acc:
                        last = pe.matmul(bank[:, :], self.zeros[0:1, 0:P], self.zeros[0:1, P:P + 512], start=start,
                                         stop=not start, skip_group_check=True)
                    return last

                def one(x, q):
                    return x[:, q, :] if isinstance(q, int) else x[:, bass.ds(q, 1), :].rearrange("p a x -> p (a x)")

                def gather(q, first=False):
                    if not first:
                        pe.wait_ge(down_used, q * 2 - 2)
                    for k in range(K):
                        for t in range(TT):
                            last = pe.matmul(wide[k // 4][:, (k % 4) * P:(k % 4 + 1) * P],
                                             self.normed[:, t, k * P:(k + 1) * P], one(self.pick[:, t], q),
                                             start=(t == 0), stop=(t == TT - 1))
                    last.then_inc(gather_ready, 1)

                def gate_up(q, parity):
                    for n in range(2):
                        pe.wait_ge(self.landed[3 * parity + n], (q + 1) * 16 + 16 * base[3 * parity + n])
                    pe.wait_ge(gather_used, q * 2 + 2)
                    if not (isinstance(q, int) and q == 0 and parity == 0):
                        pe.wait_ge(gu_used, q * 2 + parity)
                    for k in range(K):
                        for n in range(2):
                            last = pe.matmul(gu_bank[64 * n:64 * n + 64, :], self.gathered[:, k, 64 * parity:64 * parity + 64],
                                             slot(3 * parity + n, K, FF)[:, k, :], start=(k == 0), stop=(k == K - 1))
                    last.then_inc(gu_ready, 1)

                def turn(q, parity):
                    pe.wait_ge(gu_used, q * 2 + (parity + 1))
                    if not (isinstance(q, int) and q == 0 and parity == 0):
                        pe.wait_ge(hid_ready, q * 2 + parity)
                    for f in range(FT):
                        last = pe.transpose(turn_bank[:, f * P:(f + 1) * P], self.gate_up[:, parity, f * P:(f + 1) * P], ident)
                    last.then_inc(turn_ready, 1)

                def down(q):
                    for parity in range(2):
                        pe.wait_ge(self.landed[3 * parity + 2], (q + 1) * 16 + 16 * base[3 * parity + 2])
                    pe.wait_ge(hid_ready, q * 2 + 2)
                    pe.wait_ge(gather_used, q * 2 + 2)
                    for n in range(2):
                        for f in range(FT):
                            for parity in range(2):
                                last = pe.matmul(wide[n][64 * parity:64 * parity + 64, :], self.hid[:, parity, f, :],
                                                 slot(3 * parity + 2, FT, D)[:, f, n * 512:(n + 1) * 512],
                                                 start=(f == 0), stop=(f == FT - 1))
                    last.then_inc(down_ready, 1)

                def scatter(q):
                    pe.wait_ge(down_used, q * 2 + 2)
                    for k in range(K):
                        last = pe.matmul(acc[k // 2][:, (k % 2) * T:(k % 2 + 1) * T], self.slot_out[:, k * P:(k + 1) * P],
                                         one(self.put, q), start=False, stop=False, skip_group_check=True)
                    last.then_inc(scatter_done, 1)

                touch(True)
                gather(0, first=True)
                gate_up(0, 0)
                gate_up(0, 1)
                turn(0, 0)
                gather(1, first=True)
                turn(0, 1)
                with pe.Fori(1, PAIRS - 1) as q:
                    gate_up(q, 0)
                    down(q - 1)
                    gate_up(q, 1)
                    turn(q, 0)
                    gather(q + 1)
                    scatter(q - 1)
                    turn(q, 1)
                last_q = PAIRS - 1
                gate_up(last_q, 0)
                down(last_q - 1)
                gate_up(last_q, 1)
                turn(last_q, 0)
                scatter(last_q - 1)
                turn(last_q, 1)
                down(last_q)
                scatter(last_q)
                touch(False).then_inc(all_done, 1)
                pe.wait_ge(sum_ready, 4)
                for job in range(2 * TT):
                    t, half = divmod(job, 2)
                    bank = back.free(pe, job)
                    for k in range(4):
                        last = pe.transpose(bank[:, k * P:(k + 1) * P], self.sum_t[:, 4 * half + k, t * P:(t + 1) * P], ident)
                    last.then_inc(back.filled, 1)

            @block.scalar
            def _(act):
                def copy_gate_up(q, parity):
                    act.wait_ge(gu_ready, q * 2 + (parity + 1))
                    act.activation(self.gate_up[:, parity, :], gu_bank[:, :], ACT.Copy).then_inc(gu_used, 1)

                def silu(q, parity):
                    act.wait_ge(turn_ready, q * 2 + (parity + 1))
                    turned = turn_bank[:, :].rearrange("p (f x) -> p f x", f=FT)
                    act.activation(self.silu_s, turned[:, :, 0:64], ACT.Silu).then_inc(silu_ready, 1)

                def copy_out(q):
                    act.wait_ge(down_ready, q + 1)
                    for n in range(2):
                        act.activation(self.slot_out[:, n * 512:(n + 1) * 512], wide[n][:, :],
                                       ACT.Copy).then_inc(down_used, 1)

                for parity in range(2):
                    copy_gate_up(0, parity)
                silu(0, 0)
                silu(0, 1)
                with act.Fori(1, PAIRS) as q:
                    copy_gate_up(q, 0)
                    copy_out(q - 1)
                    copy_gate_up(q, 1)
                    silu(q, 0)
                    silu(q, 1)
                copy_out(PAIRS - 1)
                act.wait_ge(all_done, 1)
                for n in range(4):
                    act.activation(self.sum_t[:, 2 * n:2 * n + 2, :], acc[n][:, :].rearrange("p (k t) -> p k t", k=2),
                                   ACT.Copy).then_inc(sum_ready, 1)

            @block.vector
            def _(vec):
                def copy_gathered(q):
                    vec.wait_ge(gather_ready, q + 1)
                    for n in range(2):
                        vec.tensor_tensor(self.gathered[:, 4 * n:4 * n + 4, :], wide[n][:, :].rearrange("p (k s) -> p k s", k=4),
                                          gain[:, 4 * n:4 * n + 4].unsqueeze(2).broadcast_to([P, 4, P]),
                                          ALU.mult).then_inc(gather_used, 1)

                def multiply(q, parity):
                    vec.wait_ge(silu_ready, q * 2 + (parity + 1))
                    turned = turn_bank[:, :].rearrange("p (f x) -> p f x", f=FT)
                    vec.tensor_tensor(self.hid[:, parity], self.silu_s, turned[:, :, 64:P], ALU.mult).then_inc(hid_ready, 1)

                copy_gathered(0)
                with vec.Fori(0, PAIRS - 1) as q:
                    multiply(q, 0)
                    copy_gathered(q + 1)
                    multiply(q, 1)
                multiply(PAIRS - 1, 0)
                multiply(PAIRS - 1, 1)
                for job in range(2 * TT):
                    t, half = divmod(job, 2)
                    bank = back.ready(vec, job)
                    part = self.h[:, t, half * 512:(half + 1) * 512]
                    vec.tensor_tensor(part, part, bank[:, :], ALU.add).then_inc(back.emptied, 1)

    def general_experts(self):
        nc = self.nc
        beyond = nc.values_load(self.over_flag[0:1, 0:1].bitcast(U32), min_val=0, max_val=1)
        with nc.If(beyond != 0):
            nc.all_engine_barrier()
            self.spread_left()
            self.experts_over_all()

    def spread_left(self):
        nc = self.nc
        turned_ready, weights_t_ready = self.sem("left_turned"), self.sem("left_weights_t")
        spread = Banks(self, "spread_left", [4, 5, 6, 7])
        with nc.Block() as block:
            @block.tensor
            def _(pe):
                for t in range(TT):
                    last = pe.transpose(self.psum[2][0:EXPERTS, t * P:(t + 1) * P], self.weights_left[:, t, :], self.ident)
                last.then_inc(turned_ready, 1)
                pe.wait_ge(weights_t_ready, 1)
                for job in range(EXPERTS // 2):
                    bank = spread.free(pe, job)
                    for n in range(2):
                        e = 2 * job + n
                        last = pe.matmul(bank[:, n * T:(n + 1) * T],
                                         self.ident[0:EXPERTS, e:e + 1].broadcast_to([EXPERTS, P]),
                                         self.weights_t[0:EXPERTS, 0, :], start=True, stop=True)
                    last.then_inc(spread.filled, 1)

            @block.scalar
            def _(act):
                for job in range(EXPERTS // 2):
                    bank = spread.ready(act, job)
                    act.activation(self.expert_w[:, 2 * job:2 * job + 2, :], bank[:, :].rearrange("p (n t) -> p n t", n=2),
                                   ACT.Copy).then_inc(spread.emptied, 1)

            @block.vector
            def _(vec):
                vec.wait_ge(turned_ready, 1)
                vec.tensor_copy(self.weights_t[0:EXPERTS, 0, :], self.psum[2][0:EXPERTS, 0:T]).then_inc(weights_t_ready, 1)

    def experts_over_all(self):
        nc, xT = self.nc, self.xT
        acc = [[self.psum[2 * t + n] for n in range(2)] for t in range(TT)]
        gu = [self.psum[4 + f] for f in range(FT)]
        gu_ready, silu_ready, gu_used, hidden_ready, down_done = (
            self.sem("experts_" + n) for n in ("gate_up", "silu", "gate_up_used", "hidden", "down"))
        all_done, h_ready = self.sem("experts_all_done"), self.sem("experts_added")
        landed = [self.sem(f"expert_slot{s}_landed") for s in range(6)]

        def slot(s, *shape):
            return self.at(RING + s * SLOT, *shape)

        def load_expert(sync, i, parity, used):
            for n in range(3):
                s = 3 * parity + n
                if used:
                    sync.wait_ge(*used[n // 2])
                src = self.ins[("w_gate", "w_up", "w_down")[n]][i * 2 + parity]
                dst = slot(s, FT, D) if n == 2 else slot(s, K, FF)
                sync.dma_start(dst, src).then_inc(landed[s], 16)

        with nc.Block() as block:
            @block.sync
            def _(sync):
                for parity in range(2):
                    load_expert(sync, 0, parity, None)
                with sync.Fori(1, EXPERTS // 2) as i:
                    for parity in range(2):
                        load_expert(sync, i, parity, [(gu_ready, i * 8 + (4 * parity - 4)), (down_done, i * 2 + (parity - 1))])

            @block.tensor
            def _(pe):
                def touch(start):
                    for bank in acc[0] + acc[1]:
                        last = pe.matmul(bank[:, :], self.zeros[0:1, 0:P], self.zeros[0:1, P:P + 512], start=start,
                                         stop=not start, skip_group_check=True)
                    return last

                def gate_up(e, parity, half, used):
                    for n in range(2):
                        pe.wait_ge(landed[3 * parity + n], half * 16 + 16)
                    for f in range(FT):
                        if used:
                            pe.wait_ge(gu_used, e * 4 + (f - 3))
                        for n in range(2):
                            w = slot(3 * parity + n, K, FF)
                            for k in range(K):
                                last = pe.matmul(gu[f][:, n * T:(n + 1) * T], w[:, k, f * P:(f + 1) * P], xT[:, k, :],
                                                 start=(k == 0), stop=(k == K - 1))
                        last.then_inc(gu_ready, 1)

                def down(e, parity, half):
                    pe.wait_ge(landed[3 * parity + 2], half * 16 + 16)
                    w = slot(3 * parity + 2, FT, D)
                    for f in range(FT):
                        pe.wait_ge(hidden_ready, e * 4 + (f + 1))
                        for t in range(TT):
                            for n in range(2):
                                last = pe.matmul(acc[t][n][:, :], self.hidden[:, parity, f, t * P:(t + 1) * P],
                                                 w[:, f, n * 512:(n + 1) * 512], start=False, stop=False,
                                                 skip_group_check=True)
                    last.then_inc(down_done, 1)

                touch(True)
                gate_up(0, 0, 0, False)
                with pe.Fori(0, EXPERTS // 2 - 1) as i:
                    gate_up(i * 2 + 1, 1, i, True)
                    down(i * 2, 0, i)
                    gate_up(i * 2 + 2, 0, i + 1, True)
                    down(i * 2 + 1, 1, i)
                last_pair = EXPERTS // 2 - 1
                gate_up(EXPERTS - 1, 1, last_pair, True)
                down(EXPERTS - 2, 0, last_pair)
                down(EXPERTS - 1, 1, last_pair)
                touch(False).then_inc(all_done, 1)

            @block.scalar
            def _(act):
                def silus(e, first):
                    for f in range(FT):
                        act.wait_ge(gu_ready, e * 4 + (f + 1))
                        if not (first and f < 2):
                            act.wait_ge(gu_used, e * 4 + (f - 1))
                        act.activation(self.silu[:, f % 2, :], gu[f][:, 0:T], ACT.Silu).then_inc(silu_ready, 1)

                silus(0, True)
                with act.Fori(1, EXPERTS) as e:
                    silus(e, False)

            @block.vector
            def _(vec):
                def hiddens(e, parity, wait_down):
                    for f in range(FT):
                        vec.wait_ge(silu_ready, e * 4 + (f + 1))
                        if wait_down and f == 0:
                            vec.wait_ge(down_done, e - 1)
                        hidden = self.hidden[:, parity, f, :]
                        vec.tensor_tensor(hidden, self.silu[:, f % 2, :], gu[f][:, T:2 * T], ALU.mult).then_inc(gu_used, 1)
                        vec.wait_ge(gu_used, e * 4 + (f + 1))
                        w = self.expert_w[:, e, :] if isinstance(e, int) else \
                            self.expert_w[:, bass.ds(e, 1), :].rearrange("p a t -> p (a t)")
                        vec.tensor_tensor(hidden, hidden, w, ALU.mult).then_inc(hidden_ready, 1)

                hiddens(0, 0, False)
                hiddens(1, 1, False)
                with vec.Fori(1, EXPERTS // 2) as i:
                    hiddens(i * 2, 0, True)
                    hiddens(i * 2 + 1, 1, True)
                vec.wait_ge(all_done, 1)
                for t in range(TT):
                    for n in range(2):
                        part = self.h[:, t, n * 512:(n + 1) * 512]
                        vec.tensor_tensor(part, part, acc[t][n][:, :], ALU.add).then_inc(h_ready, 1)
                vec.wait_ge(h_ready, 4)

    def final_norm(self):
        nc, h = self.nc, self.h
        junk = self.at(WORK, TT, D)
        ss, ms, root, rstd = (self.small[:, i * 2:i * 2 + 2] for i in range(4))
        squares, mean_ready, root_ready = (self.sem(f"final_{x}") for x in ("squares", "mean", "root"))
        order = self.vec
        with nc.Block() as block:
            @block.sync
            def _(sync):
                self.issue(sync, self.first_half + RING_SLOTS)

            @block.scalar
            def _(act):
                for t in range(TT):
                    act.activation(junk[:, t, :], h[:, t, :], ACT.Square, accum_out=ss[:, t:t + 1]).then_inc(squares, 1)
                act.wait_ge(mean_ready, 1)
                act.activation(root, ms, ACT.Sqrt).then_inc(root_ready, 1)

            @block.vector
            def _(vec):
                vec.wait_ge(squares, TT)
                vec.tensor_scalar(ms, ss, 1.0 / D, EPS, ALU.mult, ALU.add).then_inc(mean_ready, 1)
                vec.wait_ge(root_ready, 1)
                order.step(vec.reciprocal(rstd, root))
                order.settle(vec)
                vec.wait_ge(self.rows2_landed, 32)
                for t in range(TT):
                    order.step(vec.scalar_tensor_tensor(out=h[:, t, :], in0=h[:, t, :], scalar=rstd[:, t:t + 1],
                                                        in1=self.rows2[:, 0:D], op0=ALU.mult, op1=ALU.mult))


    def place_second(self):
        at = self.at
        o = WORK
        self.qkv2 = at(o, 6, TT, 512)
        self.turned_in = at(o + 6144, 4, TT, 512)
        self.qk2T = at(o + 10240, 4, 4, T)
        self.mixed = at(o + 14336, TT, D)
        o = MORE
        self.masked_s = at(o, 2, T)
        self.probs = at(o + 512, 6, T)
        self.mixed_p = at(o + 2048, 2, T)
        self.probs_t = at(o + 2560, 2, T)
        self.halves = at(o + 3072, 2, 256)
        self.squares2 = at(o + 3584, TT, 512)
        self.stat2 = at(o + 4608, 8, 64)
        self.sums2 = at(o + 5120, 64)
        self.neg_max = at(o + 5184, 64)
        self.pair_rec = at(o + 5248, 8)
        self.lam_work = at(o + 5256, 160)
        self.stat3 = at(o + 5420, 8, 24)
        self.future = at(o + 5612, T)

    def project_second(self):
        nc, xT = self.nc, self.xT
        first = self.first_half
        tokens = Banks(self, "project2", [0, 1, 2, 3])
        for c in range(6):
            self.used_by[first + c] = (tokens.filled, TT * (c + 1))
        names = ("mq", "mk", "dq", "dk")
        column = (0, 1, 3, 4)
        order = self.vec
        squares, mean_ready, root_ready = (self.sem("qk_" + n) for n in ("squares", "mean", "root"))
        exp_in, exp_out = self.sem("lambda_in"), self.sem("lambda_out")
        rows, heads = self.rows2, "p (h d) -> p h d"
        sq, ms, root, rstd = (self.stat2[:, n, :] for n in range(4))
        dots, lam_exp = self.lam_work[:, 128:130], self.lam_work[:, 130:132]
        with nc.Block() as block:
            @block.sync
            def _(sync):
                self.issue(sync, first + 8)

            @block.tensor
            def _(pe):
                for c in range(6):
                    w = self.chunk(pe, first + c)
                    for t in range(TT):
                        bank = tokens.free(pe, c * TT + t)
                        for k in range(K):
                            last = pe.matmul(bank[:, :], xT[:, k, t * P:(t + 1) * P], w[:, k, :],
                                             start=(k == 0), stop=(k == K - 1))
                        last.then_inc(tokens.filled, 1)

            @block.scalar
            def _(act):
                act.wait_ge(exp_in, 1)
                act.activation(lam_exp, dots, ACT.Exp).then_inc(exp_out, 1)
                for job in range(6 * TT):
                    bank = tokens.ready(act, job)
                    act.activation(self.qkv2[:, job // TT, job % TT, :], bank[:, :], ACT.Copy).then_inc(tokens.emptied, 1)
                act.wait_ge(mean_ready, 1)
                act.activation(root, ms, ACT.Sqrt).then_inc(root_ready, 1)

            @block.vector
            def _(vec):
                o, n = ROWS2["lambda"]
                four = rows[:, o:o + n].rearrange("p (a b d) -> p a b d", a=2, b=2)
                prod = self.lam_work[:, 0:128].rearrange("p (a d) -> p a d", a=2)
                order.step(vec.tensor_tensor(prod, four[:, :, 0, :], four[:, :, 1, :], ALU.mult))
                order.settle(vec)
                vec.tensor_reduce(dots, prod, AX.X, ALU.add).then_inc(exp_in, 1)
                order.step(vec.memset(self.future[:, 0:P], 0.0))
                order.step(vec.tensor_copy(self.future[:, P:T], self.const2[:, 128:256]))
                vec.wait_ge(exp_out, 1)
                order.step(vec.scalar_tensor_tensor(out=self.lt[:, 0:1], in0=lam_exp[:, 0:1], scalar=LAMBDA_INIT,
                                                    in1=lam_exp[:, 1:2], op0=ALU.add, op1=ALU.subtract))
                for n in range(4 * TT):
                    a, t = divmod(n, TT)
                    vec.wait_ge(tokens.emptied, TT * column[a] + t + 1)
                    x = self.qkv2[:, column[a], t, :]
                    junk = self.squares2[:, n % 2, :]
                    order.step(vec.tensor_tensor(junk, x, x, ALU.mult))
                    order.settle(vec)
                    order.step(vec.tensor_reduce(sq[:, n * 8:(n + 1) * 8], junk.rearrange(heads, h=8), AX.X, ALU.add))
                order.settle(vec)
                vec.tensor_scalar(ms, sq, 1.0 / M_DIM, EPS, ALU.mult, ALU.add).then_inc(mean_ready, 1)
                vec.wait_ge(root_ready, 1)
                order.step(vec.reciprocal(rstd, root))
                order.settle(vec)
                half = M_DIM // 2
                rope = self.const2[:, 0:128].rearrange("p (a t d) -> p a t d", a=2, t=TT)
                for n in range(4 * TT):
                    a, t = divmod(n, TT)
                    x = self.qkv2[:, column[a], t, :]
                    order.step(vec.tensor_tensor(x.rearrange(heads, h=8), x.rearrange(heads, h=8),
                                                 rstd[:, n * 8:(n + 1) * 8].unsqueeze(2).broadcast_to([P, 8, M_DIM]),
                                                 ALU.mult))
                    order.settle(vec)
                    o, width = ROWS2[names[a]]
                    gain = rows[:, o:o + width].unsqueeze(1).broadcast_to([P, 512 // width, width])
                    order.step(vec.tensor_tensor(x.rearrange(heads, d=width), x.rearrange(heads, d=width), gain, ALU.mult))
                    order.settle(vec)
                    x8 = x.rearrange(heads, h=8)
                    y8 = self.turned_in[:, a, t, :].rearrange(heads, h=8)
                    cos = rope[:, 0, t, :].unsqueeze(1).broadcast_to([P, 8, half])
                    sin = rope[:, 1, t, :].unsqueeze(1).broadcast_to([P, 8, half])
                    h0 = self.halves[:, 0, :].rearrange(heads, h=8)
                    h1 = self.halves[:, 1, :].rearrange(heads, h=8)
                    for out, u, v, op in ((y8[:, :, 0:half], cos, sin, ALU.subtract), (y8[:, :, half:], sin, cos, ALU.add)):
                        order.step(vec.tensor_tensor(h0, x8[:, :, 0:half], u, ALU.mult))
                        order.step(vec.tensor_tensor(h1, x8[:, :, half:], v, ALU.mult))
                        order.settle(vec)
                        order.step(vec.tensor_tensor(out, h0, h1, op))
                        order.settle(vec)

    def attention(self):
        nc, ident = self.nc, self.ident
        turned = Banks(self, "attn_turned", [0, 1, 2, 3])
        scores = Banks(self, "attn_scores", [4, 5])
        flips = Banks(self, "attn_flips", [6, 7])
        outs = {("m", 0): self.psum[0], ("m", 1): self.psum[1], ("d", 0): self.psum[2], ("d", 1): self.psum[3]}
        items = [("m", b, r, t) for b in range(4) for r in range(2) for t in range(TT)]
        items += [("d", b, None, t) for b in range(4) for t in range(TT)]
        jobs = []
        first_job = []
        for n, (kind, b, r, t) in enumerate(items):
            first_job.append(len(jobs))
            jobs += [(n, r)] if kind == "m" else [(n, 0), (n, 1)]
        first_job.append(len(jobs))
        diff_no = {n: m for m, n in enumerate(n for n, x in enumerate(items) if x[0] == "d")}
        maxed, exped, mixed_ready, pv_done = (self.sem("attn_" + n) for n in ("max", "exp", "mixed", "pv"))
        mean_ready, root_ready = self.sem("attn_mean"), self.sem("attn_root")
        order = self.vec
        last_item = len(items)
        with nc.Block() as block:
            @block.tensor
            def _(pe):
                for job in range(4 * TT):
                    a, t = divmod(job, TT)
                    bank = turned.free(pe, job)
                    for b in range(4):
                        last = pe.transpose(bank[:, b * P:(b + 1) * P], self.turned_in[:, a, t, b * P:(b + 1) * P], ident)
                    last.then_inc(turned.filled, 1)
                pe.wait_ge(turned.emptied, 4 * TT)
                for step in range(last_item + 3):
                    if step < last_item:
                        kind, b, r, t = items[step]
                        q = 0 if kind == "m" else 2
                        n = P * (t + 1)
                        for job in range(first_job[step], first_job[step + 1]):
                            half = jobs[job][1]
                            rows = slice(64 * half, 64 * half + 64)
                            bank = scores.free(pe, job)
                            pe.matmul(bank[:, 0:n], self.qk2T[rows, q, b, t * P:(t + 1) * P], self.qk2T[rows, q + 1, b, 0:n],
                                      start=True, stop=True).then_inc(scores.filled, 1)
                    if 0 <= step - 2 < last_item:
                        i = step - 2
                        kind, b, r, t = items[i]
                        if kind == "m":
                            pe.wait_ge(exped, first_job[i + 1])
                            src = self.probs[:, first_job[i] % 6, :]
                        else:
                            pe.wait_ge(mixed_ready, diff_no[i] + 1)
                            src = self.mixed_p[:, diff_no[i] % 2, :]
                        bank = flips.free(pe, i)
                        for s in range(t + 1):
                            last = pe.transpose(bank[:, s * P:(s + 1) * P], src[:, s * P:(s + 1) * P], ident)
                        last.then_inc(flips.filled, 1)
                    if 0 <= step - 3:
                        i = step - 3
                        kind, b, r, t = items[i]
                        pe.wait_ge(flips.emptied, i + 1)
                        v, width, h = (2, 64, 2 * b + r) if kind == "m" else (5, 128, b)
                        cols = slice(h * width, (h + 1) * width)
                        for s in range(t + 1):
                            last = pe.matmul(outs[kind, t][:, cols], self.probs_t[:, i % 2, s * P:(s + 1) * P],
                                             self.qkv2[:, v, s, cols], start=(s == 0), stop=(s == t))
                        last.then_inc(pv_done, 1)

            @block.scalar
            def _(act):
                for job in range(4 * TT):
                    a, t = divmod(job, TT)
                    bank = turned.ready(act, job)
                    act.activation(self.qk2T[:, a, :, t * P:(t + 1) * P], bank[:, :].rearrange("p (b t) -> p b t", b=4),
                                   ACT.Copy).then_inc(turned.emptied, 1)
                for step in range(last_item + 2):
                    if step < last_item:
                        kind, b, r, t = items[step]
                        n = P * (t + 1)
                        for job in range(first_job[step], first_job[step + 1]):
                            act.wait_ge(maxed, job + 1)
                            if job >= 6:
                                i = jobs[job - 6][0]
                                if items[i][0] == "m":
                                    act.wait_ge(flips.filled, i + 1)
                                else:
                                    act.wait_ge(mixed_ready, diff_no[i] + 1)
                            act.activation(self.probs[:, job % 6, 0:n], self.masked_s[:, job % 2, 0:n], ACT.Exp,
                                           bias=self.neg_max[:, job:job + 1],
                                           accum_out=self.sums2[:, job:job + 1]).then_inc(exped, 1)
                    if step >= 2:
                        i = step - 2
                        n = P * (items[i][3] + 1)
                        bank = flips.ready(act, i)
                        if i >= 2:
                            act.wait_ge(pv_done, i - 1)
                        act.activation(self.probs_t[:, i % 2, 0:n], bank[:, 0:n], ACT.Copy).then_inc(flips.emptied, 1)
                act.wait_ge(mean_ready, 1)
                act.activation(self.stat3[:, 4, :], self.stat3[:, 3, :], ACT.Sqrt).then_inc(root_ready, 1)

            @block.vector
            def _(vec):
                for step in range(last_item + 1):
                    if step < last_item:
                        kind, b, r, t = items[step]
                        n = P * (t + 1)
                        for job in range(first_job[step], first_job[step + 1]):
                            bank = scores.ready(vec, job)
                            if job >= 2:
                                vec.wait_ge(exped, job - 1)
                            s = self.masked_s[:, job % 2, 0:n]
                            vec.scalar_tensor_tensor(out=s, in0=bank[:, 0:n], scalar=M_DIM ** -0.5,
                                                     in1=self.future[:, T - n:T], op0=ALU.mult,
                                                     op1=ALU.add).then_inc(scores.emptied, 1)
                            vec.wait_ge(scores.emptied, job + 1)
                            vec.tensor_reduce(self.neg_max[:, job:job + 1], s, AX.X, ALU.max,
                                              negate=True).then_inc(maxed, 1)
                    i = step - 1
                    if i >= 0 and items[i][0] == "d":
                        j0, m = first_job[i], diff_no[i]
                        n = P * (items[i][3] + 1)
                        rec = self.pair_rec[:, 2 * (m % 2):2 * (m % 2) + 2]
                        vec.wait_ge(exped, j0 + 2)
                        order.step(vec.reciprocal(rec, self.sums2[:, j0:j0 + 2]))
                        order.settle(vec)
                        order.step(vec.tensor_tensor(rec[:, 1:2], rec[:, 1:2], self.lt[:, 0:1], ALU.mult))
                        order.settle(vec)
                        if m >= 2:
                            vec.wait_ge(flips.filled, i - 1)
                        out = self.mixed_p[:, m % 2, 0:n]
                        order.step(vec.tensor_scalar(out, self.probs[:, (j0 + 1) % 6, 0:n], rec[:, 1:2], None, ALU.mult))
                        order.settle(vec)
                        vec.scalar_tensor_tensor(out=out, in0=self.probs[:, j0 % 6, 0:n], scalar=rec[:, 0:1], in1=out,
                                                 op0=ALU.mult, op1=ALU.subtract).then_inc(mixed_ready, 1)
                vec.wait_ge(pv_done, len(items))
                heads = "p (h d) -> p h d"
                sums, square, mean, root, rstd, rec = (self.stat3[:, n, :] for n in (0, 1, 3, 4, 5, 6))
                order.step(vec.reciprocal(rec[:, 0:16], self.sums2[:, 0:16]))
                order.settle(vec)
                by_tile = rec[:, 0:16].rearrange("p (h t) -> p t h", t=TT)
                mixed = self.mixed
                for t in range(TT):
                    order.step(vec.tensor_tensor(mixed[:, t, 0:512].rearrange(heads, h=8),
                                                 outs["m", t][:, :].rearrange(heads, h=8),
                                                 by_tile[:, t].unsqueeze(2).broadcast_to([P, 8, 64]), ALU.mult))
                    order.step(vec.tensor_copy(mixed[:, t, 512:1024], outs["d", t][:, :]))
                order.settle(vec)
                for t in range(TT):
                    for part, h, at in ((0, 8, t * 8), (1, 4, 16 + t * 4)):
                        x = mixed[:, t, part * 512:(part + 1) * 512]
                        order.step(vec.tensor_tensor(self.squares2[:, part, :], x, x, ALU.mult))
                        order.settle(vec)
                        order.step(vec.tensor_reduce(square[:, at:at + h], self.squares2[:, part, :].rearrange(heads, h=h),
                                                     AX.X, ALU.add))
                    order.settle(vec)
                order.step(vec.tensor_scalar(mean[:, 0:16], square[:, 0:16], 1.0 / M_DIM, EPS, ALU.mult, ALU.add))
                vec.tensor_scalar(mean[:, 16:24], square[:, 16:24], 1.0 / F_DIM, EPS, ALU.mult, ALU.add).then_inc(mean_ready, 1)
                vec.wait_ge(root_ready, 1)
                order.step(vec.reciprocal(rstd, root))
                order.settle(vec)
                order.step(vec.tensor_scalar(rstd[:, 16:24], rstd[:, 16:24], 1.0 - LAMBDA_INIT, None, ALU.mult))
                order.settle(vec)
                for t in range(TT):
                    for part, h, at, gain in ((0, 8, t * 8, "m_out"), (1, 4, 16 + t * 4, "d_out")):
                        x = mixed[:, t, part * 512:(part + 1) * 512]
                        order.step(vec.tensor_tensor(x.rearrange(heads, h=h), x.rearrange(heads, h=h),
                                                     rstd[:, at:at + h].unsqueeze(2).broadcast_to([P, h, 512 // h]), ALU.mult))
                        order.settle(vec)
                        o, n = ROWS2[gain]
                        order.step(vec.tensor_tensor(x, x, self.rows2[:, o:o + n], ALU.mult))


    def place_peer(self):
        at = self.at
        self.query_t = at(WORK, 2 * P_HEADS, T)
        self.sub_keys = at(WORK + 4096, 2 * P_HEADS, NKEYS)
        self.key_scores = at(WORK + 6144, TT, 2 * P_HEADS, NKEYS)
        self.pairs = at(WORK + 10240, P_HEADS, TOPK * TOPK)
        self.match = at(WORK + 12288, SLOTS, TOPK)
        o = RING
        self.top_s = at(o, TT, 2 * P_HEADS, TOPK)
        self.top_i = at(o + 512, TT, 2 * P_HEADS, TOPK)
        self.top_if = at(o + 1024, TT, 2 * P_HEADS, TOPK)
        self.best_s = at(o + 1536, TT, P_HEADS, TOPK)
        self.best_p = at(o + 1792, TT, P_HEADS, TOPK)
        self.best_half = at(o + 2048, 2, TT, SLOTS)
        self.best_half_f = at(o + 2560, 2, TT, SLOTS)
        self.slot_index = at(o + 3072, 2, TT, SLOTS)
        self.gates = at(o + 3584, TT, SLOTS)
        self.gate_sum = at(o + 3840, 2, TT, P_HEADS)
        self.dense = at(0, NKEYS, T)
        self.down_ring = [at(MORE + 2048 * n, 2, K, P) for n in range(2)]
        self.up_ring = [at(MORE + 4096 + 2048 * n, 2, D) for n in range(2)]
        self.hot_i = at(MORE + 8192, 8, P)
        self.hot_j = at(MORE + 9216, 8, P)
        self.gelu = at(MORE + 10240, 2, T)
        self.gated = at(MORE + 10752, 4, T)

    def peer_queries(self):
        nc, xT = self.nc, self.xT
        first = self.first_half + 8
        queries = Banks(self, "queries", [0, 1, 2, 3])
        scores = Banks(self, "key_scores", [4, 5, 6, 7])
        for c in range(4):
            self.used_by[first + c] = (queries.filled, 4 * (c + 1))
        keys_landed = self.keys_landed = self.sem("sub_keys_landed")
        with nc.Block() as block:
            @block.sync
            def _(sync):
                sync.dma_start(self.sub_keys, self.ins["sub_keys"]).then_inc(keys_landed, 16)
                self.issue(sync, first + 4)

            @block.tensor
            def _(pe):
                for c in range(4):
                    w = self.chunk(pe, first + c)
                    for n in range(4):
                        job = 4 * c + n
                        bank = queries.free(pe, job)
                        for k in range(K):
                            last = pe.matmul(bank[:, 0:T], w[:, k, n * P:(n + 1) * P], xT[:, k, :],
                                             start=(k == 0), stop=(k == K - 1))
                        last.then_inc(queries.filled, 1)
                pe.wait_ge(keys_landed, 16)
                pe.wait_ge(queries.emptied, 16)
                for job in range(4 * TT):
                    t, quad = divmod(job, 4)
                    bank = scores.free(pe, job)
                    for n in range(4):
                        hp = 4 * quad + n
                        last = pe.matmul(bank[:, n * P:(n + 1) * P], self.query_t[:, hp, t * P:(t + 1) * P],
                                         self.sub_keys[:, hp, :], start=True, stop=True)
                    last.then_inc(scores.filled, 1)

            @block.scalar
            def _(act):
                for job in range(16):
                    bank = queries.ready(act, job)
                    act.activation(self.query_t[:, job, :], bank[:, 0:T], ACT.Copy).then_inc(queries.emptied, 1)
                for job in range(4 * TT):
                    t, quad = divmod(job, 4)
                    bank = scores.ready(act, job)
                    act.activation(self.key_scores[:, t, 4 * quad:4 * quad + 4, :],
                                   bank[:, :].rearrange("p (n x) -> p n x", n=4), ACT.Copy).then_inc(scores.emptied, 1)

    def peer_select(self):
        nc = self.nc
        order = self.vec
        exp_in, exp_out, chosen = self.sem("gate_exp_in"), self.sem("gate_exp_out"), self.sem("peer_chosen")
        turned = Banks(self, "slots_turned", [0, 1, 2, 3])
        best_p = self.best_p.bitcast(U32)
        top_i = self.top_i.bitcast(U32)
        with nc.Block() as block:
            @block.vector
            def _(vec):
                def top16(values, top, index, count):
                    for n in range(count):
                        order.step(vec.max(top(n)[:, 0:8], values(n)))
                    order.settle(vec)
                    for n in range(count):
                        order.step(vec.max_index(index(n)[:, 0:8], top(n)[:, 0:8], values(n)))
                    order.settle(vec)
                    for n in range(count):
                        order.step(vec.match_replace(values(n), top(n)[:, 0:8], values(n), -3.0e38))
                    order.settle(vec)
                    for n in range(count):
                        order.step(vec.max(top(n)[:, 8:16], values(n)))
                    order.settle(vec)
                    for n in range(count):
                        order.step(vec.max_index(index(n)[:, 8:16], top(n)[:, 8:16], values(n)))
                    order.settle(vec)

                for t in range(TT):
                    top16(lambda n: self.key_scores[:, t, n, :], lambda n: self.top_s[:, t, n, :],
                          lambda n: top_i[:, t, n, :], 2 * P_HEADS)
                order.step(vec.tensor_copy(self.top_if, top_i))
                for t in range(TT):
                    s = self.top_s[:, t].rearrange("p (h a) s -> p h a s", a=2)
                    pairs = self.pairs.rearrange("p h (x y) -> p h x y", x=TOPK)
                    order.step(vec.tensor_tensor(pairs, s[:, :, 0, :].unsqueeze(3).broadcast_to([P, P_HEADS, TOPK, TOPK]),
                                                 s[:, :, 1, :].unsqueeze(2).broadcast_to([P, P_HEADS, TOPK, TOPK]), ALU.add))
                    order.settle(vec)
                    top16(lambda h: self.pairs[:, h, :], lambda h: self.best_s[:, t, h, :], lambda h: best_p[:, t, h, :],
                          P_HEADS)
                shifted = self.gates.rearrange("p t (h s) -> p t h s", h=P_HEADS)
                for t in range(TT):
                    vec.tensor_tensor(shifted[:, t], self.best_s[:, t],
                                      self.best_s[:, t, :, 0:1].broadcast_to([P, P_HEADS, TOPK]),
                                      ALU.subtract).then_inc(exp_in, 1)
                flat = best_p.rearrange("p t h s -> p t (h s)")
                half = self.best_half.bitcast(U32)
                order.step(vec.tensor_single_scalar(half[:, 0], flat, 4, ALU.logical_shift_right))
                order.step(vec.tensor_single_scalar(half[:, 1], flat, TOPK - 1, ALU.bitwise_and))
                order.settle(vec)
                order.step(vec.tensor_copy(self.best_half_f, half))
                order.settle(vec)
                for a in range(2):
                    for t in range(TT):
                        order.step(vec.tensor_tensor(self.match,
                                                     self.best_half_f[:, a, t, :].unsqueeze(2).broadcast_to([P, SLOTS, TOPK]),
                                                     self.iota[:, 0:TOPK].unsqueeze(1).broadcast_to([P, SLOTS, TOPK]),
                                                     ALU.is_equal))
                        order.settle(vec)
                        keys = self.top_if[:, t].rearrange("p (h a) s -> p h a s", a=2)[:, :, a, :]
                        m4 = self.match.rearrange("p (h s) r -> p h s r", h=P_HEADS)
                        order.step(vec.tensor_tensor(m4, m4, keys.unsqueeze(2).broadcast_to([P, P_HEADS, TOPK, TOPK]),
                                                     ALU.mult))
                        order.settle(vec)
                        order.step(vec.tensor_reduce(self.slot_index[:, a, t, :], self.match, AX.X, ALU.add))
                        order.settle(vec)
                vec.wait_ge(exp_out, 1)
                gates = self.gates.rearrange("p t (h s) -> p t h s", h=P_HEADS)
                for t in range(TT):
                    order.step(vec.tensor_reduce(self.gate_sum[:, 0, t], gates[:, t], AX.X, ALU.add))
                order.settle(vec)
                order.step(vec.reciprocal(self.gate_sum[:, 1], self.gate_sum[:, 0]))
                order.settle(vec)
                for t in range(TT):
                    order.step(vec.tensor_tensor(gates[:, t], gates[:, t],
                                                 self.gate_sum[:, 1, t].unsqueeze(2).broadcast_to([P, P_HEADS, TOPK]),
                                                 ALU.mult))
                order.settle(vec)
                vec.sem_inc(chosen, 1)

            @block.scalar
            def _(act):
                act.wait_ge(exp_in, TT)
                act.activation(self.gates, self.gates, ACT.Exp).then_inc(exp_out, 1)
                for job in range(3):
                    bank = turned.ready(act, job)
                    dst = (self.slot_i, self.slot_j, self.slot_g)[job]
                    act.activation(dst, bank[:, 0:T], ACT.Copy).then_inc(turned.emptied, 1)

            @block.tensor
            def _(pe):
                pe.wait_ge(chosen, 1)
                for job in range(3):
                    bank = turned.free(pe, job)
                    for t in range(TT):
                        src = self.gates[:, t, :] if job == 2 else self.slot_index[:, job, t, :]
                        last = pe.transpose(bank[:, t * P:(t + 1) * P], src, self.ident)
                    last.then_inc(turned.filled, 1)

    def peer_dense(self):
        nc = self.nc
        BODY, QUAD = 16, 4
        hot_ready, product_done, spread = (self.sem("dense_" + n) for n in ("one_hots", "products", "spread"))
        self.down_landed = [self.sem(f"down_ring{n}_landed") for n in range(2)]
        self.up_landed = [self.sem(f"up_ring{n}_landed") for n in range(2)]
        with nc.Block() as block:
            @block.sync
            def _(sync):
                for q in range(2):
                    sync.dma_start(self.down_ring[q], self.ins["peer_down"][q]).then_inc(self.down_landed[q], 16)
                    sync.dma_start(self.up_ring[q], self.ins["peer_up"][q]).then_inc(self.up_landed[q], 16)

            @block.vector
            def _(vec):
                def body(n0, first):
                    for u in range(BODY):
                        if not (first and u < 8):
                            vec.wait_ge(product_done, n0 + (u - 7))

                        def at_token(x):
                            return x[:, u:u + 1] if first else x[:, bass.ds(n0 + u, 1)]

                        vec.tensor_scalar(self.hot_i[:, u % 8, :], self.iota, at_token(self.slot_i), None, ALU.is_equal)
                        vec.tensor_scalar(self.hot_j[:, u % 8, :], self.iota, at_token(self.slot_j), at_token(self.slot_g),
                                          ALU.is_equal, ALU.mult).then_inc(hot_ready, 1)

                body(0, True)
                with vec.Fori(1, T // BODY) as i:
                    body(i * BODY, False)

            @block.tensor
            def _(pe):
                def body(n0, first):
                    for u in range(BODY):
                        quad, n = divmod(u, QUAD)
                        if n == 0 and not first:
                            pe.wait_ge(spread, first_quad(n0) + (quad - 3))
                        pe.wait_ge(hot_ready, n0 + (u + 1))
                        pe.matmul(self.psum[4 + quad][:, n * P:(n + 1) * P], self.hot_i[:, u % 8, :], self.hot_j[:, u % 8, :],
                                  start=True, stop=True).then_inc(product_done, 1)

                def first_quad(n0):
                    return n0 if isinstance(n0, int) else self.quad_of

                body(0, True)
                with pe.Fori(1, T // BODY) as i:
                    self.quad_of = i * (BODY // QUAD)
                    body(i * BODY, False)

            @block.scalar
            def _(act):
                def body(i, first):
                    for quad in range(BODY // QUAD):
                        act.wait_ge(product_done, i * BODY + (quad + 1) * QUAD)
                        src = self.psum[4 + quad][:, :].rearrange("p (t j) -> p j t", t=QUAD)
                        n0 = i * BODY + quad * QUAD
                        dst = self.dense[:, :, n0:n0 + QUAD] if first else self.dense[:, :, bass.ds(n0, QUAD)]
                        act.activation(dst, src, ACT.Copy).then_inc(spread, 1)

                body(0, True)
                with act.Fori(1, T // BODY) as i:
                    body(i, False)

    def peer_experts(self):
        nc, xT = self.nc, self.xT
        acc = [[self.psum[2 * t + n] for n in range(2)] for t in range(TT)]
        hid = [self.psum[4 + n] for n in range(4)]
        hid_ready, gelu_ready, gated_ready, out_done, all_done = (
            self.sem("peer_" + n) for n in ("hidden", "gelu", "gated", "out", "all"))
        zero_again, summed, stored = self.sem("zeros_again"), self.sem("peer_summed"), self.sem("stored")
        pairs = NKEYS // 2
        zeros = self.at(MORE + 11776, 320).bitcast(mybir.dt.bfloat16)
        with nc.Block() as block:
            @block.sync
            def _(sync):
                with sync.Fori(0, pairs // 2 - 1) as i:
                    for u in range(2):
                        q = i * 2 + (2 + u)
                        sync.wait_ge(hid_ready, i * 4 + 2 * (u + 1))
                        sync.dma_start(self.down_ring[u], self.ins["peer_down"][q]).then_inc(self.down_landed[u], 16)
                        sync.wait_ge(out_done, i * 4 + 2 * (u + 1))
                        sync.dma_start(self.up_ring[u], self.ins["peer_up"][q]).then_inc(self.up_landed[u], 16)
                rows = self.out.rearrange("(t p) d -> t p d", p=P)
                for t in range(TT):
                    sync.wait_ge(summed, 2 * (t + 1))
                    sync.dma_start(rows[t], self.h[:, t, :]).then_inc(stored, 16)
                sync.wait_ge(stored, 16 * TT)

            @block.tensor
            def _(pe):
                pe.wait_ge(zero_again, 1)

                def touch(start):
                    for bank in acc[0] + acc[1]:
                        last = pe.matmul(bank[:, :], zeros[0:1, 0:P], zeros[0:1, P:P + 512], start=start, stop=not start,
                                         skip_group_check=True)
                    return last

                def hidden(i, u, first):
                    ring, n = u // 2, u % 2
                    if n == 0:
                        pe.wait_ge(self.down_landed[ring], i * 16 + 16)
                    if not first:
                        pe.wait_ge(gelu_ready, i * 4 + (u - 3))
                    for k in range(K):
                        last = pe.matmul(hid[u][:, 0:T], self.down_ring[ring][:, n, k, :], xT[:, k, :],
                                         start=(k == 0), stop=(k == K - 1))
                    last.then_inc(hid_ready, 1)

                def outputs(i, u):
                    ring, n = u // 2, u % 2
                    if n == 0:
                        pe.wait_ge(self.up_landed[ring], i * 16 + 16)
                    pe.wait_ge(gated_ready, i * 4 + (u + 1))
                    for t in range(TT):
                        for c in range(2):
                            last = pe.matmul(acc[t][c][:, :], self.gated[:, u, t * P:(t + 1) * P],
                                             self.up_ring[ring][:, n, c * 512:(c + 1) * 512], start=False, stop=False,
                                             skip_group_check=True)
                    last.then_inc(out_done, 1)

                touch(True)
                for u in range(4):
                    hidden(0, u, True)
                    if u:
                        outputs(0, u - 1)
                with pe.Fori(1, pairs // 2) as i:
                    hidden(i, 0, False)
                    outputs(i - 1, 3)
                    for u in range(1, 4):
                        hidden(i, u, False)
                        outputs(i, u - 1)
                outputs(pairs // 2 - 1, 3)
                touch(False).then_inc(all_done, 1)

            @block.scalar
            def _(act):
                def body(i, first):
                    for u in range(4):
                        act.wait_ge(hid_ready, i * 4 + (u + 1))
                        if not (first and u < 2):
                            act.wait_ge(gated_ready, i * 4 + (u - 1))
                        act.activation(self.gelu[:, u % 2, :], hid[u][:, 0:T], ACT.Gelu).then_inc(gelu_ready, 1)

                body(0, True)
                with act.Fori(1, pairs // 2) as i:
                    body(i, False)

            @block.vector
            def _(vec):
                vec.memset(zeros, 0.0).then_inc(zero_again, 1)

                def body(i, first):
                    for u in range(4):
                        vec.wait_ge(gelu_ready, i * 4 + (u + 1))
                        if not first:
                            vec.wait_ge(out_done, i * 4 + (u - 3))
                        dense = self.dense[:, u, :] if first else \
                            self.dense[:, bass.ds(i * 4 + u, 1), :].rearrange("p a t -> p (a t)")
                        vec.tensor_tensor(self.gated[:, u, :], self.gelu[:, u % 2, :], dense, ALU.mult).then_inc(gated_ready, 1)

                body(0, True)
                with vec.Fori(1, pairs // 2) as i:
                    body(i, False)
                vec.wait_ge(all_done, 1)
                for t in range(TT):
                    for c in range(2):
                        part = self.h[:, t, c * 512:(c + 1) * 512]
                        vec.tensor_tensor(part, part, acc[t][c][:, :], ALU.add).then_inc(summed, 1)


def build(nc, ins, out):
    with ExitStack() as ctx:
        k = Kernel(nc, ctx, ins, out)
        k.place_first()
        k.rms_to_features("norm1", "norm1", first=True)
        k.project_first()
        k.retention()
        k.rwkv_features()
        k.rwkv_turn()
        k.rwkv_units()
        k.rwkv_scan()
        k.project_out("out1", 8, 10)
        k.end_part()
        k.rms_to_features("norm2", "norm2", scaled_at=MORE)
        k.place_experts()
        k.route_tokens()
        k.experts()
        k.general_experts()
        k.final_norm()
        k.end_part()
        k.place_second()
        k.rms_to_features("norm3", "attn")
        k.project_second()
        k.attention()
        k.project_out("out2", k.first_half + 6, k.first_half + 8 + RING_SLOTS)
        k.rms_to_features("norm4", "ffn")
        k.place_peer()
        k.peer_queries()
        k.peer_select()
        k.peer_dense()
        k.peer_experts()
    return k



def shape_constants():
    import numpy as np
    f = np.float32
    p = np.arange(P)
    chunk = p // CHUNK
    same = chunk[:, None] == chunk[None, :]
    s, t = p[:, None], p[None, :]
    pair = np.stack([same & (s < t), same & (s <= t)], 1)
    mask_a = same & (t < s)
    levels = []
    for n in range(1, 6):
        size = 2 << (n - 1)
        levels.append((s // (2 * size) == t // (2 * size)) & (s // size < t // size))
    two = np.stack([(s // 2 == t // 2) & (t < s), (s // 2 == t // 2) & (s < t)], 1)
    head = (s // 64) == (t // 64)
    ident64 = np.concatenate([np.eye(64), np.eye(64)], 0)
    half = RET_DIM // 2
    inv = f(10000.0) ** (-np.arange(half, dtype=f) / f(half))
    ang = np.arange(T, dtype=f)[:, None] * inv[None, :]
    rope = np.stack([np.cos(ang), np.sin(ang)], 0).reshape(2, TT, P, half).transpose(2, 0, 1, 3)
    const1 = np.concatenate([pair.reshape(P, -1), mask_a, np.stack(levels, 1).reshape(P, -1), two.reshape(P, -1), head,
                             ident64, rope.reshape(P, -1), np.stack([p < 64, p >= 64], 1)], 1).astype(f)
    carry = np.broadcast_to((np.arange(4 * T) % CHUNK != 0).astype(f), (P, 4 * T)).reshape(P, 4, T).copy()
    log_g = np.log(1.0 - np.exp2(-5.0 - np.arange(RET_HEADS)))
    q, k = np.arange(T)[None, :], np.arange(T)[:, None]
    cq, ck, iq, ik = q // CHUNK, k // CHUNK, q % CHUNK, k % CHUNK
    far = (iq + 1.0) + CHUNK * (cq - ck - 1.0) + (CHUNK - 1.0 - ik)
    power = np.where(cq == ck, np.abs(iq - ik), far)
    m = np.where(cq >= ck, np.exp(log_g[:, None, None] * np.maximum(power, 0)), 0.0) * RET_DIM ** -0.5
    ret = np.concatenate([m[:, 0:P, :], m[:, P:T, P:T]], 2).transpose(1, 0, 2).astype(f)
    inv2 = f(1.0) / (f(10000.0) ** (np.arange(0, M_DIM, 2, dtype=f) / f(M_DIM)))
    ang2 = np.arange(T, dtype=f)[:, None] * inv2[None, :]
    rope2 = np.stack([np.cos(ang2), np.sin(ang2)], 0).reshape(2, TT, P, M_DIM // 2).transpose(2, 0, 1, 3)
    future = np.where(np.arange(P)[None, :] > p[:, None], NEG, 0.0)
    return {"ident": np.eye(P, dtype=f), "iota": np.concatenate([np.broadcast_to(np.arange(P), (P, P)), (p % 64)[:, None], s <= t], 1).astype(f),
            "const1": const1, "carry": carry, "ret_decay": np.ascontiguousarray(ret),
            "const2": np.concatenate([rope2.reshape(P, -1), future], 1).astype(f)}


def laid_out(a):
    import numpy as np

    def chunks(w, width=512):
        return np.ascontiguousarray(w.reshape(K, P, -1, width).transpose(2, 1, 0, 3))

    def columns(v):
        return v.reshape(-1, P).T

    def row(v):
        return v.reshape(1, -1)

    w_in = a["w_in"][0]
    lay = {
        "x": a["x"][0],
        "w_in": chunks(w_in[:, 0:3584]),
        "w_in_lora": chunks(w_in[:, 3584:3840], 256)[0],
        "w_out": chunks(a["w_out"][0]),
        "w_in_2": chunks(a["w_in_2"][0]),
        "w_out_2": chunks(a["w_out_2"][0]),
        "peer_query": chunks(a["peer_query_2"][0]),
        "cols": np.concatenate([columns(a[n]) for n in (
            "norm1_gain", "norm2_gain", "attn_norm_2", "ffn_norm_2", "rwkv_mu", "rwkv_w0", "rwkv_a0", "rwkv_k_k",
            "rwkv_k_a", "rwkv_r_k")], 1),
        "lora_up": np.concatenate([np.concatenate([a["rwkv_w_up"][0], a["rwkv_a_up"][0]], 0), a["rwkv_g_up"][0]], 1),
        "rows1": np.concatenate([a["ret_gn_gain"][0], a["rwkv_gn_gain"][0], a["b_route_group"][0], a["b_route_expert"][0]]),
        "rows2": np.concatenate([a["final_norm_gain"], a["q_norm_moba_2"][0], a["k_norm_moba_2"][0],
                                 a["q_norm_diff_2"].reshape(-1), a["k_norm_diff_2"].reshape(-1)]
                                + [a[n][0] for n in ("lambda_q1_2", "lambda_k1_2", "lambda_q2_2", "lambda_k2_2")]
                                + [a["moba_out_gain_2"].reshape(-1), a["diff_out_gain_2"].reshape(-1)]),
        "route": np.concatenate([a["w_route_group"][0], a["w_route_expert"][0]], 1).reshape(K, P, 36).transpose(1, 0, 2),
        "w_gate": a["w_gate"][0].reshape(EXPERTS, K, P, FF).transpose(0, 2, 1, 3),
        "w_up": a["w_up"][0].reshape(EXPERTS, K, P, FF).transpose(0, 2, 1, 3),
        "w_down": a["w_down"][0].reshape(EXPERTS, FT, P, D).transpose(0, 2, 1, 3),
        "sub_keys": a["peer_sub_keys_2"][0].reshape(2 * P_HEADS, NKEYS, P).transpose(2, 0, 1),
        "peer_down": a["peer_down_2"][0].reshape(P, NKEYS // 2, 2, K, P).transpose(1, 4, 2, 3, 0),
        "peer_up": a["peer_up_2"][0].reshape(P, NKEYS // 2, 2, D).transpose(1, 0, 2, 3),
    }
    lay.update(shape_constants())
    return {n: np.ascontiguousarray(v) for n, v in lay.items()}


def kernel(**inputs):
    import numpy as _np
    import concourse.bacc as _bacc
    from concourse.bass_utils import run_bass_kernel_spmd as _run

    arrays = laid_out({n: _np.asarray(v) for n, v in inputs.items()})
    nc = _bacc.Bacc("TRN2", target_bir_lowering=False, num_devices=1)
    ins = {n: nc.dram_tensor(n, v.shape, F32, kind="ExternalInput").ap() for n, v in arrays.items()}
    out = nc.dram_tensor("out", (T, D), F32, kind="ExternalOutput").ap()
    build(nc, ins, out)
    r = _run(nc, [arrays], core_ids=[0])
    return r.results[0]["out"].reshape(1, T, D)
```

```python
from contextlib import ExitStack

import numpy as np

import concourse.bass as bass
from concourse import mybir

F32 = mybir.dt.float32
F32R = mybir.dt.float32r
U32 = mybir.dt.uint32
ALU = mybir.AluOpType
ACT = mybir.ActivationFunctionType
AX = mybir.AxisListType

P = 128
T = 256
TT = T // P
D = 1024
K = D // P
EPS = 1e-6

RET_HEADS, RET_DIM = 4, 128
RW_HEADS, RW_DIM = 8, 64
CHUNK = 64
CHUNKS = T // CHUNK
RET_EPS, RW_EPS = 1e-5, 64e-5
FEATURE_BLOCKS = 14

GROUPS, PER_GROUP = 4, 8
EXPERTS = GROUPS * PER_GROUP
FF = 512
FT = FF // P
PAIRS = EXPERTS // 2
SLOTS_E = 64

M_HEADS, M_DIM = 8, 64
F_HEADS, F_DIM = 4, 128
LAMBDA_INIT = 0.2
NEG = -1e30

P_HEADS = 8
NKEYS = 128
TOPK = 16
SLOTS = P_HEADS * TOPK

COLS = {}
_at = 0
for _name, _n in (("norm1", K), ("norm2", K), ("attn", K), ("ffn", K), ("mu", FEATURE_BLOCKS), ("w0", 4), ("a0", 4),
                  ("k_k", 4), ("k_a", 4), ("r_k", 4)):
    COLS[_name] = (_at, _n)
    _at += _n
N_COLS = _at

ROWS1 = {"ret_gain": (0, 512), "rw_gain": (512, 512), "route_bias": (1024, 36)}
N_ROWS1 = 1060
ROWS2 = {"final": (0, D), "mq": (1024, 64), "mk": (1088, 64), "dq": (1152, 128), "dk": (1280, 128),
         "lambda": (1408, 256), "m_out": (1664, 512), "d_out": (2176, 512)}
N_ROWS2 = 2688

SLOT = 4096
RING = 0
RING_SLOTS = 3
SPARE = RING_SLOTS * SLOT
WORK = 4 * SLOT
MORE = WORK + 16384
KEPT = MORE + 12288
END = 53200


class Order:

    def __init__(self, sem):
        self.sem, self.n = sem, 0

    def step(self, ins):
        ins.then_inc(self.sem, 1)
        self.n += 1
        return ins

    def settle(self, eng):
        eng.wait_ge(self.sem, self.n)


class Banks:

    def __init__(self, kernel, name, banks):
        self.banks = [kernel.psum[b] for b in banks]
        self.filled = kernel.sem(name + "_filled")
        self.emptied = kernel.sem(name + "_emptied")

    def free(self, pe, job):
        if job >= len(self.banks):
            pe.wait_ge(self.emptied, job - len(self.banks) + 1)
        return self.banks[job % len(self.banks)]

    def ready(self, eng, job):
        eng.wait_ge(self.filled, job + 1)
        return self.banks[job % len(self.banks)]


class Kernel:
    def __init__(self, nc, ctx, ins, out):
        self.nc, self.ctx, self.ins, self.out = nc, ctx, ins, out
        self.mem_start = -(-nc.sbuf_base // 32) * 32
        self.mem = ctx.enter_context(nc.sbuf_tensor("mem", [P, END], F32))
        self.psum = [ctx.enter_context(nc.psum_tensor(f"bank{i}", [P, 512], F32)) for i in range(8)]
        self.part_sems = []
        self.vec = Order(self.lasting_sem("vector_order"))
        self.place_kept()
        self.landed = [self.lasting_sem(f"slot{i}_landed") for i in range(6)]
        self.x_landed, self.const_landed = self.lasting_sem("x_landed"), self.lasting_sem("const_landed")
        self.loads = [0] * 6
        self.used_by = {}
        self.issued = 0
        i = self.ins
        self.chunks = [(i["w_in"][c], 512) for c in range(4)] + [(i["w_in_lora"], 256)]
        self.chunks += [(i["w_in"][c], 512) for c in range(4, 7)]
        self.chunks += [(i["w_out"][c], 512) for c in range(2)]
        self.first_half = len(self.chunks)
        self.chunks += [(i["w_in_2"][c], 512) for c in range(6)] + [(i["w_out_2"][c], 512) for c in range(2)]
        self.chunks += [(i["peer_query"][c], 512) for c in range(4)]

    def sem(self, name):
        handle = self.nc.alloc_semaphore(name=name)
        self.part_sems.append(handle)
        return handle

    def lasting_sem(self, name):
        return self.ctx.enter_context(self.nc.semaphore(name))

    def end_part(self):
        self.nc.clear_and_free_semaphores(self.part_sems)
        self.nc.all_engine_barrier()
        self.part_sems = []

    def at(self, off, *shape):
        n = int(np.prod(shape))
        assert off + n <= END, (off, shape)
        ap = self.mem[:, off:off + n]
        if len(shape) == 1:
            return ap
        names = "abcd"[:len(shape)]
        return ap.rearrange(f"p ({' '.join(names)}) -> p {' '.join(names)}",
                            **{x: s for x, s in zip(names[1:], shape[1:])})

    def parts(self, name, off, *shape):
        n = int(np.prod(shape))
        assert off + n <= END, (off, shape)
        ap = self.nc.alloc_sbuf_tensor_at(name, [P, n], F32R, offset=self.mem_start + 4 * off)[:, :]
        if len(shape) == 1:
            return ap
        names = "abcd"[:len(shape)]
        return ap.rearrange(f"p ({' '.join(names)}) -> p {' '.join(names)}",
                            **{x: s for x, s in zip(names[1:], shape[1:])})

    def place_kept(self):
        self.cursor = KEPT

        def keep(*shape):
            ap = self.at(self.cursor, *shape)
            self.cursor += int(np.prod(shape))
            return ap

        self.h = keep(TT, D)
        self.xT = keep(K, T)
        self.ident = keep(P)
        self.iota_all = keep(2 * P + 1)
        self.iota = self.iota_all[:, 0:P]
        self.slot_number = self.iota_all[:, P:P + 1]
        self.up_to = self.iota_all[:, P + 1:]
        self.cols = keep(N_COLS)
        self.small = keep(64)
        self.slot_i = keep(T)
        self.slot_j = keep(T)
        self.slot_g = keep(T)
        self.lt = keep(4)

    def col(self, name):
        o, n = COLS[name]
        return self.cols[:, o:o + n]


    def slot_of(self, c):
        return c % RING_SLOTS

    def issue(self, sync, upto):
        while self.issued < min(upto, len(self.chunks)):
            c = self.issued
            if c >= RING_SLOTS and not self.first_half <= c < self.first_half + RING_SLOTS:
                sync.wait_ge(*self.used_by[c - RING_SLOTS])
            src, n = self.chunks[c]
            s = self.slot_of(c)
            sync.dma_start(self.at(RING + s * SLOT, K, n), src).then_inc(self.landed[s], 16)
            self.loads[s] += 1
            self.issued += 1

    def plan_chunk(self, c):
        s = self.slot_of(c)
        n = sum(1 for b in range(c + 1) if self.slot_of(b) == s)
        if c >= self.first_half:
            n += EXPERTS // 2
        return s, 16 * n

    def chunk(self, pe, c):
        s, value = self.plan_chunk(c)
        pe.wait_ge(self.landed[s], value)
        return self.at(RING + s * SLOT, K, self.chunks[c][1])


    def rms_to_features(self, name, gain, first=False, scaled_at=WORK):
        nc, h, xT, ident = self.nc, self.h, self.xT, self.ident
        scaled = self.at(scaled_at, TT, D)
        ss, ms, root, rstd = (self.small[:, i * 2:i * 2 + 2] for i in range(4))
        squares, mean_ready, root_ready, scaled_ready = (
            self.sem(f"{name}_{x}") for x in ("squares", "mean", "root", "scaled"))
        turned = Banks(self, name + "_turned", [0, 1, 2, 3])
        order = self.vec
        with nc.Block() as block:
            if first:
                @block.sync
                def _(sync):
                    self.load_first(sync)

            @block.scalar
            def _(act):
                if first:
                    act.wait_ge(self.x_landed, 16)
                for t in range(TT):
                    act.activation(scaled[:, t, :], h[:, t, :], ACT.Square, accum_out=ss[:, t:t + 1]).then_inc(squares, 1)
                act.wait_ge(mean_ready, 1)
                act.activation(root, ms, ACT.Sqrt).then_inc(root_ready, 1)

            @block.vector
            def _(vec):
                vec.wait_ge(squares, TT)
                vec.tensor_scalar(ms, ss, 1.0 / D, EPS, ALU.mult, ALU.add).then_inc(mean_ready, 1)
                vec.wait_ge(root_ready, 1)
                order.step(vec.reciprocal(rstd, root))
                order.settle(vec)
                for t in range(TT):
                    vec.tensor_scalar(scaled[:, t, :], h[:, t, :], rstd[:, t:t + 1], None, ALU.mult).then_inc(scaled_ready, 1)
                if first:
                    vec.wait_ge(self.const_landed, 16 * self.n_const)
                g = self.col(gain)
                for job in range(2 * TT):
                    t, half = divmod(job, 2)
                    bank = turned.ready(vec, job)
                    ks = slice(4 * half, 4 * half + 4)
                    vec.tensor_tensor(xT[:, ks, t * P:(t + 1) * P], bank[:, :].rearrange("p (k t) -> p k t", k=4),
                                      g[:, ks].unsqueeze(2).broadcast_to([P, 4, P]), ALU.mult).then_inc(turned.emptied, 1)

            @block.tensor
            def _(pe):
                if first:
                    pe.wait_ge(self.const_landed, 16 * self.n_const)
                for job in range(2 * TT):
                    t, half = divmod(job, 2)
                    pe.wait_ge(scaled_ready, t + 1)
                    bank = turned.free(pe, job)
                    for k in range(4):
                        last = pe.transpose(bank[:, k * P:(k + 1) * P],
                                            scaled[:, t, (4 * half + k) * P:(4 * half + k + 1) * P], ident)
                    last.then_inc(turned.filled, 1)

    def load_first(self, sync):
        i = self.ins
        sync.dma_start(self.h, i["x"].rearrange("(t p) d -> p t d", p=P)).then_inc(self.x_landed, 16)
        for dst, src in self.consts:
            sync.dma_start(dst, src).then_inc(self.const_landed, 16)
        self.issue(sync, RING_SLOTS)


    def place_first(self):
        i = self.ins
        at = self.at
        o = WORK
        self.qkvg = at(o, 4, TT, 512)
        self.qkT = at(o + 4096, 2, RET_HEADS, T)
        self.rotated = at(o + 6144, 2, TT, 512)
        self.ret_decay = at(o + 8192, RET_HEADS, 384)
        self.ret_p = at(o + 9728, 2, 384)
        self.tok_b = at(o, TT, RW_HEADS, RW_DIM)
        self.tok_k = at(o + 1024, TT, RW_HEADS, RW_DIM)
        self.tok_au = at(o + 2048, TT, RW_HEADS, P)
        self.wz = at(o + 4096, TT, RW_HEADS, P)
        self.phi = at(o + 6144, CHUNKS, 4, 2, RW_DIM)
        self.q_hat = at(o + 8192, 4, T)
        self.y_local = at(o + 9216, TT, RW_HEADS, RW_DIM)
        o = WORK + 10496
        self.mixed = at(o, TT, D)
        self.tok_v = at(o + 2048, TT, RW_HEADS, RW_DIM)
        self.gate = at(o + 3072, TT, 512)
        self.tmp = at(o + 4096, 4, T)
        assert o + 5120 <= MORE
        self.lora = at(SPARE, 2, T)
        self.carry = at(SPARE + 512, 4, T)
        self.raw = at(SPARE + 1536, 4, T + 1)
        self.rows1 = at(SPARE + 2564, N_ROWS1)
        f = [at(MORE + 1024 * n, 4, T) for n in range(12)]
        self.f_r, self.f_k, self.f_v, self.f_l, self.f_a, self.f_kk, self.f_k2 = f[:7]
        self.f_b, self.f_kt, self.f_x = f[7], f[8], f[11]
        self.f_ar = at(MORE + 1024 * 9, 4, TT, 2, P)
        self.up_wa = at(MORE + 1024 * 9, 512)
        self.up_g = at(MORE + 1024 * 9 + 512, 512)
        free = RING + SLOT
        self.u_k = [at(MORE, 4, 256), at(MORE + 4608, 4, 256)]
        self.u_b = [at(MORE + 1024, 4, 256), at(MORE + 5632, 4, 256)]
        self.u_n = [at(MORE + 2048, 2, 4, P), at(free, 2, 4, P)]
        self.u_x = [at(MORE + 3072, 4, P), at(MORE + 6656, 4, P)]
        self.u_xt = [at(MORE + 3584, 4, P), at(free + 1024, 4, P)]
        self.u_p = [at(MORE + 4096, 4, P), at(free + 1536, 4, P)]
        c = self.cursor
        self.mask_pair = at(c, 2, P)
        self.mask_a = at(c + 256, P)
        self.mask_level = at(c + 384, 5, P)
        self.mask_two = at(c + 1024, 2, P)
        self.ones_head = at(c + 1280, P)
        self.ident64 = at(c + 1408, RW_DIM)
        self.rope1 = at(c + 1472, 2, TT, RET_DIM // 2)
        self.pair_ones = at(c + 1728, 2)
        self.decay_end = at(c + 1730, 4, CHUNKS)
        self.state = at(c + 1746, 4, RW_DIM)
        self.bonus = at(c + 2002, TT, RW_HEADS)
        self.stat = at(c + 2018, 12, 16)
        assert c + 2210 <= END, c + 2210
        self.consts = [(self.cols, i["cols"]), (self.ident, i["ident"]), (self.iota_all, i["iota"]),
                       (at(c, 1730), i["const1"]), (self.carry, i["carry"]),
                       (self.ret_decay, i["ret_decay"]), (at(MORE + 1024 * 9, 1024), i["lora_up"]),
                       (self.rows1, i["rows1"].partition_broadcast(P))]
        self.n_const = len(self.consts)

    def project_first(self):
        nc, xT = self.nc, self.xT
        tokens = Banks(self, "project_tokens", [0, 1, 2, 3])
        features = Banks(self, "project_features", [4, 5, 6, 7])
        raw_used, pad_ready = self.sem("raw_used"), self.sem("raw_pad_ready")
        targets = [self.lora[:, 0, :], self.lora[:, 1, :]]
        targets += [f[:, b, :] for f in (self.f_r, self.f_k, self.f_v) for b in range(4)]
        mu_of = [12, 13] + list(range(12))
        order = self.vec
        diff = self.tmp[:, 0, :]
        for c in range(4):
            self.used_by[c] = (tokens.filled, TT * (c + 1))
        for c in range(4, 8):
            self.used_by[c] = (features.filled, 2 + 4 * (c - 4))
        with nc.Block() as block:
            @block.sync
            def _(sync):
                self.issue(sync, 8 + 2)

            @block.tensor
            def _(pe):
                for c in range(4):
                    w = self.chunk(pe, c)
                    for t in range(TT):
                        bank = tokens.free(pe, c * TT + t)
                        for k in range(K):
                            last = pe.matmul(bank[:, :], xT[:, k, t * P:(t + 1) * P], w[:, k, :],
                                             start=(k == 0), stop=(k == K - 1))
                        last.then_inc(tokens.filled, 1)
                job = 0
                for c in range(4, 8):
                    w = self.chunk(pe, c)
                    for b in range(2 if c == 4 else 4):
                        bank = features.free(pe, job)
                        for k in range(K):
                            last = pe.matmul(bank[:, 0:T], w[:, k, b * P:(b + 1) * P], xT[:, k, :],
                                             start=(k == 0), stop=(k == K - 1))
                        last.then_inc(features.filled, 1)
                        job += 1

            @block.scalar
            def _(act):
                for job in range(4 * TT):
                    bank = tokens.ready(act, job)
                    act.activation(self.qkvg[:, job // TT, job % TT, :], bank[:, :], ACT.Copy).then_inc(tokens.emptied, 1)
                act.wait_ge(pad_ready, 1)
                for job in range(FEATURE_BLOCKS):
                    bank = features.ready(act, job)
                    if job >= 4:
                        act.wait_ge(raw_used, job - 3)
                    act.activation(self.raw[:, job % 4, 1:T + 1], bank[:, 0:T], ACT.Copy).then_inc(features.emptied, 1)

            @block.vector
            def _(vec):
                vec.memset(self.raw[:, :, 0:1], 0.0).then_inc(pad_ready, 1)
                cos, sin = self.rope1[:, 0], self.rope1[:, 1]
                half = RET_DIM // 2
                a = self.tmp[:, 1, :].rearrange("p (h d) -> p h d", h=4)
                b = self.tmp[:, 2, :].rearrange("p (h d) -> p h d", h=4)
                for n in range(2 * TT):
                    which, t = divmod(n, TT)
                    vec.wait_ge(tokens.emptied, n + 1)
                    x = self.qkvg[:, which, t, :].rearrange("p (h d) -> p h d", h=4)
                    y = self.rotated[:, which, t, :].rearrange("p (h d) -> p h d", h=4)
                    c4 = cos[:, t, :].unsqueeze(1).broadcast_to([P, 4, half])
                    s4 = sin[:, t, :].unsqueeze(1).broadcast_to([P, 4, half])
                    x1, x2 = x[:, :, 0:half], x[:, :, half:]
                    for out, u, v, op in ((y[:, :, 0:half], c4, s4, ALU.subtract), (y[:, :, half:], s4, c4, ALU.add)):
                        order.step(vec.tensor_tensor(a, x1, u, ALU.mult))
                        order.step(vec.tensor_tensor(b, x2, v, ALU.mult))
                        order.settle(vec)
                        order.step(vec.tensor_tensor(out, a, b, op))
                        order.settle(vec)
                mu = self.col("mu")
                for job in range(FEATURE_BLOCKS):
                    vec.wait_ge(features.emptied, job + 1)
                    now, before = self.raw[:, job % 4, 1:T + 1], self.raw[:, job % 4, 0:T]
                    order.step(vec.tensor_tensor(diff, before, now, ALU.subtract))
                    order.settle(vec)
                    vec.scalar_tensor_tensor(out=targets[job], in0=diff, scalar=mu[:, mu_of[job]:mu_of[job] + 1],
                                             in1=now, op0=ALU.mult, op1=ALU.add).then_inc(raw_used, 1)
                    vec.wait_ge(raw_used, job + 1)

    def retention(self):
        nc, ident = self.nc, self.ident
        turned = Banks(self, "ret_turned", [0, 1])
        scores = Banks(self, "ret_scores", [2, 3])
        outs = [self.psum[4], self.psum[5]]
        p_ready, outs_ready, gate_ready = self.sem("ret_p_ready"), self.sem("ret_outs_ready"), self.sem("ret_gate_ready")
        var_ready, root_ready = self.sem("ret_var_ready"), self.sem("ret_root_ready")
        scores.emptied = p_ready
        v = self.qkvg[:, 2]
        order = self.vec
        with nc.Block() as block:
            @block.tensor
            def _(pe):
                for job in range(2 * TT):
                    which, t = divmod(job, TT)
                    bank = turned.free(pe, job)
                    for h in range(RET_HEADS):
                        last = pe.transpose(bank[:, h * P:(h + 1) * P], self.rotated[:, which, t, h * P:(h + 1) * P], ident)
                    last.then_inc(turned.filled, 1)
                pe.wait_ge(turned.emptied, 2 * TT)
                for h in range(RET_HEADS + 1):
                    if h < RET_HEADS:
                        bank = scores.free(pe, h)
                        pe.matmul(bank[:, 0:T], self.qkT[:, 1, h, 0:P], self.qkT[:, 0, h, :], start=True, stop=True)
                        pe.matmul(bank[:, T:T + P], self.qkT[:, 1, h, P:T], self.qkT[:, 0, h, P:T],
                                  start=True, stop=True).then_inc(scores.filled, 1)
                    if h > 0:
                        g = h - 1
                        pe.wait_ge(p_ready, g + 1)
                        p = self.ret_p[:, g % 2]
                        hs = slice(g * P, (g + 1) * P)
                        pe.matmul(outs[0][:, hs], p[:, 0:P], v[:, 0, hs], start=True, stop=True)
                        pe.matmul(outs[1][:, hs], p[:, P:T], v[:, 0, hs], start=True, stop=False)
                        pe.matmul(outs[1][:, hs], p[:, T:T + P], v[:, 1, hs], start=False, stop=True).then_inc(outs_ready, 1)

            @block.scalar
            def _(act):
                for job in range(2 * TT):
                    which, t = divmod(job, TT)
                    bank = turned.ready(act, job)
                    act.activation(self.qkT[:, which, :, t * P:(t + 1) * P],
                                   bank[:, :].rearrange("p (h t) -> p h t", h=4), ACT.Copy).then_inc(turned.emptied, 1)
                for t in range(TT):
                    act.activation(self.rotated[:, 0, t, :], self.qkvg[:, 3, t, :], ACT.Silu).then_inc(gate_ready, 1)
                act.wait_ge(var_ready, 1)
                act.activation(self.stat[:, 4, 0:8], self.stat[:, 3, 0:8], ACT.Sqrt).then_inc(root_ready, 1)

            @block.vector
            def _(vec):
                for h in range(RET_HEADS):
                    bank = scores.ready(vec, h)
                    if h >= 2:
                        vec.wait_ge(outs_ready, h - 1)
                    vec.tensor_tensor(self.ret_p[:, h % 2], bank[:, 0:384], self.ret_decay[:, h], ALU.mult).then_inc(p_ready, 1)
                vec.wait_ge(outs_ready, RET_HEADS)
                total, mean, square, var, root, rstd = (self.stat[:, n, 0:8].rearrange("p (t h) -> p t h", t=2) for n in
                                                        (0, 1, 2, 3, 4, 5))
                centred = self.rotated[:, 1]
                sq = self.mixed[:, :, 512:1024]
                heads = "p (h d) -> p h d"

                def over(x):
                    return x.unsqueeze(2).broadcast_to([P, RET_HEADS, RET_DIM])

                for t in range(TT):
                    order.step(vec.tensor_reduce(total[:, t], outs[t][:, :].rearrange(heads, h=4), AX.X, ALU.add))
                order.settle(vec)
                order.step(vec.tensor_scalar(mean, total, 1.0 / RET_DIM, None, ALU.mult))
                order.settle(vec)
                for t in range(TT):
                    order.step(vec.tensor_tensor(centred[:, t].rearrange(heads, h=4), outs[t][:, :].rearrange(heads, h=4),
                                                 over(mean[:, t]), ALU.subtract))
                order.settle(vec)
                for t in range(TT):
                    order.step(vec.tensor_tensor(sq[:, t], centred[:, t], centred[:, t], ALU.mult))
                order.settle(vec)
                for t in range(TT):
                    order.step(vec.tensor_reduce(square[:, t], sq[:, t].rearrange(heads, h=4), AX.X, ALU.add))
                order.settle(vec)
                vec.tensor_scalar(var, square, 1.0 / RET_DIM, RET_EPS, ALU.mult, ALU.add).then_inc(var_ready, 1)
                vec.wait_ge(root_ready, 1)
                order.step(vec.reciprocal(rstd, root))
                order.settle(vec)
                o, n = ROWS1["ret_gain"]
                gain = self.rows1[:, o:o + n]
                vec.wait_ge(gate_ready, TT)
                for t in range(TT):
                    order.step(vec.tensor_tensor(sq[:, t].rearrange(heads, h=4), centred[:, t].rearrange(heads, h=4),
                                                 over(rstd[:, t]), ALU.mult))
                    order.step(vec.tensor_tensor(self.rotated[:, 0, t], self.rotated[:, 0, t], gain, ALU.mult))
                order.settle(vec)
                for t in range(TT):
                    order.step(vec.tensor_tensor(self.mixed[:, t, 0:512], sq[:, t], self.rotated[:, 0, t], ALU.mult))

    def rwkv_features(self):
        nc = self.nc
        lora_w, lora_a = Banks(self, "lora_w", [0, 1]), Banks(self, "lora_a", [2, 3])
        lora_g = Banks(self, "lora_g", [4, 5])
        norms = Banks(self, "kk_norms", [6, 7])
        bonus = Banks(self, "bonus", [0])
        squares_ready, bonus_in = self.sem("kk_squares_ready"), self.sem("bonus_in_ready")
        bounded, roots = self.sem("kk_bounded"), self.sem("kk_roots")
        tanh_ready, sig_ready = self.sem("tanh_ready"), self.sem("gate_sigmoid_ready")
        sums, excl, expd = self.sem("decay_sums_ready"), self.sem("decay_before_ready"), self.sem("decay_exps")
        order = self.vec
        f_r, f_k, f_l, f_a, f_kk, f_k2, f_x, tmp = (self.f_r, self.f_k, self.f_l, self.f_a, self.f_kk, self.f_k2,
                                                    self.f_x, self.tmp)

        def wide(name):
            return self.col(name).unsqueeze(2).broadcast_to([P, 4, T])

        with nc.Block() as block:
            @block.tensor
            def _(pe):
                pe.wait_ge(tanh_ready, 1)
                for stage, rows in ((lora_w, slice(0, 64)), (lora_a, slice(64, 128))):
                    for pair in range(2):
                        bank = stage.free(pe, pair)
                        for n in range(2):
                            b = 2 * pair + n
                            last = pe.matmul(bank[:, n * T:(n + 1) * T], self.up_wa[rows, b * P:(b + 1) * P],
                                             self.lora[rows, 0, :], start=True, stop=True)
                        last.then_inc(stage.filled, 1)
                pe.wait_ge(sig_ready, 1)
                for t in range(TT):
                    bank = lora_g.free(pe, t)
                    pe.matmul(bank[:, :], self.lora[:, 1, t * P:(t + 1) * P], self.up_g, start=True,
                              stop=True).then_inc(lora_g.filled, 1)
                pe.wait_ge(squares_ready, 1)
                for pair in range(2):
                    bank = norms.free(pe, pair)
                    pe.matmul(bank[:, :], self.ones_head, f_x[:, 2 * pair:2 * pair + 2, :], start=True,
                              stop=True).then_inc(norms.filled, 1)
                pe.wait_ge(bonus_in, 1)
                pe.wait_ge(lora_w.emptied, 2)
                bank = bonus.free(pe, 0)
                for t in range(TT):
                    for b in range(4):
                        last = pe.matmul(bank[:, t * 8 + 2 * b:t * 8 + 2 * b + 2], f_k[:, b, t * P:(t + 1) * P],
                                         self.pair_ones, start=True, stop=True)
                last.then_inc(bonus.filled, 1)

            @block.scalar
            def _(act):
                act.activation(self.lora[0:64, 0, :], self.lora[0:64, 0, :], ACT.Tanh).then_inc(tanh_ready, 1)
                act.activation(self.lora[:, 1, :], self.lora[:, 1, :], ACT.Sigmoid).then_inc(sig_ready, 1)
                for stage, dst, bias in ((lora_w, f_l, "w0"), (lora_a, f_a, "a0")):
                    for pair in range(2):
                        bank = stage.ready(act, pair)
                        for n in range(2):
                            b = 2 * pair + n
                            last = act.activation(dst[:, b, :], bank[:, n * T:(n + 1) * T], ACT.Sigmoid,
                                                  bias=self.col(bias)[:, b:b + 1])
                        last.then_inc(stage.emptied, 1)
                for t in range(TT):
                    bank = lora_g.ready(act, t)
                    act.activation(self.gate[:, t, :], bank[:, :], ACT.Copy).then_inc(lora_g.emptied, 1)
                act.wait_ge(bounded, 2)
                act.activation(f_x, tmp, ACT.Sqrt).then_inc(roots, 1)
                act.wait_ge(sums, 1)
                act.wait_ge(excl, 1)
                act.activation(f_l, f_l, ACT.Exp).then_inc(expd, 1)
                act.activation(tmp, f_x, ACT.Exp, scale=-1.0).then_inc(expd, 1)
                act.wait_ge(expd, 2)
                act.activation(f_x, f_x, ACT.Exp).then_inc(expd, 1)

            @block.vector
            def _(vec):
                order.step(vec.tensor_tensor(f_kk, f_k, wide("k_k"), ALU.mult))
                order.settle(vec)
                vec.tensor_tensor(f_x, f_kk, f_kk, ALU.mult).then_inc(squares_ready, 1)
                for pair in range(2):
                    bank = norms.ready(vec, pair)
                    vec.tensor_scalar(tmp[:, 2 * pair:2 * pair + 2, :].rearrange("p b t -> p (b t)"), bank[:, :], 1e-24,
                                      None, ALU.max).then_inc(bounded, 1)
                vec.wait_ge(roots, 1)
                order.step(vec.reciprocal(tmp, f_x))
                order.settle(vec)
                order.step(vec.tensor_tensor(f_kk, f_kk, tmp, ALU.mult))
                vec.wait_ge(lora_a.emptied, 2)
                order.settle(vec)
                order.step(vec.scalar_tensor_tensor(out=tmp, in0=f_a, scalar=1.0, in1=wide("k_a"), op0=ALU.subtract,
                                                    op1=ALU.mult))
                order.settle(vec)
                order.step(vec.scalar_tensor_tensor(out=f_k2, in0=tmp, scalar=1.0, in1=f_k, op0=ALU.add, op1=ALU.mult))
                order.settle(vec)
                order.step(vec.tensor_tensor(f_k, f_r, f_k2, ALU.mult))
                order.step(vec.tensor_tensor(f_a, f_a, f_kk, ALU.mult))
                order.settle(vec)
                vec.tensor_tensor(f_k, f_k, wide("r_k"), ALU.mult).then_inc(bonus_in, 1)
                order.step(vec.tensor_scalar(f_l, f_l, -float(np.exp(-0.5)), None, ALU.mult))
                order.settle(vec)
                flat = "p b t -> p (b t)"
                vec.tensor_tensor_scan(f_x.rearrange(flat), self.carry.rearrange(flat), f_l.rearrange(flat), 0.0,
                                       ALU.mult, ALU.add).then_inc(sums, 1)
                vec.wait_ge(sums, 1)
                vec.tensor_tensor(f_l, f_x, f_l, ALU.subtract).then_inc(excl, 1)
                vec.wait_ge(expd, 1)
                vec.wait_ge(lora_g.emptied, TT)
                pairs = "p b t a x -> p (b t) a x"
                ar = self.f_ar.rearrange(pairs)

                def tiles(x):
                    return x.rearrange("p b (t x) -> p (b t) x", t=TT)

                order.step(vec.scalar_tensor_tensor(out=ar[:, :, 0, :], in0=tiles(f_kk), scalar=-1.0, in1=tiles(f_l),
                                                    op0=ALU.mult, op1=ALU.mult))
                vec.wait_ge(expd, 2)
                order.step(vec.tensor_tensor(self.f_b, f_a, tmp, ALU.mult))
                order.step(vec.tensor_tensor(self.f_kt, f_k2, tmp, ALU.mult))
                vec.wait_ge(expd, 3)
                order.step(vec.tensor_tensor(ar[:, :, 1, :], tiles(f_r), tiles(f_x), ALU.mult))
                order.step(vec.tensor_copy(self.decay_end, f_x[:, :, CHUNK - 1::CHUNK]))
                bank = bonus.ready(vec, 0)
                order.step(vec.tensor_copy(self.bonus, bank[:, 0:16].rearrange("p (t h) -> p t h", t=2)))

    def rwkv_turn(self):
        nc, ident = self.nc, self.ident
        turned = Banks(self, "rwkv_turned", [0, 1, 2, 3])
        with nc.Block() as block:
            sources = [lambda b, t: self.f_v[:, b, t * P:(t + 1) * P], lambda b, t: self.f_ar[:, b, t, 0, :],
                       lambda b, t: self.f_b[:, b, t * P:(t + 1) * P], lambda b, t: self.f_kt[:, b, t * P:(t + 1) * P]]
            targets = [self.tok_v, self.tok_au[:, :, :, 0:RW_DIM], self.tok_b, self.tok_k]

            @block.tensor
            def _(pe):
                for job in range(4 * TT):
                    which, t = divmod(job, TT)
                    bank = turned.free(pe, job)
                    for b in range(4):
                        last = pe.transpose(bank[:, b * P:(b + 1) * P], sources[which](b, t), ident)
                    last.then_inc(turned.filled, 1)

            @block.scalar
            def _(act):
                for job in range(4 * TT):
                    which, t = divmod(job, TT)
                    bank = turned.ready(act, job)
                    act.activation(targets[which][:, t], bank[:, :].rearrange("p (h d) -> p h d", h=8),
                                   ACT.Copy).then_inc(turned.emptied, 1)

    def rwkv_units(self):
        nc = self.nc
        SETS = range(2)
        LEVELS = 5

        def of_sets(name, banks):
            return [Banks(self, f"unit_{name}{s}", [banks[s]]) for s in SETS]

        scores = Banks(self, "unit_scores", [6, 7])
        level_p, level_xt, level_x = of_sets("p", [0, 1]), of_sets("xt", [2, 3]), of_sets("x", [4, 5])
        u_in, wz_in, q_in, y_in = of_sets("u", [0, 1]), of_sets("wz", [4, 5]), of_sets("q", [0, 1]), of_sets("y", [2, 3])
        phi_in = [Banks(self, f"unit_phi{s}", [4 + s, 6 + s]) for s in SETS]
        masked = self.sem("unit_masked")
        level_masks = [self.sem(f"unit_level_masks{s}") for s in SETS]
        x_ready = [self.sem(f"unit_x_first{s}") for s in SETS]
        scores.emptied = masked
        order = self.vec

        def heads_of(bank, width):
            return bank.rearrange("p (n s) -> p n s", s=width)

        with nc.Block() as block:
            def rows(h):
                return slice(64 * (h % 2), 64 * (h % 2) + 64)

            @block.tensor
            def _(pe):
                def score(t, s):
                    cols = slice(t * P, (t + 1) * P)
                    for part in range(6):
                        kind, parity = divmod(part, 2)
                        bank = scores.free(pe, 12 * t + 6 * s + part)
                        for n in range(2):
                            h = 4 * s + parity + 2 * n
                            b, r = h // 2, rows(h)
                            if kind < 2:
                                left = (self.f_kt, self.f_b)[kind]
                                last = pe.matmul(bank[:, n * T:(n + 1) * T], left[r, b, cols],
                                                 self.f_ar[r, b, t].rearrange("p a x -> p (a x)"), start=True, stop=True)
                            else:
                                last = pe.matmul(bank[:, n * P:(n + 1) * P], self.f_ar[r, b, t, 0, :],
                                                 self.f_b[r, b, cols], start=True, stop=True)
                        last.then_inc(scores.filled, 1)

                def level_first(t, s, level):
                    done = t * LEVELS + level
                    pe.wait_ge(level_masks[s], done + 1)
                    if level == 0:
                        pe.wait_ge(x_ready[s], 2 * (t + 1))
                    else:
                        pe.wait_ge(level_x[s].emptied, done - t)
                    bank = level_p[s].free(pe, done)
                    for n in range(4):
                        last = pe.matmul(bank[:, n * P:(n + 1) * P], self.u_n[s][:, done % 2, n, :], self.u_x[s][:, n, :],
                                         start=True, stop=True)
                    last.then_inc(level_p[s].filled, 1)

                def level_second(t, s, level):
                    done = t * LEVELS + level
                    pe.wait_ge(level_p[s].emptied, done + 1)
                    bank = level_xt[s].free(pe, done)
                    for n in range(4):
                        last = pe.matmul(bank[:, n * P:(n + 1) * P], self.u_p[s][:, n, :], self.u_xt[s][:, n, :],
                                         start=True, stop=True)
                    last.then_inc(level_xt[s].filled, 1)
                    if level < LEVELS - 1:
                        bank = level_x[s].free(pe, done - t)
                        for n in range(4):
                            last = pe.matmul(bank[:, n * P:(n + 1) * P], self.u_xt[s][:, n, :], self.u_p[s][:, n, :],
                                             start=True, stop=True)
                        last.then_inc(level_x[s].filled, 1)

                def products_u(t, s):
                    bank = u_in[s].free(pe, t)
                    for n in range(4):
                        last = pe.matmul(bank[:, n * 64:(n + 1) * 64], self.u_k[s][:, n, 0:P], self.tok_v[:, t, 4 * s + n, :],
                                         start=True, stop=True)
                    last.then_inc(u_in[s].filled, 1)

                def products_wz(t, s):
                    pe.wait_ge(level_xt[s].emptied, LEVELS * (t + 1))
                    pe.wait_ge(u_in[s].emptied, t + 1)
                    bank = wz_in[s].free(pe, t)
                    for n in range(4):
                        last = pe.matmul(bank[:, n * P:(n + 1) * P], self.u_xt[s][:, n, :], self.tok_au[:, t, 4 * s + n, :],
                                         start=True, stop=True)
                    last.then_inc(wz_in[s].filled, 1)

                def products_out(t, s):
                    pe.wait_ge(wz_in[s].emptied, t + 1)
                    bank = q_in[s].free(pe, t)
                    for n in range(4):
                        h = 4 * s + n
                        last = pe.matmul(bank[rows(h), (n // 2) * P:(n // 2 + 1) * P], self.wz[:, t, h, 0:64],
                                         self.u_b[s][:, n, P:2 * P], start=True, stop=True)
                    last.then_inc(q_in[s].filled, 1)
                    bank = y_in[s].free(pe, t)
                    for n in range(4):
                        h = 4 * s + n
                        pe.matmul(bank[:, n * 64:(n + 1) * 64], self.u_k[s][:, n, P:2 * P], self.tok_v[:, t, h, :],
                                  start=True, stop=False)
                        last = pe.matmul(bank[:, n * 64:(n + 1) * 64], self.u_b[s][:, n, P:2 * P], self.wz[:, t, h, 64:P],
                                         start=False, stop=True)
                    last.then_inc(y_in[s].filled, 1)
                    for c in range(2):
                        bank = phi_in[s].free(pe, 2 * t + c)
                        r = slice(64 * c, 64 * c + 64)
                        for n in range(4):
                            h = 4 * s + n
                            out = bank[rows(h), (n // 2) * P:(n // 2 + 1) * P]
                            pe.matmul(out[:, 0:64], self.wz[r, t, h, 0:64], self.tok_b[r, t, h, :], start=True, stop=True)
                            pe.matmul(out[:, 64:P], self.tok_b[r, t, h, :], self.wz[r, t, h, 64:P], start=True, stop=False)
                            last = pe.matmul(out[:, 64:P], self.tok_k[r, t, h, :], self.tok_v[r, t, h, :],
                                             start=False, stop=True)
                        last.then_inc(phi_in[s].filled, 1)

                for t in range(TT):
                    for s in SETS:
                        if t > 0:
                            for other in SETS:
                                pe.wait_ge(phi_in[other].emptied, 2 * t)
                            pe.wait_ge(q_in[s].emptied, t)
                            pe.wait_ge(y_in[s].emptied, t)
                        score(t, s)
                    for level in range(LEVELS):
                        for s in SETS:
                            level_first(t, s, level)
                        for s in SETS:
                            level_second(t, s, level)
                    for stage in (products_u, products_wz, products_out):
                        for s in SETS:
                            stage(t, s)

            @block.scalar
            def _(act):
                for t in range(TT):
                    for level in range(LEVELS):
                        for s in SETS:
                            bank = level_p[s].ready(act, t * LEVELS + level)
                            act.activation(self.u_p[s], heads_of(bank[:, :], P), ACT.Copy).then_inc(level_p[s].emptied, 1)
                    for s in SETS:
                        bank = u_in[s].ready(act, t)
                        act.activation(self.tok_au[:, t, 4 * s:4 * s + 4, 64:P], heads_of(bank[:, 0:T], 64),
                                       ACT.Copy).then_inc(u_in[s].emptied, 1)
                    for s in SETS:
                        bank = wz_in[s].ready(act, t)
                        act.activation(self.wz[:, t, 4 * s:4 * s + 4, :], heads_of(bank[:, :], P),
                                       ACT.Copy).then_inc(wz_in[s].emptied, 1)
                    for s in SETS:
                        bank = y_in[s].ready(act, t)
                        act.activation(self.y_local[:, t, 4 * s:4 * s + 4, :], heads_of(bank[:, 0:T], 64),
                                       ACT.Copy).then_inc(y_in[s].emptied, 1)

            @block.gpsimd
            def _(pool):
                for t in range(TT):
                    for level in range(LEVELS):
                        for s in SETS:
                            if level == 0:
                                pool.wait_ge(masked, 12 * t + 6 * (s + 1))
                            if t * LEVELS + level >= 2:
                                pool.wait_ge(level_p[s].filled, t * LEVELS + level - 1)
                            pool.tensor_tensor(self.u_n[s][:, (t * LEVELS + level) % 2], self.u_b[s][:, :, 0:P],
                                               self.mask_level[:, level, :].unsqueeze(1).broadcast_to([P, 4, P]),
                                               ALU.mult).then_inc(level_masks[s], 1)

            @block.vector
            def _(vec):
                def mask_scores(t, s):
                    for part in range(6):
                        kind, parity = divmod(part, 2)
                        bank = scores.ready(vec, 12 * t + 6 * s + part)
                        if kind < 2:
                            dst = (self.u_k[s], self.u_b[s])[kind][:, parity::2, :]
                            mask = self.mask_pair.rearrange("p a x -> p (a x)").unsqueeze(1).broadcast_to([P, 2, T])
                            src = heads_of(bank[:, :], T)
                        else:
                            dst = self.u_x[s][:, parity::2, :]
                            mask = self.mask_two[:, 0, :].unsqueeze(1).broadcast_to([P, 2, P])
                            src = heads_of(bank[:, 0:T], P)
                        vec.tensor_tensor(dst, src, mask, ALU.mult).then_inc(masked, 1)
                    vec.wait_ge(masked, 12 * t + 6 * (s + 1))
                    order.step(vec.tensor_tensor(self.u_xt[s], self.u_b[s][:, :, 0:P],
                                                 self.mask_two[:, 1, :].unsqueeze(1).broadcast_to([P, 4, P]), ALU.mult))
                    order.settle(vec)
                    for x in (self.u_x[s], self.u_xt[s]):
                        vec.tensor_tensor(x, x, self.ident.unsqueeze(1).broadcast_to([P, 4, P]),
                                          ALU.add).then_inc(x_ready[s], 1)
                    vec.wait_ge(x_ready[s], 2 * (t + 1))

                def add_level(t, s, level):
                    done = t * LEVELS + level
                    bank = level_xt[s].ready(vec, done)
                    if level < LEVELS - 1:
                        level_x[s].ready(vec, done - t)
                    vec.tensor_tensor(self.u_xt[s], self.u_xt[s], heads_of(bank[:, :], P),
                                      ALU.add).then_inc(level_xt[s].emptied, 1)
                    if level < LEVELS - 1:
                        bank = level_x[s].ready(vec, done - t)
                        vec.tensor_tensor(self.u_x[s], self.u_x[s], heads_of(bank[:, :], P),
                                          ALU.add).then_inc(level_x[s].emptied, 1)
                        vec.wait_ge(level_x[s].emptied, done - t + 1)

                def finish(t, s):
                    b0 = 2 * s
                    bank = q_in[s].ready(vec, t)
                    vec.tensor_tensor(self.q_hat[:, b0:b0 + 2, t * P:(t + 1) * P], heads_of(bank[:, 0:T], P),
                                      self.f_ar[:, b0:b0 + 2, t, 1, :], ALU.add).then_inc(q_in[s].emptied, 1)
                    for c in range(2):
                        bank = phi_in[s].ready(vec, 2 * t + c)
                        src = bank[:, 0:T].rearrange("p (n a x) -> p n a x", n=2, a=2)
                        dst = self.phi[:, 2 * t + c, b0:b0 + 2]
                        order.step(vec.tensor_copy(dst[:, :, 1, :], src[:, :, 1, :]))
                        vec.tensor_tensor(dst[:, :, 0, :], src[:, :, 0, :],
                                          self.ident64.unsqueeze(1).broadcast_to([P, 2, 64]),
                                          ALU.add).then_inc(phi_in[s].emptied, 1)

                for t in range(TT):
                    for s in SETS:
                        mask_scores(t, s)
                    for level in range(LEVELS):
                        for s in SETS:
                            add_level(t, s, level)
                    for s in SETS:
                        finish(t, s)

    def rwkv_scan(self):
        nc = self.nc
        cross = [[self.psum[2 * t + half] for half in range(2)] for t in range(TT)]
        nexts = [self.psum[4], self.psum[5]]
        cross_ready, next_ready = self.sem("cross_ready"), self.sem("next_state_ready")
        state_ready, var_ready, root_ready = (self.sem(n) for n in ("state_ready", "rwkv_var_ready", "rwkv_root_ready"))
        order = self.vec
        state = self.state
        with nc.Block() as block:
            @block.tensor
            def _(pe):
                for c in range(CHUNKS):
                    t, half_t = divmod(c, 2)
                    pe.wait_ge(state_ready, 2 * c + 1)
                    for par in range(2):
                        r = slice(64 * par, 64 * par + 64)
                        for b in range(4):
                            last = pe.matmul(cross[t][par][64 * half_t:64 * half_t + 64, b * 64:(b + 1) * 64],
                                             self.q_hat[r, b, c * CHUNK:(c + 1) * CHUNK], state[r, b, :],
                                             start=True, stop=True)
                    last.then_inc(cross_ready, 1)
                    if c < CHUNKS - 1:
                        for par in range(2):
                            r = slice(64 * par, 64 * par + 64)
                            for b in range(4):
                                last = pe.matmul(nexts[par][r, b * 64:(b + 1) * 64], self.phi[r, c, b, 0, :],
                                                 state[r, b, :], start=True, stop=True)
                        last.then_inc(next_ready, 1)

            @block.scalar
            def _(act):
                act.wait_ge(var_ready, 1)
                act.activation(self.stat[:, 4, :], self.stat[:, 3, :], ACT.Sqrt).then_inc(root_ready, 1)

            @block.vector
            def _(vec):
                vec.memset(state, 0.0).then_inc(state_ready, 1)
                for c in range(CHUNKS - 1):
                    vec.wait_ge(next_ready, c + 1)
                    vec.wait_ge(cross_ready, c + 1)
                    for par in range(2):
                        r = slice(64 * par, 64 * par + 64)
                        order.step(vec.tensor_tensor(state[r], nexts[par][r, 0:T].rearrange("p (b x) -> p b x", b=4),
                                                     self.phi[r, c, :, 1, :], ALU.add))
                    order.settle(vec)
                    for par in range(2):
                        r = slice(64 * par, 64 * par + 64)
                        vec.tensor_tensor(state[r], state[r],
                                          self.decay_end[r, :, c:c + 1].broadcast_to([64, 4, RW_DIM]),
                                          ALU.mult).then_inc(state_ready, 1)
                total, mean, square, var, root, rstd = (self.stat[:, n, :].rearrange("p (t h) -> p t h", t=2)
                                                        for n in range(6))
                y, wide = self.y_local, self.tmp.rearrange("p (t n) s -> p t (n s)", t=2)
                heads = "p (h d) -> p h d"

                def over(x):
                    return x.unsqueeze(2).broadcast_to([P, RW_HEADS, RW_DIM])

                vec.wait_ge(cross_ready, CHUNKS)
                for t in range(TT):
                    for par in range(2):
                        order.step(vec.tensor_tensor(y[:, t, par::2, :], y[:, t, par::2, :],
                                                     cross[t][par][:, 0:T].rearrange(heads, h=4), ALU.add))
                order.settle(vec)
                for t in range(TT):
                    order.step(vec.tensor_reduce(total[:, t], y[:, t], AX.X, ALU.add))
                order.settle(vec)
                order.step(vec.tensor_scalar(mean, total, 1.0 / RW_DIM, None, ALU.mult))
                order.settle(vec)
                for t in range(TT):
                    order.step(vec.tensor_tensor(y[:, t], y[:, t], over(mean[:, t]), ALU.subtract))
                order.settle(vec)
                for t in range(TT):
                    order.step(vec.tensor_tensor(wide[:, t].rearrange(heads, h=8), y[:, t], y[:, t], ALU.mult))
                order.settle(vec)
                for t in range(TT):
                    order.step(vec.tensor_reduce(square[:, t], wide[:, t].rearrange(heads, h=8), AX.X, ALU.add))
                order.settle(vec)
                vec.tensor_scalar(var, square, 1.0 / RW_DIM, RW_EPS, ALU.mult, ALU.add).then_inc(var_ready, 1)
                for t in range(TT):
                    order.step(vec.tensor_tensor(wide[:, t].rearrange(heads, h=8), self.tok_v[:, t], over(self.bonus[:, t]),
                                                 ALU.mult))
                vec.wait_ge(root_ready, 1)
                order.step(vec.reciprocal(rstd, root))
                order.settle(vec)
                for t in range(TT):
                    order.step(vec.tensor_tensor(y[:, t], y[:, t], over(rstd[:, t]), ALU.mult))
                order.settle(vec)
                o, n = ROWS1["rw_gain"]
                for t in range(TT):
                    order.step(vec.tensor_tensor(y[:, t], y[:, t], self.rows1[:, o:o + n].rearrange(heads, h=8), ALU.mult))
                order.settle(vec)
                for t in range(TT):
                    order.step(vec.tensor_tensor(y[:, t], y[:, t], wide[:, t].rearrange(heads, h=8), ALU.add))
                order.settle(vec)
                for t in range(TT):
                    order.step(vec.tensor_tensor(self.mixed[:, t, 512:1024].rearrange(heads, h=8), y[:, t],
                                                 self.gate[:, t].rearrange(heads, h=8), ALU.mult))

    def project_out(self, name, first_chunk, upto):
        nc, h, xT, ident, mixed = self.nc, self.h, self.xT, self.ident, self.mixed
        turned = Banks(self, name + "_turned", [0, 1])
        sums = Banks(self, name + "_sums", [4, 5])
        for c in range(2):
            self.used_by[first_chunk + c] = (sums.filled, TT * (c + 1))
        with nc.Block() as block:
            @block.sync
            def _(sync):
                self.issue(sync, upto)

            @block.tensor
            def _(pe):
                for job in range(2 * TT):
                    t, half = divmod(job, 2)
                    bank = turned.free(pe, job)
                    for k in range(4):
                        last = pe.transpose(bank[:, k * P:(k + 1) * P], mixed[:, t, (4 * half + k) * P:(4 * half + k + 1) * P],
                                            ident)
                    last.then_inc(turned.filled, 1)
                pe.wait_ge(turned.emptied, 2 * TT)
                for c in range(2):
                    w = self.chunk(pe, first_chunk + c)
                    for t in range(TT):
                        bank = sums.free(pe, c * TT + t)
                        for k in range(K):
                            last = pe.matmul(bank[:, :], xT[:, k, t * P:(t + 1) * P], w[:, k, :],
                                             start=(k == 0), stop=(k == K - 1))
                        last.then_inc(sums.filled, 1)

            @block.scalar
            def _(act):
                for job in range(2 * TT):
                    t, half = divmod(job, 2)
                    bank = turned.ready(act, job)
                    act.activation(xT[:, 4 * half:4 * half + 4, t * P:(t + 1) * P],
                                   bank[:, :].rearrange("p (k t) -> p k t", k=4), ACT.Copy).then_inc(turned.emptied, 1)

            @block.vector
            def _(vec):
                for job in range(2 * TT):
                    c, t = divmod(job, TT)
                    bank = sums.ready(vec, job)
                    part = h[:, t, c * 512:(c + 1) * 512]
                    vec.tensor_tensor(part, part, bank[:, :], ALU.add).then_inc(sums.emptied, 1)


    def place_experts(self):
        at = self.at
        self.pick = at(WORK + 8192, TT, PAIRS, P)
        self.put = at(WORK + 12288, PAIRS, T)
        self.normed = at(MORE, TT, D)
        self.gathered = at(MORE + 2048, K, P)
        self.gate_up = at(MORE + 3072, 2, 512)
        self.hid = at(MORE + 4096, 2, FT, SLOTS_E)
        self.slot_out = at(MORE + 4608, D)
        self.silu_s = at(MORE + 5632, FT, SLOTS_E)
        self.sum_t = at(MORE + 2048, K, T)
        self.expert_w = at(WORK + 8192, EXPERTS, T)
        self.hidden = at(MORE, 2, FT, T)
        self.silu = at(MORE + 2048, 2, T)
        self.rows2 = at(MORE + 5900, N_ROWS2)
        self.const2 = at(MORE + 5900 + N_ROWS2, 256)
        o = MORE + 5900 + N_ROWS2 + 256
        self.route = at(o, K, 36)
        self.logits = at(o + 288, TT, 36)
        self.small_moe = at(o + 360, 29, 64)
        self.weights_t = at(o + 2216, 2, T)
        self.zeros = at(o + 2728, 320).bitcast(mybir.dt.bfloat16)
        self.ones = at(o + 3048, P)
        self.over_flag = at(o + 3176, 1)
        self.iota8 = self.iota[:, 0:8]
        self.weights_left = self.at(o + 3177, TT, EXPERTS)
        self.route_bias = self.at(o + 3241, GROUPS + EXPERTS)

    def route_tokens(self):
        nc = self.nc
        s = self.small_moe
        route_landed = self.sem("route_landed")
        logits_ready, exp_in, exp_out, pair_in, pair_out = (
            self.sem("route_" + n) for n in ("logits", "exp_in", "exp_out", "pair_in", "pair_out"))
        weights_ready, weights_t_ready = self.sem("route_weights"), self.sem("route_weights_t")
        zeros_ready = self.zeros_ready = self.sem("zeros_ready")
        turned_ready = self.sem("route_turned")
        spread_w, spread_n = Banks(self, "spread_weights", [4, 5]), Banks(self, "spread_slots", [6, 7])
        counts_ready, chosen_ready = self.sem("slot_counts"), self.sem("chosen_experts")
        order = self.vec
        logits = self.logits

        def tile_view(n, width):
            return s[:, n, 0:TT * width].rearrange("p (t x) -> p t x", t=TT)

        gmax, shifted, gexp, gsum, gprob = tile_view(0, 1), tile_view(1, 4), tile_view(2, 4), tile_view(3, 1), tile_view(4, 1)
        equal, count, chosen, ones = tile_view(5, 4), tile_view(6, 4), tile_view(7, 4), s[:, 8, 0:4]
        product, inside, best = tile_view(9, 32), tile_view(10, 8), tile_view(11, 8)
        index, index_f = tile_view(12, 8).bitcast(U32), tile_view(13, 8)
        diff, ratio, denom, w0, w1 = (tile_view(14 + n, 1) for n in range(5))
        pick0, pick1 = tile_view(19, 8), tile_view(20, 8)
        weights, weights_all = tile_view(21, 32), self.weights_left
        mask, running, slot, fits = (tile_view(22 + n, 32) for n in range(4))
        picked, biggest = tile_view(26, 8), s[:, 27, 0:1]
        with nc.Block() as block:
            @block.sync
            def _(sync):
                sync.dma_start(self.route, self.ins["route"]).then_inc(route_landed, 16)
                o, n = ROWS1["route_bias"]
                sync.dma_start(self.route_bias, self.ins["rows1"][o:o + n].partition_broadcast(P)).then_inc(route_landed, 16)
                for e in range(2):
                    for n in range(3):
                        self.load_weight(sync, 0, e, n)

            @block.tensor
            def _(pe):
                pe.wait_ge(route_landed, 32)
                for t in range(TT):
                    for k in range(K):
                        last = pe.matmul(self.psum[t][:, 0:36], self.xT[:, k, t * P:(t + 1) * P], self.route[:, k, :],
                                         start=(k == 0), stop=(k == K - 1))
                    last.then_inc(logits_ready, 1)
                pe.wait_ge(chosen_ready, TT)
                pe.matmul(self.psum[3][:, 0:32], self.up_to, mask[:, 0, :], start=True, stop=True)
                pe.matmul(self.psum[3][:, 32:64], self.up_to, mask[:, 1, :], start=True, stop=False)
                pe.matmul(self.psum[3][:, 32:64], self.ones, mask[:, 0, :], start=False, stop=True)
                pe.matmul(self.psum[3][:, 64:96], self.ones, mask[:, 0, :], start=True, stop=False)
                pe.matmul(self.psum[3][:, 64:96], self.ones, mask[:, 1, :], start=False,
                          stop=True).then_inc(counts_ready, 1)
                pe.wait_ge(weights_ready, TT)
                for which, src in enumerate((weights, slot)):
                    for t in range(TT):
                        last = pe.transpose(self.psum[2][0:EXPERTS, (which * TT + t) * P:(which * TT + t + 1) * P],
                                            src[:, t, :], self.ident)
                last.then_inc(turned_ready, 1)
                pe.wait_ge(weights_t_ready, 1)
                for job in range(PAIRS // 2):
                    for which, stage in enumerate((spread_w, spread_n)):
                        bank = stage.free(pe, job)
                        for n in range(2):
                            q = 2 * job + n
                            for parity in range(2):
                                e = 2 * q + parity
                                row = self.ident[0:EXPERTS, e:e + 1].broadcast_to([EXPERTS, 64])
                                last = pe.matmul(bank[64 * parity:64 * parity + 64, n * T:(n + 1) * T], row,
                                                 self.weights_t[0:EXPERTS, which, :], start=True, stop=True)
                        last.then_inc(stage.filled, 1)

            @block.scalar
            def _(act):
                act.wait_ge(exp_in, 1)
                act.activation(gexp, shifted, ACT.Exp).then_inc(exp_out, 1)
                act.wait_ge(pair_in, 1)
                act.activation(ratio, diff, ACT.Exp).then_inc(pair_out, 1)
                for job in range(PAIRS // 2):
                    bank = spread_w.ready(act, job)
                    act.activation(self.put[:, 2 * job:2 * job + 2, :], bank[:, :].rearrange("p (n t) -> p n t", n=2),
                                   ACT.Copy).then_inc(spread_w.emptied, 1)

            @block.vector
            def _(vec):
                vec.memset(self.zeros, 0.0).then_inc(zeros_ready, 1)
                order.step(vec.memset(ones, 1.0))
                order.step(vec.memset(self.ones, 1.0))
                for t in range(TT):
                    vec.wait_ge(logits_ready, t + 1)
                    order.step(vec.tensor_tensor(logits[:, t, :], self.psum[t][:, 0:36], self.route_bias, ALU.add))
                order.settle(vec)
                order.step(vec.tensor_reduce(gmax, logits[:, :, 0:GROUPS], AX.X, ALU.max))
                order.settle(vec)
                wide = gmax.broadcast_to([P, TT, GROUPS])
                order.step(vec.tensor_tensor(equal, logits[:, :, 0:GROUPS], wide, ALU.is_equal))
                vec.tensor_tensor(shifted, logits[:, :, 0:GROUPS], wide, ALU.subtract).then_inc(exp_in, 1)
                order.settle(vec)
                for t in range(TT):
                    order.step(vec.tensor_tensor_scan(count[:, t], ones, equal[:, t], 0.0, ALU.mult, ALU.add))
                order.settle(vec)
                order.step(vec.scalar_tensor_tensor(out=chosen, in0=count, scalar=1.0, in1=equal, op0=ALU.is_equal,
                                                    op1=ALU.mult))
                vec.wait_ge(exp_out, 1)
                order.step(vec.tensor_reduce(gsum, gexp, AX.X, ALU.add))
                order.settle(vec)
                order.step(vec.reciprocal(gprob, gsum))
                for t in range(TT):
                    order.step(vec.tensor_tensor(product[:, t].rearrange("p (g e) -> p g e", g=GROUPS),
                                                 logits[:, t, GROUPS:36].rearrange("p (g e) -> p g e", g=GROUPS),
                                                 chosen[:, t].unsqueeze(2).broadcast_to([P, GROUPS, PER_GROUP]), ALU.mult))
                order.settle(vec)
                for t in range(TT):
                    order.step(vec.tensor_reduce(inside[:, t], product[:, t].rearrange("p (g e) -> p e g", g=GROUPS),
                                                 AX.X, ALU.add))
                order.settle(vec)
                for t in range(TT):
                    order.step(vec.max(best[:, t], inside[:, t]))
                order.settle(vec)
                for t in range(TT):
                    order.step(vec.max_index(index[:, t], best[:, t], inside[:, t]))
                vec.tensor_tensor(diff, best[:, :, 1:2], best[:, :, 0:1], ALU.subtract).then_inc(pair_in, 1)
                order.settle(vec)
                order.step(vec.tensor_copy(index_f, index))
                order.settle(vec)
                for t in range(TT):
                    for n, pick in enumerate((pick0, picked)):
                        order.step(vec.tensor_scalar(pick[:, t], self.iota8, index_f[:, t, n:n + 1], None, ALU.is_equal))
                order.settle(vec)
                order.step(vec.tensor_tensor(picked, picked, pick0, ALU.add))
                order.settle(vec)
                for t in range(TT):
                    vec.tensor_tensor(mask[:, t].rearrange("p (g e) -> p g e", g=GROUPS),
                                      picked[:, t].unsqueeze(1).broadcast_to([P, GROUPS, PER_GROUP]),
                                      chosen[:, t].unsqueeze(2).broadcast_to([P, GROUPS, PER_GROUP]),
                                      ALU.mult).then_inc(chosen_ready, 1)
                vec.wait_ge(pair_out, 1)
                order.step(vec.tensor_scalar(denom, ratio, 1.0, None, ALU.add))
                order.settle(vec)
                order.step(vec.reciprocal(w0, denom))
                order.settle(vec)
                order.step(vec.tensor_tensor(w0, w0, gprob, ALU.mult))
                order.settle(vec)
                order.step(vec.tensor_tensor(w1, w0, ratio, ALU.mult))
                order.settle(vec)
                for t in range(TT):
                    for n, (pick, w) in enumerate(((pick0, w0), (pick1, w1))):
                        order.step(vec.tensor_scalar(pick[:, t], self.iota8, index_f[:, t, n:n + 1], w[:, t], ALU.is_equal,
                                                     ALU.mult))
                order.settle(vec)
                order.step(vec.tensor_tensor(pick0, pick0, pick1, ALU.add))
                order.settle(vec)
                for t in range(TT):
                    order.step(vec.tensor_tensor(weights_all[:, t].rearrange("p (g e) -> p g e", g=GROUPS),
                                                 pick0[:, t].unsqueeze(1).broadcast_to([P, GROUPS, PER_GROUP]),
                                                 chosen[:, t].unsqueeze(2).broadcast_to([P, GROUPS, PER_GROUP]), ALU.mult))
                vec.wait_ge(counts_ready, 1)
                running_in = self.psum[3][:, 0:64].rearrange("p (t e) -> p t e", t=TT)
                order.step(vec.tensor_tensor(running, running_in, mask, ALU.mult))
                order.step(vec.tensor_reduce(biggest, self.psum[3][:, 64:96], AX.X, ALU.max))
                order.settle(vec)
                order.step(vec.tensor_scalar(self.over_flag.bitcast(mybir.dt.int32), biggest, float(SLOTS_E), None, ALU.is_gt))
                order.step(vec.tensor_scalar(fits, running, float(SLOTS_E), None, ALU.is_le))
                order.step(vec.tensor_scalar(slot, running, -1.0, None, ALU.add))
                order.settle(vec)
                vec.tensor_tensor(weights, weights_all, fits, ALU.mult).then_inc(weights_ready, 1)
                vec.wait_ge(weights_ready, 1)
                vec.tensor_tensor(weights_all, weights_all, weights, ALU.subtract).then_inc(weights_ready, 1)
                for t in range(TT):
                    for q in range(PAIRS):
                        for n in range(2):
                            order.step(vec.tensor_scalar(self.pick[:, t, q, n * 64:(n + 1) * 64], self.iota[:, 0:64],
                                                         slot[:, t, 2 * q + n:2 * q + n + 1], None, ALU.is_equal))
                vec.wait_ge(turned_ready, 1)
                vec.tensor_copy(self.weights_t[0:EXPERTS].rearrange("p a t -> p (a t)"),
                                self.psum[2][0:EXPERTS, :]).then_inc(weights_t_ready, 1)
                for job in range(PAIRS // 2):
                    vec.wait_ge(spread_w.emptied, job + 1)
                    bank = spread_n.ready(vec, job)
                    put = self.put[:, 2 * job:2 * job + 2, :].rearrange("p n t -> p (n t)")
                    vec.scalar_tensor_tensor(out=put, in0=bank[:, :], scalar=self.slot_number, in1=put,
                                             op0=ALU.is_equal, op1=ALU.mult).then_inc(spread_n.emptied, 1)

    def load_weight(self, sync, q, parity, n):
        s = 3 * parity + n
        dst = self.at(RING + s * SLOT, FT, D) if n == 2 else self.at(RING + s * SLOT, K, FF)
        src = self.ins[("w_gate", "w_up", "w_down")[n]][q * 2 + parity]
        sync.dma_start(dst, src).then_inc(self.landed[s], 16)

    def experts(self):
        nc, ident = self.nc, self.ident
        acc = [self.psum[n] for n in range(4)]
        wide = [self.psum[4], self.psum[5]]
        gu_bank, turn_bank = self.psum[6], self.psum[7]
        base = [self.loads[s] for s in range(6)]
        for s in range(6):
            self.loads[s] += PAIRS
        (gather_ready, gather_used, gu_ready, gu_used, turn_ready, silu_ready, hid_ready, down_ready, down_used,
         scatter_done, all_done, sum_ready) = (self.sem("pair_" + n) for n in (
            "gathered", "gathered_used", "gate_up", "gate_up_used", "turned", "silu", "hidden", "down", "down_used",
            "scattered", "all", "sum_copied"))
        back = Banks(self, "sum_turned", [4, 5])
        rows_landed = self.rows2_landed = self.sem("rows2_landed")
        gain = self.col("norm2")
        order = self.vec

        def slot(s, *shape):
            return self.at(RING + s * SLOT, *shape)

        with nc.Block() as block:
            @block.sync
            def _(sync):
                sync.dma_start(self.rows2, self.ins["rows2"].partition_broadcast(P)).then_inc(rows_landed, 16)
                sync.dma_start(self.const2, self.ins["const2"]).then_inc(rows_landed, 16)
                def reload(q, parity, n):
                    sync.wait_ge(*((down_ready, q) if n == 2 else (gu_ready, q * 2 + (parity - 1))))
                    self.load_weight(sync, q, parity, n)

                reload(1, 0, 0)
                reload(1, 0, 1)
                with sync.Fori(1, PAIRS - 1) as q:
                    reload(q, 1, 0)
                    reload(q, 1, 1)
                    reload(q + 1, 0, 0)
                    reload(q + 1, 0, 1)
                    reload(q, 0, 2)
                    reload(q, 1, 2)
                for n in range(3):
                    reload(PAIRS - 1, 1, n)
                reload(PAIRS - 1, 0, 2)

            @block.tensor
            def _(pe):
                pe.wait_ge(self.zeros_ready, 1)

                def touch(start):
                    for bank in acc:
                        last = pe.matmul(bank[:, :], self.zeros[0:1, 0:P], self.zeros[0:1, P:P + 512], start=start,
                                         stop=not start, skip_group_check=True)
                    return last

                def one(x, q):
                    return x[:, q, :] if isinstance(q, int) else x[:, bass.ds(q, 1), :].rearrange("p a x -> p (a x)")

                def gather(q, first=False):
                    if not first:
                        pe.wait_ge(down_used, q * 2 - 2)
                    for k in range(K):
                        for t in range(TT):
                            last = pe.matmul(wide[k // 4][:, (k % 4) * P:(k % 4 + 1) * P],
                                             self.normed[:, t, k * P:(k + 1) * P], one(self.pick[:, t], q),
                                             start=(t == 0), stop=(t == TT - 1))
                    last.then_inc(gather_ready, 1)

                def gate_up(q, parity):
                    for n in range(2):
                        pe.wait_ge(self.landed[3 * parity + n], (q + 1) * 16 + 16 * base[3 * parity + n])
                    pe.wait_ge(gather_used, q * 2 + 2)
                    if not (isinstance(q, int) and q == 0 and parity == 0):
                        pe.wait_ge(gu_used, q * 2 + parity)
                    for k in range(K):
                        for n in range(2):
                            last = pe.matmul(gu_bank[64 * n:64 * n + 64, :], self.gathered[:, k, 64 * parity:64 * parity + 64],
                                             slot(3 * parity + n, K, FF)[:, k, :], start=(k == 0), stop=(k == K - 1))
                    last.then_inc(gu_ready, 1)

                def turn(q, parity):
                    pe.wait_ge(gu_used, q * 2 + (parity + 1))
                    if not (isinstance(q, int) and q == 0 and parity == 0):
                        pe.wait_ge(hid_ready, q * 2 + parity)
                    for f in range(FT):
                        last = pe.transpose(turn_bank[:, f * P:(f + 1) * P], self.gate_up[:, parity, f * P:(f + 1) * P], ident)
                    last.then_inc(turn_ready, 1)

                def down(q):
                    for parity in range(2):
                        pe.wait_ge(self.landed[3 * parity + 2], (q + 1) * 16 + 16 * base[3 * parity + 2])
                    pe.wait_ge(hid_ready, q * 2 + 2)
                    pe.wait_ge(gather_used, q * 2 + 2)
                    for n in range(2):
                        for f in range(FT):
                            for parity in range(2):
                                last = pe.matmul(wide[n][64 * parity:64 * parity + 64, :], self.hid[:, parity, f, :],
                                                 slot(3 * parity + 2, FT, D)[:, f, n * 512:(n + 1) * 512],
                                                 start=(f == 0), stop=(f == FT - 1))
                    last.then_inc(down_ready, 1)

                def scatter(q):
                    pe.wait_ge(down_used, q * 2 + 2)
                    for k in range(K):
                        last = pe.matmul(acc[k // 2][:, (k % 2) * T:(k % 2 + 1) * T], self.slot_out[:, k * P:(k + 1) * P],
                                         one(self.put, q), start=False, stop=False, skip_group_check=True)
                    last.then_inc(scatter_done, 1)

                touch(True)
                gather(0, first=True)
                gate_up(0, 0)
                gate_up(0, 1)
                turn(0, 0)
                gather(1, first=True)
                turn(0, 1)
                with pe.Fori(1, PAIRS - 1) as q:
                    gate_up(q, 0)
                    down(q - 1)
                    gate_up(q, 1)
                    turn(q, 0)
                    gather(q + 1)
                    scatter(q - 1)
                    turn(q, 1)
                last_q = PAIRS - 1
                gate_up(last_q, 0)
                down(last_q - 1)
                gate_up(last_q, 1)
                turn(last_q, 0)
                scatter(last_q - 1)
                turn(last_q, 1)
                down(last_q)
                scatter(last_q)
                touch(False).then_inc(all_done, 1)
                pe.wait_ge(sum_ready, 4)
                for job in range(2 * TT):
                    t, half = divmod(job, 2)
                    bank = back.free(pe, job)
                    for k in range(4):
                        last = pe.transpose(bank[:, k * P:(k + 1) * P], self.sum_t[:, 4 * half + k, t * P:(t + 1) * P], ident)
                    last.then_inc(back.filled, 1)

            @block.scalar
            def _(act):
                def copy_gate_up(q, parity):
                    act.wait_ge(gu_ready, q * 2 + (parity + 1))
                    act.activation(self.gate_up[:, parity, :], gu_bank[:, :], ACT.Copy).then_inc(gu_used, 1)

                def silu(q, parity):
                    act.wait_ge(turn_ready, q * 2 + (parity + 1))
                    turned = turn_bank[:, :].rearrange("p (f x) -> p f x", f=FT)
                    act.activation(self.silu_s, turned[:, :, 0:64], ACT.Silu).then_inc(silu_ready, 1)

                def copy_out(q):
                    act.wait_ge(down_ready, q + 1)
                    for n in range(2):
                        act.activation(self.slot_out[:, n * 512:(n + 1) * 512], wide[n][:, :],
                                       ACT.Copy).then_inc(down_used, 1)

                for parity in range(2):
                    copy_gate_up(0, parity)
                silu(0, 0)
                silu(0, 1)
                with act.Fori(1, PAIRS) as q:
                    copy_gate_up(q, 0)
                    copy_out(q - 1)
                    copy_gate_up(q, 1)
                    silu(q, 0)
                    silu(q, 1)
                copy_out(PAIRS - 1)
                act.wait_ge(all_done, 1)
                for n in range(4):
                    act.activation(self.sum_t[:, 2 * n:2 * n + 2, :], acc[n][:, :].rearrange("p (k t) -> p k t", k=2),
                                   ACT.Copy).then_inc(sum_ready, 1)

            @block.vector
            def _(vec):
                def copy_gathered(q):
                    vec.wait_ge(gather_ready, q + 1)
                    for n in range(2):
                        vec.tensor_tensor(self.gathered[:, 4 * n:4 * n + 4, :], wide[n][:, :].rearrange("p (k s) -> p k s", k=4),
                                          gain[:, 4 * n:4 * n + 4].unsqueeze(2).broadcast_to([P, 4, P]),
                                          ALU.mult).then_inc(gather_used, 1)

                def multiply(q, parity):
                    vec.wait_ge(silu_ready, q * 2 + (parity + 1))
                    turned = turn_bank[:, :].rearrange("p (f x) -> p f x", f=FT)
                    vec.tensor_tensor(self.hid[:, parity], self.silu_s, turned[:, :, 64:P], ALU.mult).then_inc(hid_ready, 1)

                copy_gathered(0)
                with vec.Fori(0, PAIRS - 1) as q:
                    multiply(q, 0)
                    copy_gathered(q + 1)
                    multiply(q, 1)
                multiply(PAIRS - 1, 0)
                multiply(PAIRS - 1, 1)
                for job in range(2 * TT):
                    t, half = divmod(job, 2)
                    bank = back.ready(vec, job)
                    part = self.h[:, t, half * 512:(half + 1) * 512]
                    vec.tensor_tensor(part, part, bank[:, :], ALU.add).then_inc(back.emptied, 1)

    def general_experts(self):
        nc = self.nc
        beyond = nc.values_load(self.over_flag[0:1, 0:1].bitcast(U32), min_val=0, max_val=1)
        with nc.If(beyond != 0):
            nc.all_engine_barrier()
            self.spread_left()
            self.experts_over_all()

    def spread_left(self):
        nc = self.nc
        turned_ready, weights_t_ready = self.sem("left_turned"), self.sem("left_weights_t")
        spread = Banks(self, "spread_left", [4, 5, 6, 7])
        with nc.Block() as block:
            @block.tensor
            def _(pe):
                for t in range(TT):
                    last = pe.transpose(self.psum[2][0:EXPERTS, t * P:(t + 1) * P], self.weights_left[:, t, :], self.ident)
                last.then_inc(turned_ready, 1)
                pe.wait_ge(weights_t_ready, 1)
                for job in range(EXPERTS // 2):
                    bank = spread.free(pe, job)
                    for n in range(2):
                        e = 2 * job + n
                        last = pe.matmul(bank[:, n * T:(n + 1) * T],
                                         self.ident[0:EXPERTS, e:e + 1].broadcast_to([EXPERTS, P]),
                                         self.weights_t[0:EXPERTS, 0, :], start=True, stop=True)
                    last.then_inc(spread.filled, 1)

            @block.scalar
            def _(act):
                for job in range(EXPERTS // 2):
                    bank = spread.ready(act, job)
                    act.activation(self.expert_w[:, 2 * job:2 * job + 2, :], bank[:, :].rearrange("p (n t) -> p n t", n=2),
                                   ACT.Copy).then_inc(spread.emptied, 1)

            @block.vector
            def _(vec):
                vec.wait_ge(turned_ready, 1)
                vec.tensor_copy(self.weights_t[0:EXPERTS, 0, :], self.psum[2][0:EXPERTS, 0:T]).then_inc(weights_t_ready, 1)

    def experts_over_all(self):
        nc, xT = self.nc, self.xT
        acc = [[self.psum[2 * t + n] for n in range(2)] for t in range(TT)]
        gu = [self.psum[4 + f] for f in range(FT)]
        gu_ready, silu_ready, gu_used, hidden_ready, down_done = (
            self.sem("experts_" + n) for n in ("gate_up", "silu", "gate_up_used", "hidden", "down"))
        all_done, h_ready = self.sem("experts_all_done"), self.sem("experts_added")
        landed = [self.sem(f"expert_slot{s}_landed") for s in range(6)]

        def slot(s, *shape):
            return self.at(RING + s * SLOT, *shape)

        def load_expert(sync, i, parity, used):
            for n in range(3):
                s = 3 * parity + n
                if used:
                    sync.wait_ge(*used[n // 2])
                src = self.ins[("w_gate", "w_up", "w_down")[n]][i * 2 + parity]
                dst = slot(s, FT, D) if n == 2 else slot(s, K, FF)
                sync.dma_start(dst, src).then_inc(landed[s], 16)

        with nc.Block() as block:
            @block.sync
            def _(sync):
                for parity in range(2):
                    load_expert(sync, 0, parity, None)
                with sync.Fori(1, EXPERTS // 2) as i:
                    for parity in range(2):
                        load_expert(sync, i, parity, [(gu_ready, i * 8 + (4 * parity - 4)), (down_done, i * 2 + (parity - 1))])

            @block.tensor
            def _(pe):
                def touch(start):
                    for bank in acc[0] + acc[1]:
                        last = pe.matmul(bank[:, :], self.zeros[0:1, 0:P], self.zeros[0:1, P:P + 512], start=start,
                                         stop=not start, skip_group_check=True)
                    return last

                def gate_up(e, parity, half, used):
                    for n in range(2):
                        pe.wait_ge(landed[3 * parity + n], half * 16 + 16)
                    for f in range(FT):
                        if used:
                            pe.wait_ge(gu_used, e * 4 + (f - 3))
                        for n in range(2):
                            w = slot(3 * parity + n, K, FF)
                            for k in range(K):
                                last = pe.matmul(gu[f][:, n * T:(n + 1) * T], w[:, k, f * P:(f + 1) * P], xT[:, k, :],
                                                 start=(k == 0), stop=(k == K - 1))
                        last.then_inc(gu_ready, 1)

                def down(e, parity, half):
                    pe.wait_ge(landed[3 * parity + 2], half * 16 + 16)
                    w = slot(3 * parity + 2, FT, D)
                    for f in range(FT):
                        pe.wait_ge(hidden_ready, e * 4 + (f + 1))
                        for t in range(TT):
                            for n in range(2):
                                last = pe.matmul(acc[t][n][:, :], self.hidden[:, parity, f, t * P:(t + 1) * P],
                                                 w[:, f, n * 512:(n + 1) * 512], start=False, stop=False,
                                                 skip_group_check=True)
                    last.then_inc(down_done, 1)

                touch(True)
                gate_up(0, 0, 0, False)
                with pe.Fori(0, EXPERTS // 2 - 1) as i:
                    gate_up(i * 2 + 1, 1, i, True)
                    down(i * 2, 0, i)
                    gate_up(i * 2 + 2, 0, i + 1, True)
                    down(i * 2 + 1, 1, i)
                last_pair = EXPERTS // 2 - 1
                gate_up(EXPERTS - 1, 1, last_pair, True)
                down(EXPERTS - 2, 0, last_pair)
                down(EXPERTS - 1, 1, last_pair)
                touch(False).then_inc(all_done, 1)

            @block.scalar
            def _(act):
                def silus(e, first):
                    for f in range(FT):
                        act.wait_ge(gu_ready, e * 4 + (f + 1))
                        if not (first and f < 2):
                            act.wait_ge(gu_used, e * 4 + (f - 1))
                        act.activation(self.silu[:, f % 2, :], gu[f][:, 0:T], ACT.Silu).then_inc(silu_ready, 1)

                silus(0, True)
                with act.Fori(1, EXPERTS) as e:
                    silus(e, False)

            @block.vector
            def _(vec):
                def hiddens(e, parity, wait_down):
                    for f in range(FT):
                        vec.wait_ge(silu_ready, e * 4 + (f + 1))
                        if wait_down and f == 0:
                            vec.wait_ge(down_done, e - 1)
                        hidden = self.hidden[:, parity, f, :]
                        vec.tensor_tensor(hidden, self.silu[:, f % 2, :], gu[f][:, T:2 * T], ALU.mult).then_inc(gu_used, 1)
                        vec.wait_ge(gu_used, e * 4 + (f + 1))
                        w = self.expert_w[:, e, :] if isinstance(e, int) else \
                            self.expert_w[:, bass.ds(e, 1), :].rearrange("p a t -> p (a t)")
                        vec.tensor_tensor(hidden, hidden, w, ALU.mult).then_inc(hidden_ready, 1)

                hiddens(0, 0, False)
                hiddens(1, 1, False)
                with vec.Fori(1, EXPERTS // 2) as i:
                    hiddens(i * 2, 0, True)
                    hiddens(i * 2 + 1, 1, True)
                vec.wait_ge(all_done, 1)
                for t in range(TT):
                    for n in range(2):
                        part = self.h[:, t, n * 512:(n + 1) * 512]
                        vec.tensor_tensor(part, part, acc[t][n][:, :], ALU.add).then_inc(h_ready, 1)
                vec.wait_ge(h_ready, 4)

    def final_norm(self):
        nc, h = self.nc, self.h
        junk = self.at(WORK, TT, D)
        ss, ms, root, rstd = (self.small[:, i * 2:i * 2 + 2] for i in range(4))
        squares, mean_ready, root_ready = (self.sem(f"final_{x}") for x in ("squares", "mean", "root"))
        order = self.vec
        with nc.Block() as block:
            @block.sync
            def _(sync):
                self.issue(sync, self.first_half + RING_SLOTS)

            @block.scalar
            def _(act):
                for t in range(TT):
                    act.activation(junk[:, t, :], h[:, t, :], ACT.Square, accum_out=ss[:, t:t + 1]).then_inc(squares, 1)
                act.wait_ge(mean_ready, 1)
                act.activation(root, ms, ACT.Sqrt).then_inc(root_ready, 1)

            @block.vector
            def _(vec):
                vec.wait_ge(squares, TT)
                vec.tensor_scalar(ms, ss, 1.0 / D, EPS, ALU.mult, ALU.add).then_inc(mean_ready, 1)
                vec.wait_ge(root_ready, 1)
                order.step(vec.reciprocal(rstd, root))
                order.settle(vec)
                vec.wait_ge(self.rows2_landed, 32)
                for t in range(TT):
                    order.step(vec.scalar_tensor_tensor(out=h[:, t, :], in0=h[:, t, :], scalar=rstd[:, t:t + 1],
                                                        in1=self.rows2[:, 0:D], op0=ALU.mult, op1=ALU.mult))


    def place_second(self):
        at = self.at
        o = WORK
        self.qkv2 = at(o, 6, TT, 512)
        self.turned_in = at(o + 6144, 4, TT, 512)
        self.qk2T = at(o + 10240, 4, 4, T)
        self.mixed = at(o + 14336, TT, D)
        o = MORE
        self.masked_s = at(o, 2, T)
        self.probs = at(o + 512, 6, T)
        self.mixed_p = at(o + 2048, 2, T)
        self.probs_t = at(o + 2560, 2, T)
        self.halves = at(o + 3072, 2, 256)
        self.squares2 = at(o + 3584, TT, 512)
        self.stat2 = at(o + 4608, 8, 64)
        self.sums2 = at(o + 5120, 64)
        self.neg_max = at(o + 5184, 64)
        self.pair_rec = at(o + 5248, 8)
        self.lam_work = at(o + 5256, 160)
        self.stat3 = at(o + 5420, 8, 24)
        self.future = at(o + 5612, T)

    def project_second(self):
        nc, xT = self.nc, self.xT
        first = self.first_half
        tokens = Banks(self, "project2", [0, 1, 2, 3])
        for c in range(6):
            self.used_by[first + c] = (tokens.filled, TT * (c + 1))
        names = ("mq", "mk", "dq", "dk")
        column = (0, 1, 3, 4)
        order = self.vec
        squares, mean_ready, root_ready = (self.sem("qk_" + n) for n in ("squares", "mean", "root"))
        exp_in, exp_out = self.sem("lambda_in"), self.sem("lambda_out")
        rows, heads = self.rows2, "p (h d) -> p h d"
        sq, ms, root, rstd = (self.stat2[:, n, :] for n in range(4))
        dots, lam_exp = self.lam_work[:, 128:130], self.lam_work[:, 130:132]
        with nc.Block() as block:
            @block.sync
            def _(sync):
                self.issue(sync, first + 8)

            @block.tensor
            def _(pe):
                for c in range(6):
                    w = self.chunk(pe, first + c)
                    for t in range(TT):
                        bank = tokens.free(pe, c * TT + t)
                        for k in range(K):
                            last = pe.matmul(bank[:, :], xT[:, k, t * P:(t + 1) * P], w[:, k, :],
                                             start=(k == 0), stop=(k == K - 1))
                        last.then_inc(tokens.filled, 1)

            @block.scalar
            def _(act):
                act.wait_ge(exp_in, 1)
                act.activation(lam_exp, dots, ACT.Exp).then_inc(exp_out, 1)
                for job in range(6 * TT):
                    bank = tokens.ready(act, job)
                    act.activation(self.qkv2[:, job // TT, job % TT, :], bank[:, :], ACT.Copy).then_inc(tokens.emptied, 1)
                act.wait_ge(mean_ready, 1)
                act.activation(root, ms, ACT.Sqrt).then_inc(root_ready, 1)

            @block.vector
            def _(vec):
                o, n = ROWS2["lambda"]
                four = rows[:, o:o + n].rearrange("p (a b d) -> p a b d", a=2, b=2)
                prod = self.lam_work[:, 0:128].rearrange("p (a d) -> p a d", a=2)
                order.step(vec.tensor_tensor(prod, four[:, :, 0, :], four[:, :, 1, :], ALU.mult))
                order.settle(vec)
                vec.tensor_reduce(dots, prod, AX.X, ALU.add).then_inc(exp_in, 1)
                order.step(vec.memset(self.future[:, 0:P], 0.0))
                order.step(vec.tensor_copy(self.future[:, P:T], self.const2[:, 128:256]))
                vec.wait_ge(exp_out, 1)
                order.step(vec.scalar_tensor_tensor(out=self.lt[:, 0:1], in0=lam_exp[:, 0:1], scalar=LAMBDA_INIT,
                                                    in1=lam_exp[:, 1:2], op0=ALU.add, op1=ALU.subtract))
                for n in range(4 * TT):
                    a, t = divmod(n, TT)
                    vec.wait_ge(tokens.emptied, TT * column[a] + t + 1)
                    x = self.qkv2[:, column[a], t, :]
                    junk = self.squares2[:, n % 2, :]
                    order.step(vec.tensor_tensor(junk, x, x, ALU.mult))
                    order.settle(vec)
                    order.step(vec.tensor_reduce(sq[:, n * 8:(n + 1) * 8], junk.rearrange(heads, h=8), AX.X, ALU.add))
                order.settle(vec)
                vec.tensor_scalar(ms, sq, 1.0 / M_DIM, EPS, ALU.mult, ALU.add).then_inc(mean_ready, 1)
                vec.wait_ge(root_ready, 1)
                order.step(vec.reciprocal(rstd, root))
                order.settle(vec)
                half = M_DIM // 2
                rope = self.const2[:, 0:128].rearrange("p (a t d) -> p a t d", a=2, t=TT)
                for n in range(4 * TT):
                    a, t = divmod(n, TT)
                    x = self.qkv2[:, column[a], t, :]
                    order.step(vec.tensor_tensor(x.rearrange(heads, h=8), x.rearrange(heads, h=8),
                                                 rstd[:, n * 8:(n + 1) * 8].unsqueeze(2).broadcast_to([P, 8, M_DIM]),
                                                 ALU.mult))
                    order.settle(vec)
                    o, width = ROWS2[names[a]]
                    gain = rows[:, o:o + width].unsqueeze(1).broadcast_to([P, 512 // width, width])
                    order.step(vec.tensor_tensor(x.rearrange(heads, d=width), x.rearrange(heads, d=width), gain, ALU.mult))
                    order.settle(vec)
                    x8 = x.rearrange(heads, h=8)
                    y8 = self.turned_in[:, a, t, :].rearrange(heads, h=8)
                    cos = rope[:, 0, t, :].unsqueeze(1).broadcast_to([P, 8, half])
                    sin = rope[:, 1, t, :].unsqueeze(1).broadcast_to([P, 8, half])
                    h0 = self.halves[:, 0, :].rearrange(heads, h=8)
                    h1 = self.halves[:, 1, :].rearrange(heads, h=8)
                    for out, u, v, op in ((y8[:, :, 0:half], cos, sin, ALU.subtract), (y8[:, :, half:], sin, cos, ALU.add)):
                        order.step(vec.tensor_tensor(h0, x8[:, :, 0:half], u, ALU.mult))
                        order.step(vec.tensor_tensor(h1, x8[:, :, half:], v, ALU.mult))
                        order.settle(vec)
                        order.step(vec.tensor_tensor(out, h0, h1, op))
                        order.settle(vec)

    def attention(self):
        nc, ident = self.nc, self.ident
        turned = Banks(self, "attn_turned", [0, 1, 2, 3])
        scores = Banks(self, "attn_scores", [4, 5])
        flips = Banks(self, "attn_flips", [6, 7])
        outs = {("m", 0): self.psum[0], ("m", 1): self.psum[1], ("d", 0): self.psum[2], ("d", 1): self.psum[3]}
        items = [("m", b, r, t) for b in range(4) for r in range(2) for t in range(TT)]
        items += [("d", b, None, t) for b in range(4) for t in range(TT)]
        jobs = []
        first_job = []
        for n, (kind, b, r, t) in enumerate(items):
            first_job.append(len(jobs))
            jobs += [(n, r)] if kind == "m" else [(n, 0), (n, 1)]
        first_job.append(len(jobs))
        diff_no = {n: m for m, n in enumerate(n for n, x in enumerate(items) if x[0] == "d")}
        maxed, exped, mixed_ready, pv_done = (self.sem("attn_" + n) for n in ("max", "exp", "mixed", "pv"))
        mean_ready, root_ready = self.sem("attn_mean"), self.sem("attn_root")
        order = self.vec
        last_item = len(items)
        with nc.Block() as block:
            @block.tensor
            def _(pe):
                for job in range(4 * TT):
                    a, t = divmod(job, TT)
                    bank = turned.free(pe, job)
                    for b in range(4):
                        last = pe.transpose(bank[:, b * P:(b + 1) * P], self.turned_in[:, a, t, b * P:(b + 1) * P], ident)
                    last.then_inc(turned.filled, 1)
                pe.wait_ge(turned.emptied, 4 * TT)
                for step in range(last_item + 3):
                    if step < last_item:
                        kind, b, r, t = items[step]
                        q = 0 if kind == "m" else 2
                        n = P * (t + 1)
                        for job in range(first_job[step], first_job[step + 1]):
                            half = jobs[job][1]
                            rows = slice(64 * half, 64 * half + 64)
                            bank = scores.free(pe, job)
                            pe.matmul(bank[:, 0:n], self.qk2T[rows, q, b, t * P:(t + 1) * P], self.qk2T[rows, q + 1, b, 0:n],
                                      start=True, stop=True).then_inc(scores.filled, 1)
                    if 0 <= step - 2 < last_item:
                        i = step - 2
                        kind, b, r, t = items[i]
                        if kind == "m":
                            pe.wait_ge(exped, first_job[i + 1])
                            src = self.probs[:, first_job[i] % 6, :]
                        else:
                            pe.wait_ge(mixed_ready, diff_no[i] + 1)
                            src = self.mixed_p[:, diff_no[i] % 2, :]
                        bank = flips.free(pe, i)
                        for s in range(t + 1):
                            last = pe.transpose(bank[:, s * P:(s + 1) * P], src[:, s * P:(s + 1) * P], ident)
                        last.then_inc(flips.filled, 1)
                    if 0 <= step - 3:
                        i = step - 3
                        kind, b, r, t = items[i]
                        pe.wait_ge(flips.emptied, i + 1)
                        v, width, h = (2, 64, 2 * b + r) if kind == "m" else (5, 128, b)
                        cols = slice(h * width, (h + 1) * width)
                        for s in range(t + 1):
                            last = pe.matmul(outs[kind, t][:, cols], self.probs_t[:, i % 2, s * P:(s + 1) * P],
                                             self.qkv2[:, v, s, cols], start=(s == 0), stop=(s == t))
                        last.then_inc(pv_done, 1)

            @block.scalar
            def _(act):
                for job in range(4 * TT):
                    a, t = divmod(job, TT)
                    bank = turned.ready(act, job)
                    act.activation(self.qk2T[:, a, :, t * P:(t + 1) * P], bank[:, :].rearrange("p (b t) -> p b t", b=4),
                                   ACT.Copy).then_inc(turned.emptied, 1)
                for step in range(last_item + 2):
                    if step < last_item:
                        kind, b, r, t = items[step]
                        n = P * (t + 1)
                        for job in range(first_job[step], first_job[step + 1]):
                            act.wait_ge(maxed, job + 1)
                            if job >= 6:
                                i = jobs[job - 6][0]
                                if items[i][0] == "m":
                                    act.wait_ge(flips.filled, i + 1)
                                else:
                                    act.wait_ge(mixed_ready, diff_no[i] + 1)
                            act.activation(self.probs[:, job % 6, 0:n], self.masked_s[:, job % 2, 0:n], ACT.Exp,
                                           bias=self.neg_max[:, job:job + 1],
                                           accum_out=self.sums2[:, job:job + 1]).then_inc(exped, 1)
                    if step >= 2:
                        i = step - 2
                        n = P * (items[i][3] + 1)
                        bank = flips.ready(act, i)
                        if i >= 2:
                            act.wait_ge(pv_done, i - 1)
                        act.activation(self.probs_t[:, i % 2, 0:n], bank[:, 0:n], ACT.Copy).then_inc(flips.emptied, 1)
                act.wait_ge(mean_ready, 1)
                act.activation(self.stat3[:, 4, :], self.stat3[:, 3, :], ACT.Sqrt).then_inc(root_ready, 1)

            @block.vector
            def _(vec):
                for step in range(last_item + 1):
                    if step < last_item:
                        kind, b, r, t = items[step]
                        n = P * (t + 1)
                        for job in range(first_job[step], first_job[step + 1]):
                            bank = scores.ready(vec, job)
                            if job >= 2:
                                vec.wait_ge(exped, job - 1)
                            s = self.masked_s[:, job % 2, 0:n]
                            vec.scalar_tensor_tensor(out=s, in0=bank[:, 0:n], scalar=M_DIM ** -0.5,
                                                     in1=self.future[:, T - n:T], op0=ALU.mult,
                                                     op1=ALU.add).then_inc(scores.emptied, 1)
                            vec.wait_ge(scores.emptied, job + 1)
                            vec.tensor_reduce(self.neg_max[:, job:job + 1], s, AX.X, ALU.max,
                                              negate=True).then_inc(maxed, 1)
                    i = step - 1
                    if i >= 0 and items[i][0] == "d":
                        j0, m = first_job[i], diff_no[i]
                        n = P * (items[i][3] + 1)
                        rec = self.pair_rec[:, 2 * (m % 2):2 * (m % 2) + 2]
                        vec.wait_ge(exped, j0 + 2)
                        order.step(vec.reciprocal(rec, self.sums2[:, j0:j0 + 2]))
                        order.settle(vec)
                        order.step(vec.tensor_tensor(rec[:, 1:2], rec[:, 1:2], self.lt[:, 0:1], ALU.mult))
                        order.settle(vec)
                        if m >= 2:
                            vec.wait_ge(flips.filled, i - 1)
                        out = self.mixed_p[:, m % 2, 0:n]
                        order.step(vec.tensor_scalar(out, self.probs[:, (j0 + 1) % 6, 0:n], rec[:, 1:2], None, ALU.mult))
                        order.settle(vec)
                        vec.scalar_tensor_tensor(out=out, in0=self.probs[:, j0 % 6, 0:n], scalar=rec[:, 0:1], in1=out,
                                                 op0=ALU.mult, op1=ALU.subtract).then_inc(mixed_ready, 1)
                vec.wait_ge(pv_done, len(items))
                heads = "p (h d) -> p h d"
                sums, square, mean, root, rstd, rec = (self.stat3[:, n, :] for n in (0, 1, 3, 4, 5, 6))
                order.step(vec.reciprocal(rec[:, 0:16], self.sums2[:, 0:16]))
                order.settle(vec)
                by_tile = rec[:, 0:16].rearrange("p (h t) -> p t h", t=TT)
                mixed = self.mixed
                for t in range(TT):
                    order.step(vec.tensor_tensor(mixed[:, t, 0:512].rearrange(heads, h=8),
                                                 outs["m", t][:, :].rearrange(heads, h=8),
                                                 by_tile[:, t].unsqueeze(2).broadcast_to([P, 8, 64]), ALU.mult))
                    order.step(vec.tensor_copy(mixed[:, t, 512:1024], outs["d", t][:, :]))
                order.settle(vec)
                for t in range(TT):
                    for part, h, at in ((0, 8, t * 8), (1, 4, 16 + t * 4)):
                        x = mixed[:, t, part * 512:(part + 1) * 512]
                        order.step(vec.tensor_tensor(self.squares2[:, part, :], x, x, ALU.mult))
                        order.settle(vec)
                        order.step(vec.tensor_reduce(square[:, at:at + h], self.squares2[:, part, :].rearrange(heads, h=h),
                                                     AX.X, ALU.add))
                    order.settle(vec)
                order.step(vec.tensor_scalar(mean[:, 0:16], square[:, 0:16], 1.0 / M_DIM, EPS, ALU.mult, ALU.add))
                vec.tensor_scalar(mean[:, 16:24], square[:, 16:24], 1.0 / F_DIM, EPS, ALU.mult, ALU.add).then_inc(mean_ready, 1)
                vec.wait_ge(root_ready, 1)
                order.step(vec.reciprocal(rstd, root))
                order.settle(vec)
                order.step(vec.tensor_scalar(rstd[:, 16:24], rstd[:, 16:24], 1.0 - LAMBDA_INIT, None, ALU.mult))
                order.settle(vec)
                for t in range(TT):
                    for part, h, at, gain in ((0, 8, t * 8, "m_out"), (1, 4, 16 + t * 4, "d_out")):
                        x = mixed[:, t, part * 512:(part + 1) * 512]
                        order.step(vec.tensor_tensor(x.rearrange(heads, h=h), x.rearrange(heads, h=h),
                                                     rstd[:, at:at + h].unsqueeze(2).broadcast_to([P, h, 512 // h]), ALU.mult))
                        order.settle(vec)
                        o, n = ROWS2[gain]
                        order.step(vec.tensor_tensor(x, x, self.rows2[:, o:o + n], ALU.mult))


    def place_peer(self):
        at = self.at
        self.query_t = at(WORK, 2 * P_HEADS, T)
        self.sub_keys = at(WORK + 4096, 2 * P_HEADS, NKEYS)
        self.key_scores = at(WORK + 6144, TT, 2 * P_HEADS, NKEYS)
        self.pairs = at(WORK + 10240, P_HEADS, TOPK * TOPK)
        self.match = at(WORK + 12288, SLOTS, TOPK)
        o = RING
        self.top_s = at(o, TT, 2 * P_HEADS, TOPK)
        self.top_i = at(o + 512, TT, 2 * P_HEADS, TOPK)
        self.top_if = at(o + 1024, TT, 2 * P_HEADS, TOPK)
        self.best_s = at(o + 1536, TT, P_HEADS, TOPK)
        self.best_p = at(o + 1792, TT, P_HEADS, TOPK)
        self.best_half = at(o + 2048, 2, TT, SLOTS)
        self.best_half_f = at(o + 2560, 2, TT, SLOTS)
        self.slot_index = at(o + 3072, 2, TT, SLOTS)
        self.gates = at(o + 3584, TT, SLOTS)
        self.gate_sum = at(o + 3840, 2, TT, P_HEADS)
        self.dense = at(0, NKEYS, T)
        self.down_ring = [at(MORE + 2048 * n, 2, K, P) for n in range(2)]
        self.up_ring = [at(MORE + 4096 + 2048 * n, 2, D) for n in range(2)]
        self.x_parts = self.parts("x_parts", MORE + 8192, K, 2, T)
        o = KEPT + TT * D
        self.hot_j = at(o, 16, P)
        self.hot_i = at(self.cursor, 16, P)
        self.down_high = self.parts("down_high", o, 2, K, P)
        self.down_low = [self.parts(f"down_low{n}", MORE + 2048 * n, 2, K, P) for n in range(2)]
        self.up_high = self.parts("up_high", o + 2048, 2, D)
        self.up_low = [self.parts(f"up_low{n}", MORE + 4096 + 2048 * n, 2, D) for n in range(2)]
        self.gelu = at(o + 4096, 2, T)
        self.gated_high = self.parts("gated_high", o + 4608, 2, T)
        self.gated_low = self.parts("gated_low", o + 5120, 2, T)

    def peer_queries(self):
        nc, xT = self.nc, self.xT
        first = self.first_half + 8
        queries = Banks(self, "queries", [0, 1, 2, 3])
        scores = Banks(self, "key_scores", [4, 5, 6, 7])
        for c in range(4):
            self.used_by[first + c] = (queries.filled, 4 * (c + 1))
        keys_landed = self.keys_landed = self.sem("sub_keys_landed")
        with nc.Block() as block:
            @block.sync
            def _(sync):
                sync.dma_start(self.sub_keys, self.ins["sub_keys"]).then_inc(keys_landed, 16)
                self.issue(sync, first + 4)

            @block.tensor
            def _(pe):
                for c in range(4):
                    w = self.chunk(pe, first + c)
                    for n in range(4):
                        job = 4 * c + n
                        bank = queries.free(pe, job)
                        for k in range(K):
                            last = pe.matmul(bank[:, 0:T], w[:, k, n * P:(n + 1) * P], xT[:, k, :],
                                             start=(k == 0), stop=(k == K - 1))
                        last.then_inc(queries.filled, 1)
                pe.wait_ge(keys_landed, 16)
                pe.wait_ge(queries.emptied, 16)
                for job in range(4 * TT):
                    t, quad = divmod(job, 4)
                    bank = scores.free(pe, job)
                    for n in range(4):
                        hp = 4 * quad + n
                        last = pe.matmul(bank[:, n * P:(n + 1) * P], self.query_t[:, hp, t * P:(t + 1) * P],
                                         self.sub_keys[:, hp, :], start=True, stop=True)
                    last.then_inc(scores.filled, 1)

            @block.scalar
            def _(act):
                for job in range(16):
                    bank = queries.ready(act, job)
                    act.activation(self.query_t[:, job, :], bank[:, 0:T], ACT.Copy).then_inc(queries.emptied, 1)
                for job in range(4 * TT):
                    t, quad = divmod(job, 4)
                    bank = scores.ready(act, job)
                    act.activation(self.key_scores[:, t, 4 * quad:4 * quad + 4, :],
                                   bank[:, :].rearrange("p (n x) -> p n x", n=4), ACT.Copy).then_inc(scores.emptied, 1)

    def peer_select(self):
        nc = self.nc
        order = self.vec
        exp_in, exp_out, chosen = self.sem("gate_exp_in"), self.sem("gate_exp_out"), self.sem("peer_chosen")
        turned = Banks(self, "slots_turned", [0, 1, 2, 3])
        x_high_ready, x_low_ready = self.sem("x_high"), self.sem("x_low")
        best_p = self.best_p.bitcast(U32)
        top_i = self.top_i.bitcast(U32)
        with nc.Block() as block:
            @block.vector
            def _(vec):
                def top16(values, top, index, count):
                    for n in range(count):
                        order.step(vec.max(top(n)[:, 0:8], values(n)))
                    order.settle(vec)
                    for n in range(count):
                        order.step(vec.max_index(index(n)[:, 0:8], top(n)[:, 0:8], values(n)))
                    order.settle(vec)
                    for n in range(count):
                        order.step(vec.match_replace(values(n), top(n)[:, 0:8], values(n), -3.0e38))
                    order.settle(vec)
                    for n in range(count):
                        order.step(vec.max(top(n)[:, 8:16], values(n)))
                    order.settle(vec)
                    for n in range(count):
                        order.step(vec.max_index(index(n)[:, 8:16], top(n)[:, 8:16], values(n)))
                    order.settle(vec)

                for t in range(TT):
                    top16(lambda n: self.key_scores[:, t, n, :], lambda n: self.top_s[:, t, n, :],
                          lambda n: top_i[:, t, n, :], 2 * P_HEADS)
                order.step(vec.tensor_copy(self.top_if, top_i))
                for t in range(TT):
                    s = self.top_s[:, t].rearrange("p (h a) s -> p h a s", a=2)
                    pairs = self.pairs.rearrange("p h (x y) -> p h x y", x=TOPK)
                    order.step(vec.tensor_tensor(pairs, s[:, :, 0, :].unsqueeze(3).broadcast_to([P, P_HEADS, TOPK, TOPK]),
                                                 s[:, :, 1, :].unsqueeze(2).broadcast_to([P, P_HEADS, TOPK, TOPK]), ALU.add))
                    order.settle(vec)
                    top16(lambda h: self.pairs[:, h, :], lambda h: self.best_s[:, t, h, :], lambda h: best_p[:, t, h, :],
                          P_HEADS)
                shifted = self.gates.rearrange("p t (h s) -> p t h s", h=P_HEADS)
                for t in range(TT):
                    vec.tensor_tensor(shifted[:, t], self.best_s[:, t],
                                      self.best_s[:, t, :, 0:1].broadcast_to([P, P_HEADS, TOPK]),
                                      ALU.subtract).then_inc(exp_in, 1)
                flat = best_p.rearrange("p t h s -> p t (h s)")
                half = self.best_half.bitcast(U32)
                order.step(vec.tensor_single_scalar(half[:, 0], flat, 4, ALU.logical_shift_right))
                order.step(vec.tensor_single_scalar(half[:, 1], flat, TOPK - 1, ALU.bitwise_and))
                order.settle(vec)
                order.step(vec.tensor_copy(self.best_half_f, half))
                order.settle(vec)
                for a in range(2):
                    for t in range(TT):
                        order.step(vec.tensor_tensor(self.match,
                                                     self.best_half_f[:, a, t, :].unsqueeze(2).broadcast_to([P, SLOTS, TOPK]),
                                                     self.iota[:, 0:TOPK].unsqueeze(1).broadcast_to([P, SLOTS, TOPK]),
                                                     ALU.is_equal))
                        order.settle(vec)
                        keys = self.top_if[:, t].rearrange("p (h a) s -> p h a s", a=2)[:, :, a, :]
                        m4 = self.match.rearrange("p (h s) r -> p h s r", h=P_HEADS)
                        order.step(vec.tensor_tensor(m4, m4, keys.unsqueeze(2).broadcast_to([P, P_HEADS, TOPK, TOPK]),
                                                     ALU.mult))
                        order.settle(vec)
                        order.step(vec.tensor_reduce(self.slot_index[:, a, t, :], self.match, AX.X, ALU.add))
                        order.settle(vec)
                vec.wait_ge(exp_out, 1)
                gates = self.gates.rearrange("p t (h s) -> p t h s", h=P_HEADS)
                for t in range(TT):
                    order.step(vec.tensor_reduce(self.gate_sum[:, 0, t], gates[:, t], AX.X, ALU.add))
                order.settle(vec)
                order.step(vec.reciprocal(self.gate_sum[:, 1], self.gate_sum[:, 0]))
                order.settle(vec)
                for t in range(TT):
                    order.step(vec.tensor_tensor(gates[:, t], gates[:, t],
                                                 self.gate_sum[:, 1, t].unsqueeze(2).broadcast_to([P, P_HEADS, TOPK]),
                                                 ALU.mult))
                order.settle(vec)
                vec.sem_inc(chosen, 1)

            @block.gpsimd
            def _(pool):
                pool.wait_ge(x_high_ready, 1)
                pool.tensor_tensor(self.x_parts[:, :, 1, :], self.xT, self.x_parts[:, :, 0, :],
                                   ALU.subtract).then_inc(x_low_ready, 1)

            @block.scalar
            def _(act):
                act.activation(self.x_parts[:, :, 0, :], self.xT, ACT.Copy).then_inc(x_high_ready, 1)
                act.wait_ge(exp_in, TT)
                act.activation(self.gates, self.gates, ACT.Exp).then_inc(exp_out, 1)
                for job in range(3):
                    bank = turned.ready(act, job)
                    dst = (self.slot_i, self.slot_j, self.slot_g)[job]
                    act.activation(dst, bank[:, 0:T], ACT.Copy).then_inc(turned.emptied, 1)

            @block.tensor
            def _(pe):
                pe.wait_ge(chosen, 1)
                for job in range(3):
                    bank = turned.free(pe, job)
                    for t in range(TT):
                        src = self.gates[:, t, :] if job == 2 else self.slot_index[:, job, t, :]
                        last = pe.transpose(bank[:, t * P:(t + 1) * P], src, self.ident)
                    last.then_inc(turned.filled, 1)

    def peer_dense(self):
        nc = self.nc
        BODY, QUAD = 16, 4
        second_ready, first_ready, gated_ready, product_done, spread = (
            self.sem("dense_" + n) for n in ("second_one_hots", "first_one_hots", "gated_one_hots", "products", "spread"))
        self.down_landed = [self.sem(f"down_ring{n}_landed") for n in range(2)]
        self.up_landed = [self.sem(f"up_ring{n}_landed") for n in range(2)]
        with nc.Block() as block:
            @block.sync
            def _(sync):
                for q in range(2):
                    sync.dma_start(self.down_ring[q], self.ins["peer_down"][q]).then_inc(self.down_landed[q], 16)
                    sync.dma_start(self.up_ring[q], self.ins["peer_up"][q]).then_inc(self.up_landed[q], 16)

            def at_quad(x, n0):
                part = x[:, n0:n0 + QUAD] if isinstance(n0, int) else x[:, bass.ds(n0, QUAD)]
                return part.unsqueeze(2).broadcast_to([P, QUAD, P])

            def slots(quad):
                return slice(quad * QUAD, quad * QUAD + QUAD)

            @block.vector
            def _(vec):
                rows = self.iota.unsqueeze(1).broadcast_to([P, QUAD, P])

                def body(i, first):
                    for quad in range(BODY // QUAD):
                        n0 = i * BODY + quad * QUAD
                        if not first:
                            vec.wait_ge(product_done, i * 4 + (quad - 3))
                        vec.tensor_tensor(self.hot_j[:, slots(quad), :], rows, at_quad(self.slot_j, n0),
                                          ALU.is_equal).then_inc(second_ready, 1)
                        vec.tensor_tensor(self.hot_i[:, slots(quad), :], rows, at_quad(self.slot_i, n0),
                                          ALU.is_equal).then_inc(first_ready, 1)

                body(0, True)
                with vec.Fori(1, T // BODY) as i:
                    body(i, False)

            @block.gpsimd
            def _(pool):
                def body(i):
                    for quad in range(BODY // QUAD):
                        hot = self.hot_j[:, slots(quad), :]
                        pool.wait_ge(second_ready, i * 4 + (quad + 1))
                        pool.tensor_tensor(hot, hot, at_quad(self.slot_g, i * BODY + quad * QUAD),
                                           ALU.mult).then_inc(gated_ready, 1)

                body(0)
                with pool.Fori(1, T // BODY) as i:
                    body(i)

            @block.tensor
            def _(pe):
                def body(i, first):
                    for quad in range(BODY // QUAD):
                        pe.wait_ge(first_ready, i * 4 + (quad + 1))
                        pe.wait_ge(gated_ready, i * 4 + (quad + 1))
                        if not first:
                            pe.wait_ge(spread, i * 4 + (quad - 3))
                        for n in range(QUAD):
                            u = quad * QUAD + n
                            last = pe.matmul(self.psum[4 + quad][:, n * P:(n + 1) * P], self.hot_i[:, u, :],
                                             self.hot_j[:, u, :], start=True, stop=True)
                        last.then_inc(product_done, 1)

                body(0, True)
                with pe.Fori(1, T // BODY) as i:
                    body(i, False)

            @block.scalar
            def _(act):
                def body(i, first):
                    for quad in range(BODY // QUAD):
                        act.wait_ge(product_done, i * 4 + (quad + 1))
                        src = self.psum[4 + quad][:, :].rearrange("p (t j) -> p j t", t=QUAD)
                        n0 = i * BODY + quad * QUAD
                        dst = self.dense[:, :, n0:n0 + QUAD] if first else self.dense[:, :, bass.ds(n0, QUAD)]
                        act.activation(dst, src, ACT.Copy).then_inc(spread, 1)

                body(0, True)
                with act.Fori(1, T // BODY) as i:
                    body(i, False)

    def peer_experts(self):
        nc = self.nc
        acc = [[self.psum[2 * t + n] for n in range(2)] for t in range(TT)]
        hid = [self.psum[4 + n] for n in range(4)]
        (down_high_ready, down_low_ready, up_high_ready, up_low_ready, hid_ready, hid_copied, hid_summed, gelu_ready, gated_ready,
         gated_high_ready, gated_low_ready, out_done, all_done) = (self.sem("peer_" + n) for n in (
            "down_high", "down_low", "up_high", "up_low", "hidden", "hidden_copied", "hidden_summed", "gelu", "gated", "gated_high",
            "gated_low", "out", "all"))
        zero_again, summed, stored = self.sem("zeros_again"), self.sem("peer_summed"), self.sem("stored")
        pairs = NKEYS // 2
        zeros = self.at(KEPT + TT * D + 5632, 320).bitcast(mybir.dt.bfloat16)
        with nc.Block() as block:
            @block.sync
            def _(sync):
                with sync.Fori(0, pairs // 2 - 1) as i:
                    for u in range(2):
                        q = i * 2 + (2 + u)
                        sync.wait_ge(hid_ready, i * 4 + 2 * (u + 1))
                        sync.dma_start(self.down_ring[u], self.ins["peer_down"][q]).then_inc(self.down_landed[u], 16)
                        sync.wait_ge(out_done, i * 4 + 2 * (u + 1))
                        sync.dma_start(self.up_ring[u], self.ins["peer_up"][q]).then_inc(self.up_landed[u], 16)
                rows = self.out.rearrange("(t p) d -> t p d", p=P)
                for t in range(TT):
                    sync.wait_ge(summed, 2 * (t + 1))
                    sync.dma_start(rows[t], self.h[:, t, :]).then_inc(stored, 16)
                sync.wait_ge(stored, 16 * TT)

            @block.tensor
            def _(pe):
                pe.wait_ge(zero_again, 1)

                def touch(start):
                    for bank in acc[0] + acc[1]:
                        last = pe.matmul(bank[:, :], zeros[0:1, 0:P], zeros[0:1, P:P + 512], start=start, stop=not start,
                                         skip_group_check=True)
                    return last

                def hidden(i, u, first):
                    pe.wait_ge(down_low_ready, i * 4 + (u + 1))
                    if not first:
                        pe.wait_ge(hid_summed, i * 4 + (u - 3))
                    low = self.down_low[u // 2][:, u % 2]
                    for k in range(K):
                        pe.matmul(hid[u][:, :], self.down_high[:, u % 2, k, :],
                                  self.x_parts[:, k].rearrange("p a t -> p (a t)"), start=(k == 0), stop=False)
                        last = pe.matmul(hid[u][:, 0:T], low[:, k, :], self.x_parts[:, k, 0, :], start=False,
                                         stop=(k == K - 1))
                    last.then_inc(hid_ready, 1)

                def outputs(i, u):
                    pe.wait_ge(up_low_ready, i * 4 + (u + 1))
                    pe.wait_ge(gated_low_ready, i * 4 + (u + 1))
                    low = self.up_low[u // 2][:, u % 2]
                    for t in range(TT):
                        tokens = slice(t * P, (t + 1) * P)
                        for gated, up in ((self.gated_high, self.up_high[:, u % 2]), (self.gated_high, low),
                                          (self.gated_low, self.up_high[:, u % 2])):
                            for c in range(2):
                                last = pe.matmul(acc[t][c][:, :], gated[:, u % 2, tokens], up[:, c * 512:(c + 1) * 512],
                                                 start=False, stop=False, skip_group_check=True)
                    last.then_inc(out_done, 1)

                touch(True)
                for u in range(4):
                    hidden(0, u, True)
                    if u:
                        outputs(0, u - 1)
                with pe.Fori(1, pairs // 2) as i:
                    hidden(i, 0, False)
                    outputs(i - 1, 3)
                    for u in range(1, 4):
                        hidden(i, u, False)
                        outputs(i, u - 1)
                outputs(pairs // 2 - 1, 3)
                touch(False).then_inc(all_done, 1)

            @block.scalar
            def _(act):
                def split_down(i, u, first=False):
                    if u % 2 == 0:
                        act.wait_ge(self.down_landed[u // 2], i * 16 + 16)
                    if not (first and u < 2):
                        act.wait_ge(hid_ready, i * 4 + (u - 1))
                    act.activation(self.down_high[:, u % 2], self.down_ring[u // 2][:, u % 2],
                                   ACT.Copy).then_inc(down_high_ready, 1)

                def step(i, u, first=False):
                    if u % 2 == 0:
                        act.wait_ge(self.up_landed[u // 2], i * 16 + 16)
                    if not (first and u < 2):
                        act.wait_ge(out_done, i * 4 + (u - 1))
                    act.activation(self.up_high[:, u % 2], self.up_ring[u // 2][:, u % 2],
                                   ACT.Copy).then_inc(up_high_ready, 1)
                    act.wait_ge(hid_summed, i * 4 + (u + 1))
                    act.activation(self.gelu[:, u % 2, :], self.gelu[:, u % 2, :], ACT.Gelu).then_inc(gelu_ready, 1)
                    act.wait_ge(gated_ready, i * 4 + (u + 1))
                    act.activation(self.gated_high[:, u % 2, :], self.gelu[:, u % 2, :],
                                   ACT.Copy).then_inc(gated_high_ready, 1)

                split_down(0, 0, first=True)
                for u in range(3):
                    split_down(0, u + 1, first=True)
                    step(0, u, first=True)
                with act.Fori(1, pairs // 2) as i:
                    split_down(i, 0)
                    step(i - 1, 3)
                    for u in range(3):
                        split_down(i, u + 1)
                        step(i, u)
                step(pairs // 2 - 1, 3)

            @block.vector
            def _(vec):
                vec.memset(zeros, 0.0).then_inc(zero_again, 1)

                def split_down(i, u):
                    vec.wait_ge(down_high_ready, i * 4 + (u + 1))
                    whole, low = self.down_ring[u // 2], self.down_low[u // 2]
                    vec.tensor_tensor(low[:, u % 2], whole[:, u % 2], self.down_high[:, u % 2],
                                      ALU.subtract).then_inc(down_low_ready, 1)

                def step(i, u, first=False):
                    vec.wait_ge(hid_ready, i * 4 + (u + 1))
                    if not (first and u < 2):
                        vec.wait_ge(gated_low_ready, i * 4 + (u - 1))
                    gelu = self.gelu[:, u % 2, :]
                    vec.tensor_copy(gelu, hid[u][:, 0:T]).then_inc(hid_copied, 1)
                    vec.wait_ge(hid_copied, i * 4 + (u + 1))
                    vec.tensor_tensor(gelu, gelu, hid[u][:, T:2 * T], ALU.add).then_inc(hid_summed, 1)
                    vec.wait_ge(up_high_ready, i * 4 + (u + 1))
                    whole, low = self.up_ring[u // 2], self.up_low[u // 2]
                    vec.tensor_tensor(low[:, u % 2], whole[:, u % 2], self.up_high[:, u % 2],
                                      ALU.subtract).then_inc(up_low_ready, 1)
                    vec.wait_ge(gelu_ready, i * 4 + (u + 1))
                    dense = self.dense[:, 4 * i + u, :] if isinstance(i, int) else \
                        self.dense[:, bass.ds(i * 4 + u, 1), :].rearrange("p a t -> p (a t)")
                    vec.tensor_tensor(gelu, gelu, dense, ALU.mult).then_inc(gated_ready, 1)
                    vec.wait_ge(gated_high_ready, i * 4 + (u + 1))
                    vec.tensor_tensor(self.gated_low[:, u % 2, :], gelu, self.gated_high[:, u % 2, :],
                                      ALU.subtract).then_inc(gated_low_ready, 1)

                split_down(0, 0)
                for u in range(3):
                    split_down(0, u + 1)
                    step(0, u, first=True)
                with vec.Fori(1, pairs // 2) as i:
                    split_down(i, 0)
                    step(i - 1, 3)
                    for u in range(3):
                        split_down(i, u + 1)
                        step(i, u)
                step(pairs // 2 - 1, 3)
                vec.wait_ge(all_done, 1)
                for t in range(TT):
                    for c in range(2):
                        part = self.h[:, t, c * 512:(c + 1) * 512]
                        vec.tensor_tensor(part, part, acc[t][c][:, :], ALU.add).then_inc(summed, 1)


def build(nc, ins, out):
    with ExitStack() as ctx:
        k = Kernel(nc, ctx, ins, out)
        k.place_first()
        k.rms_to_features("norm1", "norm1", first=True)
        k.project_first()
        k.retention()
        k.rwkv_features()
        k.rwkv_turn()
        k.rwkv_units()
        k.rwkv_scan()
        k.project_out("out1", 8, 10)
        k.end_part()
        k.rms_to_features("norm2", "norm2", scaled_at=MORE)
        k.place_experts()
        k.route_tokens()
        k.experts()
        k.general_experts()
        k.final_norm()
        k.end_part()
        k.place_second()
        k.rms_to_features("norm3", "attn")
        k.project_second()
        k.attention()
        k.project_out("out2", k.first_half + 6, k.first_half + 8 + RING_SLOTS)
        k.rms_to_features("norm4", "ffn")
        k.place_peer()
        k.peer_queries()
        k.peer_select()
        k.peer_dense()
        k.peer_experts()
    return k



def shape_constants():
    import numpy as np
    f = np.float32
    p = np.arange(P)
    chunk = p // CHUNK
    same = chunk[:, None] == chunk[None, :]
    s, t = p[:, None], p[None, :]
    pair = np.stack([same & (s < t), same & (s <= t)], 1)
    mask_a = same & (t < s)
    levels = []
    for n in range(1, 6):
        size = 2 << (n - 1)
        levels.append((s // (2 * size) == t // (2 * size)) & (s // size < t // size))
    two = np.stack([(s // 2 == t // 2) & (t < s), (s // 2 == t // 2) & (s < t)], 1)
    head = (s // 64) == (t // 64)
    ident64 = np.concatenate([np.eye(64), np.eye(64)], 0)
    half = RET_DIM // 2
    inv = f(10000.0) ** (-np.arange(half, dtype=f) / f(half))
    ang = np.arange(T, dtype=f)[:, None] * inv[None, :]
    rope = np.stack([np.cos(ang), np.sin(ang)], 0).reshape(2, TT, P, half).transpose(2, 0, 1, 3)
    const1 = np.concatenate([pair.reshape(P, -1), mask_a, np.stack(levels, 1).reshape(P, -1), two.reshape(P, -1), head,
                             ident64, rope.reshape(P, -1), np.stack([p < 64, p >= 64], 1)], 1).astype(f)
    carry = np.broadcast_to((np.arange(4 * T) % CHUNK != 0).astype(f), (P, 4 * T)).reshape(P, 4, T).copy()
    log_g = np.log(1.0 - np.exp2(-5.0 - np.arange(RET_HEADS)))
    q, k = np.arange(T)[None, :], np.arange(T)[:, None]
    cq, ck, iq, ik = q // CHUNK, k // CHUNK, q % CHUNK, k % CHUNK
    far = (iq + 1.0) + CHUNK * (cq - ck - 1.0) + (CHUNK - 1.0 - ik)
    power = np.where(cq == ck, np.abs(iq - ik), far)
    m = np.where(cq >= ck, np.exp(log_g[:, None, None] * np.maximum(power, 0)), 0.0) * RET_DIM ** -0.5
    ret = np.concatenate([m[:, 0:P, :], m[:, P:T, P:T]], 2).transpose(1, 0, 2).astype(f)
    inv2 = f(1.0) / (f(10000.0) ** (np.arange(0, M_DIM, 2, dtype=f) / f(M_DIM)))
    ang2 = np.arange(T, dtype=f)[:, None] * inv2[None, :]
    rope2 = np.stack([np.cos(ang2), np.sin(ang2)], 0).reshape(2, TT, P, M_DIM // 2).transpose(2, 0, 1, 3)
    future = np.where(np.arange(P)[None, :] > p[:, None], NEG, 0.0)
    return {"ident": np.eye(P, dtype=f), "iota": np.concatenate([np.broadcast_to(np.arange(P), (P, P)), (p % 64)[:, None], s <= t], 1).astype(f),
            "const1": const1, "carry": carry, "ret_decay": np.ascontiguousarray(ret),
            "const2": np.concatenate([rope2.reshape(P, -1), future], 1).astype(f)}


def laid_out(a):
    import numpy as np

    def chunks(w, width=512):
        return np.ascontiguousarray(w.reshape(K, P, -1, width).transpose(2, 1, 0, 3))

    def columns(v):
        return v.reshape(-1, P).T

    def row(v):
        return v.reshape(1, -1)

    w_in = a["w_in"][0]
    lay = {
        "x": a["x"][0],
        "w_in": chunks(w_in[:, 0:3584]),
        "w_in_lora": chunks(w_in[:, 3584:3840], 256)[0],
        "w_out": chunks(a["w_out"][0]),
        "w_in_2": chunks(a["w_in_2"][0]),
        "w_out_2": chunks(a["w_out_2"][0]),
        "peer_query": chunks(a["peer_query_2"][0]),
        "cols": np.concatenate([columns(a[n]) for n in (
            "norm1_gain", "norm2_gain", "attn_norm_2", "ffn_norm_2", "rwkv_mu", "rwkv_w0", "rwkv_a0", "rwkv_k_k",
            "rwkv_k_a", "rwkv_r_k")], 1),
        "lora_up": np.concatenate([np.concatenate([a["rwkv_w_up"][0], a["rwkv_a_up"][0]], 0), a["rwkv_g_up"][0]], 1),
        "rows1": np.concatenate([a["ret_gn_gain"][0], a["rwkv_gn_gain"][0], a["b_route_group"][0], a["b_route_expert"][0]]),
        "rows2": np.concatenate([a["final_norm_gain"], a["q_norm_moba_2"][0], a["k_norm_moba_2"][0],
                                 a["q_norm_diff_2"].reshape(-1), a["k_norm_diff_2"].reshape(-1)]
                                + [a[n][0] for n in ("lambda_q1_2", "lambda_k1_2", "lambda_q2_2", "lambda_k2_2")]
                                + [a["moba_out_gain_2"].reshape(-1), a["diff_out_gain_2"].reshape(-1)]),
        "route": np.concatenate([a["w_route_group"][0], a["w_route_expert"][0]], 1).reshape(K, P, 36).transpose(1, 0, 2),
        "w_gate": a["w_gate"][0].reshape(EXPERTS, K, P, FF).transpose(0, 2, 1, 3),
        "w_up": a["w_up"][0].reshape(EXPERTS, K, P, FF).transpose(0, 2, 1, 3),
        "w_down": a["w_down"][0].reshape(EXPERTS, FT, P, D).transpose(0, 2, 1, 3),
        "sub_keys": a["peer_sub_keys_2"][0].reshape(2 * P_HEADS, NKEYS, P).transpose(2, 0, 1),
        "peer_down": a["peer_down_2"][0].reshape(P, NKEYS // 2, 2, K, P).transpose(1, 4, 2, 3, 0),
        "peer_up": a["peer_up_2"][0].reshape(P, NKEYS // 2, 2, D).transpose(1, 0, 2, 3),
    }
    lay.update(shape_constants())
    return {n: np.ascontiguousarray(v) for n, v in lay.items()}


def kernel(**inputs):
    import numpy as _np
    import concourse.bacc as _bacc
    from concourse.bass_utils import run_bass_kernel_spmd as _run

    arrays = laid_out({n: _np.asarray(v) for n, v in inputs.items()})
    nc = _bacc.Bacc("TRN2", target_bir_lowering=False, num_devices=1)
    ins = {n: nc.dram_tensor(n, v.shape, F32, kind="ExternalInput").ap() for n, v in arrays.items()}
    out = nc.dram_tensor("out", (T, D), F32, kind="ExternalOutput").ap()
    build(nc, ins, out)
    r = _run(nc, [arrays], core_ids=[0])
    return r.results[0]["out"].reshape(1, T, D)
```

```python
from contextlib import ExitStack

import numpy as np

import concourse.bass as bass
from concourse import mybir

F32 = mybir.dt.float32
F32R = mybir.dt.float32r
U32 = mybir.dt.uint32
ALU = mybir.AluOpType
ACT = mybir.ActivationFunctionType
AX = mybir.AxisListType

P = 128
T = 256
TT = T // P
D = 1024
K = D // P
EPS = 1e-6

RET_HEADS, RET_DIM = 4, 128
RW_HEADS, RW_DIM = 8, 64
CHUNK = 64
CHUNKS = T // CHUNK
RET_EPS, RW_EPS = 1e-5, 64e-5
FEATURE_BLOCKS = 14

GROUPS, PER_GROUP = 4, 8
EXPERTS = GROUPS * PER_GROUP
FF = 512
FT = FF // P
PAIRS = EXPERTS // 2
SLOTS_E = 64

M_HEADS, M_DIM = 8, 64
F_HEADS, F_DIM = 4, 128
LAMBDA_INIT = 0.2
SECOND_ORDER = (0, 1, 3, 4, 2, 5)
NEG = -1e30

P_HEADS = 8
NKEYS = 128
TOPK = 16
SLOTS = P_HEADS * TOPK
PAIRS_IN = 4 * TOPK + (TOPK - 4) * 4
EARLY = 16

COLS = {}
_at = 0
for _name, _n in (("norm1", K), ("norm2", K), ("attn", K), ("ffn", K), ("mu", FEATURE_BLOCKS), ("w0", 4), ("a0", 4),
                  ("k_k", 4), ("k_a", 4), ("r_k", 4)):
    COLS[_name] = (_at, _n)
    _at += _n
N_COLS = _at

ROWS1 = {"ret_gain": (0, 512), "rw_gain": (512, 512), "route_bias": (1024, 36)}
N_ROWS1 = 1060
ROWS2 = {"final": (0, D), "mq": (1024, 64), "mk": (1088, 64), "dq": (1152, 128), "dk": (1280, 128),
         "lambda": (1408, 256), "m_out": (1664, 512), "d_out": (2176, 512)}
N_ROWS2 = 2688

SLOT = 4096
RING = 0
RING_SLOTS = 3
SPARE = RING_SLOTS * SLOT
WORK = 4 * SLOT
MORE = WORK + 16384
KEPT = MORE + 12288
END = 53200


class Order:

    def __init__(self, sem):
        self.sem, self.n = sem, 0

    def step(self, ins):
        ins.then_inc(self.sem, 1)
        self.n += 1
        return ins

    def settle(self, eng):
        eng.wait_ge(self.sem, self.n)


class Banks:

    def __init__(self, kernel, name, banks):
        self.banks = [kernel.psum[b] for b in banks]
        self.filled = kernel.sem(name + "_filled")
        self.emptied = kernel.sem(name + "_emptied")

    def free(self, pe, job):
        if job >= len(self.banks):
            pe.wait_ge(self.emptied, job - len(self.banks) + 1)
        return self.banks[job % len(self.banks)]

    def ready(self, eng, job):
        eng.wait_ge(self.filled, job + 1)
        return self.banks[job % len(self.banks)]


class Split:

    RING = 4

    def __init__(self, kernel, name, at, ring_at, first, x_in_order=True):
        self.kernel, self.first, self.x_in_order = kernel, first, x_in_order
        self.x_high = kernel.parts(name + "_x_high", at, K, T)
        self.x_low = kernel.parts(name + "_x_low", at + K * T, K, T)
        self.w_high = kernel.parts(name + "_w_high", ring_at, self.RING, 512)
        self.x_high_ready, self.x_low_ready, self.high_ready, self.low_ready, self.high_used = (
            kernel.sem(f"{name}_{n}") for n in ("x_high", "x_low", "w_high", "w_low", "w_high_used"))

    def x_highs(self, act):
        for n in range(4):
            act.activation(self.x_high[:, 2 * n:2 * n + 2, :], self.kernel.xT[:, 2 * n:2 * n + 2, :],
                           ACT.Copy).then_inc(self.x_high_ready, 1)

    def x_lows(self, vec):
        for n in range(4):
            ks = slice(2 * n, 2 * n + 2)
            vec.wait_ge(self.x_high_ready, n + 1)
            vec.tensor_tensor(self.x_low[:, ks, :], self.kernel.xT[:, ks, :], self.x_high[:, ks, :],
                              ALU.subtract).then_inc(self.x_low_ready, 1)

    def high(self, act, c, k):
        step = c * K + k
        if k == 0:
            self.whole = self.kernel.chunk(act, self.first + c)
        if step >= self.RING:
            act.wait_ge(self.high_used, step - self.RING + 1)
        act.activation(self.w_high[:, step % self.RING, :], self.whole[:, k, :], ACT.Copy).then_inc(self.high_ready, 1)

    def lows(self, pool, chunks):
        for c in range(chunks):
            slot = self.kernel.slot_of(self.first + c)
            whole, low = self.kernel.at(RING + slot * SLOT, K, 512), self.kernel.w_low[slot]
            for k in range(K):
                step = c * K + k
                pool.wait_ge(self.high_ready, step + 1)
                pool.tensor_tensor(low[k // 4][:, k % 4, :], whole[:, k, :], self.w_high[:, step % self.RING, :],
                                   ALU.subtract).then_inc(self.low_ready, 1)

    def products(self, pe, c, banks):
        free = [banks.free(pe, c * TT + t) for t in range(TT)]
        low = self.kernel.w_low[self.kernel.slot_of(self.first + c)]
        for k in range(K):
            step = c * K + k
            if c == 0:
                pe.wait_ge(self.x_low_ready, k // 2 + 1 if self.x_in_order else 4)
            pe.wait_ge(self.low_ready, step + 1)
            high = self.w_high[:, step % self.RING, :]
            for t in range(TT):
                tokens = slice(t * P, (t + 1) * P)
                pe.matmul(free[t][:, :], self.x_high[:, k, tokens], high, start=(k == 0), stop=False)
                used = pe.matmul(free[t][:, :], self.x_low[:, k, tokens], high, start=False, stop=False)
                last = pe.matmul(free[t][:, :], self.x_high[:, k, tokens], low[k // 4][:, k % 4, :], start=False,
                                 stop=(k == K - 1))
                if k == K - 1:
                    last.then_inc(banks.filled, 1)
            used.then_inc(self.high_used, 1)


class Kernel:
    def __init__(self, nc, ctx, ins, out):
        self.nc, self.ctx, self.ins, self.out = nc, ctx, ins, out
        self.mem_start = -(-nc.sbuf_base // 32) * 32
        self.mem = ctx.enter_context(nc.sbuf_tensor("mem", [P, END], F32))
        self.psum = [ctx.enter_context(nc.psum_tensor(f"bank{i}", [P, 512], F32)) for i in range(8)]
        self.part_sems = []
        self.vec = Order(self.lasting_sem("vector_order"))
        self.place_kept()
        self.landed = [self.lasting_sem(f"slot{i}_landed") for i in range(6)]
        self.x_landed, self.const_landed = self.lasting_sem("x_landed"), self.lasting_sem("const_landed")
        self.loads = [0] * 6
        self.w_low = [[self.parts(f"slot{s}_low{half}", RING + s * SLOT + half * SLOT // 2, K // 2, 512) for half in range(2)]
                      for s in range(RING_SLOTS)]
        self.used_by = {}
        self.issued = 0
        i = self.ins
        self.chunks = [(i["w_in"][c], 512) for c in range(4)] + [(i["w_in_lora"], 256)]
        self.chunks += [(i["w_in"][c], 512) for c in range(4, 7)]
        self.chunks += [(i["w_out"][c], 512) for c in range(2)]
        self.first_half = len(self.chunks)
        self.chunks += [(i["w_in_2"][c], 512) for c in SECOND_ORDER] + [(i["w_out_2"][c], 512) for c in range(2)]
        self.chunks += [(i["peer_query"][c], 512) for c in range(4)]

    def sem(self, name):
        handle = self.nc.alloc_semaphore(name=name)
        self.part_sems.append(handle)
        return handle

    def lasting_sem(self, name):
        return self.ctx.enter_context(self.nc.semaphore(name))

    def end_part(self):
        self.nc.clear_and_free_semaphores(self.part_sems)
        self.nc.all_engine_barrier()
        self.part_sems = []

    def at(self, off, *shape):
        n = int(np.prod(shape))
        assert off + n <= END, (off, shape)
        ap = self.mem[:, off:off + n]
        if len(shape) == 1:
            return ap
        names = "abcd"[:len(shape)]
        return ap.rearrange(f"p ({' '.join(names)}) -> p {' '.join(names)}",
                            **{x: s for x, s in zip(names[1:], shape[1:])})

    def parts(self, name, off, *shape):
        n = int(np.prod(shape))
        assert off + n <= END, (off, shape)
        ap = self.nc.alloc_sbuf_tensor_at(name, [P, n], F32R, offset=self.mem_start + 4 * off)[:, :]
        if len(shape) == 1:
            return ap
        names = "abcd"[:len(shape)]
        return ap.rearrange(f"p ({' '.join(names)}) -> p {' '.join(names)}",
                            **{x: s for x, s in zip(names[1:], shape[1:])})

    def place_kept(self):
        self.cursor = KEPT

        def keep(*shape):
            ap = self.at(self.cursor, *shape)
            self.cursor += int(np.prod(shape))
            return ap

        self.h = keep(TT, D)
        self.xT = keep(K, T)
        self.ident = keep(P)
        self.iota_all = keep(2 * P + 1)
        self.iota = self.iota_all[:, 0:P]
        self.slot_number = self.iota_all[:, P:P + 1]
        self.up_to = self.iota_all[:, P + 1:]
        self.cols = keep(N_COLS)
        self.small = keep(64)
        self.slot_i = keep(T)
        self.slot_j = keep(T)
        self.slot_g = keep(T)
        self.lt = keep(4)

    def col(self, name):
        o, n = COLS[name]
        return self.cols[:, o:o + n]


    def slot_of(self, c):
        return c % RING_SLOTS

    def issue(self, sync, upto):
        while self.issued < min(upto, len(self.chunks)):
            c = self.issued
            if c >= RING_SLOTS and not self.first_half <= c < self.first_half + RING_SLOTS:
                sync.wait_ge(*self.used_by[c - RING_SLOTS])
            src, n = self.chunks[c]
            s = self.slot_of(c)
            sync.dma_start(self.at(RING + s * SLOT, K, n), src).then_inc(self.landed[s], 16)
            self.loads[s] += 1
            self.issued += 1

    def plan_chunk(self, c):
        s = self.slot_of(c)
        n = sum(1 for b in range(c + 1) if self.slot_of(b) == s)
        if c >= self.first_half:
            n += EXPERTS // 2
        return s, 16 * n

    def chunk(self, pe, c):
        s, value = self.plan_chunk(c)
        pe.wait_ge(self.landed[s], value)
        return self.at(RING + s * SLOT, K, self.chunks[c][1])


    def rms_to_features(self, name, gain, first=False, scaled_at=WORK):
        nc, h, xT, ident = self.nc, self.h, self.xT, self.ident
        scaled = self.at(scaled_at, TT, D)
        ss, ms, root, rstd = (self.small[:, i * 2:i * 2 + 2] for i in range(4))
        squares, mean_ready, root_ready, scaled_ready = (
            self.sem(f"{name}_{x}") for x in ("squares", "mean", "root", "scaled"))
        turned = Banks(self, name + "_turned", [0, 1, 2, 3])
        order = self.vec
        with nc.Block() as block:
            if first:
                @block.sync
                def _(sync):
                    self.load_first(sync)

            @block.scalar
            def _(act):
                if first:
                    act.wait_ge(self.x_landed, 16)
                for t in range(TT):
                    act.activation(scaled[:, t, :], h[:, t, :], ACT.Square, accum_out=ss[:, t:t + 1]).then_inc(squares, 1)
                act.wait_ge(mean_ready, 1)
                act.activation(root, ms, ACT.Sqrt).then_inc(root_ready, 1)

            @block.vector
            def _(vec):
                vec.wait_ge(squares, TT)
                vec.tensor_scalar(ms, ss, 1.0 / D, EPS, ALU.mult, ALU.add).then_inc(mean_ready, 1)
                vec.wait_ge(root_ready, 1)
                order.step(vec.reciprocal(rstd, root))
                order.settle(vec)
                for t in range(TT):
                    vec.tensor_scalar(scaled[:, t, :], h[:, t, :], rstd[:, t:t + 1], None, ALU.mult).then_inc(scaled_ready, 1)
                if first:
                    vec.wait_ge(self.const_landed, 16 * self.n_const)
                g = self.col(gain)
                for job in range(2 * TT):
                    t, half = divmod(job, 2)
                    bank = turned.ready(vec, job)
                    ks = slice(4 * half, 4 * half + 4)
                    vec.tensor_tensor(xT[:, ks, t * P:(t + 1) * P], bank[:, :].rearrange("p (k t) -> p k t", k=4),
                                      g[:, ks].unsqueeze(2).broadcast_to([P, 4, P]), ALU.mult).then_inc(turned.emptied, 1)

            @block.tensor
            def _(pe):
                if first:
                    pe.wait_ge(self.const_landed, 16 * self.n_const)
                for job in range(2 * TT):
                    t, half = divmod(job, 2)
                    pe.wait_ge(scaled_ready, t + 1)
                    bank = turned.free(pe, job)
                    for k in range(4):
                        last = pe.transpose(bank[:, k * P:(k + 1) * P],
                                            scaled[:, t, (4 * half + k) * P:(4 * half + k + 1) * P], ident)
                    last.then_inc(turned.filled, 1)

    def load_first(self, sync):
        i = self.ins
        sync.dma_start(self.h, i["x"].rearrange("(t p) d -> p t d", p=P)).then_inc(self.x_landed, 16)
        for dst, src in self.consts:
            sync.dma_start(dst, src).then_inc(self.const_landed, 16)
        self.issue(sync, RING_SLOTS)


    def place_first(self):
        i = self.ins
        at = self.at
        o = WORK
        self.qkvg = at(o, 4, TT, 512)
        self.qkT = at(o + 4096, 2, RET_HEADS, T)
        self.rotated = at(o + 6144, 2, TT, 512)
        self.ret_decay = at(o + 8192, RET_HEADS, 384)
        self.ret_p = at(o + 9728, 2, 384)
        self.tok_b = at(o, TT, RW_HEADS, RW_DIM)
        self.tok_k = at(o + 1024, TT, RW_HEADS, RW_DIM)
        self.tok_au = at(o + 2048, TT, RW_HEADS, P)
        self.wz = at(o + 4096, TT, RW_HEADS, P)
        self.phi = at(o + 6144, CHUNKS, 4, 2, RW_DIM)
        self.q_hat = at(o + 8192, 4, T)
        self.y_local = at(o + 9216, TT, RW_HEADS, RW_DIM)
        o = WORK + 10496
        self.mixed = at(o, TT, D)
        self.tok_v = at(o + 2048, TT, RW_HEADS, RW_DIM)
        self.gate = at(o + 3072, TT, 512)
        self.tmp = at(o + 4096, 4, T)
        assert o + 5120 <= MORE
        self.lora = at(SPARE, 2, T)
        self.carry = at(SPARE + 512, 4, T)
        self.raw = at(SPARE + 1536, 4, T + 1)
        self.rows1 = at(SPARE + 2564, N_ROWS1)
        f = [at(MORE + 1024 * n, 4, T) for n in range(12)]
        self.f_r, self.f_k, self.f_v, self.f_l, self.f_a, self.f_kk, self.f_k2 = f[:7]
        self.f_b, self.f_kt, self.f_x = f[7], f[8], f[11]
        self.f_ar = at(MORE + 1024 * 9, 4, TT, 2, P)
        self.up_wa = at(MORE + 1024 * 9, 512)
        self.up_g = at(MORE + 1024 * 9 + 512, 512)
        free = RING + SLOT
        self.u_k = [at(MORE, 4, 256), at(MORE + 4608, 4, 256)]
        self.u_b = [at(MORE + 1024, 4, 256), at(MORE + 5632, 4, 256)]
        self.u_n = [at(MORE + 2048, 2, 4, P), at(free, 2, 4, P)]
        self.u_x = [at(MORE + 3072, 4, P), at(MORE + 6656, 4, P)]
        self.u_xt = [at(MORE + 3584, 4, P), at(free + 1024, 4, P)]
        self.u_p = [at(MORE + 4096, 4, P), at(free + 1536, 4, P)]
        c = self.cursor
        self.mask_pair = at(c, 2, P)
        self.mask_level = at(c + 256, 5, P)
        self.mask_two = at(c + 896, 2, P)
        self.ones_head = at(c + 1152, P)
        self.ident64 = at(c + 1280, RW_DIM)
        self.rope1 = at(c + 1344, 2, TT, RET_DIM // 2)
        self.pair_ones = at(c + 1600, 2)
        self.decay_end = at(c + 1602, 4, CHUNKS)
        self.state = at(c + 1618, 4, RW_DIM)
        self.bonus = at(c + 1874, TT, RW_HEADS)
        self.stat = at(c + 1890, 12, 16)
        assert c + 2082 <= END
        self.consts = [(self.cols, i["cols"]), (self.ident, i["ident"]), (self.iota_all, i["iota"]),
                       (at(c, 1602), i["const1"]), (self.carry, i["carry"]),
                       (self.ret_decay, i["ret_decay"]), (at(MORE + 1024 * 9, 1024), i["lora_up"]),
                       (self.rows1, i["rows1"].partition_broadcast(P))]
        self.n_const = len(self.consts)

    def project_and_retain(self):
        nc, xT, ident = self.nc, self.xT, self.ident
        tokens = Banks(self, "project_tokens", [0, 1, 2, 3])
        features = Banks(self, "project_features", [6, 7])
        split = Split(self, "first", MORE + 3072, MORE + 7168, 0)
        raw_used, pad_ready = self.sem("raw_used"), self.sem("raw_pad_ready")
        targets = [self.lora[:, 0, :], self.lora[:, 1, :]]
        targets += [f[:, b, :] for f in (self.f_r, self.f_k, self.f_v) for b in range(4)]
        mu_of = [12, 13] + list(range(12))
        turned = Banks(self, "ret_turned", [0, 1])
        scores = Banks(self, "ret_scores", [2, 3])
        outs = [self.psum[4], self.psum[5]]
        p_ready, outs_ready, gate_ready = self.sem("ret_p_ready"), self.sem("ret_outs_ready"), self.sem("ret_gate_ready")
        var_ready, root_ready, rotated_ready = (self.sem("ret_" + n) for n in ("var_ready", "root_ready", "rotated"))
        scores.emptied = p_ready
        values = self.qkvg[:, 2]
        TURN, FIRST_HEAD, NORM, SCALE = 1, 2, 7, 9
        order = self.vec
        diff = self.tmp[:, 0, :]
        for c in range(4):
            self.used_by[c] = (tokens.filled, TT * (c + 1))
        for c in range(4, 8):
            self.used_by[c] = (features.filled, 2 + 4 * (c - 4))
        with nc.Block() as block:
            @block.sync
            def _(sync):
                self.issue(sync, 8 + 2)

            @block.tensor
            def _(pe):
                def turn_queries_keys():
                    pe.wait_ge(tokens.emptied, 4 * TT)
                    pe.wait_ge(rotated_ready, 4 * TT)
                    for job in range(2 * TT):
                        which, t = divmod(job, TT)
                        bank = turned.free(pe, job)
                        for h in range(RET_HEADS):
                            last = pe.transpose(bank[:, h * P:(h + 1) * P], self.rotated[:, which, t, h * P:(h + 1) * P],
                                                ident)
                        last.then_inc(turned.filled, 1)

                def head_scores(h):
                    if h == 0:
                        pe.wait_ge(turned.emptied, 2 * TT)
                    bank = scores.free(pe, h)
                    pe.matmul(bank[:, 0:T], self.qkT[:, 1, h, 0:P], self.qkT[:, 0, h, :], start=True, stop=True)
                    pe.matmul(bank[:, T:T + P], self.qkT[:, 1, h, P:T], self.qkT[:, 0, h, P:T],
                              start=True, stop=True).then_inc(scores.filled, 1)

                def head_out(h):
                    pe.wait_ge(p_ready, h + 1)
                    p = self.ret_p[:, h % 2]
                    hs = slice(h * P, (h + 1) * P)
                    pe.matmul(outs[0][:, hs], p[:, 0:P], values[:, 0, hs], start=True, stop=True)
                    pe.matmul(outs[1][:, hs], p[:, P:T], values[:, 0, hs], start=True, stop=False)
                    pe.matmul(outs[1][:, hs], p[:, T:T + P], values[:, 1, hs], start=False,
                              stop=True).then_inc(outs_ready, 1)

                for c in range(4):
                    split.products(pe, c, tokens)
                job = 0
                for c in range(4, 8):
                    w = self.chunk(pe, c)
                    for b in range(2 if c == 4 else 4):
                        bank = features.free(pe, job)
                        for k in range(K):
                            last = pe.matmul(bank[:, 0:T], w[:, k, b * P:(b + 1) * P], xT[:, k, :],
                                             start=(k == 0), stop=(k == K - 1))
                        last.then_inc(features.filled, 1)
                        if job == TURN:
                            turn_queries_keys()
                        h = job - FIRST_HEAD
                        if 0 <= h < RET_HEADS:
                            head_scores(h)
                        if 0 < h <= RET_HEADS:
                            head_out(h - 1)
                        job += 1

            @block.scalar
            def _(act):
                def copy_out(c):
                    for job in range(c * TT, (c + 1) * TT):
                        bank = tokens.ready(act, job)
                        act.activation(self.qkvg[:, c, job % TT, :], bank[:, :], ACT.Copy).then_inc(tokens.emptied, 1)

                split.x_highs(act)
                for c in range(4):
                    for k in range(K):
                        if c > 0 and k == K // 2:
                            copy_out(c - 1)
                        split.high(act, c, k)
                copy_out(3)
                act.wait_ge(pad_ready, 1)
                for job in range(FEATURE_BLOCKS):
                    bank = features.ready(act, job)
                    if job >= 4:
                        act.wait_ge(raw_used, job - 3)
                    act.activation(self.raw[:, job % 4, 1:T + 1], bank[:, 0:T], ACT.Copy).then_inc(features.emptied, 1)
                    if job == TURN:
                        for n in range(2 * TT):
                            which, t = divmod(n, TT)
                            bank = turned.ready(act, n)
                            act.activation(self.qkT[:, which, :, t * P:(t + 1) * P],
                                           bank[:, :].rearrange("p (h t) -> p h t", h=4), ACT.Copy).then_inc(turned.emptied, 1)
                        for t in range(TT):
                            act.activation(self.rotated[:, 0, t, :], self.qkvg[:, 3, t, :],
                                           ACT.Silu).then_inc(gate_ready, 1)
                    if job == SCALE:
                        act.wait_ge(var_ready, 1)
                        act.activation(self.stat[:, 4, 0:8], self.stat[:, 3, 0:8], ACT.Sqrt).then_inc(root_ready, 1)

            @block.gpsimd
            def _(pool):
                split.lows(pool, 4)

            @block.vector
            def _(vec):
                split.x_lows(vec)
                vec.memset(self.raw[:, :, 0:1], 0.0).then_inc(pad_ready, 1)
                cos, sin = self.rope1[:, 0], self.rope1[:, 1]
                half, rotations = RET_DIM // 2, 0
                a = self.tmp[:, 1, :].rearrange("p (h d) -> p h d", h=4)
                b = self.tmp[:, 2, :].rearrange("p (h d) -> p h d", h=4)
                for n in range(2 * TT):
                    which, t = divmod(n, TT)
                    vec.wait_ge(tokens.emptied, n + 1)
                    x = self.qkvg[:, which, t, :].rearrange("p (h d) -> p h d", h=4)
                    y = self.rotated[:, which, t, :].rearrange("p (h d) -> p h d", h=4)
                    c4 = cos[:, t, :].unsqueeze(1).broadcast_to([P, 4, half])
                    s4 = sin[:, t, :].unsqueeze(1).broadcast_to([P, 4, half])
                    x1, x2 = x[:, :, 0:half], x[:, :, half:]
                    for out, u, v, op in ((y[:, :, 0:half], c4, s4, ALU.subtract), (y[:, :, half:], s4, c4, ALU.add)):
                        order.step(vec.tensor_tensor(a, x1, u, ALU.mult))
                        order.step(vec.tensor_tensor(b, x2, v, ALU.mult))
                        order.settle(vec)
                        vec.tensor_tensor(out, a, b, op).then_inc(rotated_ready, 1)
                        rotations += 1
                        vec.wait_ge(rotated_ready, rotations)
                total, mean, square, var, root, rstd = (self.stat[:, n, 0:8].rearrange("p (t h) -> p t h", t=2) for n in
                                                        (0, 1, 2, 3, 4, 5))
                centred = self.rotated[:, 1]
                sq = self.mixed[:, :, 512:1024]
                heads = "p (h d) -> p h d"

                def over(x):
                    return x.unsqueeze(2).broadcast_to([P, RET_HEADS, RET_DIM])

                def decay_scores(h):
                    bank = scores.ready(vec, h)
                    if h >= 2:
                        vec.wait_ge(outs_ready, h - 1)
                    vec.tensor_tensor(self.ret_p[:, h % 2], bank[:, 0:384], self.ret_decay[:, h], ALU.mult).then_inc(p_ready, 1)

                def centre_and_square():
                    vec.wait_ge(outs_ready, RET_HEADS)
                    for t in range(TT):
                        order.step(vec.tensor_reduce(total[:, t], outs[t][:, :].rearrange(heads, h=4), AX.X, ALU.add))
                    order.settle(vec)
                    order.step(vec.tensor_scalar(mean, total, 1.0 / RET_DIM, None, ALU.mult))
                    order.settle(vec)
                    for t in range(TT):
                        order.step(vec.tensor_tensor(centred[:, t].rearrange(heads, h=4), outs[t][:, :].rearrange(heads, h=4),
                                                     over(mean[:, t]), ALU.subtract))
                    order.settle(vec)
                    for t in range(TT):
                        order.step(vec.tensor_tensor(sq[:, t], centred[:, t], centred[:, t], ALU.mult))
                    order.settle(vec)
                    for t in range(TT):
                        order.step(vec.tensor_reduce(square[:, t], sq[:, t].rearrange(heads, h=4), AX.X, ALU.add))
                    order.settle(vec)
                    vec.tensor_scalar(var, square, 1.0 / RET_DIM, RET_EPS, ALU.mult, ALU.add).then_inc(var_ready, 1)

                def scale_and_gate():
                    vec.wait_ge(root_ready, 1)
                    order.step(vec.reciprocal(rstd, root))
                    order.settle(vec)
                    o, n = ROWS1["ret_gain"]
                    vec.wait_ge(gate_ready, TT)
                    for t in range(TT):
                        order.step(vec.tensor_tensor(sq[:, t].rearrange(heads, h=4), centred[:, t].rearrange(heads, h=4),
                                                     over(rstd[:, t]), ALU.mult))
                        order.step(vec.tensor_tensor(self.rotated[:, 0, t], self.rotated[:, 0, t], self.rows1[:, o:o + n],
                                                     ALU.mult))
                    order.settle(vec)
                    for t in range(TT):
                        order.step(vec.tensor_tensor(self.mixed[:, t, 0:512], sq[:, t], self.rotated[:, 0, t], ALU.mult))

                mu = self.col("mu")
                for job in range(FEATURE_BLOCKS):
                    vec.wait_ge(features.emptied, job + 1)
                    now, before = self.raw[:, job % 4, 1:T + 1], self.raw[:, job % 4, 0:T]
                    order.step(vec.tensor_tensor(diff, before, now, ALU.subtract))
                    order.settle(vec)
                    vec.scalar_tensor_tensor(out=targets[job], in0=diff, scalar=mu[:, mu_of[job]:mu_of[job] + 1],
                                             in1=now, op0=ALU.mult, op1=ALU.add).then_inc(raw_used, 1)
                    vec.wait_ge(raw_used, job + 1)
                    if 0 <= job - FIRST_HEAD < RET_HEADS:
                        decay_scores(job - FIRST_HEAD)
                    if job == NORM:
                        centre_and_square()
                    if job == SCALE:
                        scale_and_gate()

    def rwkv_features(self):
        nc = self.nc
        lora_w, lora_a = Banks(self, "lora_w", [0, 1]), Banks(self, "lora_a", [2, 3])
        lora_g = Banks(self, "lora_g", [4, 5])
        norms = Banks(self, "kk_norms", [6, 7])
        bonus = Banks(self, "bonus", [0])
        squares_ready, bonus_in = self.sem("kk_squares_ready"), self.sem("bonus_in_ready")
        bounded, roots = self.sem("kk_bounded"), self.sem("kk_roots")
        tanh_ready, sig_ready = self.sem("tanh_ready"), self.sem("gate_sigmoid_ready")
        sums, excl, expd = self.sem("decay_sums_ready"), self.sem("decay_before_ready"), self.sem("decay_exps")
        order = self.vec
        f_r, f_k, f_l, f_a, f_kk, f_k2, f_x, tmp = (self.f_r, self.f_k, self.f_l, self.f_a, self.f_kk, self.f_k2,
                                                    self.f_x, self.tmp)

        def wide(name):
            return self.col(name).unsqueeze(2).broadcast_to([P, 4, T])

        with nc.Block() as block:
            @block.tensor
            def _(pe):
                pe.wait_ge(tanh_ready, 1)
                for stage, rows in ((lora_w, slice(0, 64)), (lora_a, slice(64, 128))):
                    for pair in range(2):
                        bank = stage.free(pe, pair)
                        for n in range(2):
                            b = 2 * pair + n
                            last = pe.matmul(bank[:, n * T:(n + 1) * T], self.up_wa[rows, b * P:(b + 1) * P],
                                             self.lora[rows, 0, :], start=True, stop=True)
                        last.then_inc(stage.filled, 1)
                pe.wait_ge(sig_ready, 1)
                for t in range(TT):
                    bank = lora_g.free(pe, t)
                    pe.matmul(bank[:, :], self.lora[:, 1, t * P:(t + 1) * P], self.up_g, start=True,
                              stop=True).then_inc(lora_g.filled, 1)
                pe.wait_ge(squares_ready, 1)
                for pair in range(2):
                    bank = norms.free(pe, pair)
                    pe.matmul(bank[:, :], self.ones_head, f_x[:, 2 * pair:2 * pair + 2, :], start=True,
                              stop=True).then_inc(norms.filled, 1)
                pe.wait_ge(bonus_in, 1)
                pe.wait_ge(lora_w.emptied, 2)
                bank = bonus.free(pe, 0)
                for t in range(TT):
                    for b in range(4):
                        last = pe.matmul(bank[:, t * 8 + 2 * b:t * 8 + 2 * b + 2], f_k[:, b, t * P:(t + 1) * P],
                                         self.pair_ones, start=True, stop=True)
                last.then_inc(bonus.filled, 1)

            @block.scalar
            def _(act):
                act.activation(self.lora[0:64, 0, :], self.lora[0:64, 0, :], ACT.Tanh).then_inc(tanh_ready, 1)
                act.activation(self.lora[:, 1, :], self.lora[:, 1, :], ACT.Sigmoid).then_inc(sig_ready, 1)
                for stage, dst, bias in ((lora_w, f_l, "w0"), (lora_a, f_a, "a0")):
                    for pair in range(2):
                        bank = stage.ready(act, pair)
                        for n in range(2):
                            b = 2 * pair + n
                            last = act.activation(dst[:, b, :], bank[:, n * T:(n + 1) * T], ACT.Sigmoid,
                                                  bias=self.col(bias)[:, b:b + 1])
                        last.then_inc(stage.emptied, 1)
                for t in range(TT):
                    bank = lora_g.ready(act, t)
                    act.activation(self.gate[:, t, :], bank[:, :], ACT.Copy).then_inc(lora_g.emptied, 1)
                act.wait_ge(bounded, 2)
                act.activation(f_x, tmp, ACT.Sqrt).then_inc(roots, 1)
                act.wait_ge(sums, 1)
                act.wait_ge(excl, 1)
                act.activation(f_l, f_l, ACT.Exp).then_inc(expd, 1)
                act.activation(tmp, f_x, ACT.Exp, scale=-1.0).then_inc(expd, 1)
                act.wait_ge(expd, 2)
                act.activation(f_x, f_x, ACT.Exp).then_inc(expd, 1)

            @block.vector
            def _(vec):
                order.step(vec.tensor_tensor(f_kk, f_k, wide("k_k"), ALU.mult))
                order.settle(vec)
                vec.tensor_tensor(f_x, f_kk, f_kk, ALU.mult).then_inc(squares_ready, 1)
                for pair in range(2):
                    bank = norms.ready(vec, pair)
                    vec.tensor_scalar(tmp[:, 2 * pair:2 * pair + 2, :].rearrange("p b t -> p (b t)"), bank[:, :], 1e-24,
                                      None, ALU.max).then_inc(bounded, 1)
                vec.wait_ge(roots, 1)
                order.step(vec.reciprocal(tmp, f_x))
                order.settle(vec)
                order.step(vec.tensor_tensor(f_kk, f_kk, tmp, ALU.mult))
                vec.wait_ge(lora_a.emptied, 2)
                order.settle(vec)
                order.step(vec.scalar_tensor_tensor(out=tmp, in0=f_a, scalar=1.0, in1=wide("k_a"), op0=ALU.subtract,
                                                    op1=ALU.mult))
                order.settle(vec)
                order.step(vec.scalar_tensor_tensor(out=f_k2, in0=tmp, scalar=1.0, in1=f_k, op0=ALU.add, op1=ALU.mult))
                order.settle(vec)
                order.step(vec.tensor_tensor(f_k, f_r, f_k2, ALU.mult))
                order.step(vec.tensor_tensor(f_a, f_a, f_kk, ALU.mult))
                order.settle(vec)
                vec.tensor_tensor(f_k, f_k, wide("r_k"), ALU.mult).then_inc(bonus_in, 1)
                order.step(vec.tensor_scalar(f_l, f_l, -float(np.exp(-0.5)), None, ALU.mult))
                order.settle(vec)
                flat = "p b t -> p (b t)"
                vec.tensor_tensor_scan(f_x.rearrange(flat), self.carry.rearrange(flat), f_l.rearrange(flat), 0.0,
                                       ALU.mult, ALU.add).then_inc(sums, 1)
                vec.wait_ge(sums, 1)
                vec.tensor_tensor(f_l, f_x, f_l, ALU.subtract).then_inc(excl, 1)
                vec.wait_ge(expd, 1)
                vec.wait_ge(lora_g.emptied, TT)
                pairs = "p b t a x -> p (b t) a x"
                ar = self.f_ar.rearrange(pairs)

                def tiles(x):
                    return x.rearrange("p b (t x) -> p (b t) x", t=TT)

                order.step(vec.scalar_tensor_tensor(out=ar[:, :, 0, :], in0=tiles(f_kk), scalar=-1.0, in1=tiles(f_l),
                                                    op0=ALU.mult, op1=ALU.mult))
                vec.wait_ge(expd, 2)
                order.step(vec.tensor_tensor(self.f_b, f_a, tmp, ALU.mult))
                order.step(vec.tensor_tensor(self.f_kt, f_k2, tmp, ALU.mult))
                vec.wait_ge(expd, 3)
                order.step(vec.tensor_tensor(ar[:, :, 1, :], tiles(f_r), tiles(f_x), ALU.mult))
                order.step(vec.tensor_copy(self.decay_end, f_x[:, :, CHUNK - 1::CHUNK]))
                bank = bonus.ready(vec, 0)
                order.step(vec.tensor_copy(self.bonus, bank[:, 0:16].rearrange("p (t h) -> p t h", t=2)))

    def rwkv_turn(self):
        nc, ident = self.nc, self.ident
        turned = Banks(self, "rwkv_turned", [0, 1, 2, 3])
        with nc.Block() as block:
            sources = [lambda b, t: self.f_v[:, b, t * P:(t + 1) * P], lambda b, t: self.f_ar[:, b, t, 0, :],
                       lambda b, t: self.f_b[:, b, t * P:(t + 1) * P], lambda b, t: self.f_kt[:, b, t * P:(t + 1) * P]]
            targets = [self.tok_v, self.tok_au[:, :, :, 0:RW_DIM], self.tok_b, self.tok_k]

            @block.tensor
            def _(pe):
                for job in range(4 * TT):
                    which, t = divmod(job, TT)
                    bank = turned.free(pe, job)
                    for b in range(4):
                        last = pe.transpose(bank[:, b * P:(b + 1) * P], sources[which](b, t), ident)
                    last.then_inc(turned.filled, 1)

            @block.scalar
            def _(act):
                for job in range(4 * TT):
                    which, t = divmod(job, TT)
                    bank = turned.ready(act, job)
                    act.activation(targets[which][:, t], bank[:, :].rearrange("p (h d) -> p h d", h=8),
                                   ACT.Copy).then_inc(turned.emptied, 1)

    def rwkv_units(self):
        nc = self.nc
        SETS = range(2)
        LEVELS = 5

        def of_sets(name, banks):
            return [Banks(self, f"unit_{name}{s}", [banks[s]]) for s in SETS]

        scores = Banks(self, "unit_scores", [6, 7])
        level_p, level_xt, level_x = of_sets("p", [0, 1]), of_sets("xt", [2, 3]), of_sets("x", [4, 5])
        u_in, wz_in, q_in, y_in = of_sets("u", [0, 1]), of_sets("wz", [4, 5]), of_sets("q", [0, 1]), of_sets("y", [2, 3])
        phi_in = [Banks(self, f"unit_phi{s}", [4 + s, 6 + s]) for s in SETS]
        masked = self.sem("unit_masked")
        level_masks = [self.sem(f"unit_level_masks{s}") for s in SETS]
        x_ready = [self.sem(f"unit_x_first{s}") for s in SETS]
        scores.emptied = masked
        order = self.vec

        def heads_of(bank, width):
            return bank.rearrange("p (n s) -> p n s", s=width)

        with nc.Block() as block:
            def rows(h):
                return slice(64 * (h % 2), 64 * (h % 2) + 64)

            @block.tensor
            def _(pe):
                def score(t, s):
                    cols = slice(t * P, (t + 1) * P)
                    for part in range(6):
                        kind, parity = divmod(part, 2)
                        bank = scores.free(pe, 12 * t + 6 * s + part)
                        for n in range(2):
                            h = 4 * s + parity + 2 * n
                            b, r = h // 2, rows(h)
                            if kind < 2:
                                left = (self.f_kt, self.f_b)[kind]
                                last = pe.matmul(bank[:, n * T:(n + 1) * T], left[r, b, cols],
                                                 self.f_ar[r, b, t].rearrange("p a x -> p (a x)"), start=True, stop=True)
                            else:
                                last = pe.matmul(bank[:, n * P:(n + 1) * P], self.f_ar[r, b, t, 0, :],
                                                 self.f_b[r, b, cols], start=True, stop=True)
                        last.then_inc(scores.filled, 1)

                def level_first(t, s, level):
                    done = t * LEVELS + level
                    pe.wait_ge(level_masks[s], done + 1)
                    if level == 0:
                        pe.wait_ge(x_ready[s], 2 * (t + 1))
                    else:
                        pe.wait_ge(level_x[s].emptied, done - t)
                    bank = level_p[s].free(pe, done)
                    for n in range(4):
                        last = pe.matmul(bank[:, n * P:(n + 1) * P], self.u_n[s][:, done % 2, n, :], self.u_x[s][:, n, :],
                                         start=True, stop=True)
                    last.then_inc(level_p[s].filled, 1)

                def level_second(t, s, level):
                    done = t * LEVELS + level
                    pe.wait_ge(level_p[s].emptied, done + 1)
                    bank = level_xt[s].free(pe, done)
                    for n in range(4):
                        last = pe.matmul(bank[:, n * P:(n + 1) * P], self.u_p[s][:, n, :], self.u_xt[s][:, n, :],
                                         start=True, stop=True)
                    last.then_inc(level_xt[s].filled, 1)
                    if level < LEVELS - 1:
                        bank = level_x[s].free(pe, done - t)
                        for n in range(4):
                            last = pe.matmul(bank[:, n * P:(n + 1) * P], self.u_xt[s][:, n, :], self.u_p[s][:, n, :],
                                             start=True, stop=True)
                        last.then_inc(level_x[s].filled, 1)

                def products_u(t, s):
                    bank = u_in[s].free(pe, t)
                    for n in range(4):
                        last = pe.matmul(bank[:, n * 64:(n + 1) * 64], self.u_k[s][:, n, 0:P], self.tok_v[:, t, 4 * s + n, :],
                                         start=True, stop=True)
                    last.then_inc(u_in[s].filled, 1)

                def products_wz(t, s):
                    pe.wait_ge(level_xt[s].emptied, LEVELS * (t + 1))
                    pe.wait_ge(u_in[s].emptied, t + 1)
                    bank = wz_in[s].free(pe, t)
                    for n in range(4):
                        last = pe.matmul(bank[:, n * P:(n + 1) * P], self.u_xt[s][:, n, :], self.tok_au[:, t, 4 * s + n, :],
                                         start=True, stop=True)
                    last.then_inc(wz_in[s].filled, 1)

                def products_out(t, s):
                    pe.wait_ge(wz_in[s].emptied, t + 1)
                    bank = q_in[s].free(pe, t)
                    for n in range(4):
                        h = 4 * s + n
                        last = pe.matmul(bank[rows(h), (n // 2) * P:(n // 2 + 1) * P], self.wz[:, t, h, 0:64],
                                         self.u_b[s][:, n, P:2 * P], start=True, stop=True)
                    last.then_inc(q_in[s].filled, 1)
                    bank = y_in[s].free(pe, t)
                    for n in range(4):
                        h = 4 * s + n
                        pe.matmul(bank[:, n * 64:(n + 1) * 64], self.u_k[s][:, n, P:2 * P], self.tok_v[:, t, h, :],
                                  start=True, stop=False)
                        last = pe.matmul(bank[:, n * 64:(n + 1) * 64], self.u_b[s][:, n, P:2 * P], self.wz[:, t, h, 64:P],
                                         start=False, stop=True)
                    last.then_inc(y_in[s].filled, 1)
                    for c in range(2):
                        bank = phi_in[s].free(pe, 2 * t + c)
                        r = slice(64 * c, 64 * c + 64)
                        for n in range(4):
                            h = 4 * s + n
                            out = bank[rows(h), (n // 2) * P:(n // 2 + 1) * P]
                            pe.matmul(out[:, 0:64], self.wz[r, t, h, 0:64], self.tok_b[r, t, h, :], start=True, stop=True)
                            pe.matmul(out[:, 64:P], self.tok_b[r, t, h, :], self.wz[r, t, h, 64:P], start=True, stop=False)
                            last = pe.matmul(out[:, 64:P], self.tok_k[r, t, h, :], self.tok_v[r, t, h, :],
                                             start=False, stop=True)
                        last.then_inc(phi_in[s].filled, 1)

                for t in range(TT):
                    for s in SETS:
                        if t > 0:
                            for other in SETS:
                                pe.wait_ge(phi_in[other].emptied, 2 * t)
                            pe.wait_ge(q_in[s].emptied, t)
                            pe.wait_ge(y_in[s].emptied, t)
                        score(t, s)
                    for level in range(LEVELS):
                        for s in SETS:
                            level_first(t, s, level)
                        for s in SETS:
                            level_second(t, s, level)
                    for stage in (products_u, products_wz, products_out):
                        for s in SETS:
                            stage(t, s)

            @block.scalar
            def _(act):
                for t in range(TT):
                    for level in range(LEVELS):
                        for s in SETS:
                            bank = level_p[s].ready(act, t * LEVELS + level)
                            act.activation(self.u_p[s], heads_of(bank[:, :], P), ACT.Copy).then_inc(level_p[s].emptied, 1)
                    for s in SETS:
                        bank = u_in[s].ready(act, t)
                        act.activation(self.tok_au[:, t, 4 * s:4 * s + 4, 64:P], heads_of(bank[:, 0:T], 64),
                                       ACT.Copy).then_inc(u_in[s].emptied, 1)
                    for s in SETS:
                        bank = wz_in[s].ready(act, t)
                        act.activation(self.wz[:, t, 4 * s:4 * s + 4, :], heads_of(bank[:, :], P),
                                       ACT.Copy).then_inc(wz_in[s].emptied, 1)
                    for s in SETS:
                        bank = y_in[s].ready(act, t)
                        act.activation(self.y_local[:, t, 4 * s:4 * s + 4, :], heads_of(bank[:, 0:T], 64),
                                       ACT.Copy).then_inc(y_in[s].emptied, 1)

            @block.gpsimd
            def _(pool):
                for t in range(TT):
                    for level in range(LEVELS):
                        for s in SETS:
                            if level == 0:
                                pool.wait_ge(masked, 12 * t + 6 * (s + 1))
                            if t * LEVELS + level >= 2:
                                pool.wait_ge(level_p[s].filled, t * LEVELS + level - 1)
                            pool.tensor_tensor(self.u_n[s][:, (t * LEVELS + level) % 2], self.u_b[s][:, :, 0:P],
                                               self.mask_level[:, level, :].unsqueeze(1).broadcast_to([P, 4, P]),
                                               ALU.mult).then_inc(level_masks[s], 1)

            @block.vector
            def _(vec):
                def mask_scores(t, s):
                    for part in range(6):
                        kind, parity = divmod(part, 2)
                        bank = scores.ready(vec, 12 * t + 6 * s + part)
                        if kind < 2:
                            dst = (self.u_k[s], self.u_b[s])[kind][:, parity::2, :]
                            mask = self.mask_pair.rearrange("p a x -> p (a x)").unsqueeze(1).broadcast_to([P, 2, T])
                            src = heads_of(bank[:, :], T)
                        else:
                            dst = self.u_x[s][:, parity::2, :]
                            mask = self.mask_two[:, 0, :].unsqueeze(1).broadcast_to([P, 2, P])
                            src = heads_of(bank[:, 0:T], P)
                        vec.tensor_tensor(dst, src, mask, ALU.mult).then_inc(masked, 1)
                    vec.wait_ge(masked, 12 * t + 6 * (s + 1))
                    order.step(vec.tensor_tensor(self.u_xt[s], self.u_b[s][:, :, 0:P],
                                                 self.mask_two[:, 1, :].unsqueeze(1).broadcast_to([P, 4, P]), ALU.mult))
                    order.settle(vec)
                    for x in (self.u_x[s], self.u_xt[s]):
                        vec.tensor_tensor(x, x, self.ident.unsqueeze(1).broadcast_to([P, 4, P]),
                                          ALU.add).then_inc(x_ready[s], 1)
                    vec.wait_ge(x_ready[s], 2 * (t + 1))

                def add_level(t, s, level):
                    done = t * LEVELS + level
                    bank = level_xt[s].ready(vec, done)
                    if level < LEVELS - 1:
                        level_x[s].ready(vec, done - t)
                    vec.tensor_tensor(self.u_xt[s], self.u_xt[s], heads_of(bank[:, :], P),
                                      ALU.add).then_inc(level_xt[s].emptied, 1)
                    if level < LEVELS - 1:
                        bank = level_x[s].ready(vec, done - t)
                        vec.tensor_tensor(self.u_x[s], self.u_x[s], heads_of(bank[:, :], P),
                                          ALU.add).then_inc(level_x[s].emptied, 1)
                        vec.wait_ge(level_x[s].emptied, done - t + 1)

                def finish(t, s):
                    b0 = 2 * s
                    bank = q_in[s].ready(vec, t)
                    vec.tensor_tensor(self.q_hat[:, b0:b0 + 2, t * P:(t + 1) * P], heads_of(bank[:, 0:T], P),
                                      self.f_ar[:, b0:b0 + 2, t, 1, :], ALU.add).then_inc(q_in[s].emptied, 1)
                    for c in range(2):
                        bank = phi_in[s].ready(vec, 2 * t + c)
                        src = bank[:, 0:T].rearrange("p (n a x) -> p n a x", n=2, a=2)
                        dst = self.phi[:, 2 * t + c, b0:b0 + 2]
                        order.step(vec.tensor_copy(dst[:, :, 1, :], src[:, :, 1, :]))
                        vec.tensor_tensor(dst[:, :, 0, :], src[:, :, 0, :],
                                          self.ident64.unsqueeze(1).broadcast_to([P, 2, 64]),
                                          ALU.add).then_inc(phi_in[s].emptied, 1)

                for t in range(TT):
                    for s in SETS:
                        mask_scores(t, s)
                    for level in range(LEVELS):
                        for s in SETS:
                            add_level(t, s, level)
                    for s in SETS:
                        finish(t, s)

    def rwkv_scan(self):
        nc = self.nc
        cross = [[self.psum[2 * t + half] for half in range(2)] for t in range(TT)]
        nexts = [self.psum[4], self.psum[5]]
        cross_ready, next_ready = self.sem("cross_ready"), self.sem("next_state_ready")
        state_ready, var_ready, root_ready = (self.sem(n) for n in ("state_ready", "rwkv_var_ready", "rwkv_root_ready"))
        order = self.vec
        state = self.state
        with nc.Block() as block:
            @block.tensor
            def _(pe):
                for c in range(CHUNKS):
                    t, half_t = divmod(c, 2)
                    pe.wait_ge(state_ready, 2 * c + 1)
                    for par in range(2):
                        r = slice(64 * par, 64 * par + 64)
                        for b in range(4):
                            last = pe.matmul(cross[t][par][64 * half_t:64 * half_t + 64, b * 64:(b + 1) * 64],
                                             self.q_hat[r, b, c * CHUNK:(c + 1) * CHUNK], state[r, b, :],
                                             start=True, stop=True)
                    last.then_inc(cross_ready, 1)
                    if c < CHUNKS - 1:
                        for par in range(2):
                            r = slice(64 * par, 64 * par + 64)
                            for b in range(4):
                                last = pe.matmul(nexts[par][r, b * 64:(b + 1) * 64], self.phi[r, c, b, 0, :],
                                                 state[r, b, :], start=True, stop=True)
                        last.then_inc(next_ready, 1)

            @block.scalar
            def _(act):
                act.wait_ge(var_ready, 1)
                act.activation(self.stat[:, 4, :], self.stat[:, 3, :], ACT.Sqrt).then_inc(root_ready, 1)

            @block.vector
            def _(vec):
                vec.memset(state, 0.0).then_inc(state_ready, 1)
                for c in range(CHUNKS - 1):
                    vec.wait_ge(next_ready, c + 1)
                    vec.wait_ge(cross_ready, c + 1)
                    for par in range(2):
                        r = slice(64 * par, 64 * par + 64)
                        order.step(vec.tensor_tensor(state[r], nexts[par][r, 0:T].rearrange("p (b x) -> p b x", b=4),
                                                     self.phi[r, c, :, 1, :], ALU.add))
                    order.settle(vec)
                    for par in range(2):
                        r = slice(64 * par, 64 * par + 64)
                        vec.tensor_tensor(state[r], state[r],
                                          self.decay_end[r, :, c:c + 1].broadcast_to([64, 4, RW_DIM]),
                                          ALU.mult).then_inc(state_ready, 1)
                total, mean, square, var, root, rstd = (self.stat[:, n, :].rearrange("p (t h) -> p t h", t=2)
                                                        for n in range(6))
                y, wide = self.y_local, self.tmp.rearrange("p (t n) s -> p t (n s)", t=2)
                heads = "p (h d) -> p h d"

                def over(x):
                    return x.unsqueeze(2).broadcast_to([P, RW_HEADS, RW_DIM])

                vec.wait_ge(cross_ready, CHUNKS)
                for t in range(TT):
                    for par in range(2):
                        order.step(vec.tensor_tensor(y[:, t, par::2, :], y[:, t, par::2, :],
                                                     cross[t][par][:, 0:T].rearrange(heads, h=4), ALU.add))
                order.settle(vec)
                for t in range(TT):
                    order.step(vec.tensor_reduce(total[:, t], y[:, t], AX.X, ALU.add))
                order.settle(vec)
                order.step(vec.tensor_scalar(mean, total, 1.0 / RW_DIM, None, ALU.mult))
                order.settle(vec)
                for t in range(TT):
                    order.step(vec.tensor_tensor(y[:, t], y[:, t], over(mean[:, t]), ALU.subtract))
                order.settle(vec)
                for t in range(TT):
                    order.step(vec.tensor_tensor(wide[:, t].rearrange(heads, h=8), y[:, t], y[:, t], ALU.mult))
                order.settle(vec)
                for t in range(TT):
                    order.step(vec.tensor_reduce(square[:, t], wide[:, t].rearrange(heads, h=8), AX.X, ALU.add))
                order.settle(vec)
                vec.tensor_scalar(var, square, 1.0 / RW_DIM, RW_EPS, ALU.mult, ALU.add).then_inc(var_ready, 1)
                for t in range(TT):
                    order.step(vec.tensor_tensor(wide[:, t].rearrange(heads, h=8), self.tok_v[:, t], over(self.bonus[:, t]),
                                                 ALU.mult))
                vec.wait_ge(root_ready, 1)
                order.step(vec.reciprocal(rstd, root))
                order.settle(vec)
                for t in range(TT):
                    order.step(vec.tensor_tensor(y[:, t], y[:, t], over(rstd[:, t]), ALU.mult))
                order.settle(vec)
                o, n = ROWS1["rw_gain"]
                for t in range(TT):
                    order.step(vec.tensor_tensor(y[:, t], y[:, t], self.rows1[:, o:o + n].rearrange(heads, h=8), ALU.mult))
                order.settle(vec)
                for t in range(TT):
                    order.step(vec.tensor_tensor(y[:, t], y[:, t], wide[:, t].rearrange(heads, h=8), ALU.add))
                order.settle(vec)
                for t in range(TT):
                    order.step(vec.tensor_tensor(self.mixed[:, t, 512:1024].rearrange(heads, h=8), y[:, t],
                                                 self.gate[:, t].rearrange(heads, h=8), ALU.mult))

    def project_out(self, name, first_chunk, upto):
        nc, h, ident, mixed = self.nc, self.h, self.ident, self.mixed
        split = Split(self, name, MORE, MORE + 4096, first_chunk, x_in_order=False)
        turned = Banks(self, name + "_turned", [0, 1, 2, 3])
        sums = Banks(self, name + "_sums", [4, 5, 6, 7])
        for c in range(2):
            self.used_by[first_chunk + c] = (sums.filled, TT * (c + 1))
        with nc.Block() as block:
            @block.sync
            def _(sync):
                self.issue(sync, upto)

            @block.tensor
            def _(pe):
                for job in range(2 * TT):
                    t, half = divmod(job, 2)
                    bank = turned.free(pe, job)
                    for k in range(4):
                        last = pe.transpose(bank[:, k * P:(k + 1) * P], mixed[:, t, (4 * half + k) * P:(4 * half + k + 1) * P],
                                            ident)
                    last.then_inc(turned.filled, 1)
                for c in range(2):
                    split.products(pe, c, sums)

            @block.scalar
            def _(act):
                for job in range(2 * TT):
                    t, half = divmod(job, 2)
                    bank = turned.ready(act, job)
                    act.activation(split.x_high[:, 4 * half:4 * half + 4, t * P:(t + 1) * P],
                                   bank[:, :].rearrange("p (k t) -> p k t", k=4), ACT.Copy).then_inc(split.x_high_ready, 1)
                for c in range(2):
                    for k in range(K):
                        split.high(act, c, k)

            @block.gpsimd
            def _(pool):
                split.lows(pool, 2)

            @block.vector
            def _(vec):
                for job in range(2 * TT):
                    t, half = divmod(job, 2)
                    bank = turned.ready(vec, job)
                    vec.wait_ge(split.x_high_ready, job + 1)
                    part = slice(4 * half, 4 * half + 4), slice(t * P, (t + 1) * P)
                    vec.tensor_tensor(split.x_low[:, part[0], part[1]], bank[:, :].rearrange("p (k t) -> p k t", k=4),
                                      split.x_high[:, part[0], part[1]], ALU.subtract).then_inc(split.x_low_ready, 1)
                for job in range(2 * TT):
                    c, t = divmod(job, TT)
                    bank = sums.ready(vec, job)
                    part = h[:, t, c * 512:(c + 1) * 512]
                    vec.tensor_tensor(part, part, bank[:, :], ALU.add).then_inc(sums.emptied, 1)


    def place_experts(self):
        at = self.at
        self.pick = at(WORK + 8192, TT, PAIRS, P)
        self.put = at(WORK + 12288, PAIRS, T)
        self.normed = at(MORE, TT, D)
        self.gathered = at(MORE + 2048, K, P)
        self.gate_up = at(MORE + 3072, 2, 512)
        self.hid = at(MORE + 4096, 2, FT, SLOTS_E)
        self.slot_out = at(MORE + 4608, D)
        self.silu_s = at(MORE + 5632, FT, SLOTS_E)
        self.sum_t = at(MORE + 2048, K, T)
        self.selector = at(self.cursor, PAIRS, P)
        self.expert_w = at(WORK + 8192, EXPERTS, T)
        self.hidden = at(MORE, 2, FT, T)
        self.silu = at(MORE + 2048, 2, T)
        self.rows2 = at(MORE + 5900, N_ROWS2)
        self.const2 = at(MORE + 5900 + N_ROWS2, 256)
        o = MORE + 5900 + N_ROWS2 + 256
        self.route = at(o, K, 36)
        self.logits = at(o + 288, TT, 36)
        self.small_moe = at(o + 360, 29, 64)
        self.weights_t = at(o + 2216, 2, T)
        self.zeros = at(o + 2728, 320).bitcast(mybir.dt.bfloat16)
        self.ones = at(o + 3048, P)
        self.over_flag = at(o + 3176, 1)
        self.iota8 = self.iota[:, 0:8]
        self.weights_left = self.at(o + 3177, TT, EXPERTS)
        self.route_bias = self.at(o + 3241, GROUPS + EXPERTS)

    def route_tokens(self):
        nc = self.nc
        s = self.small_moe
        route_landed = self.sem("route_landed")
        logits_ready, exp_in, exp_out, pair_in, pair_out = (
            self.sem("route_" + n) for n in ("logits", "exp_in", "exp_out", "pair_in", "pair_out"))
        weights_ready, selector_ready = self.sem("route_weights"), self.sem("selector")
        zeros_ready = self.zeros_ready = self.sem("zeros_ready")
        counts_ready, chosen_ready = self.sem("slot_counts"), self.sem("chosen_experts")
        order = self.vec
        logits = self.logits

        def tile_view(n, width):
            return s[:, n, 0:TT * width].rearrange("p (t x) -> p t x", t=TT)

        gmax, shifted, gexp, gsum, gprob = tile_view(0, 1), tile_view(1, 4), tile_view(2, 4), tile_view(3, 1), tile_view(4, 1)
        equal, count, chosen, ones = tile_view(5, 4), tile_view(6, 4), tile_view(7, 4), s[:, 8, 0:4]
        product, inside, best = tile_view(9, 32), tile_view(10, 8), tile_view(11, 8)
        index, index_f = tile_view(12, 8).bitcast(U32), tile_view(13, 8)
        diff, ratio, denom, w0, w1 = (tile_view(14 + n, 1) for n in range(5))
        pick0, pick1 = tile_view(19, 8), tile_view(20, 8)
        weights, weights_all = tile_view(21, 32), self.weights_left
        mask, running, slot, fits = (tile_view(22 + n, 32) for n in range(4))
        picked, biggest = tile_view(26, 8), s[:, 27, 0:1]
        self.slot_weights, self.slots = weights, slot
        with nc.Block() as block:
            @block.sync
            def _(sync):
                sync.dma_start(self.route, self.ins["route"]).then_inc(route_landed, 16)
                o, n = ROWS1["route_bias"]
                sync.dma_start(self.route_bias, self.ins["rows1"][o:o + n].partition_broadcast(P)).then_inc(route_landed, 16)
                for e in range(2):
                    for n in range(3):
                        self.load_weight(sync, 0, e, n)

            @block.tensor
            def _(pe):
                pe.wait_ge(route_landed, 32)
                for t in range(TT):
                    for k in range(K):
                        last = pe.matmul(self.psum[t][:, 0:36], self.xT[:, k, t * P:(t + 1) * P], self.route[:, k, :],
                                         start=(k == 0), stop=(k == K - 1))
                    last.then_inc(logits_ready, 1)
                pe.wait_ge(chosen_ready, TT)
                pe.matmul(self.psum[3][:, 0:32], self.up_to, mask[:, 0, :], start=True, stop=True)
                pe.matmul(self.psum[3][:, 32:64], self.up_to, mask[:, 1, :], start=True, stop=False)
                pe.matmul(self.psum[3][:, 32:64], self.ones, mask[:, 0, :], start=False, stop=True)
                pe.matmul(self.psum[3][:, 64:96], self.ones, mask[:, 0, :], start=True, stop=False)
                pe.matmul(self.psum[3][:, 64:96], self.ones, mask[:, 1, :], start=False,
                          stop=True).then_inc(counts_ready, 1)

            @block.gpsimd
            def _(pool):
                pool.tensor_copy(self.selector[0:EXPERTS].rearrange("p q (e s) -> p (q e) s", e=2),
                                 self.ident[0:EXPERTS, 0:EXPERTS].unsqueeze(2).broadcast_to([EXPERTS, EXPERTS, 64])
                                 ).then_inc(selector_ready, 1)

            @block.scalar
            def _(act):
                act.wait_ge(exp_in, 1)
                act.activation(gexp, shifted, ACT.Exp).then_inc(exp_out, 1)
                act.wait_ge(pair_in, 1)
                act.activation(ratio, diff, ACT.Exp).then_inc(pair_out, 1)

            @block.vector
            def _(vec):
                vec.memset(self.zeros, 0.0).then_inc(zeros_ready, 1)
                order.step(vec.memset(ones, 1.0))
                order.step(vec.memset(self.ones, 1.0))
                for t in range(TT):
                    vec.wait_ge(logits_ready, t + 1)
                    order.step(vec.tensor_tensor(logits[:, t, :], self.psum[t][:, 0:36], self.route_bias, ALU.add))
                order.settle(vec)
                order.step(vec.tensor_reduce(gmax, logits[:, :, 0:GROUPS], AX.X, ALU.max))
                order.settle(vec)
                wide = gmax.broadcast_to([P, TT, GROUPS])
                order.step(vec.tensor_tensor(equal, logits[:, :, 0:GROUPS], wide, ALU.is_equal))
                vec.tensor_tensor(shifted, logits[:, :, 0:GROUPS], wide, ALU.subtract).then_inc(exp_in, 1)
                order.settle(vec)
                for t in range(TT):
                    order.step(vec.tensor_tensor_scan(count[:, t], ones, equal[:, t], 0.0, ALU.mult, ALU.add))
                order.settle(vec)
                order.step(vec.scalar_tensor_tensor(out=chosen, in0=count, scalar=1.0, in1=equal, op0=ALU.is_equal,
                                                    op1=ALU.mult))
                vec.wait_ge(exp_out, 1)
                order.step(vec.tensor_reduce(gsum, gexp, AX.X, ALU.add))
                order.settle(vec)
                order.step(vec.reciprocal(gprob, gsum))
                for t in range(TT):
                    order.step(vec.tensor_tensor(product[:, t].rearrange("p (g e) -> p g e", g=GROUPS),
                                                 logits[:, t, GROUPS:36].rearrange("p (g e) -> p g e", g=GROUPS),
                                                 chosen[:, t].unsqueeze(2).broadcast_to([P, GROUPS, PER_GROUP]), ALU.mult))
                order.settle(vec)
                for t in range(TT):
                    order.step(vec.tensor_reduce(inside[:, t], product[:, t].rearrange("p (g e) -> p e g", g=GROUPS),
                                                 AX.X, ALU.add))
                order.settle(vec)
                for t in range(TT):
                    order.step(vec.max(best[:, t], inside[:, t]))
                order.settle(vec)
                for t in range(TT):
                    order.step(vec.max_index(index[:, t], best[:, t], inside[:, t]))
                vec.tensor_tensor(diff, best[:, :, 1:2], best[:, :, 0:1], ALU.subtract).then_inc(pair_in, 1)
                order.settle(vec)
                order.step(vec.tensor_copy(index_f, index))
                order.settle(vec)
                for t in range(TT):
                    for n, pick in enumerate((pick0, picked)):
                        order.step(vec.tensor_scalar(pick[:, t], self.iota8, index_f[:, t, n:n + 1], None, ALU.is_equal))
                order.settle(vec)
                order.step(vec.tensor_tensor(picked, picked, pick0, ALU.add))
                order.settle(vec)
                for t in range(TT):
                    vec.tensor_tensor(mask[:, t].rearrange("p (g e) -> p g e", g=GROUPS),
                                      picked[:, t].unsqueeze(1).broadcast_to([P, GROUPS, PER_GROUP]),
                                      chosen[:, t].unsqueeze(2).broadcast_to([P, GROUPS, PER_GROUP]),
                                      ALU.mult).then_inc(chosen_ready, 1)
                vec.wait_ge(pair_out, 1)
                order.step(vec.tensor_scalar(denom, ratio, 1.0, None, ALU.add))
                order.settle(vec)
                order.step(vec.reciprocal(w0, denom))
                order.settle(vec)
                order.step(vec.tensor_tensor(w0, w0, gprob, ALU.mult))
                order.settle(vec)
                order.step(vec.tensor_tensor(w1, w0, ratio, ALU.mult))
                order.settle(vec)
                for t in range(TT):
                    for n, (pick, w) in enumerate(((pick0, w0), (pick1, w1))):
                        order.step(vec.tensor_scalar(pick[:, t], self.iota8, index_f[:, t, n:n + 1], w[:, t], ALU.is_equal,
                                                     ALU.mult))
                order.settle(vec)
                order.step(vec.tensor_tensor(pick0, pick0, pick1, ALU.add))
                order.settle(vec)
                for t in range(TT):
                    order.step(vec.tensor_tensor(weights_all[:, t].rearrange("p (g e) -> p g e", g=GROUPS),
                                                 pick0[:, t].unsqueeze(1).broadcast_to([P, GROUPS, PER_GROUP]),
                                                 chosen[:, t].unsqueeze(2).broadcast_to([P, GROUPS, PER_GROUP]), ALU.mult))
                vec.wait_ge(counts_ready, 1)
                running_in = self.psum[3][:, 0:64].rearrange("p (t e) -> p t e", t=TT)
                order.step(vec.tensor_tensor(running, running_in, mask, ALU.mult))
                order.step(vec.tensor_reduce(biggest, self.psum[3][:, 64:96], AX.X, ALU.max))
                order.settle(vec)
                order.step(vec.tensor_scalar(self.over_flag.bitcast(mybir.dt.int32), biggest, float(SLOTS_E), None, ALU.is_gt))
                order.step(vec.tensor_scalar(fits, running, float(SLOTS_E), None, ALU.is_le))
                order.step(vec.tensor_scalar(slot, running, -1.0, None, ALU.add))
                order.settle(vec)
                vec.tensor_tensor(weights, weights_all, fits, ALU.mult).then_inc(weights_ready, 1)
                vec.wait_ge(weights_ready, 1)
                vec.tensor_tensor(weights_all, weights_all, weights, ALU.subtract).then_inc(weights_ready, 1)
                for t in range(TT):
                    for q in range(PAIRS):
                        for n in range(2):
                            order.step(vec.tensor_scalar(self.pick[:, t, q, n * 64:(n + 1) * 64], self.iota[:, 0:64],
                                                         slot[:, t, 2 * q + n:2 * q + n + 1], None, ALU.is_equal))

    def load_weight(self, sync, q, parity, n):
        s = 3 * parity + n
        dst = self.at(RING + s * SLOT, FT, D) if n == 2 else self.at(RING + s * SLOT, K, FF)
        src = self.ins[("w_gate", "w_up", "w_down")[n]][q * 2 + parity]
        sync.dma_start(dst, src).then_inc(self.landed[s], 16)

    def experts(self):
        nc, ident = self.nc, self.ident
        acc = [self.psum[n] for n in range(4)]
        wide = [self.psum[4], self.psum[5]]
        gu_bank, turn_bank = self.psum[6], self.psum[7]
        base = [self.loads[s] for s in range(6)]
        for s in range(6):
            self.loads[s] += PAIRS
        (gather_ready, gather_used, gu_ready, gu_used, turn_ready, silu_ready, hid_ready, down_ready, down_used,
         scatter_done, all_done, sum_ready) = (self.sem("pair_" + n) for n in (
            "gathered", "gathered_used", "gate_up", "gate_up_used", "turned", "silu", "hidden", "down", "down_used",
            "scattered", "all", "sum_copied"))
        back = Banks(self, "sum_turned", [4, 5])
        slots_turned, slots_t_ready = self.sem("slots_turned"), self.sem("slots_t_ready")
        spread, weights_spread = Banks(self, "spread", [0, 1, 2, 3]), self.sem("weights_spread")
        rows_landed = self.rows2_landed = self.sem("rows2_landed")
        gain = self.col("norm2")
        order = self.vec

        def slot(s, *shape):
            return self.at(RING + s * SLOT, *shape)

        with nc.Block() as block:
            @block.sync
            def _(sync):
                sync.dma_start(self.rows2, self.ins["rows2"].partition_broadcast(P)).then_inc(rows_landed, 16)
                sync.dma_start(self.const2, self.ins["const2"]).then_inc(rows_landed, 16)
                def reload(q, parity, n):
                    sync.wait_ge(*((down_ready, q) if n == 2 else (gu_ready, q * 2 + (parity - 1))))
                    self.load_weight(sync, q, parity, n)

                reload(1, 0, 0)
                reload(1, 0, 1)
                with sync.Fori(1, PAIRS - 1) as q:
                    reload(q, 1, 0)
                    reload(q, 1, 1)
                    reload(q + 1, 0, 0)
                    reload(q + 1, 0, 1)
                    reload(q, 0, 2)
                    reload(q, 1, 2)
                for n in range(3):
                    reload(PAIRS - 1, 1, n)
                reload(PAIRS - 1, 0, 2)

            @block.tensor
            def _(pe):
                pe.wait_ge(self.zeros_ready, 1)

                def touch(start):
                    for bank in acc:
                        last = pe.matmul(bank[:, :], self.zeros[0:1, 0:P], self.zeros[0:1, P:P + 512], start=start,
                                         stop=not start, skip_group_check=True)
                    return last

                def one(x, q):
                    return x[:, q, :] if isinstance(q, int) else x[:, bass.ds(q, 1), :].rearrange("p a x -> p (a x)")

                def gather(q, first=False):
                    if not first:
                        pe.wait_ge(down_used, q * 2 - 2)
                    for k in range(K):
                        for t in range(TT):
                            last = pe.matmul(wide[k // 4][:, (k % 4) * P:(k % 4 + 1) * P],
                                             self.normed[:, t, k * P:(k + 1) * P], one(self.pick[:, t], q),
                                             start=(t == 0), stop=(t == TT - 1))
                    last.then_inc(gather_ready, 1)

                def gate_up(q, parity):
                    for n in range(2):
                        pe.wait_ge(self.landed[3 * parity + n], (q + 1) * 16 + 16 * base[3 * parity + n])
                    pe.wait_ge(gather_used, q * 2 + 2)
                    if not (isinstance(q, int) and q == 0 and parity == 0):
                        pe.wait_ge(gu_used, q * 2 + parity)
                    for k in range(K):
                        for n in range(2):
                            last = pe.matmul(gu_bank[64 * n:64 * n + 64, :], self.gathered[:, k, 64 * parity:64 * parity + 64],
                                             slot(3 * parity + n, K, FF)[:, k, :], start=(k == 0), stop=(k == K - 1))
                    last.then_inc(gu_ready, 1)

                def turn(q, parity):
                    pe.wait_ge(gu_used, q * 2 + (parity + 1))
                    if not (isinstance(q, int) and q == 0 and parity == 0):
                        pe.wait_ge(hid_ready, q * 2 + parity)
                    for f in range(FT):
                        last = pe.transpose(turn_bank[:, f * P:(f + 1) * P], self.gate_up[:, parity, f * P:(f + 1) * P], ident)
                    last.then_inc(turn_ready, 1)

                def down(q):
                    for parity in range(2):
                        pe.wait_ge(self.landed[3 * parity + 2], (q + 1) * 16 + 16 * base[3 * parity + 2])
                    pe.wait_ge(hid_ready, q * 2 + 2)
                    pe.wait_ge(gather_used, q * 2 + 2)
                    for n in range(2):
                        for f in range(FT):
                            for parity in range(2):
                                last = pe.matmul(wide[n][64 * parity:64 * parity + 64, :], self.hid[:, parity, f, :],
                                                 slot(3 * parity + 2, FT, D)[:, f, n * 512:(n + 1) * 512],
                                                 start=(f == 0), stop=(f == FT - 1))
                    last.then_inc(down_ready, 1)

                def scatter(q):
                    pe.wait_ge(down_used, q * 2 + 2)
                    for k in range(K):
                        last = pe.matmul(acc[k // 2][:, (k % 2) * T:(k % 2 + 1) * T], self.slot_out[:, k * P:(k + 1) * P],
                                         one(self.put, q), start=False, stop=False, skip_group_check=True)
                    last.then_inc(scatter_done, 1)

                for which, src in enumerate((self.slot_weights, self.slots)):
                    for t in range(TT):
                        last = pe.transpose(self.psum[3][0:EXPERTS, (which * TT + t) * P:(which * TT + t + 1) * P],
                                            src[:, t, :], ident)
                last.then_inc(slots_turned, 1)
                gather(0, first=True)
                gate_up(0, 0)
                gate_up(0, 1)
                turn(0, 0)
                gather(1, first=True)
                turn(0, 1)
                gate_up(1, 0)
                down(0)
                gate_up(1, 1)
                turn(1, 0)
                gather(2)
                pe.wait_ge(slots_t_ready, 1)
                for q in range(PAIRS):
                    pe.matmul(spread.free(pe, q)[:, :], self.selector[0:EXPERTS, q, :],
                              self.weights_t[0:EXPERTS].rearrange("p a t -> p (a t)"),
                              start=True, stop=True).then_inc(spread.filled, 1)
                pe.wait_ge(spread.emptied, PAIRS)
                touch(True)
                scatter(0)
                turn(1, 1)
                with pe.Fori(2, PAIRS - 1) as q:
                    gate_up(q, 0)
                    down(q - 1)
                    gate_up(q, 1)
                    turn(q, 0)
                    gather(q + 1)
                    scatter(q - 1)
                    turn(q, 1)
                last_q = PAIRS - 1
                gate_up(last_q, 0)
                down(last_q - 1)
                gate_up(last_q, 1)
                turn(last_q, 0)
                scatter(last_q - 1)
                turn(last_q, 1)
                down(last_q)
                scatter(last_q)
                touch(False).then_inc(all_done, 1)
                pe.wait_ge(sum_ready, 4)
                for job in range(2 * TT):
                    t, half = divmod(job, 2)
                    bank = back.free(pe, job)
                    for k in range(4):
                        last = pe.transpose(bank[:, k * P:(k + 1) * P], self.sum_t[:, 4 * half + k, t * P:(t + 1) * P], ident)
                    last.then_inc(back.filled, 1)

            @block.scalar
            def _(act):
                def copy_gate_up(q, parity):
                    act.wait_ge(gu_ready, q * 2 + (parity + 1))
                    act.activation(self.gate_up[:, parity, :], gu_bank[:, :], ACT.Copy).then_inc(gu_used, 1)

                def silu(q, parity):
                    act.wait_ge(turn_ready, q * 2 + (parity + 1))
                    turned = turn_bank[:, :].rearrange("p (f x) -> p f x", f=FT)
                    act.activation(self.silu_s, turned[:, :, 0:64], ACT.Silu).then_inc(silu_ready, 1)

                def copy_out(q):
                    act.wait_ge(down_ready, q + 1)
                    for n in range(2):
                        act.activation(self.slot_out[:, n * 512:(n + 1) * 512], wide[n][:, :],
                                       ACT.Copy).then_inc(down_used, 1)

                for parity in range(2):
                    copy_gate_up(0, parity)
                silu(0, 0)
                silu(0, 1)
                copy_gate_up(1, 0)
                copy_out(0)
                copy_gate_up(1, 1)
                silu(1, 0)
                for q in range(PAIRS):
                    act.activation(self.put[:, q, :], spread.ready(act, q)[:, 0:T], ACT.Copy).then_inc(weights_spread, 1)
                silu(1, 1)
                with act.Fori(2, PAIRS) as q:
                    copy_gate_up(q, 0)
                    copy_out(q - 1)
                    copy_gate_up(q, 1)
                    silu(q, 0)
                    silu(q, 1)
                copy_out(PAIRS - 1)
                act.wait_ge(all_done, 1)
                for n in range(4):
                    act.activation(self.sum_t[:, 2 * n:2 * n + 2, :], acc[n][:, :].rearrange("p (k t) -> p k t", k=2),
                                   ACT.Copy).then_inc(sum_ready, 1)

            @block.vector
            def _(vec):
                def copy_gathered(q):
                    vec.wait_ge(gather_ready, q + 1)
                    for n in range(2):
                        vec.tensor_tensor(self.gathered[:, 4 * n:4 * n + 4, :], wide[n][:, :].rearrange("p (k s) -> p k s", k=4),
                                          gain[:, 4 * n:4 * n + 4].unsqueeze(2).broadcast_to([P, 4, P]),
                                          ALU.mult).then_inc(gather_used, 1)

                def multiply(q, parity):
                    vec.wait_ge(silu_ready, q * 2 + (parity + 1))
                    turned = turn_bank[:, :].rearrange("p (f x) -> p f x", f=FT)
                    vec.tensor_tensor(self.hid[:, parity], self.silu_s, turned[:, :, 64:P], ALU.mult).then_inc(hid_ready, 1)

                vec.wait_ge(slots_turned, 1)
                vec.tensor_copy(self.weights_t[0:EXPERTS].rearrange("p a t -> p (a t)"),
                                self.psum[3][0:EXPERTS, :]).then_inc(slots_t_ready, 1)
                copy_gathered(0)
                multiply(0, 0)
                copy_gathered(1)
                multiply(0, 1)
                multiply(1, 0)
                copy_gathered(2)
                for q in range(PAIRS):
                    vec.wait_ge(weights_spread, q + 1)
                    vec.scalar_tensor_tensor(out=self.put[:, q, :], in0=spread.ready(vec, q)[:, T:2 * T],
                                             scalar=self.slot_number, in1=self.put[:, q, :],
                                             op0=ALU.is_equal, op1=ALU.mult).then_inc(spread.emptied, 1)
                multiply(1, 1)
                with vec.Fori(2, PAIRS - 1) as q:
                    multiply(q, 0)
                    copy_gathered(q + 1)
                    multiply(q, 1)
                multiply(PAIRS - 1, 0)
                multiply(PAIRS - 1, 1)
                for job in range(2 * TT):
                    t, half = divmod(job, 2)
                    bank = back.ready(vec, job)
                    part = self.h[:, t, half * 512:(half + 1) * 512]
                    vec.tensor_tensor(part, part, bank[:, :], ALU.add).then_inc(back.emptied, 1)

    def general_experts(self):
        nc = self.nc
        beyond = nc.values_load(self.over_flag[0:1, 0:1].bitcast(U32), min_val=0, max_val=1)
        with nc.If(beyond != 0):
            nc.all_engine_barrier()
            self.spread_left()
            self.experts_over_all()

    def spread_left(self):
        nc = self.nc
        turned_ready, weights_t_ready = self.sem("left_turned"), self.sem("left_weights_t")
        spread = Banks(self, "spread_left", [4, 5, 6, 7])
        with nc.Block() as block:
            @block.tensor
            def _(pe):
                for t in range(TT):
                    last = pe.transpose(self.psum[2][0:EXPERTS, t * P:(t + 1) * P], self.weights_left[:, t, :], self.ident)
                last.then_inc(turned_ready, 1)
                pe.wait_ge(weights_t_ready, 1)
                for job in range(EXPERTS // 2):
                    bank = spread.free(pe, job)
                    for n in range(2):
                        e = 2 * job + n
                        last = pe.matmul(bank[:, n * T:(n + 1) * T],
                                         self.ident[0:EXPERTS, e:e + 1].broadcast_to([EXPERTS, P]),
                                         self.weights_t[0:EXPERTS, 0, :], start=True, stop=True)
                    last.then_inc(spread.filled, 1)

            @block.scalar
            def _(act):
                for job in range(EXPERTS // 2):
                    bank = spread.ready(act, job)
                    act.activation(self.expert_w[:, 2 * job:2 * job + 2, :], bank[:, :].rearrange("p (n t) -> p n t", n=2),
                                   ACT.Copy).then_inc(spread.emptied, 1)

            @block.vector
            def _(vec):
                vec.wait_ge(turned_ready, 1)
                vec.tensor_copy(self.weights_t[0:EXPERTS, 0, :], self.psum[2][0:EXPERTS, 0:T]).then_inc(weights_t_ready, 1)

    def experts_over_all(self):
        nc, xT = self.nc, self.xT
        acc = [[self.psum[2 * t + n] for n in range(2)] for t in range(TT)]
        gu = [self.psum[4 + f] for f in range(FT)]
        gu_ready, silu_ready, gu_used, hidden_ready, down_done = (
            self.sem("experts_" + n) for n in ("gate_up", "silu", "gate_up_used", "hidden", "down"))
        all_done, h_ready = self.sem("experts_all_done"), self.sem("experts_added")
        landed = [self.sem(f"expert_slot{s}_landed") for s in range(6)]

        def slot(s, *shape):
            return self.at(RING + s * SLOT, *shape)

        def load_expert(sync, i, parity, used):
            for n in range(3):
                s = 3 * parity + n
                if used:
                    sync.wait_ge(*used[n // 2])
                src = self.ins[("w_gate", "w_up", "w_down")[n]][i * 2 + parity]
                dst = slot(s, FT, D) if n == 2 else slot(s, K, FF)
                sync.dma_start(dst, src).then_inc(landed[s], 16)

        with nc.Block() as block:
            @block.sync
            def _(sync):
                for parity in range(2):
                    load_expert(sync, 0, parity, None)
                with sync.Fori(1, EXPERTS // 2) as i:
                    for parity in range(2):
                        load_expert(sync, i, parity, [(gu_ready, i * 8 + (4 * parity - 4)), (down_done, i * 2 + (parity - 1))])

            @block.tensor
            def _(pe):
                def touch(start):
                    for bank in acc[0] + acc[1]:
                        last = pe.matmul(bank[:, :], self.zeros[0:1, 0:P], self.zeros[0:1, P:P + 512], start=start,
                                         stop=not start, skip_group_check=True)
                    return last

                def gate_up(e, parity, half, used):
                    for n in range(2):
                        pe.wait_ge(landed[3 * parity + n], half * 16 + 16)
                    for f in range(FT):
                        if used:
                            pe.wait_ge(gu_used, e * 4 + (f - 3))
                        for n in range(2):
                            w = slot(3 * parity + n, K, FF)
                            for k in range(K):
                                last = pe.matmul(gu[f][:, n * T:(n + 1) * T], w[:, k, f * P:(f + 1) * P], xT[:, k, :],
                                                 start=(k == 0), stop=(k == K - 1))
                        last.then_inc(gu_ready, 1)

                def down(e, parity, half):
                    pe.wait_ge(landed[3 * parity + 2], half * 16 + 16)
                    w = slot(3 * parity + 2, FT, D)
                    for f in range(FT):
                        pe.wait_ge(hidden_ready, e * 4 + (f + 1))
                        for t in range(TT):
                            for n in range(2):
                                last = pe.matmul(acc[t][n][:, :], self.hidden[:, parity, f, t * P:(t + 1) * P],
                                                 w[:, f, n * 512:(n + 1) * 512], start=False, stop=False,
                                                 skip_group_check=True)
                    last.then_inc(down_done, 1)

                touch(True)
                gate_up(0, 0, 0, False)
                with pe.Fori(0, EXPERTS // 2 - 1) as i:
                    gate_up(i * 2 + 1, 1, i, True)
                    down(i * 2, 0, i)
                    gate_up(i * 2 + 2, 0, i + 1, True)
                    down(i * 2 + 1, 1, i)
                last_pair = EXPERTS // 2 - 1
                gate_up(EXPERTS - 1, 1, last_pair, True)
                down(EXPERTS - 2, 0, last_pair)
                down(EXPERTS - 1, 1, last_pair)
                touch(False).then_inc(all_done, 1)

            @block.scalar
            def _(act):
                def silus(e, first):
                    for f in range(FT):
                        act.wait_ge(gu_ready, e * 4 + (f + 1))
                        if not (first and f < 2):
                            act.wait_ge(gu_used, e * 4 + (f - 1))
                        act.activation(self.silu[:, f % 2, :], gu[f][:, 0:T], ACT.Silu).then_inc(silu_ready, 1)

                silus(0, True)
                with act.Fori(1, EXPERTS) as e:
                    silus(e, False)

            @block.vector
            def _(vec):
                def hiddens(e, parity, wait_down):
                    for f in range(FT):
                        vec.wait_ge(silu_ready, e * 4 + (f + 1))
                        if wait_down and f == 0:
                            vec.wait_ge(down_done, e - 1)
                        hidden = self.hidden[:, parity, f, :]
                        vec.tensor_tensor(hidden, self.silu[:, f % 2, :], gu[f][:, T:2 * T], ALU.mult).then_inc(gu_used, 1)
                        vec.wait_ge(gu_used, e * 4 + (f + 1))
                        w = self.expert_w[:, e, :] if isinstance(e, int) else \
                            self.expert_w[:, bass.ds(e, 1), :].rearrange("p a t -> p (a t)")
                        vec.tensor_tensor(hidden, hidden, w, ALU.mult).then_inc(hidden_ready, 1)

                hiddens(0, 0, False)
                hiddens(1, 1, False)
                with vec.Fori(1, EXPERTS // 2) as i:
                    hiddens(i * 2, 0, True)
                    hiddens(i * 2 + 1, 1, True)
                vec.wait_ge(all_done, 1)
                for t in range(TT):
                    for n in range(2):
                        part = self.h[:, t, n * 512:(n + 1) * 512]
                        vec.tensor_tensor(part, part, acc[t][n][:, :], ALU.add).then_inc(h_ready, 1)
                vec.wait_ge(h_ready, 4)

    def final_norm(self):
        nc, h = self.nc, self.h
        junk = self.at(WORK, TT, D)
        ss, ms, root, rstd = (self.small[:, i * 2:i * 2 + 2] for i in range(4))
        squares, mean_ready, root_ready = (self.sem(f"final_{x}") for x in ("squares", "mean", "root"))
        order = self.vec
        with nc.Block() as block:
            @block.sync
            def _(sync):
                self.issue(sync, self.first_half + RING_SLOTS)

            @block.scalar
            def _(act):
                for t in range(TT):
                    act.activation(junk[:, t, :], h[:, t, :], ACT.Square, accum_out=ss[:, t:t + 1]).then_inc(squares, 1)
                act.wait_ge(mean_ready, 1)
                act.activation(root, ms, ACT.Sqrt).then_inc(root_ready, 1)

            @block.vector
            def _(vec):
                vec.wait_ge(squares, TT)
                vec.tensor_scalar(ms, ss, 1.0 / D, EPS, ALU.mult, ALU.add).then_inc(mean_ready, 1)
                vec.wait_ge(root_ready, 1)
                order.step(vec.reciprocal(rstd, root))
                order.settle(vec)
                vec.wait_ge(self.rows2_landed, 32)
                for t in range(TT):
                    order.step(vec.scalar_tensor_tensor(out=h[:, t, :], in0=h[:, t, :], scalar=rstd[:, t:t + 1],
                                                        in1=self.rows2[:, 0:D], op0=ALU.mult, op1=ALU.mult))


    def place_second(self):
        at = self.at
        o = WORK
        self.qkv2 = at(o, 6, TT, 512)
        self.turned_in = at(o + 6144, 4, TT, 512)
        self.qk2T = at(o + 10240, 4, 4, T)
        self.mixed = at(o + 14336, TT, D)
        o = MORE
        self.masked_s = at(o, 2, T)
        self.probs = at(o + 512, 6, T)
        self.mixed_p = at(o + 2048, 2, T)
        self.probs_t = at(o + 2560, 2, T)
        self.halves = at(o + 3072, 2, 256)
        self.squares2 = at(o + 3584, TT, 512)
        self.stat2 = at(o + 4608, 8, 64)
        self.sums2 = at(o + 5120, 64)
        self.neg_max = at(o + 5184, 64)
        self.pair_rec = at(o + 5248, 8)
        self.lam_work = at(o + 5256, 160)
        self.stat3 = at(o + 5420, 8, 24)
        self.future = at(o + 5612, T)

    def project_second(self):
        nc, xT = self.nc, self.xT
        first = self.first_half
        tokens = Banks(self, "project2", [0, 1, 2, 3])
        split = Split(self, "second", WORK + 10240, WORK + 14336, first)
        for c in range(6):
            self.used_by[first + c] = (tokens.filled, TT * (c + 1))
        names = ("mq", "mk", "dq", "dk")
        column = (0, 1, 3, 4)
        order = self.vec
        squares, mean_ready, root_ready = (self.sem("qk_" + n) for n in ("squares", "mean", "root"))
        exp_in, exp_out = self.sem("lambda_in"), self.sem("lambda_out")
        rows, heads = self.rows2, "p (h d) -> p h d"
        sq, ms, root, rstd = (self.stat2[:, n, :] for n in range(4))
        dots, lam_exp = self.lam_work[:, 128:130], self.lam_work[:, 130:132]
        with nc.Block() as block:
            @block.sync
            def _(sync):
                self.issue(sync, first + 8)

            @block.tensor
            def _(pe):
                for c in range(6):
                    split.products(pe, c, tokens)

            @block.gpsimd
            def _(pool):
                split.lows(pool, 6)

            @block.scalar
            def _(act):
                def copy_out(c):
                    for t in range(TT):
                        bank = tokens.ready(act, c * TT + t)
                        act.activation(self.qkv2[:, SECOND_ORDER[c], t, :], bank[:, :], ACT.Copy).then_inc(tokens.emptied, 1)

                split.x_highs(act)
                act.wait_ge(exp_in, 1)
                act.activation(lam_exp, dots, ACT.Exp).then_inc(exp_out, 1)
                for c in range(6):
                    for k in range(K):
                        if c > 0 and k == K // 2:
                            copy_out(c - 1)
                        if c in (3, 5) and k == 0:
                            of_group = slice(32 * (c // 2 - 1), 32 * (c // 2))
                            act.wait_ge(mean_ready, c // 2)
                            act.activation(root[:, of_group], ms[:, of_group], ACT.Sqrt).then_inc(root_ready, 1)
                        split.high(act, c, k)
                copy_out(5)

            @block.vector
            def _(vec):
                split.x_lows(vec)
                o, n = ROWS2["lambda"]
                four = rows[:, o:o + n].rearrange("p (a b d) -> p a b d", a=2, b=2)
                prod = self.lam_work[:, 0:128].rearrange("p (a d) -> p a d", a=2)
                order.step(vec.tensor_tensor(prod, four[:, :, 0, :], four[:, :, 1, :], ALU.mult))
                order.settle(vec)
                vec.tensor_reduce(dots, prod, AX.X, ALU.add).then_inc(exp_in, 1)
                order.step(vec.memset(self.future[:, 0:P], 0.0))
                order.step(vec.tensor_copy(self.future[:, P:T], self.const2[:, 128:256]))
                vec.wait_ge(exp_out, 1)
                order.step(vec.scalar_tensor_tensor(out=self.lt[:, 0:1], in0=lam_exp[:, 0:1], scalar=LAMBDA_INIT,
                                                    in1=lam_exp[:, 1:2], op0=ALU.add, op1=ALU.subtract))
                half = M_DIM // 2
                rope = self.const2[:, 0:128].rearrange("p (a t d) -> p a t d", a=2, t=TT)
                for group in range(2):
                    of_group = slice(32 * group, 32 * group + 32)
                    for n in range(2 * TT * group, 2 * TT * (group + 1)):
                        a, t = divmod(n, TT)
                        vec.wait_ge(tokens.emptied, n + 1)
                        x = self.qkv2[:, column[a], t, :]
                        junk = self.squares2[:, n % 2, :]
                        order.step(vec.tensor_tensor(junk, x, x, ALU.mult))
                        order.settle(vec)
                        order.step(vec.tensor_reduce(sq[:, n * 8:(n + 1) * 8], junk.rearrange(heads, h=8), AX.X, ALU.add))
                    order.settle(vec)
                    vec.tensor_scalar(ms[:, of_group], sq[:, of_group], 1.0 / M_DIM, EPS, ALU.mult,
                                      ALU.add).then_inc(mean_ready, 1)
                    vec.wait_ge(root_ready, group + 1)
                    order.step(vec.reciprocal(rstd[:, of_group], root[:, of_group]))
                    order.settle(vec)
                    for n in range(2 * TT * group, 2 * TT * (group + 1)):
                        a, t = divmod(n, TT)
                        x = self.qkv2[:, column[a], t, :]
                        order.step(vec.tensor_tensor(x.rearrange(heads, h=8), x.rearrange(heads, h=8),
                                                     rstd[:, n * 8:(n + 1) * 8].unsqueeze(2).broadcast_to([P, 8, M_DIM]),
                                                     ALU.mult))
                        order.settle(vec)
                        o, width = ROWS2[names[a]]
                        gain = rows[:, o:o + width].unsqueeze(1).broadcast_to([P, 512 // width, width])
                        order.step(vec.tensor_tensor(x.rearrange(heads, d=width), x.rearrange(heads, d=width), gain, ALU.mult))
                        order.settle(vec)
                        x8 = x.rearrange(heads, h=8)
                        y8 = self.turned_in[:, a, t, :].rearrange(heads, h=8)
                        cos = rope[:, 0, t, :].unsqueeze(1).broadcast_to([P, 8, half])
                        sin = rope[:, 1, t, :].unsqueeze(1).broadcast_to([P, 8, half])
                        h0 = self.halves[:, 0, :].rearrange(heads, h=8)
                        h1 = self.halves[:, 1, :].rearrange(heads, h=8)
                        for out, u, v, op in ((y8[:, :, 0:half], cos, sin, ALU.subtract), (y8[:, :, half:], sin, cos, ALU.add)):
                            order.step(vec.tensor_tensor(h0, x8[:, :, 0:half], u, ALU.mult))
                            order.step(vec.tensor_tensor(h1, x8[:, :, half:], v, ALU.mult))
                            order.settle(vec)
                            order.step(vec.tensor_tensor(out, h0, h1, op))
                            order.settle(vec)

    def attention(self):
        nc, ident = self.nc, self.ident
        turned = Banks(self, "attn_turned", [0, 1, 2, 3])
        scores = Banks(self, "attn_scores", [4, 5])
        flips = Banks(self, "attn_flips", [6, 7])
        outs = {("m", 0): self.psum[0], ("m", 1): self.psum[1], ("d", 0): self.psum[2], ("d", 1): self.psum[3]}
        items = [("m", b, r, t) for b in range(4) for r in range(2) for t in range(TT)]
        items += [("d", b, None, t) for b in range(4) for t in range(TT)]
        jobs = []
        first_job = []
        for n, (kind, b, r, t) in enumerate(items):
            first_job.append(len(jobs))
            jobs += [(n, r)] if kind == "m" else [(n, 0), (n, 1)]
        first_job.append(len(jobs))
        diff_no = {n: m for m, n in enumerate(n for n, x in enumerate(items) if x[0] == "d")}
        maxed, exped, mixed_ready, pv_done = (self.sem("attn_" + n) for n in ("max", "exp", "mixed", "pv"))
        mean_ready, root_ready = self.sem("attn_mean"), self.sem("attn_root")
        order = self.vec
        last_item = len(items)
        FINISH_STEP = M_HEADS * TT + 4
        with nc.Block() as block:
            @block.tensor
            def _(pe):
                for job in range(4 * TT):
                    a, t = divmod(job, TT)
                    bank = turned.free(pe, job)
                    for b in range(4):
                        last = pe.transpose(bank[:, b * P:(b + 1) * P], self.turned_in[:, a, t, b * P:(b + 1) * P], ident)
                    last.then_inc(turned.filled, 1)
                pe.wait_ge(turned.emptied, 4 * TT)
                for step in range(last_item + 3):
                    if step < last_item:
                        kind, b, r, t = items[step]
                        q = 0 if kind == "m" else 2
                        n = P * (t + 1)
                        for job in range(first_job[step], first_job[step + 1]):
                            half = jobs[job][1]
                            rows = slice(64 * half, 64 * half + 64)
                            bank = scores.free(pe, job)
                            pe.matmul(bank[:, 0:n], self.qk2T[rows, q, b, t * P:(t + 1) * P], self.qk2T[rows, q + 1, b, 0:n],
                                      start=True, stop=True).then_inc(scores.filled, 1)
                    if 0 <= step - 2 < last_item:
                        i = step - 2
                        kind, b, r, t = items[i]
                        if kind == "m":
                            pe.wait_ge(exped, first_job[i + 1])
                            src = self.probs[:, first_job[i] % 6, :]
                        else:
                            pe.wait_ge(mixed_ready, diff_no[i] + 1)
                            src = self.mixed_p[:, diff_no[i] % 2, :]
                        bank = flips.free(pe, i)
                        for s in range(t + 1):
                            last = pe.transpose(bank[:, s * P:(s + 1) * P], src[:, s * P:(s + 1) * P], ident)
                        last.then_inc(flips.filled, 1)
                    if 0 <= step - 3:
                        i = step - 3
                        kind, b, r, t = items[i]
                        pe.wait_ge(flips.emptied, i + 1)
                        v, width, h = (2, 64, 2 * b + r) if kind == "m" else (5, 128, b)
                        cols = slice(h * width, (h + 1) * width)
                        for s in range(t + 1):
                            last = pe.matmul(outs[kind, t][:, cols], self.probs_t[:, i % 2, s * P:(s + 1) * P],
                                             self.qkv2[:, v, s, cols], start=(s == 0), stop=(s == t))
                        last.then_inc(pv_done, 1)

            @block.scalar
            def _(act):
                for job in range(4 * TT):
                    a, t = divmod(job, TT)
                    bank = turned.ready(act, job)
                    act.activation(self.qk2T[:, a, :, t * P:(t + 1) * P], bank[:, :].rearrange("p (b t) -> p b t", b=4),
                                   ACT.Copy).then_inc(turned.emptied, 1)
                for step in range(last_item + 2):
                    if step == FINISH_STEP:
                        act.wait_ge(mean_ready, 1)
                        act.activation(self.stat3[:, 4, 0:16], self.stat3[:, 3, 0:16], ACT.Sqrt).then_inc(root_ready, 1)
                    if step < last_item:
                        kind, b, r, t = items[step]
                        n = P * (t + 1)
                        for job in range(first_job[step], first_job[step + 1]):
                            act.wait_ge(maxed, job + 1)
                            if job >= 6:
                                i = jobs[job - 6][0]
                                if items[i][0] == "m":
                                    act.wait_ge(flips.filled, i + 1)
                                else:
                                    act.wait_ge(mixed_ready, diff_no[i] + 1)
                            act.activation(self.probs[:, job % 6, 0:n], self.masked_s[:, job % 2, 0:n], ACT.Exp,
                                           bias=self.neg_max[:, job:job + 1],
                                           accum_out=self.sums2[:, job:job + 1]).then_inc(exped, 1)
                    if step >= 2:
                        i = step - 2
                        n = P * (items[i][3] + 1)
                        bank = flips.ready(act, i)
                        if i >= 2:
                            act.wait_ge(pv_done, i - 1)
                        act.activation(self.probs_t[:, i % 2, 0:n], bank[:, 0:n], ACT.Copy).then_inc(flips.emptied, 1)
                act.wait_ge(mean_ready, 2)
                act.activation(self.stat3[:, 4, 16:24], self.stat3[:, 3, 16:24], ACT.Sqrt).then_inc(root_ready, 1)

            @block.vector
            def _(vec):
                heads = "p (h d) -> p h d"
                square, mean, root, rstd, by_sum = (self.stat3[:, n, :] for n in (1, 3, 4, 5, 6))

                def finish(kind):
                    part, h, width, gain, scale = {"m": (0, M_HEADS, M_DIM, "m_out", 1.0),
                                                   "d": (1, F_HEADS, F_DIM, "d_out", 1.0 - LAMBDA_INIT)}[kind]
                    at = 16 * part
                    of_kind = slice(at, at + TT * h)
                    x = [self.mixed[:, t, part * 512:(part + 1) * 512].rearrange(heads, h=h) for t in range(TT)]
                    vec.wait_ge(pv_done, len(items) if kind == "d" else M_HEADS * TT)
                    if kind == "m":
                        order.step(vec.reciprocal(by_sum[:, 0:16], self.sums2[:, 0:16]))
                        order.settle(vec)
                        by_tile = by_sum[:, 0:16].rearrange("p (h t) -> p t h", t=TT)
                        for t in range(TT):
                            order.step(vec.tensor_tensor(x[t], outs["m", t][:, :].rearrange(heads, h=h),
                                                         by_tile[:, t].unsqueeze(2).broadcast_to([P, h, width]), ALU.mult))
                    else:
                        for t in range(TT):
                            order.step(vec.tensor_copy(x[t], outs["d", t][:, :].rearrange(heads, h=h)))
                    order.settle(vec)
                    squared = [self.squares2[:, t, :].rearrange(heads, h=h) for t in range(TT)]
                    for t in range(TT):
                        order.step(vec.tensor_tensor(squared[t], x[t], x[t], ALU.mult))
                    order.settle(vec)
                    for t in range(TT):
                        order.step(vec.tensor_reduce(square[:, at + t * h:at + (t + 1) * h], squared[t], AX.X, ALU.add))
                    order.settle(vec)
                    vec.tensor_scalar(mean[:, of_kind], square[:, of_kind], 1.0 / width, EPS, ALU.mult,
                                      ALU.add).then_inc(mean_ready, 1)
                    vec.wait_ge(root_ready, part + 1)
                    order.step(vec.reciprocal(rstd[:, of_kind], root[:, of_kind]))
                    order.settle(vec)
                    o, n = ROWS2[gain]
                    for t in range(TT):
                        order.step(vec.tensor_tensor(x[t], x[t], rstd[:, at + t * h:at + (t + 1) * h].unsqueeze(2).broadcast_to(
                            [P, h, width]), ALU.mult))
                    order.settle(vec)
                    for t in range(TT):
                        flat = self.mixed[:, t, part * 512:(part + 1) * 512]
                        order.step(vec.scalar_tensor_tensor(out=flat, in0=flat, scalar=scale, in1=self.rows2[:, o:o + n],
                                                            op0=ALU.mult, op1=ALU.mult))

                for step in range(last_item + 1):
                    if step == FINISH_STEP:
                        finish("m")
                    if step < last_item:
                        kind, b, r, t = items[step]
                        n = P * (t + 1)
                        for job in range(first_job[step], first_job[step + 1]):
                            bank = scores.ready(vec, job)
                            if job >= 2:
                                vec.wait_ge(exped, job - 1)
                            s = self.masked_s[:, job % 2, 0:n]
                            vec.scalar_tensor_tensor(out=s, in0=bank[:, 0:n], scalar=M_DIM ** -0.5,
                                                     in1=self.future[:, T - n:T], op0=ALU.mult,
                                                     op1=ALU.add).then_inc(scores.emptied, 1)
                            vec.wait_ge(scores.emptied, job + 1)
                            vec.tensor_reduce(self.neg_max[:, job:job + 1], s, AX.X, ALU.max,
                                              negate=True).then_inc(maxed, 1)
                    i = step - 1
                    if i >= 0 and items[i][0] == "d":
                        j0, m = first_job[i], diff_no[i]
                        n = P * (items[i][3] + 1)
                        rec = self.pair_rec[:, 2 * (m % 2):2 * (m % 2) + 2]
                        vec.wait_ge(exped, j0 + 2)
                        order.step(vec.reciprocal(rec, self.sums2[:, j0:j0 + 2]))
                        order.settle(vec)
                        order.step(vec.tensor_tensor(rec[:, 1:2], rec[:, 1:2], self.lt[:, 0:1], ALU.mult))
                        order.settle(vec)
                        if m >= 2:
                            vec.wait_ge(flips.filled, i - 1)
                        out = self.mixed_p[:, m % 2, 0:n]
                        order.step(vec.tensor_scalar(out, self.probs[:, (j0 + 1) % 6, 0:n], rec[:, 1:2], None, ALU.mult))
                        order.settle(vec)
                        vec.scalar_tensor_tensor(out=out, in0=self.probs[:, j0 % 6, 0:n], scalar=rec[:, 0:1], in1=out,
                                                 op0=ALU.mult, op1=ALU.subtract).then_inc(mixed_ready, 1)
                finish("d")


    def place_peer(self):
        at = self.at
        self.query_t = at(WORK, 2 * P_HEADS, T)
        self.sub_keys = at(WORK + 4096, 2 * P_HEADS, NKEYS)
        self.key_scores = at(WORK + 6144, TT, 2 * P_HEADS, NKEYS)
        self.pairs = at(WORK + 10240, P_HEADS, PAIRS_IN)
        self.best_quarter = at(WORK + 11136, 2, TT, SLOTS)
        self.best_quarter_f = at(WORK + 11648, 2, TT, SLOTS)
        self.match = at(WORK + 12288, SLOTS, TOPK)
        o = SPARE
        self.top_s = at(o, TT, 2 * P_HEADS, TOPK)
        self.top_i = at(o + 512, TT, 2 * P_HEADS, TOPK)
        self.top_if = at(o + 1024, TT, 2 * P_HEADS, TOPK)
        self.best_s = at(o + 1536, TT, P_HEADS, TOPK)
        self.best_p = at(o + 1792, TT, P_HEADS, TOPK)
        self.best_half = at(o + 2048, 2, TT, SLOTS)
        self.best_half_f = at(o + 2560, 2, TT, SLOTS)
        self.slot_index = at(o + 3072, 2, TT, SLOTS)
        self.gates = at(o + 3584, TT, SLOTS)
        self.gate_sum = at(o + 3840, 2, TT, P_HEADS)
        self.dense = at(0, NKEYS, T)
        self.down_ring = [at(MORE + 2048 * n, 2, K, P) for n in range(2)]
        self.up_ring = [at(MORE + 4096 + 2048 * n, 2, D) for n in range(2)]
        self.x_parts = self.parts("x_parts", MORE + 8192, K, 2, T)
        self.early = at(MORE, EARLY, T)
        self.early_ring = [at(MORE + 4096 + 2048 * n, 2, K, P) for n in range(2)]
        self.early_high = [self.parts(f"early_high{n}", RING + 2048 * n, 2, K, P) for n in range(2)]
        self.early_low = [self.parts(f"early_low{n}", RING + 4096 + 2048 * n, 2, K, P) for n in range(2)]
        o = KEPT + TT * D
        self.hot_j = at(o, 16, P)
        self.hot_i = at(self.cursor, 16, P)
        self.down_high = self.parts("down_high", o, 2, K, P)
        self.down_low = [self.parts(f"down_low{n}", MORE + 2048 * n, 2, K, P) for n in range(2)]
        self.up_high = self.parts("up_high", o + 2048, 2, D)
        self.up_low = [self.parts(f"up_low{n}", MORE + 4096 + 2048 * n, 2, D) for n in range(2)]
        self.gelu = at(o + 4096, 2, T)
        self.gated_high = self.parts("gated_high", o + 4608, 2, T)
        self.gated_low = self.parts("gated_low", o + 5120, 2, T)

    def top16(self, vec, values, top, index, count):
        order = self.vec
        for half in range(2):
            best = slice(8 * half, 8 * half + 8)
            for n in range(count):
                order.step(vec.max(top(n)[:, best], values(n)))
            order.settle(vec)
            for n in range(count):
                order.step(vec.max_index(index(n)[:, best], top(n)[:, best], values(n)))
            order.settle(vec)
            if half == 0:
                for n in range(count):
                    order.step(vec.match_replace(values(n), top(n)[:, best], values(n), -3.0e38))
                order.settle(vec)

    def peer_queries(self):
        nc, xT = self.nc, self.xT
        first = self.first_half + 8
        queries = Banks(self, "queries", [0, 1, 2, 3])
        scores = Banks(self, "key_scores", [4, 5, 6, 7])
        for c in range(4):
            self.used_by[first + c] = (queries.filled, 4 * (c + 1))
        keys_landed = self.keys_landed = self.sem("sub_keys_landed")
        x_high_ready, x_low_ready = self.sem("x_high"), self.sem("x_low")
        self.early_landed = [self.sem(f"early_ring{n}_landed") for n in range(2)]
        top_i = self.top_i.bitcast(U32)
        with nc.Block() as block:
            @block.sync
            def _(sync):
                sync.dma_start(self.sub_keys, self.ins["sub_keys"]).then_inc(keys_landed, 16)
                self.issue(sync, first + 4)
                for u in range(2):
                    sync.dma_start(self.early_ring[u], self.ins["peer_down"][u]).then_inc(self.early_landed[u], 16)

            @block.tensor
            def _(pe):
                def query(c):
                    w = self.chunk(pe, first + c)
                    for n in range(4):
                        job = 4 * c + n
                        bank = queries.free(pe, job)
                        for k in range(K):
                            last = pe.matmul(bank[:, 0:T], w[:, k, n * P:(n + 1) * P], xT[:, k, :],
                                             start=(k == 0), stop=(k == K - 1))
                        last.then_inc(queries.filled, 1)

                def score(c):
                    pe.wait_ge(queries.emptied, 4 * (c + 1))
                    for t in range(TT):
                        bank = scores.free(pe, TT * c + t)
                        for n in range(4):
                            hp = 4 * c + n
                            last = pe.matmul(bank[:, n * P:(n + 1) * P], self.query_t[:, hp, t * P:(t + 1) * P],
                                             self.sub_keys[:, hp, :], start=True, stop=True)
                        last.then_inc(scores.filled, 1)

                query(0)
                pe.wait_ge(keys_landed, 16)
                for c in range(4):
                    score(c)
                    if c < 3:
                        query(c + 1)

            @block.scalar
            def _(act):
                act.activation(self.x_parts[:, :, 0, :], xT, ACT.Copy).then_inc(x_high_ready, 1)
                for c in range(4):
                    for n in range(4):
                        bank = queries.ready(act, 4 * c + n)
                        act.activation(self.query_t[:, 4 * c + n, :], bank[:, 0:T], ACT.Copy).then_inc(queries.emptied, 1)
                    for t in range(TT):
                        bank = scores.ready(act, TT * c + t)
                        act.activation(self.key_scores[:, t, 4 * c:4 * c + 4, :],
                                       bank[:, :].rearrange("p (n x) -> p n x", n=4), ACT.Copy).then_inc(scores.emptied, 1)

            @block.vector
            def _(vec):
                vec.wait_ge(x_high_ready, 1)
                vec.tensor_tensor(self.x_parts[:, :, 1, :], xT, self.x_parts[:, :, 0, :],
                                  ALU.subtract).then_inc(x_low_ready, 1)
                for c in range(4):
                    vec.wait_ge(scores.emptied, TT * (c + 1))
                    rows = [(t, 4 * c + n) for t in range(TT) for n in range(4)]
                    self.top16(vec, lambda n: self.key_scores[:, rows[n][0], rows[n][1], :],
                               lambda n: self.top_s[:, rows[n][0], rows[n][1], :],
                               lambda n: top_i[:, rows[n][0], rows[n][1], :], len(rows))

    def peer_select(self):
        nc = self.nc
        order = self.vec
        exp_in, exp_out, chosen = self.sem("gate_exp_in"), self.sem("gate_exp_out"), self.sem("peer_chosen")
        turned = Banks(self, "slots_turned", [0, 1, 2, 3])
        high_ready, low_ready, hid_ready, gelu_ready = (self.sem("early_" + n) for n in ("high", "low", "hidden", "gelu"))
        landed = self.early_landed
        best_p = self.best_p.bitcast(U32)
        top_i = self.top_i.bitcast(U32)
        with nc.Block() as block:
            @block.sync
            def _(sync):
                with sync.Fori(1, EARLY // 4) as i:
                    for u in range(2):
                        sync.wait_ge(low_ready, i * 4 + (2 * u - 2))
                        sync.dma_start(self.early_ring[u], self.ins["peer_down"][i * 2 + u]).then_inc(landed[u], 16)

            @block.vector
            def _(vec):
                order.step(vec.tensor_copy(self.top_if, top_i))
                for t in range(TT):
                    s = self.top_s[:, t].rearrange("p (h a) s -> p h a s", a=2)
                    for x, y, at in ((slice(0, 4), slice(0, TOPK), 0), (slice(4, TOPK), slice(0, 4), 4 * TOPK)):
                        nx, ny = x.stop - x.start, y.stop - y.start
                        order.step(vec.tensor_tensor(
                            self.pairs[:, :, at:at + nx * ny].rearrange("p h (x y) -> p h x y", x=nx),
                            s[:, :, 0, x].unsqueeze(3).broadcast_to([P, P_HEADS, nx, ny]),
                            s[:, :, 1, y].unsqueeze(2).broadcast_to([P, P_HEADS, nx, ny]), ALU.add))
                    order.settle(vec)
                    self.top16(vec, lambda h: self.pairs[:, h, :], lambda h: self.best_s[:, t, h, :], lambda h: best_p[:, t, h, :],
                          P_HEADS)
                shifted = self.gates.rearrange("p t (h s) -> p t h s", h=P_HEADS)
                for t in range(TT):
                    vec.tensor_tensor(shifted[:, t], self.best_s[:, t],
                                      self.best_s[:, t, :, 0:1].broadcast_to([P, P_HEADS, TOPK]),
                                      ALU.subtract).then_inc(exp_in, 1)
                flat = best_p.rearrange("p t h s -> p t (h s)")
                half, quarter = self.best_half.bitcast(U32), self.best_quarter.bitcast(U32)
                order.step(vec.tensor_single_scalar(half[:, 0], flat, 4, ALU.logical_shift_right))
                order.step(vec.tensor_single_scalar(half[:, 1], flat, TOPK - 1, ALU.bitwise_and))
                order.step(vec.tensor_single_scalar(quarter[:, 0], flat, 2, ALU.logical_shift_right))
                order.step(vec.tensor_single_scalar(quarter[:, 1], flat, 3, ALU.bitwise_and))
                order.settle(vec)
                order.step(vec.tensor_copy(self.best_half_f, half))
                order.step(vec.tensor_copy(self.best_quarter_f, quarter))
                order.settle(vec)
                second_part = self.slot_index[:, 0]
                order.step(vec.tensor_scalar(second_part, self.best_half_f[:, 0], 4.0, None, ALU.is_ge))
                order.step(vec.scalar_tensor_tensor(out=self.best_quarter_f[:, 0], in0=self.best_quarter_f[:, 0],
                                                    scalar=-12.0, in1=self.best_half_f[:, 0], op0=ALU.add,
                                                    op1=ALU.subtract))
                order.step(vec.tensor_tensor(self.best_quarter_f[:, 1], self.best_quarter_f[:, 1],
                                             self.best_half_f[:, 1], ALU.subtract))
                order.settle(vec)
                for n in range(2):
                    order.step(vec.tensor_tensor(self.best_quarter_f[:, n], self.best_quarter_f[:, n], second_part, ALU.mult))
                order.settle(vec)
                order.step(vec.tensor_tensor(self.best_half_f, self.best_half_f, self.best_quarter_f, ALU.add))
                order.settle(vec)
                for a in range(2):
                    for t in range(TT):
                        order.step(vec.tensor_tensor(self.match,
                                                     self.best_half_f[:, a, t, :].unsqueeze(2).broadcast_to([P, SLOTS, TOPK]),
                                                     self.iota[:, 0:TOPK].unsqueeze(1).broadcast_to([P, SLOTS, TOPK]),
                                                     ALU.is_equal))
                        order.settle(vec)
                        keys = self.top_if[:, t].rearrange("p (h a) s -> p h a s", a=2)[:, :, a, :]
                        m4 = self.match.rearrange("p (h s) r -> p h s r", h=P_HEADS)
                        order.step(vec.tensor_tensor(m4, m4, keys.unsqueeze(2).broadcast_to([P, P_HEADS, TOPK, TOPK]),
                                                     ALU.mult))
                        order.settle(vec)
                        order.step(vec.tensor_reduce(self.slot_index[:, a, t, :], self.match, AX.X, ALU.add))
                        order.settle(vec)
                vec.wait_ge(exp_out, 1)
                gates = self.gates.rearrange("p t (h s) -> p t h s", h=P_HEADS)
                for t in range(TT):
                    order.step(vec.tensor_reduce(self.gate_sum[:, 0, t], gates[:, t], AX.X, ALU.add))
                order.settle(vec)
                order.step(vec.reciprocal(self.gate_sum[:, 1], self.gate_sum[:, 0]))
                order.settle(vec)
                for t in range(TT):
                    order.step(vec.tensor_tensor(gates[:, t], gates[:, t],
                                                 self.gate_sum[:, 1, t].unsqueeze(2).broadcast_to([P, P_HEADS, TOPK]),
                                                 ALU.mult))
                order.settle(vec)
                vec.sem_inc(chosen, 1)

            @block.gpsimd
            def _(pool):
                with pool.Fori(0, EARLY // 4) as i:
                    for u in range(4):
                        pool.wait_ge(high_ready, i * 4 + (u + 1))
                        pool.tensor_tensor(self.early_low[u // 2][:, u % 2], self.early_ring[u // 2][:, u % 2],
                                           self.early_high[u // 2][:, u % 2], ALU.subtract).then_inc(low_ready, 1)

            @block.scalar
            def _(act):

                def split(i, u, first=False):
                    if u % 2 == 0:
                        act.wait_ge(landed[u // 2], i * 16 + 16)
                    if not first:
                        act.wait_ge(hid_ready, i * 4 + (u - 3))
                    act.activation(self.early_high[u // 2][:, u % 2], self.early_ring[u // 2][:, u % 2],
                                   ACT.Copy).then_inc(high_ready, 1)

                def gelu(i, u):
                    act.wait_ge(hid_ready, i * 4 + (u + 1))
                    early = self.early[:, 4 * i + u, :] if isinstance(i, int) else \
                        self.early[:, bass.ds(i * 4 + u, 1), :].rearrange("p a t -> p (a t)")
                    act.activation(early, self.psum[4 + u][:, 0:T], ACT.Gelu).then_inc(gelu_ready, 1)

                def body(i):
                    split(i, 0)
                    gelu(i - 1, 3)
                    for u in range(1, 4):
                        split(i, u)
                        gelu(i, u - 1)

                split(0, 0, first=True)
                for u in range(1, 4):
                    split(0, u, first=True)
                    gelu(0, u - 1)
                with act.Fori(1, EARLY // 4 - 1) as i:
                    body(i)
                act.wait_ge(exp_in, TT)
                act.activation(self.gates, self.gates, ACT.Exp).then_inc(exp_out, 1)
                body(EARLY // 4 - 1)
                gelu(EARLY // 4 - 1, 3)
                for job in range(3):
                    bank = turned.ready(act, job)
                    dst = (self.slot_i, self.slot_j, self.slot_g)[job]
                    act.activation(dst, bank[:, 0:T], ACT.Copy).then_inc(turned.emptied, 1)

            @block.tensor
            def _(pe):
                def hidden(i, u, first=False):
                    pe.wait_ge(low_ready, i * 4 + (u + 1))
                    if not first:
                        pe.wait_ge(gelu_ready, i * 4 + (u - 3))
                    bank, high, low = self.psum[4 + u], self.early_high[u // 2][:, u % 2], self.early_low[u // 2][:, u % 2]
                    for k in range(K):
                        x_high, x_low = self.x_parts[:, k, 0, :], self.x_parts[:, k, 1, :]
                        pe.matmul(bank[:, 0:T], high[:, k, :], x_high, start=(k == 0), stop=False)
                        pe.matmul(bank[:, 0:T], high[:, k, :], x_low, start=False, stop=False)
                        last = pe.matmul(bank[:, 0:T], low[:, k, :], x_high, start=False, stop=(k == K - 1))
                    last.then_inc(hid_ready, 1)

                for u in range(4):
                    hidden(0, u, first=True)
                with pe.Fori(1, EARLY // 4) as i:
                    for u in range(4):
                        hidden(i, u)
                pe.wait_ge(chosen, 1)
                for job in range(3):
                    bank = turned.free(pe, job)
                    for t in range(TT):
                        src = self.gates[:, t, :] if job == 2 else self.slot_index[:, job, t, :]
                        last = pe.transpose(bank[:, t * P:(t + 1) * P], src, self.ident)
                    last.then_inc(turned.filled, 1)

    def peer_dense(self):
        nc = self.nc
        BODY, QUAD = 16, 4
        second_ready, first_ready, gated_ready, product_done, spread = (
            self.sem("dense_" + n) for n in ("second_one_hots", "first_one_hots", "gated_one_hots", "products", "spread"))
        self.down_landed = [self.sem(f"down_ring{n}_landed") for n in range(2)]
        self.up_landed = [self.sem(f"up_ring{n}_landed") for n in range(2)]
        with nc.Block() as block:
            @block.sync
            def _(sync):
                for q in range(2):
                    sync.dma_start(self.up_ring[q], self.ins["peer_up"][q]).then_inc(self.up_landed[q], 16)

            def at_quad(x, n0):
                part = x[:, n0:n0 + QUAD] if isinstance(n0, int) else x[:, bass.ds(n0, QUAD)]
                return part.unsqueeze(2).broadcast_to([P, QUAD, P])

            def slots(quad):
                return slice(quad * QUAD, quad * QUAD + QUAD)

            @block.vector
            def _(vec):
                rows = self.iota.unsqueeze(1).broadcast_to([P, QUAD, P])

                def body(i, first):
                    for quad in range(BODY // QUAD):
                        n0 = i * BODY + quad * QUAD
                        if not first:
                            vec.wait_ge(product_done, i * 4 + (quad - 3))
                        vec.tensor_tensor(self.hot_j[:, slots(quad), :], rows, at_quad(self.slot_j, n0),
                                          ALU.is_equal).then_inc(second_ready, 1)
                        vec.tensor_tensor(self.hot_i[:, slots(quad), :], rows, at_quad(self.slot_i, n0),
                                          ALU.is_equal).then_inc(first_ready, 1)

                body(0, True)
                with vec.Fori(1, T // BODY) as i:
                    body(i, False)

            @block.gpsimd
            def _(pool):
                def body(i):
                    for quad in range(BODY // QUAD):
                        hot = self.hot_j[:, slots(quad), :]
                        pool.wait_ge(second_ready, i * 4 + (quad + 1))
                        pool.tensor_tensor(hot, hot, at_quad(self.slot_g, i * BODY + quad * QUAD),
                                           ALU.mult).then_inc(gated_ready, 1)

                body(0)
                with pool.Fori(1, T // BODY) as i:
                    body(i)

            @block.tensor
            def _(pe):
                def body(i, first):
                    for quad in range(BODY // QUAD):
                        pe.wait_ge(first_ready, i * 4 + (quad + 1))
                        pe.wait_ge(gated_ready, i * 4 + (quad + 1))
                        if not first:
                            pe.wait_ge(spread, i * 4 + (quad - 3))
                        for n in range(QUAD):
                            u = quad * QUAD + n
                            last = pe.matmul(self.psum[4 + quad][:, n * P:(n + 1) * P], self.hot_i[:, u, :],
                                             self.hot_j[:, u, :], start=True, stop=True)
                        last.then_inc(product_done, 1)

                body(0, True)
                with pe.Fori(1, T // BODY) as i:
                    body(i, False)

            @block.scalar
            def _(act):
                def body(i, first):
                    for quad in range(BODY // QUAD):
                        act.wait_ge(product_done, i * 4 + (quad + 1))
                        src = self.psum[4 + quad][:, :].rearrange("p (t j) -> p j t", t=QUAD)
                        n0 = i * BODY + quad * QUAD
                        dst = self.dense[:, :, n0:n0 + QUAD] if first else self.dense[:, :, bass.ds(n0, QUAD)]
                        act.activation(dst, src, ACT.Copy).then_inc(spread, 1)

                body(0, True)
                with act.Fori(1, T // BODY) as i:
                    body(i, False)

    def peer_experts(self):
        nc = self.nc
        acc = [[self.psum[2 * t + n] for n in range(2)] for t in range(TT)]
        hid = [self.psum[4 + n] for n in range(4)]
        (down_high_ready, down_low_ready, up_high_ready, up_low_ready, hid_ready, hid_copied, hid_summed, gelu_ready, gated_ready,
         gated_high_ready, gated_low_ready, out_done, all_done) = (self.sem("peer_" + n) for n in (
            "down_high", "down_low", "up_high", "up_low", "hidden", "hidden_copied", "hidden_summed", "gelu", "gated", "gated_high",
            "gated_low", "out", "all"))
        zero_again, summed, stored = self.sem("zeros_again"), self.sem("peer_summed"), self.sem("stored")
        pairs, start = NKEYS // 2, EARLY // 4
        zeros = self.at(KEPT + TT * D + 5632, 320).bitcast(mybir.dt.bfloat16)
        with nc.Block() as block:
            @block.sync
            def _(sync):
                def load_down(q, u):
                    sync.dma_start(self.down_ring[u], self.ins["peer_down"][q]).then_inc(self.down_landed[u], 16)

                def load_up(q, u):
                    sync.dma_start(self.up_ring[u], self.ins["peer_up"][q]).then_inc(self.up_landed[u], 16)

                e = EARLY // 2
                for q in range(2, e + 2):
                    sync.wait_ge(out_done, 2 * (q - 1))
                    load_up(q, q % 2)
                    if q in (e // 2, e):
                        u = q // (e // 2) - 1
                        sync.wait_ge(gated_ready, (u + 1) * EARLY // 2)
                        load_down(e + u, u)
                with sync.Fori(EARLY // 4 + 1, pairs // 2) as i:
                    for u in range(2):
                        q = i * 2 + u
                        sync.wait_ge(hid_ready, i * 4 + (2 * u - 2 - EARLY))
                        load_down(q, u)
                        sync.wait_ge(out_done, i * 4 + (2 * u - 2))
                        load_up(q, u)
                rows = self.out.rearrange("(t p) d -> t p d", p=P)
                for t in range(TT):
                    sync.wait_ge(summed, 2 * (t + 1))
                    sync.dma_start(rows[t], self.h[:, t, :]).then_inc(stored, 16)
                sync.wait_ge(stored, 16 * TT)

            @block.tensor
            def _(pe):
                pe.wait_ge(zero_again, 1)

                def touch(start):
                    for bank in acc[0] + acc[1]:
                        last = pe.matmul(bank[:, :], zeros[0:1, 0:P], zeros[0:1, P:P + 512], start=start, stop=not start,
                                         skip_group_check=True)
                    return last

                def hidden(i, u, first):
                    pe.wait_ge(down_low_ready, i * 4 + (u + 1 - EARLY))
                    if not first:
                        pe.wait_ge(hid_summed, i * 4 + (u - 3 - EARLY))
                    low = self.down_low[u // 2][:, u % 2]
                    for k in range(K):
                        pe.matmul(hid[u][:, :], self.down_high[:, u % 2, k, :],
                                  self.x_parts[:, k].rearrange("p a t -> p (a t)"), start=(k == 0), stop=False)
                        last = pe.matmul(hid[u][:, 0:T], low[:, k, :], self.x_parts[:, k, 0, :], start=False,
                                         stop=(k == K - 1))
                    last.then_inc(hid_ready, 1)

                def outputs(i, u):
                    pe.wait_ge(up_low_ready, i * 4 + (u + 1))
                    pe.wait_ge(gated_low_ready, i * 4 + (u + 1))
                    low = self.up_low[u // 2][:, u % 2]
                    for t in range(TT):
                        tokens = slice(t * P, (t + 1) * P)
                        for gated, up in ((self.gated_high, self.up_high[:, u % 2]), (self.gated_high, low),
                                          (self.gated_low, self.up_high[:, u % 2])):
                            for c in range(2):
                                last = pe.matmul(acc[t][c][:, :], gated[:, u % 2, tokens], up[:, c * 512:(c + 1) * 512],
                                                 start=False, stop=False, skip_group_check=True)
                    last.then_inc(out_done, 1)

                touch(True)
                with pe.Fori(0, start - 1) as i:
                    for u in range(4):
                        outputs(i, u)
                for u in range(3):
                    outputs(start - 1, u)
                for u in range(4):
                    hidden(start, u, True)
                    outputs(*((start, u - 1) if u else (start - 1, 3)))
                with pe.Fori(start + 1, pairs // 2) as i:
                    hidden(i, 0, False)
                    outputs(i - 1, 3)
                    for u in range(1, 4):
                        hidden(i, u, False)
                        outputs(i, u - 1)
                outputs(pairs // 2 - 1, 3)
                touch(False).then_inc(all_done, 1)

            @block.scalar
            def _(act):
                def split_down(i, u, first=False):
                    if u % 2 == 0:
                        act.wait_ge(self.down_landed[u // 2], i * 16 + (16 - 4 * EARLY))
                    if not (first and u < 2):
                        act.wait_ge(hid_ready, i * 4 + (u - 1 - EARLY))
                    act.activation(self.down_high[:, u % 2], self.down_ring[u // 2][:, u % 2],
                                   ACT.Copy).then_inc(down_high_ready, 1)

                def step(i, u, first=False, early=False):
                    if u % 2 == 0:
                        act.wait_ge(self.up_landed[u // 2], i * 16 + 16)
                    if not (first and u < 2):
                        act.wait_ge(out_done, i * 4 + (u - 1))
                    act.activation(self.up_high[:, u % 2], self.up_ring[u // 2][:, u % 2],
                                   ACT.Copy).then_inc(up_high_ready, 1)
                    if not early:
                        act.wait_ge(hid_summed, i * 4 + (u + 1 - EARLY))
                        act.activation(self.gelu[:, u % 2, :], self.gelu[:, u % 2, :], ACT.Gelu).then_inc(gelu_ready, 1)
                    act.wait_ge(gated_ready, i * 4 + (u + 1))
                    act.activation(self.gated_high[:, u % 2, :], self.gelu[:, u % 2, :],
                                   ACT.Copy).then_inc(gated_high_ready, 1)

                for u in range(4):
                    step(0, u, first=True, early=True)
                with act.Fori(1, start - 1) as i:
                    for u in range(4):
                        step(i, u, early=True)
                for u in range(3):
                    step(start - 1, u, early=True)
                split_down(start, 0, first=True)
                step(start - 1, 3, early=True)
                for u in range(3):
                    split_down(start, u + 1, first=True)
                    step(start, u)
                with act.Fori(start + 1, pairs // 2) as i:
                    split_down(i, 0)
                    step(i - 1, 3)
                    for u in range(3):
                        split_down(i, u + 1)
                        step(i, u)
                step(pairs // 2 - 1, 3)

            @block.vector
            def _(vec):
                vec.memset(zeros, 0.0).then_inc(zero_again, 1)

                def split_down(i, u):
                    vec.wait_ge(down_high_ready, i * 4 + (u + 1 - EARLY))
                    whole, low = self.down_ring[u // 2], self.down_low[u // 2]
                    vec.tensor_tensor(low[:, u % 2], whole[:, u % 2], self.down_high[:, u % 2],
                                      ALU.subtract).then_inc(down_low_ready, 1)

                def split_up(i, u):
                    vec.wait_ge(up_high_ready, i * 4 + (u + 1))
                    whole, low = self.up_ring[u // 2], self.up_low[u // 2]
                    vec.tensor_tensor(low[:, u % 2], whole[:, u % 2], self.up_high[:, u % 2],
                                      ALU.subtract).then_inc(up_low_ready, 1)

                def step(i, u, first=False, early=False):
                    if not (first and u < 2):
                        vec.wait_ge(gated_low_ready, i * 4 + (u - 1))
                    gelu = self.gelu[:, u % 2, :]
                    if not early:
                        vec.wait_ge(hid_ready, i * 4 + (u + 1 - EARLY))
                        vec.tensor_copy(gelu, hid[u][:, 0:T]).then_inc(hid_copied, 1)
                        vec.wait_ge(hid_copied, i * 4 + (u + 1 - EARLY))
                        vec.tensor_tensor(gelu, gelu, hid[u][:, T:2 * T], ALU.add).then_inc(hid_summed, 1)
                    if not early:
                        split_up(i, u)
                        vec.wait_ge(gelu_ready, i * 4 + (u + 1 - EARLY))

                    def of_j(x):
                        return x[:, 4 * i + u, :] if isinstance(i, int) else \
                            x[:, bass.ds(i * 4 + u, 1), :].rearrange("p a t -> p (a t)")

                    vec.tensor_tensor(gelu, of_j(self.early) if early else gelu, of_j(self.dense),
                                      ALU.mult).then_inc(gated_ready, 1)
                    if early:
                        split_up(i, u)
                    vec.wait_ge(gated_high_ready, i * 4 + (u + 1))
                    vec.tensor_tensor(self.gated_low[:, u % 2, :], gelu, self.gated_high[:, u % 2, :],
                                      ALU.subtract).then_inc(gated_low_ready, 1)

                for u in range(4):
                    step(0, u, first=True, early=True)
                with vec.Fori(1, start - 1) as i:
                    for u in range(4):
                        step(i, u, early=True)
                for u in range(3):
                    step(start - 1, u, early=True)
                split_down(start, 0)
                step(start - 1, 3, early=True)
                for u in range(3):
                    split_down(start, u + 1)
                    step(start, u)
                with vec.Fori(start + 1, pairs // 2) as i:
                    split_down(i, 0)
                    step(i - 1, 3)
                    for u in range(3):
                        split_down(i, u + 1)
                        step(i, u)
                step(pairs // 2 - 1, 3)
                vec.wait_ge(all_done, 1)
                for t in range(TT):
                    for c in range(2):
                        part = self.h[:, t, c * 512:(c + 1) * 512]
                        vec.tensor_tensor(part, part, acc[t][c][:, :], ALU.add).then_inc(summed, 1)


def build(nc, ins, out):
    with ExitStack() as ctx:
        k = Kernel(nc, ctx, ins, out)
        k.place_first()
        k.rms_to_features("norm1", "norm1", first=True)
        k.project_and_retain()
        k.rwkv_features()
        k.rwkv_turn()
        k.rwkv_units()
        k.rwkv_scan()
        k.project_out("out1", 8, 10)
        k.end_part()
        k.rms_to_features("norm2", "norm2", scaled_at=MORE)
        k.place_experts()
        k.route_tokens()
        k.experts()
        k.general_experts()
        k.final_norm()
        k.end_part()
        k.place_second()
        k.rms_to_features("norm3", "attn")
        k.project_second()
        k.attention()
        k.project_out("out2", k.first_half + 6, k.first_half + 8 + RING_SLOTS)
        k.rms_to_features("norm4", "ffn")
        k.place_peer()
        k.peer_queries()
        k.peer_select()
        k.peer_dense()
        k.peer_experts()
    return k



def shape_constants():
    import numpy as np
    f = np.float32
    p = np.arange(P)
    chunk = p // CHUNK
    same = chunk[:, None] == chunk[None, :]
    s, t = p[:, None], p[None, :]
    pair = np.stack([same & (s < t), same & (s <= t)], 1)
    levels = []
    for n in range(1, 6):
        size = 2 << (n - 1)
        levels.append((s // (2 * size) == t // (2 * size)) & (s // size < t // size))
    two = np.stack([(s // 2 == t // 2) & (t < s), (s // 2 == t // 2) & (s < t)], 1)
    head = (s // 64) == (t // 64)
    ident64 = np.concatenate([np.eye(64), np.eye(64)], 0)
    half = RET_DIM // 2
    inv = f(10000.0) ** (-np.arange(half, dtype=f) / f(half))
    ang = np.arange(T, dtype=f)[:, None] * inv[None, :]
    rope = np.stack([np.cos(ang), np.sin(ang)], 0).reshape(2, TT, P, half).transpose(2, 0, 1, 3)
    const1 = np.concatenate([pair.reshape(P, -1), np.stack(levels, 1).reshape(P, -1), two.reshape(P, -1), head,
                             ident64, rope.reshape(P, -1), np.stack([p < 64, p >= 64], 1)], 1).astype(f)
    carry = np.broadcast_to((np.arange(4 * T) % CHUNK != 0).astype(f), (P, 4 * T)).reshape(P, 4, T).copy()
    log_g = np.log(1.0 - np.exp2(-5.0 - np.arange(RET_HEADS)))
    q, k = np.arange(T)[None, :], np.arange(T)[:, None]
    cq, ck, iq, ik = q // CHUNK, k // CHUNK, q % CHUNK, k % CHUNK
    far = (iq + 1.0) + CHUNK * (cq - ck - 1.0) + (CHUNK - 1.0 - ik)
    power = np.where(cq == ck, np.abs(iq - ik), far)
    m = np.where(cq >= ck, np.exp(log_g[:, None, None] * np.maximum(power, 0)), 0.0) * RET_DIM ** -0.5
    ret = np.concatenate([m[:, 0:P, :], m[:, P:T, P:T]], 2).transpose(1, 0, 2).astype(f)
    inv2 = f(1.0) / (f(10000.0) ** (np.arange(0, M_DIM, 2, dtype=f) / f(M_DIM)))
    ang2 = np.arange(T, dtype=f)[:, None] * inv2[None, :]
    rope2 = np.stack([np.cos(ang2), np.sin(ang2)], 0).reshape(2, TT, P, M_DIM // 2).transpose(2, 0, 1, 3)
    future = np.where(np.arange(P)[None, :] > p[:, None], NEG, 0.0)
    return {"ident": np.eye(P, dtype=f), "iota": np.concatenate([np.broadcast_to(np.arange(P), (P, P)), (p % 64)[:, None], s <= t], 1).astype(f),
            "const1": const1, "carry": carry, "ret_decay": np.ascontiguousarray(ret),
            "const2": np.concatenate([rope2.reshape(P, -1), future], 1).astype(f)}


def laid_out(a):
    import numpy as np

    def chunks(w, width=512):
        return np.ascontiguousarray(w.reshape(K, P, -1, width).transpose(2, 1, 0, 3))

    def columns(v):
        return v.reshape(-1, P).T

    def row(v):
        return v.reshape(1, -1)

    w_in = a["w_in"][0]
    lay = {
        "x": a["x"][0],
        "w_in": chunks(w_in[:, 0:3584]),
        "w_in_lora": chunks(w_in[:, 3584:3840], 256)[0],
        "w_out": chunks(a["w_out"][0]),
        "w_in_2": chunks(a["w_in_2"][0]),
        "w_out_2": chunks(a["w_out_2"][0]),
        "peer_query": chunks(a["peer_query_2"][0]),
        "cols": np.concatenate([columns(a[n]) for n in (
            "norm1_gain", "norm2_gain", "attn_norm_2", "ffn_norm_2", "rwkv_mu", "rwkv_w0", "rwkv_a0", "rwkv_k_k",
            "rwkv_k_a", "rwkv_r_k")], 1),
        "lora_up": np.concatenate([np.concatenate([a["rwkv_w_up"][0], a["rwkv_a_up"][0]], 0), a["rwkv_g_up"][0]], 1),
        "rows1": np.concatenate([a["ret_gn_gain"][0], a["rwkv_gn_gain"][0], a["b_route_group"][0], a["b_route_expert"][0]]),
        "rows2": np.concatenate([a["final_norm_gain"], a["q_norm_moba_2"][0], a["k_norm_moba_2"][0],
                                 a["q_norm_diff_2"].reshape(-1), a["k_norm_diff_2"].reshape(-1)]
                                + [a[n][0] for n in ("lambda_q1_2", "lambda_k1_2", "lambda_q2_2", "lambda_k2_2")]
                                + [a["moba_out_gain_2"].reshape(-1), a["diff_out_gain_2"].reshape(-1)]),
        "route": np.concatenate([a["w_route_group"][0], a["w_route_expert"][0]], 1).reshape(K, P, 36).transpose(1, 0, 2),
        "w_gate": a["w_gate"][0].reshape(EXPERTS, K, P, FF).transpose(0, 2, 1, 3),
        "w_up": a["w_up"][0].reshape(EXPERTS, K, P, FF).transpose(0, 2, 1, 3),
        "w_down": a["w_down"][0].reshape(EXPERTS, FT, P, D).transpose(0, 2, 1, 3),
        "sub_keys": a["peer_sub_keys_2"][0].reshape(2 * P_HEADS, NKEYS, P).transpose(2, 0, 1),
        "peer_down": a["peer_down_2"][0].reshape(P, NKEYS // 2, 2, K, P).transpose(1, 4, 2, 3, 0),
        "peer_up": a["peer_up_2"][0].reshape(P, NKEYS // 2, 2, D).transpose(1, 0, 2, 3),
    }
    lay.update(shape_constants())
    return {n: np.ascontiguousarray(v) for n, v in lay.items()}


def kernel(**inputs):
    import numpy as _np
    import concourse.bacc as _bacc
    from concourse.bass_utils import run_bass_kernel_spmd as _run

    arrays = laid_out({n: _np.asarray(v) for n, v in inputs.items()})
    nc = _bacc.Bacc("TRN2", target_bir_lowering=False, num_devices=1)
    ins = {n: nc.dram_tensor(n, v.shape, F32, kind="ExternalInput").ap() for n, v in arrays.items()}
    out = nc.dram_tensor("out", (T, D), F32, kind="ExternalOutput").ap()
    build(nc, ins, out)
    r = _run(nc, [arrays], core_ids=[0])
    return r.results[0]["out"].reshape(1, T, D)
```
